# Optimizing a Trainium2 kernel written in Bass

```python
import math
import jax
import jax.numpy as jnp
from jax import lax
import numpy as np

D_MODEL = 1024
BATCH = 1
SEQ = 1024
DEPTH = 2
DEC_BATCH = 8
DEC_SEQ = 1
PAST_LEN = 1024
PAGE_SIZE = 128

HEAD_DIM = 64
N_ATT_HEADS = 8
N_KV_HEADS = 2
GQA = N_ATT_HEADS // N_KV_HEADS
IDX_HEADS = 4
IDX_DIM = 64
TOPK_MAX = 256
CONV_WIDTH = 3
CONV_CH = 512
RWKV_HEADS = 8
RWKV_DIM = RWKV_HEADS * HEAD_DIM
LORA_W = 64
LORA_A = 64
LORA_G = 128
GN_EPS = 64e-5
CMP_BLOCK = 32
SEL_BLOCK = 64
CMP_PER_SEL = SEL_BLOCK // CMP_BLOCK
N_SEL_BLOCKS = 8
WINDOW = 512
N_BUCKETS = 32
MAX_DISTANCE = 128
N_EXPERTS = 16
N_GROUPS = 4
EXPERTS_PER_GROUP = N_EXPERTS // N_GROUPS
TOP_K = 2
D_EXPERT = 512
ROUTE_BLOCK = 128
Q_BLOCK = 128
N_EVEN = (DEPTH + 1) // 2
N_ODD = DEPTH // 2
RMS_EPS = 1e-6
NEG = -1e30
FORCE = 1e9
A_Q = N_ATT_HEADS * HEAD_DIM
A_KV = 2 * N_KV_HEADS * HEAD_DIM
MIX_WIDTH = A_Q + CONV_CH
EVEN_SPLITS = (A_Q, A_KV, IDX_HEADS * IDX_DIM, IDX_DIM, IDX_HEADS, CONV_CH, CONV_CH, CONV_CH)
P_EVEN = A_Q + A_KV + IDX_HEADS * IDX_DIM + IDX_DIM + IDX_HEADS + 3 * CONV_CH
C_SPLITS = (RWKV_DIM, RWKV_DIM, RWKV_DIM, LORA_W, LORA_A, LORA_G)
P_C = 3 * RWKV_DIM + LORA_W + LORA_A + LORA_G
ODD_SPLITS = (P_C, A_Q, A_KV, A_KV, A_KV, 3 * N_ATT_HEADS)
P_ODD = P_C + A_Q + 3 * A_KV + 3 * N_ATT_HEADS

kernel_name = 'hybrid_dsa_shortconv_rwkv7_nsa_moe_step'

def split_cols(z, sizes):
    return jnp.split(z, np.cumsum(sizes)[:-1].tolist(), axis=-1)

def rms_norm(x, g):
    xf = x.astype(jnp.float32)
    y = xf * lax.rsqrt(jnp.mean(xf * xf, axis=-1, keepdims=True) + RMS_EPS)
    return (y * g.astype(jnp.float32)).astype(x.dtype)

def norm_keys(kv, g):
    return jnp.stack([rms_norm(kv[:, :, 0], g), kv[:, :, 1]], axis=2)

def ada_mod(c, w, b):
    m = jax.nn.silu(c) @ w + b
    return [u[:, None, :] for u in jnp.split(m, 6, axis=-1)]

def modulate(x, g, shift, scale):
    return rms_norm(x, g) * (1 + scale) + shift

def t5_bucket(dist):
    dist = jnp.maximum(dist, 0)
    exact = N_BUCKETS // 2
    far = exact + (jnp.log(jnp.maximum(dist, 1).astype(jnp.float32) / exact)
                   / math.log(MAX_DISTANCE / exact) * (N_BUCKETS - exact)).astype(jnp.int32)
    return jnp.where(dist < exact, dist, jnp.minimum(far, N_BUCKETS - 1))

def masked_softmax(logits, mask):
    p = jax.nn.softmax(jnp.where(mask, logits, NEG), axis=-1)
    return jnp.where(mask, p, 0.0)

def to_blocks(x):
    b, s = x.shape[:2]
    return jnp.moveaxis(x.reshape(b, s // Q_BLOCK, Q_BLOCK, *x.shape[2:]), 1, 0)

def from_blocks(y):
    nb, b, qb = y.shape[:3]
    return jnp.moveaxis(y, 0, 1).reshape(b, nb * qb, *y.shape[3:])

def gather_pages(pool, page_table):
    g = pool[page_table]
    return g.reshape(g.shape[0], -1, *g.shape[3:])

def short_conv(u, buf, w, bias):
    t = u.shape[1]
    up = jnp.concatenate([buf, u], axis=1)
    y = bias + w[0] * up[:, 0:t]
    for j in range(1, CONV_WIDTH):
        y = y + w[j] * up[:, j:j + t]
    return y, up[:, -(CONV_WIDTH - 1):]

def dsa_core(q, qi, wi, t_pos, kidx, gather_kv, rel_bias, n_keep):
    b, t = q.shape[:2]
    f32 = jnp.float32
    s_pos = jnp.arange(kidx.shape[1])
    rel = jax.nn.relu(jnp.einsum('bthd,bsd->bths', qi.astype(f32), kidx.astype(f32)))
    score = jnp.einsum('bths,bth->bts', rel, wi.astype(f32)) * (IDX_HEADS * IDX_DIM) ** -0.5
    score = jnp.where(s_pos[None, None, :] <= t_pos[None, :, None], score, NEG)
    _, idx = lax.top_k(score, n_keep)
    k_sel, v_sel = gather_kv(idx)
    dist = t_pos[None, :, None] - idx
    bias = rel_bias[t5_bucket(dist)].reshape(b, t, n_keep, N_KV_HEADS, GQA).transpose(0, 1, 3, 4, 2)
    qg = q.reshape(b, t, N_KV_HEADS, GQA, HEAD_DIM)
    logits = jnp.einsum('bthgd,btnhd->bthgn', qg, k_sel).astype(f32) * HEAD_DIM ** -0.5 + bias
    p = masked_softmax(logits, (dist >= 0)[:, :, None, None, :])
    o = jnp.einsum('bthgn,btnhd->bthgd', p, v_sel.astype(f32))
    return o.reshape(b, t, A_Q).astype(q.dtype)

def even_project(h, w_in, q_norm, k_norm):
    b, t, _ = h.shape
    q, kv, qi, ki, wi, bg, cg, xin = split_cols(h @ w_in, EVEN_SPLITS)
    q = rms_norm(q.reshape(b, t, N_ATT_HEADS, HEAD_DIM), q_norm)
    kv = norm_keys(kv.reshape(b, t, 2, N_KV_HEADS, HEAD_DIM), k_norm)
    qi = qi.reshape(b, t, IDX_HEADS, IDX_DIM)
    return q, kv, qi, ki, wi, bg, cg, xin

def even_mixer_prompt(h, w_in, w_out, q_norm, k_norm, conv_w, conv_b, rel_bias):
    b, s, _ = h.shape
    q, kv, qi, ki, wi, bg, cg, xin = even_project(h, w_in, q_norm, k_norm)
    bi = jnp.arange(b)[:, None, None]

    def gather_kv(idx):
        sel = kv[bi, idx]
        return sel[:, :, :, 0], sel[:, :, :, 1]

    n_keep = min(TOPK_MAX, s // 4)

    def block(args):
        qb, qib, wib, tb = args
        return dsa_core(qb, qib, wib, tb, ki, gather_kv, rel_bias, n_keep)

    o_a = from_blocks(lax.map(block, (to_blocks(q), to_blocks(qi), to_blocks(wi),
                                      jnp.arange(s).reshape(-1, Q_BLOCK))))
    zero_buf = jnp.zeros((b, CONV_WIDTH - 1, CONV_CH), h.dtype)
    y_b, conv_state = short_conv(cg * xin, zero_buf, conv_w, conv_b)
    out = jnp.concatenate([o_a, bg * y_b], axis=-1) @ w_out
    return out, kv, ki, conv_state

def even_mixer_sample(h, kv_pool, kidx_pool, conv_buf, page_table, w_in, w_out, q_norm, k_norm,
                      conv_w, conv_b, rel_bias):
    b, t, _ = h.shape
    past = page_table.shape[1] * PAGE_SIZE
    q, kv, qi, ki, wi, bg, cg, xin = even_project(h, w_in, q_norm, k_norm)
    kidx_all = jnp.concatenate([gather_pages(kidx_pool, page_table), ki], axis=1)
    bi = jnp.arange(b)[:, None, None]

    def gather_kv(idx):
        pidx = jnp.minimum(idx, past - 1)
        sel_past = kv_pool[page_table[bi, pidx // PAGE_SIZE], pidx % PAGE_SIZE]
        sel_new = kv[bi, jnp.clip(idx - past, 0, t - 1)]
        sel = jnp.where((idx < past)[..., None, None, None], sel_past, sel_new)
        return sel[:, :, :, 0], sel[:, :, :, 1]

    n_keep = min(TOPK_MAX, (past + t) // 4)
    o_a = dsa_core(q, qi, wi, past + jnp.arange(t), kidx_all, gather_kv, rel_bias, n_keep)
    y_b, conv_state = short_conv(cg * xin, conv_buf, conv_w, conv_b)
    out = jnp.concatenate([o_a, bg * y_b], axis=-1) @ w_out
    return out, kv, ki, conv_state

def rwkv_mix(z, z_prev, wkv0, mu, w0, w_up, a0, a_up, g_up, k_k, k_a, r_k, ln_w, ln_b):
    b, t, _ = z.shape
    f32 = jnp.float32
    z_shift = jnp.concatenate([z_prev[:, None, :], z[:, :-1]], axis=1)
    zm = z + (z_shift - z) * mu
    r, k, v, wd, ad, gd = split_cols(zm, C_SPLITS)
    w_log = -jax.nn.softplus(-(w0 + jnp.tanh(wd) @ w_up).astype(f32)) - 0.5
    decay = jnp.exp(-jnp.exp(w_log))
    a = jax.nn.sigmoid((a0 + ad @ a_up).astype(f32))
    g = (jax.nn.sigmoid(gd) @ g_up).astype(f32)

    def heads(u):
        return u.astype(f32).reshape(b, t, RWKV_HEADS, HEAD_DIM)

    kk = heads(k * k_k)
    kk = kk / jnp.maximum(jnp.sqrt(jnp.sum(kk * kk, axis=-1, keepdims=True)), 1e-12)
    r, v, a, decay = heads(r), heads(v), heads(a), heads(decay)
    ka = k_a.astype(f32).reshape(RWKV_HEADS, HEAD_DIM)
    k = heads(k) * (1 + (a - 1) * ka)

    def step(S, inp):
        r_t, w_t, k_t, v_t, kk_t, a_t = inp
        sa = jnp.einsum('bhvk,bhk->bhv', S, -kk_t)
        S = (S * w_t[:, :, None, :] + sa[..., None] * (kk_t * a_t)[:, :, None, :]
             + v_t[..., None] * k_t[:, :, None, :])
        return S, jnp.einsum('bhvk,bhk->bhv', S, r_t)

    seq = tuple(jnp.moveaxis(u, 1, 0) for u in (r, decay, k, v, kk, a))
    S, y = lax.scan(step, wkv0.astype(f32), seq)
    y = jnp.moveaxis(y, 0, 1)
    y_mean = jnp.mean(y, axis=-1, keepdims=True)
    y_var = jnp.mean(jnp.square(y - y_mean), axis=-1, keepdims=True)
    yn = ((y - y_mean) * lax.rsqrt(y_var + GN_EPS)).reshape(b, t, RWKV_DIM) * ln_w + ln_b
    bonus = (jnp.sum(r * k * r_k.astype(f32), axis=-1, keepdims=True) * v).reshape(b, t, RWKV_DIM)
    out = (yn + bonus) * g
    return out.astype(z.dtype), S.astype(wkv0.dtype), z[:, -1]

def nsa_compress(rows, pe, w):
    b, L = rows.shape[:2]
    nc = L // CMP_BLOCK
    blk = rows[:, :nc * CMP_BLOCK].reshape(b, nc, CMP_BLOCK, N_KV_HEADS, HEAD_DIM) + pe[:, None, :]
    return jnp.einsum('bnrhd,rde->bnhe', blk, w.reshape(CMP_BLOCK, HEAD_DIM, HEAD_DIM))

def nsa_compress_kv(kvc, pe, w, k_norm_c):
    kc = rms_norm(nsa_compress(kvc[:, :, 0], pe[0], w[0]), k_norm_c)
    vc = nsa_compress(kvc[:, :, 1], pe[1], w[1])
    return kc, vc

def nsa_core(q, gates, t_pos, kc, vc, slc_gather, n_slc, n_sel, kw, vw, w_pos, rel_bias):
    b, t = q.shape[:2]
    f32 = jnp.float32
    scale = HEAD_DIM ** -0.5
    qg = q.reshape(b, t, N_KV_HEADS, GQA, HEAD_DIM)
    bias_hg = rel_bias.reshape(N_BUCKETS, N_KV_HEADS, GQA)
    nc = kc.shape[1]
    c_end = jnp.arange(nc) * CMP_BLOCK + CMP_BLOCK - 1
    dist_c = t_pos[:, None] - c_end[None, :]
    bias_c = jnp.moveaxis(bias_hg[t5_bucket(dist_c)], 1, -1)
    lc = jnp.einsum('bthgd,bnhd->bthgn', qg, kc).astype(f32) * scale + bias_c
    pc = masked_softmax(lc, (dist_c >= 0)[None, :, None, None, :])
    oc = jnp.einsum('bthgn,bnhd->bthgd', pc, vc.astype(f32))
    ps = jnp.sum(pc, axis=3)
    ps = jnp.pad(ps, ((0, 0), (0, 0), (0, 0), (0, n_slc * CMP_PER_SEL - nc)))
    ps = ps.reshape(b, t, N_KV_HEADS, n_slc, CMP_PER_SEL).sum(-1)
    j = jnp.arange(n_slc)
    cur = (t_pos // SEL_BLOCK)[:, None]
    forced = (j[None, :] == 0) | (j[None, :] == cur) | (j[None, :] == cur - 1)
    score = jnp.where(forced[None, :, None, :], FORCE, ps)
    score = jnp.where((j[None, :] * SEL_BLOCK <= t_pos[:, None])[None, :, None, :], score, NEG)
    _, blk = lax.top_k(score, n_sel)
    ks, vs = slc_gather(blk)
    ns = n_sel * SEL_BLOCK
    pos_s = (blk[..., None] * SEL_BLOCK + jnp.arange(SEL_BLOCK)).reshape(b, t, N_KV_HEADS, ns)
    dist_s = t_pos[None, :, None, None] - pos_s
    bias_s = jnp.moveaxis(bias_hg[t5_bucket(dist_s), jnp.arange(N_KV_HEADS)[None, None, :, None]], 3, -1)
    ls = jnp.einsum('bthgd,bthnd->bthgn', qg, ks.reshape(b, t, N_KV_HEADS, ns, HEAD_DIM)).astype(f32) * scale + bias_s
    p_s = masked_softmax(ls, (dist_s >= 0)[:, :, :, None, :])
    o_s = jnp.einsum('bthgn,bthnd->bthgd', p_s, vs.reshape(b, t, N_KV_HEADS, ns, HEAD_DIM).astype(f32))
    dist_w = t_pos[:, None] - w_pos[None, :]
    valid_w = (dist_w >= 0) & (dist_w < WINDOW) & (w_pos[None, :] >= 0)
    bias_w = jnp.moveaxis(bias_hg[t5_bucket(dist_w)], 1, -1)
    lw = jnp.einsum('bthgd,bshd->bthgs', qg, kw).astype(f32) * scale + bias_w
    pw = masked_softmax(lw, valid_w[None, :, None, None, :])
    o_w = jnp.einsum('bthgs,bshd->bthgd', pw, vw.astype(f32))
    g = gates.reshape(b, t, 3, N_KV_HEADS, GQA)[..., None].astype(f32)
    o = g[:, :, 0] * oc + g[:, :, 1] * o_s + g[:, :, 2] * o_w
    return o.reshape(b, t, A_Q).astype(q.dtype)

def odd_project(h, w_in, q_norm, k_norm):
    b, t, _ = h.shape
    zc, q, kvc, kvs, kvw, gates = split_cols(h @ w_in, ODD_SPLITS)
    kv_shape = (b, t, 2, N_KV_HEADS, HEAD_DIM)
    q = rms_norm(q.reshape(b, t, N_ATT_HEADS, HEAD_DIM), q_norm)
    kvc = kvc.reshape(kv_shape)
    kvs = norm_keys(kvs.reshape(kv_shape), k_norm[1])
    kvw = norm_keys(kvw.reshape(kv_shape), k_norm[2])
    gates = jax.nn.sigmoid(gates.reshape(b, t, 3, N_ATT_HEADS))
    return zc, q, kvc, kvs, kvw, gates

def odd_mixer_prompt(h, w_in, w_out, cp, q_norm, k_norm, cmp_pe, cmp_w, rel_bias):
    b, s, _ = h.shape
    zc, q, kvc, kvs, kvw, gates = odd_project(h, w_in, q_norm, k_norm)
    o_c, wkv, shift = rwkv_mix(zc, jnp.zeros((b, P_C), h.dtype),
                               jnp.zeros((b, RWKV_HEADS, HEAD_DIM, HEAD_DIM), h.dtype), *cp)
    kc, vc = nsa_compress_kv(kvc, cmp_pe, cmp_w, k_norm[0])
    n_slc = -(-s // SEL_BLOCK)
    n_sel = min(N_SEL_BLOCKS, n_slc)
    kvb = kvs.reshape(b, n_slc, SEL_BLOCK, 2, N_KV_HEADS, HEAD_DIM).transpose(0, 4, 1, 2, 3, 5)
    bi = jnp.arange(b)[:, None, None, None]
    hi = jnp.arange(N_KV_HEADS)[None, None, :, None]

    def slc_gather(blk):
        sel = kvb[bi, hi, blk]
        return sel[..., 0, :], sel[..., 1, :]

    kvw_pad = jnp.pad(kvw, ((0, 0), (WINDOW, 0), (0, 0), (0, 0), (0, 0)))

    def block(args):
        i, qb, gb = args
        q0 = i * Q_BLOCK
        win = lax.dynamic_slice_in_dim(kvw_pad, q0, WINDOW + Q_BLOCK, axis=1)
        w_pos = q0 - WINDOW + jnp.arange(WINDOW + Q_BLOCK)
        return nsa_core(qb, gb, q0 + jnp.arange(Q_BLOCK), kc, vc, slc_gather, n_slc, n_sel,
                        win[:, :, 0], win[:, :, 1], w_pos, rel_bias)

    o_d = from_blocks(lax.map(block, (jnp.arange(s // Q_BLOCK), to_blocks(q), to_blocks(gates))))
    out = jnp.concatenate([o_c, o_d], axis=-1) @ w_out
    return out, wkv, shift, kvc, kvs, kvw[:, -min(WINDOW, s):]

def odd_mixer_sample(h, wkv0, shift0, cmp_pool, slc_pool, win_buf, page_table, w_in, w_out, cp,
                     q_norm, k_norm, cmp_pe, cmp_w, rel_bias):
    b, t, _ = h.shape
    past = page_table.shape[1] * PAGE_SIZE
    zc, q, kvc, kvs, kvw, gates = odd_project(h, w_in, q_norm, k_norm)
    o_c, wkv, shift = rwkv_mix(zc, shift0, wkv0, *cp)
    kvc_all = jnp.concatenate([gather_pages(cmp_pool, page_table), kvc], axis=1)
    kc, vc = nsa_compress_kv(kvc_all, cmp_pe, cmp_w, k_norm[0])
    n_slc = -(-(past + t) // SEL_BLOCK)
    n_sel = min(N_SEL_BLOCKS, n_slc)
    n_past_blk = past // SEL_BLOCK
    n_new_blk = -(-t // SEL_BLOCK)
    per_page = PAGE_SIZE // SEL_BLOCK
    pool_blocks = slc_pool.reshape(slc_pool.shape[0], per_page, SEL_BLOCK, 2, N_KV_HEADS, HEAD_DIM)
    new_blocks = jnp.pad(kvs, ((0, 0), (0, n_new_blk * SEL_BLOCK - t), (0, 0), (0, 0), (0, 0)))
    new_blocks = new_blocks.reshape(b, n_new_blk, SEL_BLOCK, 2, N_KV_HEADS, HEAD_DIM)
    bi = jnp.arange(b)[:, None, None, None]
    hi = jnp.arange(N_KV_HEADS)[None, None, :, None]

    def slc_gather(blk):
        pb = jnp.minimum(blk, n_past_blk - 1)
        sel_past = pool_blocks[page_table[bi, pb // per_page], pb % per_page, :, :, hi]
        sel_new = new_blocks[bi, jnp.clip(blk - n_past_blk, 0, n_new_blk - 1), :, :, hi]
        sel = jnp.where((blk < n_past_blk)[..., None, None, None], sel_past, sel_new)
        return sel[..., 0, :], sel[..., 1, :]

    w_eff = win_buf.shape[1]
    kvw_all = jnp.concatenate([win_buf, kvw], axis=1)
    w_pos = past - w_eff + jnp.arange(w_eff + t)
    o_d = nsa_core(q, gates, past + jnp.arange(t), kc, vc, slc_gather, n_slc, n_sel,
                   kvw_all[:, :, 0], kvw_all[:, :, 1], w_pos, rel_bias)
    out = jnp.concatenate([o_c, o_d], axis=-1) @ w_out
    return out, wkv, shift, kvc, kvs, kvw_all[:, -w_eff:]

def route(x, w_router, b_router):
    n = x.shape[0]
    s = jax.nn.sigmoid(x.astype(jnp.float32) @ w_router.astype(jnp.float32))
    sel = (s + b_router.astype(jnp.float32)).reshape(n, N_GROUPS, EXPERTS_PER_GROUP)
    grp = jnp.sum(lax.top_k(sel, TOP_K)[0], axis=-1)
    g_best = jnp.argmax(grp, axis=-1)
    within = sel[jnp.arange(n), g_best]
    _, i2 = lax.top_k(within, TOP_K)
    idx = g_best[:, None] * EXPERTS_PER_GROUP + i2
    w = jnp.take_along_axis(s, idx, axis=-1)
    return idx, w / jnp.sum(w, axis=-1, keepdims=True)

def moe_ffn(h, w_router, b_router, w_gate, w_up, w_down):
    shp = h.shape
    x = h.reshape(-1, shp[-1])
    n = x.shape[0]
    idx, wts = route(x, w_router, b_router)
    flat_e = idx.reshape(-1)
    n_asg = flat_e.shape[0]
    order = jnp.argsort(flat_e)
    sorted_e = flat_e[order]
    counts = jnp.zeros((N_EXPERTS,), jnp.int32).at[flat_e].add(1)
    padded = (counts + ROUTE_BLOCK - 1) // ROUTE_BLOCK * ROUTE_BLOCK
    pad_end = jnp.cumsum(padded)
    pad_start = pad_end - padded
    start = jnp.cumsum(counts) - counts
    dest = pad_start[sorted_e] + jnp.arange(n_asg) - start[sorted_e]
    n_blocks = -(-n_asg // ROUTE_BLOCK) + N_EXPERTS
    tok = order // TOP_K
    slot_tok = jnp.zeros((n_blocks * ROUTE_BLOCK,), jnp.int32).at[dest].set(tok)
    block_e = jnp.minimum(jnp.searchsorted(pad_end, jnp.arange(n_blocks) * ROUTE_BLOCK, side='right'),
                          N_EXPERTS - 1)

    def expert_block(args):
        e, toks = args
        xb = x[toks]
        return (jax.nn.silu(xb @ w_gate[e]) * (xb @ w_up[e])) @ w_down[e]

    y_slots = lax.map(expert_block, (block_e, slot_tok.reshape(n_blocks, ROUTE_BLOCK)))
    y_asg = y_slots.reshape(n_blocks * ROUTE_BLOCK, -1)[dest] * wts.reshape(-1)[order][:, None].astype(x.dtype)
    return jax.ops.segment_sum(y_asg, tok, num_segments=n).reshape(shp)

def setup_inputs(seed: int = 0) -> dict:
    key = jax.random.key(seed)
    keys = iter(jax.random.split(key, 64))

    def nrm(shape, scale):
        return jax.random.normal(next(keys), shape, jnp.float32) * scale

    def gain(shape):
        return 1.0 + nrm(shape, 0.02)

    n_pages = PAST_LEN // PAGE_SIZE
    n_pool = (5 * DEC_BATCH * n_pages + 3) // 4
    perm = jax.random.permutation(next(keys), n_pool).astype(jnp.int32)
    page_table = perm[:DEC_BATCH * n_pages].reshape(DEC_BATCH, n_pages)
    w_eff = min(WINDOW, PAST_LEN)
    kv_row = (2, N_KV_HEADS, HEAD_DIM)
    return {
        'x_prompt': nrm((BATCH, SEQ, D_MODEL), 1.0),
        'x_sample': nrm((DEC_BATCH, DEC_SEQ, D_MODEL), 1.0),
        'c_prompt': nrm((BATCH, D_MODEL), 1.0),
        'c_sample': nrm((DEC_BATCH, D_MODEL), 1.0),
        'page_table': page_table,
        'cache_a_kv': nrm((N_EVEN, n_pool, PAGE_SIZE) + kv_row, 1.0),
        'cache_a_kidx': nrm((N_EVEN, n_pool, PAGE_SIZE, IDX_DIM), 1.0),
        'state_b_conv': nrm((N_EVEN, DEC_BATCH, CONV_WIDTH - 1, CONV_CH), 1.0),
        'state_c_wkv': nrm((N_ODD, DEC_BATCH, RWKV_HEADS, HEAD_DIM, HEAD_DIM), 0.3),
        'state_c_shift': nrm((N_ODD, DEC_BATCH, P_C), 1.0),
        'cache_d_cmp': nrm((N_ODD, n_pool, PAGE_SIZE) + kv_row, 1.0),
        'cache_d_slc': nrm((N_ODD, n_pool, PAGE_SIZE) + kv_row, 1.0),
        'cache_d_win': nrm((N_ODD, DEC_BATCH, w_eff) + kv_row, 1.0),
        'rel_bias': nrm((N_BUCKETS, N_ATT_HEADS), 0.5),
        'w_router': nrm((D_MODEL, N_EXPERTS), D_MODEL ** -0.5),
        'b_router': nrm((N_EXPERTS,), 0.01),
        'w_ada': nrm((DEPTH, D_MODEL, 6 * D_MODEL), 0.5 * D_MODEL ** -0.5),
        'b_ada': nrm((DEPTH, 6 * D_MODEL), 0.02),
        'g_norm_mix': gain((DEPTH, D_MODEL)),
        'g_norm_ffn': gain((DEPTH, D_MODEL)),
        'w_expert_gate': nrm((DEPTH, N_EXPERTS, D_MODEL, D_EXPERT), D_MODEL ** -0.5),
        'w_expert_up': nrm((DEPTH, N_EXPERTS, D_MODEL, D_EXPERT), D_MODEL ** -0.5),
        'w_expert_down': nrm((DEPTH, N_EXPERTS, D_EXPERT, D_MODEL), D_EXPERT ** -0.5),
        'e_w_in': nrm((N_EVEN, D_MODEL, P_EVEN), D_MODEL ** -0.5),
        'e_w_out': nrm((N_EVEN, MIX_WIDTH, D_MODEL), MIX_WIDTH ** -0.5),
        'a_q_norm': gain((N_EVEN, HEAD_DIM)),
        'a_k_norm': gain((N_EVEN, HEAD_DIM)),
        'b_conv_w': nrm((N_EVEN, CONV_WIDTH, CONV_CH), 0.5),
        'b_conv_b': nrm((N_EVEN, CONV_CH), 0.02),
        'o_w_in': nrm((N_ODD, D_MODEL, P_ODD), D_MODEL ** -0.5),
        'o_w_out': nrm((N_ODD, MIX_WIDTH, D_MODEL), MIX_WIDTH ** -0.5),
        'c_mu': jax.random.uniform(next(keys), (N_ODD, P_C), jnp.float32),
        'c_w0': nrm((N_ODD, RWKV_DIM), 0.5),
        'c_w_up': nrm((N_ODD, LORA_W, RWKV_DIM), 0.1),
        'c_a0': nrm((N_ODD, RWKV_DIM), 0.5),
        'c_a_up': nrm((N_ODD, LORA_A, RWKV_DIM), 0.1),
        'c_g_up': nrm((N_ODD, LORA_G, RWKV_DIM), LORA_G ** -0.5),
        'c_k_k': 0.85 + nrm((N_ODD, RWKV_DIM), 0.05),
        'c_k_a': 1.0 + nrm((N_ODD, RWKV_DIM), 0.05),
        'c_r_k': nrm((N_ODD, RWKV_HEADS, HEAD_DIM), 0.1),
        'c_ln_w': gain((N_ODD, RWKV_DIM)),
        'c_ln_b': nrm((N_ODD, RWKV_DIM), 0.02),
        'd_q_norm': gain((N_ODD, HEAD_DIM)),
        'd_k_norm': gain((N_ODD, 3, HEAD_DIM)),
        'd_cmp_pe': nrm((N_ODD, 2, CMP_BLOCK, HEAD_DIM), 0.1),
        'd_cmp_w': nrm((N_ODD, 2, CMP_BLOCK * HEAD_DIM, HEAD_DIM), (CMP_BLOCK * HEAD_DIM) ** -0.5),
    }

def reference(x_prompt, x_sample, c_prompt, c_sample, page_table,
              cache_a_kv, cache_a_kidx, state_b_conv, state_c_wkv, state_c_shift,
              cache_d_cmp, cache_d_slc, cache_d_win,
              rel_bias, w_router, b_router, w_ada, b_ada, g_norm_mix, g_norm_ffn,
              w_expert_gate, w_expert_up, w_expert_down,
              e_w_in, e_w_out, a_q_norm, a_k_norm, b_conv_w, b_conv_b,
              o_w_in, o_w_out, c_mu, c_w0, c_w_up, c_a0, c_a_up, c_g_up, c_k_k, c_k_a, c_r_k,
              c_ln_w, c_ln_b, d_q_norm, d_k_norm, d_cmp_pe, d_cmp_w):
    xp, xs = x_prompt, x_sample
    a_kv_p, a_kidx_p, b_conv_p, a_kv_s, a_kidx_s, b_conv_s = [], [], [], [], [], []
    c_wkv_p, c_shift_p, d_cmp_p, d_slc_p, d_win_p = [], [], [], [], []
    c_wkv_s, c_shift_s, d_cmp_s, d_slc_s, d_win_s = [], [], [], [], []
    for l in range(DEPTH):
        li = l // 2
        mp = ada_mod(c_prompt, w_ada[l], b_ada[l])
        ms = ada_mod(c_sample, w_ada[l], b_ada[l])
        hp = modulate(xp, g_norm_mix[l], mp[0], mp[1])
        hs = modulate(xs, g_norm_mix[l], ms[0], ms[1])
        if l % 2 == 0:
            ew = (e_w_in[li], e_w_out[li], a_q_norm[li], a_k_norm[li], b_conv_w[li], b_conv_b[li], rel_bias)
            op, kv, ki, cv = even_mixer_prompt(hp, *ew)
            a_kv_p.append(kv)
            a_kidx_p.append(ki)
            b_conv_p.append(cv)
            osm, kv, ki, cv = even_mixer_sample(hs, cache_a_kv[li], cache_a_kidx[li], state_b_conv[li],
                                                page_table, *ew)
            a_kv_s.append(kv)
            a_kidx_s.append(ki)
            b_conv_s.append(cv)
        else:
            cp = (c_mu[li], c_w0[li], c_w_up[li], c_a0[li], c_a_up[li], c_g_up[li], c_k_k[li],
                  c_k_a[li], c_r_k[li], c_ln_w[li], c_ln_b[li])
            ow = (o_w_in[li], o_w_out[li], cp, d_q_norm[li], d_k_norm[li], d_cmp_pe[li], d_cmp_w[li], rel_bias)
            op, wkv, sh, kvc, kvs, kvw = odd_mixer_prompt(hp, *ow)
            c_wkv_p.append(wkv)
            c_shift_p.append(sh)
            d_cmp_p.append(kvc)
            d_slc_p.append(kvs)
            d_win_p.append(kvw)
            osm, wkv, sh, kvc, kvs, kvw = odd_mixer_sample(hs, state_c_wkv[li], state_c_shift[li],
                                                           cache_d_cmp[li], cache_d_slc[li], cache_d_win[li],
                                                           page_table, *ow)
            c_wkv_s.append(wkv)
            c_shift_s.append(sh)
            d_cmp_s.append(kvc)
            d_slc_s.append(kvs)
            d_win_s.append(kvw)
        xp = xp + mp[2] * op
        xs = xs + ms[2] * osm
        ex = (w_router, b_router, w_expert_gate[l], w_expert_up[l], w_expert_down[l])
        xp = xp + mp[5] * moe_ffn(modulate(xp, g_norm_ffn[l], mp[3], mp[4]), *ex)
        xs = xs + ms[5] * moe_ffn(modulate(xs, g_norm_ffn[l], ms[3], ms[4]), *ex)
    return (xp, xs,
            jnp.stack(a_kv_p), jnp.stack(a_kidx_p), jnp.stack(b_conv_p),
            jnp.stack(c_wkv_p), jnp.stack(c_shift_p), jnp.stack(d_cmp_p), jnp.stack(d_slc_p), jnp.stack(d_win_p),
            jnp.stack(a_kv_s), jnp.stack(a_kidx_s), jnp.stack(b_conv_s),
            jnp.stack(c_wkv_s), jnp.stack(c_shift_s), jnp.stack(d_cmp_s), jnp.stack(d_slc_s), jnp.stack(d_win_s))


_drawn_inputs = setup_inputs


def setup_inputs(seed=0):
    import zlib

    import numpy as np

    out = dict(_drawn_inputs(seed))
    spreads = {}
    factors = {'cache_d_slc': 5.796,
     'a_q_norm': 6.599,
     'a_k_norm': 4.607,
     'b_conv_b': 3.876,
     'c_k_k': 12.047,
     'c_ln_w': 18.866,
     'c_ln_b': 21.782,
     'd_q_norm': 8.0,
     'd_k_norm': 4.033,
     'd_cmp_pe': 3.403}
    for name, (base, spread) in spreads.items():
        noise = np.random.default_rng([zlib.crc32(name.encode()), seed]).standard_normal(out[name].shape)
        drawn = base * np.exp(spread * noise) if base else spread * noise
        out[name] = jnp.asarray(drawn.astype(out[name].dtype))
    for name, factor in factors.items():
        out[name] = (out[name] * factor).astype(out[name].dtype)
    return out
```

```python
from contextlib import ExitStack

import numpy as np

import concourse.bass as bass
from concourse import mybir

F32 = mybir.dt.float32
U32 = mybir.dt.uint32
I32 = mybir.dt.int32
ALU = mybir.AluOpType
ACT = mybir.ActivationFunctionType
AX = mybir.AxisListType

P = 128
D = 1024
SEQ = 1024
DEPTH = 2
NB = 8
TILES = SEQ // P
TOK = SEQ + NB
KC = D // P
HD = 64
NH = 8
NKV = 2
GQA = NH // NKV
PAST = 1024
PAGE = 128
PAGES = PAST // PAGE
A_Q = NH * HD
KVW = NKV * HD
A_KV = 2 * KVW
IDXH = 4
TOPK = 256
CONV = 512
P_EVEN = A_Q + A_KV + IDXH * HD + HD + IDXH + 3 * CONV
RW = 512
P_C = 3 * RW + 64 + 64 + 128
P_ODD = P_C + A_Q + 3 * A_KV + 3 * NH
CMP = 32
NCMP = SEQ // CMP
SEL = 64
NSEL = SEQ // SEL
WINDOW = 512
NBUCK = 32
NEXP = 16
NGRP = 4
DEXP = 512
ROUTE_BLOCK = 128
RMS_EPS = 1e-6
GN_EPS = 64e-5
NEG = -1e30
FORCE = 1e9
TAKEN = -3e38
CH = 32

E_Q, E_K, E_V, E_QI, E_KI, E_WI = 0, 512, 640, 768, 1024, 1088
E_BG, E_CG, E_XIN = 1092, 1604, 2116
O_R, O_K, O_V, O_WD, O_AD, O_GD = 0, 512, 1024, 1536, 1600, 1664
O_Q, O_KVC, O_KVS, O_KVW, O_G = 1792, 2304, 2560, 2816, 3072

LEAD = 2
Z_S = LEAD + SEQ

OH0 = 1280
OH_W = OH0 + 1280


def t5_onehot():
    dist = np.maximum(np.arange(OH_W) - OH0, 0)
    exact = NBUCK // 2
    far = exact + (np.log(np.maximum(dist, 1).astype(np.float32) / np.float32(exact))
                   / np.float32(np.log(128 / exact)) * np.float32(NBUCK - exact)).astype(np.int32)
    bucket = np.where(dist < exact, dist, np.minimum(far, NBUCK - 1))
    return (bucket[None, :] == np.arange(NBUCK)[:, None]).astype(np.float32)


def signals(nc, ctx, names):
    return [ctx.enter_context(nc.semaphore(n)) for n in names.split()]


def tile_of(nc, ctx, name, shape, dt=F32):
    return ctx.enter_context(nc.sbuf_tensor(name, shape, dt, allow_name_mangling=True))


def bank_of(nc, ctx, name, shape):
    return ctx.enter_context(nc.psum_tensor(name, shape, F32, allow_name_mangling=True))


def clear_signals(nc, sems, pool_dma=()):
    for s in pool_dma:
        nc.gpsimd.dma_reset(range(s.num, s.num + 1))
    for s in sems:
        nc.gpsimd.sem_clear(s)
    nc.all_engine_barrier()


class InOrder:

    def __init__(self, eng):
        self.eng = eng
        self.count = {}

    def __call__(self, ins, sem, n=1):
        ins.then_inc(sem, n)
        self.count[sem.num] = self.count.get(sem.num, 0) + n
        self.eng.wait_ge(sem, self.count[sem.num])


def stage_constants(nc, G):
    with ExitStack() as c:
        zeroed, made, stored, started = signals(nc, c, "zeroed ident_made lead_stored x_loaded")
        with nc.Block() as block:

            @block.gpsimd
            def _(pool):
                pool.memset(G["ident"][:, :], 0.0).then_inc(zeroed, 1)
                pool.memset(G["ones"][:, :], 1.0).then_inc(zeroed, 1)
                pool.memset(G["featT"][0:LEAD, :, :], 0.0).then_inc(zeroed, 1)
                pool.wait_ge(zeroed, 3)
                pool.affine_select(out=G["ident"][:, :], in_=G["ident"][:, :], compare_op=ALU.not_equal,
                                   fill=1.0, base=0, pattern=[[-1, P]], channel_multiplier=1).then_inc(made, 1)
                pool.wait_ge(made, 1)

            @block.sync
            def _(sp):
                sp.dma_start(G["x"][:, 0:TILES, :],
                             G["x_prompt"][0].rearrange("(t p) d -> p t d", p=P)).then_inc(started, 16)
                sp.dma_start(G["x"][0:NB, TILES, :], G["x_sample"][:, 0, :]).then_inc(started, 16)
                sp.wait_ge(zeroed, 3)
                lead = G["featT"][0:LEAD, :, :].rearrange("p k n -> p (k n)")
                sp.dma_start(G["z_even"][0:LEAD, :], lead[:, 0:P_EVEN])\
                  .then_inc(stored, 16)
                sp.dma_start(G["z_odd"][0:LEAD, :], lead[:, 0:P_ODD])\
                  .then_inc(stored, 16)
                sp.wait_ge(stored, 32)
                sp.wait_ge(started, 32)
        clear_signals(nc, [zeroed, made, stored, started])


def stage_ada(nc, G):
    N = 6 * D
    NQ = 4
    rows = 1 + NB
    with ExitStack() as c:
        c_sb = tile_of(nc, c, "c_rows", [rows, D])
        cT = tile_of(nc, c, "cT", [P, KC, rows])
        ct_ps = bank_of(nc, c, "cT_ps", [P, KC, rows])
        sems = signals(nc, c, "c_loaded silu_done cT_transposed cT_ready")
        c_loaded, silu_done, cT_transposed, cT_ready = sems
        with nc.Block() as block:

            @block.sync
            def _(sp):
                sp.dma_start(c_sb[0:1, :], G["c_prompt"]).then_inc(c_loaded, 16)
                sp.dma_start(c_sb[1:rows, :], G["c_sample"]).then_inc(c_loaded, 16)

            @block.scalar
            def _(act):
                act.wait_ge(c_loaded, 32)
                act.activation(c_sb[:, :], c_sb[:, :], ACT.Silu).then_inc(silu_done, 1)

            @block.tensor
            def _(pe):
                pe.wait_ge(silu_done, 1)
                for k in range(KC):
                    last = pe.transpose(ct_ps[:, k, :], c_sb[:, k * P:(k + 1) * P], G["ident"][0:rows, 0:rows])
                last.then_inc(cT_transposed, 1)

            @block.vector
            def _(dve):
                dve.wait_ge(cT_transposed, 1)
                dve.tensor_copy(cT[:, :, :], ct_ps[:, :, :]).then_inc(cT_ready, 1)
                dve.wait_ge(cT_ready, 1)
        clear_signals(nc, sems)

        w = [tile_of(nc, c, f"w_ada{i}", [P, KC, 512]) for i in range(NQ)]
        bias = tile_of(nc, c, "b_ada_rows", [rows, NQ * 512])
        m_sb = tile_of(nc, c, "mod_rows", [rows, NQ * 512])
        acc = [bank_of(nc, c, f"mod_ps{i}", [rows, 512]) for i in range(NQ)]
        sems = signals(nc, c, "w0 w1 w2 w3 b_loaded mod_summed mod_ready mod_stored")
        w_loaded, (b_loaded, mod_summed, mod_ready, mod_stored) = sems[0:4], sems[4:]
        for layer in range(DEPTH):
            w_view = G["w_ada"][layer].rearrange("(k p) n -> p k n", p=P)
            with nc.Fori(0, N // (NQ * 512)) as j:
                with nc.Block() as block:

                    @block.sync
                    def _(sp):
                        for q in range(NQ):
                            sp.dma_start(w[q][:, :, :], w_view[:, :, bass.ds(j * (NQ * 512) + q * 512, 512)])\
                              .then_inc(w_loaded[q], 16)
                            if q == 0:
                                sp.dma_start(bias[:, :], G["b_ada"][layer, bass.ds(j * (NQ * 512), NQ * 512)]
                                             .partition_broadcast(rows)).then_inc(b_loaded, 16)
                        sp.wait_ge(mod_ready, NQ)
                        sp.dma_start(G["mod"][:, layer, bass.ds(j * (NQ * 512), NQ * 512)], m_sb[:, :])\
                          .then_inc(mod_stored, 16)
                        sp.wait_ge(mod_stored, 16)

                    @block.tensor
                    def _(pe):
                        for q in range(NQ):
                            pe.wait_ge(w_loaded[q], 16)
                            for k in range(KC):
                                last = pe.matmul(acc[q][:, :], cT[:, k, :], w[q][:, k, :],
                                                 start=(k == 0), stop=(k == KC - 1))
                            last.then_inc(mod_summed, 1)

                    @block.vector
                    def _(dve):
                        dve.wait_ge(b_loaded, 16)
                        for q in range(NQ):
                            dve.wait_ge(mod_summed, q + 1)
                            dve.tensor_tensor(m_sb[:, q * 512:(q + 1) * 512], acc[q][:, :],
                                              bias[:, q * 512:(q + 1) * 512], ALU.add).then_inc(mod_ready, 1)
                clear_signals(nc, sems)


def stage_modulate(nc, G, layer, gain_dram, first, rows_dram=None):
    x, featT = G["x"], G["featT"]
    with ExitStack() as c:
        gain = tile_of(nc, c, "gain_b", [P, D])
        amp = tile_of(nc, c, "amp_b", [P, 2, D])
        shift = tile_of(nc, c, "shift_b", [P, 2, D])
        h = tile_of(nc, c, "h_tile", [P, D])
        junk = tile_of(nc, c, "sq_rows", [P, D])
        ss = tile_of(nc, c, "h_ss", [P, 2])
        hT_ps = bank_of(nc, c, "hT_ps", [P, KC, P])
        loaded, made = setup = signals(nc, c, "mod_loaded amp_made")
        with nc.Block() as block:

            @block.sync
            def _(sp):
                sp.dma_start(gain[:, :], gain_dram.partition_broadcast(P)).then_inc(loaded, 16)
                for j, dst in ((first + 1, amp), (first, shift)):
                    cols = slice(j * D, (j + 1) * D)
                    sp.dma_start(dst[:, 0, :], G["mod"][0, layer, cols].partition_broadcast(P)).then_inc(loaded, 16)
                    sp.dma_start(dst[0:NB, 1, :], G["mod"][1:1 + NB, layer, cols]).then_inc(loaded, 16)

            @block.vector
            def _(dve):
                dve.wait_ge(loaded, 16 * 5)
                for kind, rows in ((0, P), (1, NB)):
                    dve.scalar_tensor_tensor(amp[0:rows, kind, :], amp[0:rows, kind, :], 1.0, gain[0:rows, :],
                                             ALU.add, ALU.mult).then_inc(made, 1)
                dve.wait_ge(made, 2)
        clear_signals(nc, setup)

        sems = signals(nc, c, "squares_summed mean_made rms_made rstd_made h_made h_transposed h_stored")
        squares_summed, mean_made, rms_made, rstd_made, h_made, h_transposed, h_stored = sems

        def one_tile(t, rows, kind):
            with nc.Block() as block:

                @block.sync
                def _(sp):
                    if rows_dram is not None:
                        sp.wait_ge(h_made, 1)
                        sp.dma_start(rows_dram[bass.ds(t * P, rows), :], h[0:rows, :]).then_inc(h_stored, 16)
                        sp.wait_ge(h_stored, 16)

                @block.scalar
                def _(act):
                    act.activation(junk[0:rows, :], x[0:rows, t, :], ACT.Square, accum_out=ss[0:rows, 0:1])\
                       .then_inc(squares_summed, 1)
                    act.wait_ge(mean_made, 1)
                    act.activation(ss[0:rows, 1:2], ss[0:rows, 1:2], ACT.Sqrt).then_inc(rms_made, 1)
                    act.wait_ge(rms_made, 1)
                    act.wait_ge(h_transposed, 2)
                    act.copy(featT[:, KC // 2:KC, bass.ds(t * P, rows)], hT_ps[:, KC // 2:KC, 0:rows])

                @block.vector
                def _(dve):
                    step = InOrder(dve)
                    dve.wait_ge(squares_summed, 1)
                    step(dve.tensor_scalar(ss[0:rows, 1:2], ss[0:rows, 0:1], 1.0 / D, RMS_EPS, ALU.mult, ALU.add),
                         mean_made)
                    dve.wait_ge(rms_made, 1)
                    step(dve.reciprocal(ss[0:rows, 0:1], ss[0:rows, 1:2]), rstd_made)
                    step(dve.scalar_tensor_tensor(h[0:rows, :], x[0:rows, t, :], ss[0:rows, 0:1],
                                                  amp[0:rows, kind, :], ALU.mult, ALU.mult), rstd_made)
                    step(dve.tensor_tensor(h[0:rows, :], h[0:rows, :], shift[0:rows, kind, :], ALU.add), h_made)
                    dve.wait_ge(h_transposed, 1)
                    dve.tensor_copy(featT[:, 0:KC // 2, bass.ds(t * P, rows)], hT_ps[:, 0:KC // 2, 0:rows])

                @block.tensor
                def _(pe):
                    pe.wait_ge(h_made, 1)
                    for k in range(KC):
                        last = pe.transpose(hT_ps[:, k, 0:rows], h[0:rows, k * P:(k + 1) * P],
                                            G["ident"][0:rows, 0:rows])
                        if k in (KC // 2 - 1, KC - 1):
                            last.then_inc(h_transposed, 1)
            clear_signals(nc, sems)

        with nc.Fori(0, TILES) as t:
            one_tile(t, P, 0)
        one_tile(TILES, NB, 1)


def stage_project(nc, G, w_dram, width, prompt_rows, sample_rows):
    featT = G["featT"]
    w_view = w_dram.rearrange("(k p) n -> p k n", p=P)
    NM = TILES + 1
    with ExitStack() as c:
        w = tile_of(nc, c, "w_cols", [P, KC, 512])
        out = tile_of(nc, c, "z_cols", [P, NM, 512])
        acc = [bank_of(nc, c, f"z_ps{i}", [P, 512]) for i in range(4)]
        sems = signals(nc, c, "w_loaded z_summed z_copied_dve z_copied_act z_stored")
        w_loaded, z_summed, copied_dve, copied_act, z_stored = sems

        def one_chunk(c0, n):
            with nc.Block() as block:

                @block.sync
                def _(sp):
                    for half in range(2):
                        ks = slice(half * KC // 2, (half + 1) * KC // 2)
                        sp.dma_start(w[:, ks, 0:n], w_view[:, ks, bass.ds(c0, n)]).then_inc(w_loaded, 16)
                    for m in range(TILES):
                        sp.wait_ge(copied_dve if m % 2 == 0 else copied_act, m // 2 + 1)
                        sp.dma_start(prompt_rows[m * P:(m + 1) * P, bass.ds(c0, n)], out[:, m, 0:n])\
                          .then_inc(z_stored, 16)
                    sp.wait_ge(copied_dve, TILES // 2 + 1)
                    sp.dma_start(sample_rows[:, bass.ds(c0, n)], out[0:NB, TILES, 0:n]).then_inc(z_stored, 16)
                    sp.wait_ge(z_stored, 16 * NM)

                @block.tensor
                def _(pe):
                    pe.wait_ge(w_loaded, 32)
                    for m in range(NM):
                        rows = P if m < TILES else NB
                        if m >= 4:
                            pe.wait_ge(copied_dve if m % 2 == 0 else copied_act, (m - 4) // 2 + 1)
                        for k in range(KC):
                            last = pe.matmul(acc[m % 4][0:rows, 0:n], featT[:, k, m * P:m * P + rows], w[:, k, 0:n],
                                             start=(k == 0), stop=(k == KC - 1))
                        last.then_inc(z_summed, 1)

                @block.vector
                def _(dve):
                    for m in range(0, NM, 2):
                        rows = P if m < TILES else NB
                        dve.wait_ge(z_summed, m + 1)
                        dve.tensor_copy(out[0:rows, m, 0:n], acc[m % 4][0:rows, 0:n]).then_inc(copied_dve, 1)

                @block.scalar
                def _(act):
                    for m in range(1, NM, 2):
                        act.wait_ge(z_summed, m + 1)
                        act.copy(out[:, m, 0:n], acc[m % 4][:, 0:n]).then_inc(copied_act, 1)
            clear_signals(nc, sems)

        full = width // 512
        with nc.Fori(0, full) as j:
            one_chunk(j * 512, 512)
        if width % 512:
            one_chunk(full * 512, width % 512)


def stage_residual_project(nc, G, layer, w_dram, gate_row):
    featT, x = G["featT"], G["x"]
    w_view = w_dram.rearrange("(k p) n -> p k n", p=P)
    NM = TILES + 1
    with ExitStack() as c:
        w = tile_of(nc, c, "w_out_cols", [P, KC, 512])
        gate = tile_of(nc, c, "gate_cols", [P, 2, 512])
        gated = tile_of(nc, c, "gated", [P, 512])
        acc = [bank_of(nc, c, f"mix_ps{i}", [P, 512]) for i in range(4)]
        sems = signals(nc, c, "w_loaded gate_loaded mix_summed mix_gated x_added")
        w_loaded, gate_loaded, mix_summed, mix_gated, x_added = sems
        for c0 in range(0, D, 512):
            cols = slice(gate_row * D + c0, gate_row * D + c0 + 512)
            with nc.Block() as block:

                @block.sync
                def _(sp):
                    sp.dma_start(w[:, :, :], w_view[:, :, c0:c0 + 512]).then_inc(w_loaded, 16)
                    sp.dma_start(gate[:, 0, :], G["mod"][0, layer, cols].partition_broadcast(P))\
                      .then_inc(gate_loaded, 16)
                    sp.dma_start(gate[0:NB, 1, :], G["mod"][1:1 + NB, layer, cols]).then_inc(gate_loaded, 16)

                @block.tensor
                def _(pe):
                    pe.wait_ge(w_loaded, 16)
                    for m in range(NM):
                        rows = P if m < TILES else NB
                        if m >= 4:
                            pe.wait_ge(mix_gated, m - 3)
                        for k in range(KC):
                            last = pe.matmul(acc[m % 4][0:rows, :], featT[:, k, m * P:m * P + rows], w[:, k, :],
                                             start=(k == 0), stop=(k == KC - 1))
                        last.then_inc(mix_summed, 1)

                @block.vector
                def _(dve):
                    step = InOrder(dve)
                    dve.wait_ge(gate_loaded, 32)
                    for m in range(NM):
                        rows, kind = (P, 0) if m < TILES else (NB, 1)
                        dve.wait_ge(mix_summed, m + 1)
                        step(dve.tensor_tensor(gated[0:rows, :], acc[m % 4][0:rows, :], gate[0:rows, kind, :],
                                               ALU.mult), mix_gated)
                        step(dve.tensor_tensor(x[0:rows, m, c0:c0 + 512], x[0:rows, m, c0:c0 + 512],
                                               gated[0:rows, :], ALU.add), x_added)
            clear_signals(nc, sems)


def alloc_banks(nc, c, G):
    G["near"] = tile_of(nc, c, "near_bias", [P, NH, 2 * P])
    G["far_mask"] = tile_of(nc, c, "causal_bank", [P, 15 * P])
    G["row_bias"] = tile_of(nc, c, "row_bias", [NB * NH, PAST + 1])


def stage_banks(nc, G, cmp_bias=None):
    near, far_mask, row_bias = G["near"], G["far_mask"], G["row_bias"]
    with ExitStack() as c:
        oh = tile_of(nc, c, "t5_oh", [NBUCK, OH_W])
        rev = tile_of(nc, c, "t5_rev", [NBUCK, PAST + 1])
        table = tile_of(nc, c, "bias_table", [NBUCK, NH])
        farthest = tile_of(nc, c, "bias_far", [NBUCK, NH])
        rel8 = tile_of(nc, c, "bias_rel8", [NBUCK, NB, NH])
        col_ps = [bank_of(nc, c, f"near_ps{i}", [P, 64, NH]) for i in range(2)]
        row_ps = bank_of(nc, c, "row_ps", [NB * NH, 512])
        sems = signals(nc, c, "tables_loaded table_made cols_summed cols_copied row_summed row_copied filled masked")
        tables_loaded, table_made, cols_summed, cols_copied, row_summed, row_copied, filled, masked = sems
        near_groups = [(near[:, :, g * 64:(g + 1) * 64], [P - (g * 64 + i) for i in range(64)]) for g in range(4)]
        if cmp_bias is not None:
            near_groups.append((cmp_bias[:, :, :], [865 - CMP * i for i in range(64)]))

        with nc.Block() as block:

            @block.gpsimd
            def _(pool):
                pool.memset(far_mask[:, :], 0.0).then_inc(filled, 1)
                pool.wait_ge(filled, 1)
                pool.affine_select(out=far_mask[:, :], in_=far_mask[:, :], compare_op=ALU.is_ge, fill=NEG,
                                   base=896, pattern=[[-1, 15 * P]], channel_multiplier=1).then_inc(masked, 1)
                pool.wait_ge(masked, 1)

            @block.sync
            def _(sp):
                sp.dma_start(oh[:, :], G["t5_onehot"]).then_inc(tables_loaded, 16)
                sp.dma_start(rev[:, :], G["t5_onehot_rev"]).then_inc(tables_loaded, 16)
                sp.dma_start(table[:, :], G["rel_bias"]).then_inc(tables_loaded, 16)
                sp.dma_start(farthest[:, :], G["rel_bias"][NBUCK - 1].partition_broadcast(NBUCK))\
                  .then_inc(tables_loaded, 16)

            @block.vector
            def _(dve):
                step = InOrder(dve)
                dve.wait_ge(tables_loaded, 64)
                step(dve.tensor_tensor(table[:, :], table[:, :], farthest[:, :], ALU.subtract), table_made)
                for b in range(NB):
                    step(dve.tensor_copy(rel8[:, b, :], table[:, :]), table_made)
                for i, (dst, dist) in enumerate(near_groups):
                    dve.wait_ge(cols_summed, i + 1)
                    step(dve.tensor_copy(dst, col_ps[i % 2][:, 0:len(dist), :].rearrange("p x h -> p h x")), cols_copied)

            @block.tensor
            def _(pe):
                pe.wait_ge(table_made, 1 + NB)
                for i, (dst, dist) in enumerate(near_groups):
                    if i >= 2:
                        pe.wait_ge(cols_copied, i - 1)
                    for x, d in enumerate(dist):
                        last = pe.matmul(col_ps[i % 2][:, x, :], oh[:, OH0 + d:OH0 + d + P], table[:, :],
                                         start=True, stop=True)
                    last.then_inc(cols_summed, 1)
                for i, (a, b) in enumerate(((0, 512), (512, 1024), (1024, 1025))):
                    if i:
                        pe.wait_ge(row_copied, i)
                    pe.matmul(row_ps[:, 0:b - a], rel8[:, :, :].rearrange("r b h -> r (b h)"), rev[:, a:b],
                              start=True, stop=True).then_inc(row_summed, 1)

            @block.scalar
            def _(act):
                for i, (a, b) in enumerate(((0, 512), (512, 1024), (1024, 1025))):
                    act.wait_ge(row_summed, i + 1)
                    act.copy(row_bias[:, a:b], row_ps[:, 0:b - a]).then_inc(row_copied, 1)
        clear_signals(nc, sems)


class Attend:
    def __init__(self, nc, c):
        self.lg_ps = [bank_of(nc, c, f"lg_ps{i}", [P, 1024]) for i in range(2)]
        self.t_ps = bank_of(nc, c, "t_ps", [P, 8, P])
        self.o_ps = [bank_of(nc, c, f"o_ps{i}", [P, HD]) for i in range(2)]
        self.lg = [tile_of(nc, c, f"lg{i}", [P, P + 1024]) for i in range(2)]
        self.prob = [tile_of(nc, c, f"prob{i}", [P, 1024]) for i in range(2)]
        self.probT = [tile_of(nc, c, f"probT{i}", [P, 8, P]) for i in range(2)]
        self.nmax = tile_of(nc, c, "nmax", [P, 2])
        self.sum = tile_of(nc, c, "esum", [P, 16])
        self.rsum = tile_of(nc, c, "rsum", [P, 2])
        self.sems = signals(nc, c, "lg_summed lg_masked rowmax_made exp_done p_transposed pT_copied pv_summed "
                                   "o_scaled o_added")
        (self.lg_summed, self.lg_masked, self.rowmax_made, self.exp_done, self.p_transposed, self.pT_copied,
         self.pv_summed, self.o_scaled, self.o_added) = self.sems

    def tensor(self, pe, units, ident):
        n = len(units)
        for i in range(n + 2):
            if i < n:
                lhsT, keys = units[i][0], units[i][1]
                if i >= 2:
                    pe.wait_ge(self.lg_masked, i - 1)
                at = 0
                for ap, width in keys:
                    last = pe.matmul(self.lg_ps[i % 2][:, at:at + width], lhsT, ap, start=True, stop=True)
                    at += width
                last.then_inc(self.lg_summed, 1)
            if 1 <= i <= n:
                u = i - 1
                pe.wait_ge(self.exp_done, u + 1)
                if u >= 1:
                    pe.wait_ge(self.pT_copied, u)
                for j in range(len(units[u][5])):
                    last = pe.transpose(self.t_ps[:, j, :], self.prob[u % 2][:, j * P:(j + 1) * P], ident[:, :])
                last.then_inc(self.p_transposed, 1)
            if i >= 2:
                u = i - 2
                pe.wait_ge(self.pT_copied, u + 1)
                if u >= 2:
                    pe.wait_ge(self.o_scaled, u - 1)
                values = units[u][5]
                for j, v in enumerate(values):
                    last = pe.matmul(self.o_ps[u % 2][:, :], self.probT[u % 2][:, j, :], v,
                                     start=(j == 0), stop=(j == len(values) - 1))
                last.then_inc(self.pv_summed, 1)

    def vector(self, dve, step, units, near, out, gates):
        n = len(units)
        for i in range(n + 2):
            if i < n:
                _, keys, mask, at, head, values, _ = units[i]
                width = len(values) * P
                lg = self.lg[i % 2]
                dve.wait_ge(self.lg_summed, i + 1)
                if i >= 2:
                    dve.wait_ge(self.exp_done, i - 1)
                step(dve.tensor_tensor(lg[:, P:P + width], self.lg_ps[i % 2][:, 0:width], mask, ALU.add),
                     self.lg_masked)
                step(dve.tensor_tensor(lg[:, bass.ds(at, 2 * P)], lg[:, bass.ds(at, 2 * P)], near[:, head, :],
                                       ALU.add), self.o_added)
                step(dve.tensor_reduce(self.nmax[:, i % 2:i % 2 + 1], lg[:, P:P + width], AX.X, ALU.max, negate=True),
                     self.rowmax_made)
            if i >= 2:
                u = i - 2
                head, gate = units[u][4], units[u][6]
                r = self.rsum[:, u % 2:u % 2 + 1]
                step(dve.reciprocal(r, self.sum[:, u:u + 1]), self.o_added)
                if gates is not None:
                    step(dve.tensor_tensor(r, r, gates[:, gate:gate + 1], ALU.mult), self.o_added)
                dve.wait_ge(self.pv_summed, u + 1)
                if gates is None:
                    step(dve.tensor_scalar(out[:, head, :], self.o_ps[u % 2][:, :], r, None, ALU.mult), self.o_scaled)
                else:
                    step(dve.scalar_tensor_tensor(out[:, head, :], self.o_ps[u % 2][:, :], r, out[:, head, :],
                                                  ALU.mult, ALU.add), self.o_scaled)

    def scalar(self, act, units):
        n = len(units)
        for i in range(n + 1):
            if i < n:
                width = len(units[i][5]) * P
                act.wait_ge(self.rowmax_made, i + 1)
                if i >= 2:
                    act.wait_ge(self.p_transposed, i - 1)
                act.activation(self.prob[i % 2][:, 0:width], self.lg[i % 2][:, P:P + width], ACT.Exp,
                               bias=self.nmax[:, i % 2:i % 2 + 1], accum_out=self.sum[:, i:i + 1])\
                   .then_inc(self.exp_done, 1)
            if i >= 1:
                u = i - 1
                nb = len(units[u][5])
                act.wait_ge(self.p_transposed, u + 1)
                if u >= 2:
                    act.wait_ge(self.pv_summed, u - 1)
                act.copy(self.probT[u % 2][:, 0:nb, :], self.t_ps[:, 0:nb, :]).then_inc(self.pT_copied, 1)


def stage_even_prompt(nc, G):
    ident, featT, near, far_mask, z = G["ident"], G["featT"], G["near"], G["far_mask"], G["z_even"]
    kv_out = G["a_kv_p"][0, 0].rearrange("s two kv d -> s (two kv d)")
    with ExitStack() as c:
        zt = tile_of(nc, c, "zt", [P, E_BG])
        cx = [tile_of(nc, c, f"cx{j}", [P, 2, CONV]) for j in range(3)]
        bg = tile_of(nc, c, "bg", [P, CONV])
        cw = tile_of(nc, c, "cw", [P, 4, CONV])
        gq = tile_of(nc, c, "gq", [P, HD])
        gk = tile_of(nc, c, "gk", [P, HD])
        sq = tile_of(nc, c, "sq", [P, 10, HD])
        rms = tile_of(nc, c, "rms", [P, 3, 10])
        qn = tile_of(nc, c, "qn", [P, 5, NKV, HD])
        kid = tile_of(nc, c, "kid", [P, 2, HD])
        qTz = tile_of(nc, c, "qTz", [P, NH, P])
        qiT = tile_of(nc, c, "qiT", [P, 2, P])
        KT = tile_of(nc, c, "KT", [P, SEQ])
        KiT = tile_of(nc, c, "KiT", [P, SEQ])
        V = tile_of(nc, c, "V", [P, TILES, P])
        rel = tile_of(nc, c, "rel", [P, SEQ])
        score = tile_of(nc, c, "score", [P, SEQ])
        top8 = tile_of(nc, c, "top8", [P, 8])
        wi = tile_of(nc, c, "wi", [P, IDXH])
        cat = tile_of(nc, c, "cat", [P, D])
        o = cat[:, 0:A_Q].rearrange("p (h d) -> p h d", h=NH)
        att = Attend(nc, c)
        t_ps = att.t_ps

        loaded, cleared, scaled = setup = signals(nc, c, "weights_loaded buffers_cleared gain_scaled")
        with nc.Block() as block:

            @block.sync
            def _(sp):
                for j in range(3):
                    sp.dma_start(cw[:, j, :], G["b_conv_w"][0, j].partition_broadcast(P)).then_inc(loaded, 16)
                sp.dma_start(cw[:, 3, :], G["b_conv_b"][0].partition_broadcast(P)).then_inc(loaded, 16)
                sp.dma_start(gq[:, :], G["a_q_norm"][0].partition_broadcast(P)).then_inc(loaded, 16)
                sp.dma_start(gk[:, :], G["a_k_norm"][0].partition_broadcast(P)).then_inc(loaded, 16)

            @block.gpsimd
            def _(pool):
                for buf in (qTz[:, :, :], KT[:, :], KiT[:, :], V[:, :, :], att.lg[0][:, :], att.lg[1][:, :]):
                    pool.memset(buf, 0.0).then_inc(cleared, 1)

            @block.vector
            def _(dve):
                dve.wait_ge(loaded, 96)
                dve.tensor_scalar(gq[:, :], gq[:, :], HD ** -0.5, None, ALU.mult).then_inc(scaled, 1)
        clear_signals(nc, setup)

        names = signals(nc, c, "z_loaded conv_loaded normed kn_ready mean_made rms_made kid_copied v_copied "
                               "qk_transposed q_copied keys_copied idx_summed idx_relu score_step picked "
                               "u_made conv_step conv_made kv_stored cat_transposed")
        (z_loaded, conv_loaded, normed, kn_ready, mean_made, rms_made, kid_copied, v_copied, qk_transposed,
         q_copied, keys_copied, idx_summed, idx_relu, score_step, picked, u_made, conv_step, conv_made, kv_stored,
         cat_transposed) = names

        with nc.Fori(0, TILES) as t:
            units = [(qTz[:, h, :], [(KT[:, 0:512], 512), (KT[:, 512:1024], 512)], score[:, :], t * P, h,
                      [V[:, j, (h // GQA) * HD:(h // GQA + 1) * HD] for j in range(TILES)], None)
                     for h in range(NH)]
            with nc.Block() as block:

                @block.sync
                def _(sp):
                    sp.dma_start(zt[:, :], z[bass.ds(t * P + LEAD, P), 0:E_BG]).then_inc(z_loaded, 16)
                    for j in range(3):
                        sp.dma_start(cx[j][:, :, :].rearrange("p a n -> p (a n)"),
                                     z[bass.ds(t * P + LEAD - j, P), E_CG:P_EVEN]).then_inc(conv_loaded, 16)
                    sp.dma_start(bg[:, :], z[bass.ds(t * P + LEAD, P), E_BG:E_CG]).then_inc(conv_loaded, 16)
                    sp.wait_ge(z_loaded, 16)
                    sp.dma_start(kv_out[bass.ds(t * P, P), KVW:A_KV], zt[:, E_V:E_QI]).then_inc(kv_stored, 16)
                    sp.dma_start(G["a_kidx_p"][0, 0, bass.ds(t * P, P), :], zt[:, E_KI:E_WI]).then_inc(kv_stored, 16)
                    sp.wait_ge(kn_ready, 1)
                    sp.dma_start(kv_out[bass.ds(t * P, P), 0:KVW], qn[:, 4, :, :].rearrange("p a d -> p (a d)"))\
                      .then_inc(kv_stored, 16)
                    sp.wait_ge(u_made, 3)
                    sp.dma_start(G["b_conv_p"][0, 0], cx[0][P - 2:P, 0, :]).then_inc(kv_stored, 16)
                    sp.wait_ge(kv_stored, 64)

                @block.gpsimd
                def _(pool):
                    step = InOrder(pool)
                    pool.wait_ge(conv_loaded, 64)
                    for j in range(3):
                        step(pool.tensor_tensor(cx[j][:, 0, :], cx[j][:, 0, :], cx[j][:, 1, :], ALU.mult), u_made)
                    for j in (2, 1, 0):
                        step(pool.tensor_tensor(cx[j][:, 1, :], cx[j][:, 0, :], cw[:, 2 - j, :], ALU.mult), conv_step)
                    step(pool.tensor_tensor(cx[2][:, 1, :], cx[2][:, 1, :], cw[:, 3, :], ALU.add), conv_step)
                    step(pool.tensor_tensor(cx[2][:, 1, :], cx[2][:, 1, :], cx[1][:, 1, :], ALU.add), conv_step)
                    step(pool.tensor_tensor(cx[2][:, 1, :], cx[2][:, 1, :], cx[0][:, 1, :], ALU.add), conv_step)
                    step(pool.tensor_tensor(cat[:, A_Q:D], cx[2][:, 1, :], bg[:, :], ALU.mult), conv_made)

                @block.scalar
                def _(act):
                    act.wait_ge(z_loaded, 16)
                    for a in range(2):
                        act.copy(kid[:, a, :], zt[:, E_KI:E_WI]).then_inc(kid_copied, 1)
                    act.copy(V[:, t, :], zt[:, E_V:E_QI]).then_inc(v_copied, 1)
                    act.wait_ge(mean_made, 1)
                    act.activation(rms[:, 1, :], rms[:, 0, :], ACT.Sqrt).then_inc(rms_made, 1)
                    act.wait_ge(qk_transposed, 1)
                    act.copy(KT[:, bass.ds(t * P, P)], t_ps[:, 4, :]).then_inc(keys_copied, 1)
                    act.copy(qiT[:, :, :], t_ps[:, 5:7, :]).then_inc(keys_copied, 1)
                    act.copy(KiT[:, bass.ds(t * P, P)], t_ps[:, 7, :]).then_inc(keys_copied, 1)
                    for i in range(IDXH):
                        act.wait_ge(idx_summed, i + 1)
                        if i:
                            act.wait_ge(score_step, i)
                        act.activation(rel[:, :], att.lg_ps[i % 2][:, :], ACT.Relu).then_inc(idx_relu, 1)
                    att.scalar(act, units)
                    act.wait_ge(cat_transposed, 1)
                    act.copy(featT[:, KC // 2:KC, bass.ds(t * P, P)], t_ps[:, KC // 2:KC, :])

                @block.tensor
                def _(pe):
                    pe.wait_ge(kn_ready, 1)
                    for g in range(5):
                        pe.transpose(t_ps[:, g, :], qn[:, g, :, :].rearrange("p a d -> p (a d)"), ident[:, :])
                    pe.wait_ge(z_loaded, 16)
                    for g in range(2):
                        pe.transpose(t_ps[:, 5 + g, :], zt[:, E_QI + g * P:E_QI + (g + 1) * P], ident[:, :])
                    pe.wait_ge(kid_copied, 2)
                    pe.transpose(t_ps[:, 7, :], kid[:, :, :].rearrange("p a d -> p (a d)"), ident[:, :])\
                      .then_inc(qk_transposed, 1)
                    pe.wait_ge(keys_copied, 3)
                    for i in range(IDXH):
                        if i >= 2:
                            pe.wait_ge(idx_relu, i - 1)
                        half = slice((i % 2) * HD, (i % 2 + 1) * HD)
                        for s in range(2):
                            last = pe.matmul(att.lg_ps[i % 2][:, s * 512:(s + 1) * 512], qiT[half, i // 2, :],
                                             KiT[half, s * 512:(s + 1) * 512], start=True, stop=True)
                        last.then_inc(idx_summed, 1)
                    pe.wait_ge(q_copied, 2)
                    pe.wait_ge(idx_relu, IDXH)
                    pe.wait_ge(v_copied, 1)
                    att.tensor(pe, units, ident)
                    pe.wait_ge(att.o_scaled, NH)
                    pe.wait_ge(conv_made, 1)
                    for k in range(KC):
                        last = pe.transpose(t_ps[:, k, :], cat[:, k * P:(k + 1) * P], ident[:, :])
                    last.then_inc(cat_transposed, 1)

                @block.vector
                def _(dve):
                    step = InOrder(dve)
                    dve.wait_ge(z_loaded, 16)
                    qk = zt[:, 0:10 * HD].rearrange("p (h d) -> p h d", d=HD)
                    step(dve.tensor_tensor(sq[:, :, :], qk, qk, ALU.mult), normed)
                    step(dve.tensor_reduce(rms[:, 0, :], sq[:, :, :], AX.X, ALU.add), normed)
                    step(dve.tensor_scalar(rms[:, 0, :], rms[:, 0, :], 1.0 / HD, RMS_EPS, ALU.mult, ALU.add),
                         mean_made)
                    step(dve.tensor_scalar(wi[:, :], zt[:, E_WI:E_BG], (IDXH * HD) ** -0.5, None, ALU.mult), normed)
                    dve.wait_ge(rms_made, 1)
                    step(dve.reciprocal(rms[:, 2, :], rms[:, 1, :]), normed)
                    for kv in range(NKV):
                        cols = slice(kv * GQA * HD, (kv + 1) * GQA * HD)
                        r = rms[:, 2, kv * GQA:(kv + 1) * GQA].unsqueeze(2).broadcast_to([P, GQA, HD])
                        step(dve.tensor_tensor(qn[:, 0:GQA, kv, :], zt[:, cols].rearrange("p (g d) -> p g d", d=HD),
                                               r, ALU.mult), normed)
                        step(dve.tensor_tensor(qn[:, 0:GQA, kv, :], qn[:, 0:GQA, kv, :],
                                               gq[:, :].unsqueeze(1).broadcast_to([P, GQA, HD]), ALU.mult), normed)
                    r = rms[:, 2, NH:NH + NKV].unsqueeze(2).broadcast_to([P, NKV, HD])
                    step(dve.tensor_tensor(qn[:, GQA, :, :], zt[:, E_K:E_V].rearrange("p (g d) -> p g d", d=HD),
                                           r, ALU.mult), normed)
                    step(dve.tensor_tensor(qn[:, GQA, :, :], qn[:, GQA, :, :],
                                           gk[:, :].unsqueeze(1).broadcast_to([P, NKV, HD]), ALU.mult), kn_ready)
                    dve.wait_ge(qk_transposed, 1)
                    for kv in range(NKV):
                        half = slice(kv * HD, (kv + 1) * HD)
                        step(dve.tensor_copy(qTz[half, kv * GQA:(kv + 1) * GQA, :], t_ps[half, 0:GQA, :]), q_copied)
                    causal = far_mask[:, bass.ds(896 - t * P, SEQ)]
                    for i in range(IDXH):
                        dve.wait_ge(idx_relu, i + 1)
                        step(dve.scalar_tensor_tensor(score[:, :], rel[:, :], wi[:, i:i + 1],
                                                      causal if i == 0 else score[:, :], ALU.mult, ALU.add),
                             score_step)
                    for _ in range(TOPK // 8):
                        step(dve.max(top8[:, :], score[:, :]), picked)
                        step(dve.match_replace(score[:, :], top8[:, :], score[:, :], TAKEN), picked)
                    step(dve.tensor_scalar(score[:, :], score[:, :], TAKEN / 2, NEG, ALU.is_gt, ALU.mult), picked)
                    step(dve.tensor_tensor(score[:, :], score[:, :], causal, ALU.add), picked)
                    att.vector(dve, step, units, near, o, None)
                    dve.wait_ge(cat_transposed, 1)
                    dve.tensor_copy(featT[:, 0:KC // 2, bass.ds(t * P, P)], t_ps[:, 0:KC // 2, :])
            clear_signals(nc, names + att.sems)


class SampleState:

    def __init__(self, nc, c):
        self.Qz = tile_of(nc, c, "Qz", [P, NB, NH])
        self.KnT = tile_of(nc, c, "KnT", [P, 2, NB])
        self.Vn = tile_of(nc, c, "Vn", [1, 2, NB, P])
        self.mask = tile_of(nc, c, "s_mask", [NB * NH, PAST + 1])
        self.scale = tile_of(nc, c, "s_scale", [NB * NH, 3])
        self.oT = tile_of(nc, c, "s_oT", [P, NB * NH])
        self.cat = tile_of(nc, c, "s_cat", [NB, D])


def sample_logits(nc, G, st, name, load_keys, n_tiles, branch, V, kidx=None):
    ident = G["ident"]
    past = n_tiles * P
    Ls, Rs = G["s_logits"], G["s_rel"]
    with ExitStack() as c:
        K = tile_of(nc, c, "s_K", [P, n_tiles, P])
        KT = tile_of(nc, c, "s_KT", [P, past + 1])
        Qb = tile_of(nc, c, "s_Qb", [P, NH])
        L = tile_of(nc, c, "s_L", [NH, past + 1])
        Ki = tile_of(nc, c, "s_Ki", [P, n_tiles, HD])
        KiT = tile_of(nc, c, "s_KiT", [HD, past + 1])
        Qib = tile_of(nc, c, "s_Qib", [HD, IDXH])
        R = tile_of(nc, c, "s_R", [IDXH, past + 1])
        t_ps = bank_of(nc, c, "s_t_ps", [P, 8, P])
        ti_ps = bank_of(nc, c, "s_ti_ps", [HD, 8, P])
        l_ps = bank_of(nc, c, "s_l_ps", [NH, 1024])
        new_ps = bank_of(nc, c, "s_new_ps", [NH, 2])
        sems = signals(nc, c, "keys_loaded kidx_loaded staged k_transposed kT_copied ki_transposed kiT_copied "
                              "l_summed l_copied r_summed r_copied l_stored")
        (keys_loaded, kidx_loaded, staged, k_transposed, kT_copied, ki_transposed, kiT_copied, l_summed, l_copied,
         r_summed, r_copied, l_stored) = sems
        spans = [(a, min(a + 512, past)) for a in range(0, past, 512)]

        with nc.Fori(0, NB) as b:
            with nc.Block() as block:

                @block.sync
                def _(sp):
                    load_keys(sp, b, K, V, Ki, keys_loaded, kidx_loaded)
                    sp.wait_ge(l_copied, 2)
                    sp.dma_start(Ls[bass.ds(b * NH, NH), 0:past + 1], L[:, :]).then_inc(l_stored, 16)
                    if kidx:
                        sp.wait_ge(r_copied, 2)
                        sp.dma_start(Rs[b], R[:, :]).then_inc(l_stored, 16)
                    sp.wait_ge(l_stored, 32 if kidx else 16)

                @block.vector
                def _(dve):
                    dve.tensor_copy(Qb[:, :], st.Qz[:, b, :]).then_inc(staged, 1)
                    dve.tensor_copy(KT[:, past:past + 1], st.KnT[:, branch, bass.ds(b, 1)]).then_inc(staged, 1)
                    if kidx:
                        dve.tensor_copy(Qib[:, :], kidx[0][:, b, :]).then_inc(staged, 1)
                        dve.tensor_copy(KiT[:, past:past + 1], kidx[1][:, bass.ds(b, 1)]).then_inc(staged, 1)
                        dve.wait_ge(ki_transposed, 1)
                        dve.tensor_copy(KiT[:, 0:past], ti_ps[:, 0:n_tiles, :].rearrange("p j s -> p (j s)"))\
                           .then_inc(kiT_copied, 1)
                    dve.wait_ge(l_summed, 1)
                    dve.tensor_copy(L[:, 0:past], l_ps[:, 0:past]).then_inc(l_copied, 1)
                    dve.tensor_copy(L[:, past:past + 1], new_ps[:, 0:1]).then_inc(l_copied, 1)

                @block.scalar
                def _(act):
                    act.wait_ge(k_transposed, 1)
                    act.copy(KT[:, 0:past], t_ps[:, 0:n_tiles, :].rearrange("p j s -> p (j s)")).then_inc(kT_copied, 1)
                    if kidx:
                        act.wait_ge(r_summed, 1)
                        act.activation(R[:, 0:past], l_ps[0:IDXH, 0:past], ACT.Relu).then_inc(r_copied, 1)
                        act.activation(R[:, past:past + 1], new_ps[0:IDXH, 1:2], ACT.Relu).then_inc(r_copied, 1)

                @block.tensor
                def _(pe):
                    pe.wait_ge(keys_loaded, 16 * 2 * n_tiles)
                    for j in range(n_tiles):
                        last = pe.transpose(t_ps[:, j, :], K[:, j, :], ident[:, :])
                    last.then_inc(k_transposed, 1)
                    if kidx:
                        pe.wait_ge(kidx_loaded, 16 * n_tiles)
                        for j in range(n_tiles):
                            last = pe.transpose(ti_ps[:, j, :], Ki[:, j, :], ident[:, :])
                        last.then_inc(ki_transposed, 1)
                    pe.wait_ge(staged, 4 if kidx else 2)
                    pe.wait_ge(kT_copied, 1)
                    for a, e in spans:
                        pe.matmul(l_ps[:, a:e], Qb[:, :], KT[:, a:e], start=True, stop=True)
                    pe.matmul(new_ps[:, 0:1], Qb[:, :], KT[:, past:past + 1], start=True, stop=True)\
                      .then_inc(l_summed, 1)
                    if kidx:
                        pe.wait_ge(kiT_copied, 1)
                        pe.wait_ge(l_copied, 2)
                        for a, e in spans:
                            pe.matmul(l_ps[0:IDXH, a:e], Qib[:, :], KiT[:, a:e], start=True, stop=True)
                        pe.matmul(new_ps[0:IDXH, 1:2], Qib[:, :], KiT[:, past:past + 1], start=True, stop=True)\
                          .then_inc(r_summed, 1)
            clear_signals(nc, sems)


def sample_attend(nc, G, st, n_tiles, branch, V, first_key, gate, accumulate):
    ident, row_bias = G["ident"], G["row_bias"]
    past = n_tiles * P
    W = past + 1
    R = NB * NH
    with ExitStack() as c:
        S = tile_of(nc, c, "s_S", [R, W])
        PT = tile_of(nc, c, "s_PT", [P, n_tiles, R])
        PTn = tile_of(nc, c, "s_PTn", [1, R])
        mx = tile_of(nc, c, "s_mx", [R, 4])
        t_ps = bank_of(nc, c, "s_pt_ps", [P, n_tiles, R])
        tn_ps = bank_of(nc, c, "s_ptn_ps", [1, R])
        o_ps = bank_of(nc, c, "s_o_ps", [P, R])
        sems = signals(nc, c, "l_loaded masked max_made exp_done scaled transposed pT_copied o_summed")
        l_loaded, masked, max_made, exp_done, scaled, transposed, pT_copied, o_summed = sems
        with nc.Block() as block:

            @block.sync
            def _(sp):
                sp.dma_start(S[:, :], G["s_logits"][:, 0:W]).then_inc(l_loaded, 16)

            @block.vector
            def _(dve):
                step = InOrder(dve)
                dve.wait_ge(l_loaded, 16)
                step(dve.tensor_tensor(S[:, :], S[:, :], row_bias[:, first_key:first_key + W], ALU.add), masked)
                step(dve.tensor_tensor(S[:, :], S[:, :], st.mask[:, first_key:first_key + W], ALU.add), masked)
                step(dve.tensor_reduce(mx[:, 0:1], S[:, :], AX.X, ALU.max, negate=True), max_made)
                dve.wait_ge(exp_done, 1)
                step(dve.reciprocal(mx[:, 2:3], mx[:, 1:2]), masked)
                step(dve.tensor_scalar(S[:, :], S[:, :], mx[:, 2:3], st.scale[:, gate:gate + 1], ALU.mult, ALU.mult),
                     scaled)
                dve.wait_ge(transposed, 1)
                dve.tensor_copy(PT[:, :, :], t_ps[:, :, :]).then_inc(pT_copied, 1)
                dve.tensor_copy(PTn[:, :], tn_ps[:, :]).then_inc(pT_copied, 1)
                dve.wait_ge(o_summed, 1)
                if accumulate:
                    step(dve.tensor_tensor(st.oT[:, :], st.oT[:, :], o_ps[:, :], ALU.add), masked)
                else:
                    step(dve.tensor_copy(st.oT[:, :], o_ps[:, :]), masked)

            @block.scalar
            def _(act):
                act.wait_ge(max_made, 1)
                act.activation(S[:, :], S[:, :], ACT.Exp, bias=mx[:, 0:1], accum_out=mx[:, 1:2]).then_inc(exp_done, 1)

            @block.tensor
            def _(pe):
                pe.wait_ge(scaled, 1)
                for j in range(n_tiles):
                    pe.transpose(t_ps[:, j, :], S[:, j * P:(j + 1) * P], ident[0:R, 0:R])
                pe.transpose(tn_ps[:, :], S[:, past:W], ident[0:R, 0:R]).then_inc(transposed, 1)
                pe.wait_ge(pT_copied, 2)
                for b in range(NB):
                    cols = slice(b * NH, (b + 1) * NH)
                    for j in range(n_tiles):
                        pe.matmul(o_ps[:, cols], V[:, b * n_tiles + j, :], PT[:, j, cols], start=(j == 0), stop=False)
                    last = pe.matmul(o_ps[:, cols], st.Vn[0:1, branch, b, :], PTn[:, cols], start=False, stop=True)
                last.then_inc(o_summed, 1)
        clear_signals(nc, sems)


def sample_concat(nc, G, st, layer_kind="even"):
    ident, featT = G["ident"], G["featT"]
    R = NB * NH
    with ExitStack() as c:
        rows = tile_of(nc, c, "s_orow", [R, P])
        o_ps = bank_of(nc, c, "s_or_ps", [R, P])
        t_ps = bank_of(nc, c, "s_cat_ps", [P, KC, NB])
        sems = signals(nc, c, "o_transposed o_copied o_stored cat_loaded cat_transposed")
        o_transposed, o_copied, o_stored, cat_loaded, cat_transposed = sems
        odd = layer_kind == "odd"
        at = A_Q if odd else 0
        with nc.Block() as block:

            @block.tensor
            def _(pe):
                pe.transpose(o_ps[:, :], st.oT[:, :], ident[:, :]).then_inc(o_transposed, 1)
                pe.wait_ge(cat_loaded, 48 if odd else 32)
                for k in range(KC):
                    last = pe.transpose(t_ps[:, k, :], st.cat[:, k * P:(k + 1) * P], ident[0:NB, 0:NB])
                last.then_inc(cat_transposed, 1)

            @block.vector
            def _(dve):
                dve.wait_ge(o_transposed, 1)
                dve.tensor_copy(rows[:, :], o_ps[:, :]).then_inc(o_copied, 1)
                dve.wait_ge(cat_transposed, 1)
                dve.tensor_copy(featT[:, :, SEQ:TOK], t_ps[:, :, :])

            @block.sync
            def _(sp):
                sp.wait_ge(o_copied, 1)
                sp.dma_start(G["s_rows"], rows[:, :]).then_inc(o_stored, 16)
                sp.wait_ge(o_stored, 16)
                for kv in range(NKV):
                    src = G["s_rows"].rearrange("(b a g) n -> b a g n", b=NB, a=NKV)[:, kv, :, kv * HD:(kv + 1) * HD]
                    cols = slice(at + kv * GQA * HD, at + (kv + 1) * GQA * HD)
                    sp.dma_start(st.cat[:, cols].rearrange("b (g d) -> b g d", d=HD), src).then_inc(cat_loaded, 16)
                if odd:
                    sp.dma_start(st.cat[:, 0:RW].rearrange("b (h d) -> b h d", d=HD),
                                 G["s_rows_c"].rearrange("(b h) d -> b h d", h=NH)).then_inc(cat_loaded, 16)
        clear_signals(nc, sems)


def page_loads(sp, G, b, cache, sources):
    n_pool = cache.shape[0]
    for j in range(PAGES):
        page = sp.value_load(G["page_table"][bass.ds(b, 1), j:j + 1], min_val=0, max_val=n_pool - 1)
        for dst, cache_view, sem in sources:
            sp.dma_start(dst(j), cache_view(page)).then_inc(sem, 16)


def stage_even_sample(nc, G):
    ident = G["ident"]
    z = G["z_even"]
    kv_cache = G["cache_a_kv"][0].rearrange("n s two kv d -> n s (two kv d)")
    ki_cache = G["cache_a_kidx"][0]
    kv_out = G["a_kv_s"][0].rearrange("b one two kv d -> b (one two kv d)")
    R = NB * NH
    with ExitStack() as c:
        st = SampleState(nc, c)
        wi = tile_of(nc, c, "s_wi", [NB, IDXH])
        QiT = tile_of(nc, c, "s_QiT", [HD, NB, IDXH])
        KiN = tile_of(nc, c, "s_KiN", [HD, NB])
        expand = tile_of(nc, c, "s_expand", [NB, R])

        with ExitStack() as c2:
            zs = tile_of(nc, c2, "s_z", [NB, P_EVEN])
            buf = tile_of(nc, c2, "s_buf", [NB, 2, CONV])
            cw = tile_of(nc, c2, "s_cw", [NB, 4, CONV])
            tmp = tile_of(nc, c2, "s_tmp", [NB, 3, CONV])
            gq = tile_of(nc, c2, "s_gq", [NB, HD])
            gk = tile_of(nc, c2, "s_gk", [NB, HD])
            qn = tile_of(nc, c2, "s_qn", [NB, 5, NKV, HD])
            sq = tile_of(nc, c2, "s_sq", [NB, 10, HD])
            rms = tile_of(nc, c2, "s_rms", [NB, 3, 10])
            t_ps = bank_of(nc, c2, "s_prep_ps", [P, 5, NB])
            i_ps = bank_of(nc, c2, "s_prepi_ps", [HD, 5, NB])
            sems = signals(nc, c2, "z_loaded w_loaded cleared expand_cut1 expand_made normed mean_made rms_made kn_ready "
                                   "transposed conv_step u_made conv_made stored")
            (z_loaded, w_loaded, cleared, expand_cut1, expand_made, normed, mean_made, rms_made, kn_ready, transposed,
             conv_step, u_made, conv_made, stored) = sems
            with nc.Block() as block:

                @block.sync
                def _(sp):
                    sp.dma_start(zs[:, :], z[Z_S:Z_S + NB, :]).then_inc(z_loaded, 16)
                    sp.dma_start(st.Vn[0:1, 0, :, :], z[Z_S:Z_S + NB, E_V:E_QI].unsqueeze(0)).then_inc(z_loaded, 16)
                    for j in range(3):
                        sp.dma_start(cw[:, j, :], G["b_conv_w"][0, j].partition_broadcast(NB)).then_inc(w_loaded, 16)
                    sp.dma_start(cw[:, 3, :], G["b_conv_b"][0].partition_broadcast(NB)).then_inc(w_loaded, 16)
                    sp.dma_start(gq[:, :], G["a_q_norm"][0].partition_broadcast(NB)).then_inc(w_loaded, 16)
                    sp.dma_start(gk[:, :], G["a_k_norm"][0].partition_broadcast(NB)).then_inc(w_loaded, 16)
                    sp.dma_start(buf[:, :, :], G["state_b_conv"][0]).then_inc(w_loaded, 16)
                    sp.wait_ge(z_loaded, 32)
                    sp.wait_ge(w_loaded, 112)
                    sp.dma_start(kv_out[:, KVW:A_KV], zs[:, E_V:E_QI]).then_inc(stored, 16)
                    sp.dma_start(G["a_kidx_s"][0, :, 0, :], zs[:, E_KI:E_WI]).then_inc(stored, 16)
                    sp.dma_start(G["b_conv_s"][0, :, 0, :], buf[:, 1, :]).then_inc(stored, 16)
                    sp.wait_ge(kn_ready, 1)
                    sp.dma_start(kv_out[:, 0:KVW], qn[:, 4, :, :].rearrange("p a d -> p (a d)")).then_inc(stored, 16)
                    sp.wait_ge(u_made, 1)
                    sp.dma_start(G["b_conv_s"][0, :, 1, :], tmp[:, 0, :]).then_inc(stored, 16)
                    sp.wait_ge(stored, 80)

                @block.gpsimd
                def _(pool):
                    step = InOrder(pool)
                    pool.memset(st.mask[:, :], 0.0).then_inc(cleared, 1)
                    pool.memset(st.scale[:, :], 1.0).then_inc(cleared, 1)
                    pool.memset(expand[:, :], 1.0).then_inc(cleared, 1)
                    pool.memset(st.Qz[:, :, :], 0.0).then_inc(cleared, 1)
                    pool.wait_ge(cleared, 4)
                    step(pool.affine_select(out=expand[:, :], in_=expand[:, :], compare_op=ALU.is_ge, fill=0.0,
                                            base=0, pattern=[[1, R]], channel_multiplier=-NH), expand_cut1)
                    step(pool.affine_select(out=expand[:, :], in_=expand[:, :], compare_op=ALU.is_ge, fill=0.0,
                                            base=NH - 1, pattern=[[-1, R]], channel_multiplier=NH), expand_made)
                    pool.wait_ge(z_loaded, 32)
                    pool.wait_ge(w_loaded, 112)
                    step(pool.tensor_tensor(tmp[:, 0, :], zs[:, E_CG:E_XIN], zs[:, E_XIN:P_EVEN], ALU.mult), u_made)
                    step(pool.tensor_tensor(tmp[:, 1, :], buf[:, 0, :], cw[:, 0, :], ALU.mult), conv_step)
                    step(pool.tensor_tensor(tmp[:, 1, :], tmp[:, 1, :], cw[:, 3, :], ALU.add), conv_step)
                    step(pool.tensor_tensor(tmp[:, 2, :], buf[:, 1, :], cw[:, 1, :], ALU.mult), conv_step)
                    step(pool.tensor_tensor(tmp[:, 1, :], tmp[:, 1, :], tmp[:, 2, :], ALU.add), conv_step)
                    step(pool.tensor_tensor(tmp[:, 2, :], tmp[:, 0, :], cw[:, 2, :], ALU.mult), conv_step)
                    step(pool.tensor_tensor(tmp[:, 1, :], tmp[:, 1, :], tmp[:, 2, :], ALU.add), conv_step)
                    step(pool.tensor_tensor(st.cat[:, A_Q:D], tmp[:, 1, :], zs[:, E_BG:E_CG], ALU.mult), conv_made)

                @block.scalar
                def _(act):
                    act.wait_ge(mean_made, 1)
                    act.activation(rms[:, 1, :], rms[:, 0, :], ACT.Sqrt).then_inc(rms_made, 1)

                @block.tensor
                def _(pe):
                    pe.wait_ge(kn_ready, 1)
                    for g in range(5):
                        pe.transpose(t_ps[:, g, :], qn[:, g, :, :].rearrange("p a d -> p (a d)"), ident[0:NB, 0:NB])
                    for g in range(5):
                        last = pe.transpose(i_ps[:, g, :], zs[:, E_QI + g * HD:E_QI + (g + 1) * HD], ident[0:NB, 0:NB])
                    last.then_inc(transposed, 1)

                @block.vector
                def _(dve):
                    step = InOrder(dve)
                    dve.wait_ge(z_loaded, 32)
                    dve.wait_ge(w_loaded, 112)
                    step(dve.tensor_scalar(gq[:, :], gq[:, :], HD ** -0.5, None, ALU.mult), normed)
                    qk = zs[:, 0:10 * HD].rearrange("p (h d) -> p h d", d=HD)
                    step(dve.tensor_tensor(sq[:, :, :], qk, qk, ALU.mult), normed)
                    step(dve.tensor_reduce(rms[:, 0, :], sq[:, :, :], AX.X, ALU.add), normed)
                    step(dve.tensor_scalar(rms[:, 0, :], rms[:, 0, :], 1.0 / HD, RMS_EPS, ALU.mult, ALU.add),
                         mean_made)
                    step(dve.tensor_scalar(wi[:, :], zs[:, E_WI:E_BG], (IDXH * HD) ** -0.5, None, ALU.mult), normed)
                    dve.wait_ge(rms_made, 1)
                    step(dve.reciprocal(rms[:, 2, :], rms[:, 1, :]), normed)
                    for kv in range(NKV):
                        cols = slice(kv * GQA * HD, (kv + 1) * GQA * HD)
                        r = rms[:, 2, kv * GQA:(kv + 1) * GQA].unsqueeze(2).broadcast_to([NB, GQA, HD])
                        step(dve.tensor_tensor(qn[:, 0:GQA, kv, :], zs[:, cols].rearrange("p (g d) -> p g d", d=HD),
                                               r, ALU.mult), normed)
                        step(dve.tensor_tensor(qn[:, 0:GQA, kv, :], qn[:, 0:GQA, kv, :],
                                               gq[:, :].unsqueeze(1).broadcast_to([NB, GQA, HD]), ALU.mult), normed)
                    r = rms[:, 2, NH:NH + NKV].unsqueeze(2).broadcast_to([NB, NKV, HD])
                    step(dve.tensor_tensor(qn[:, GQA, :, :], zs[:, E_K:E_V].rearrange("p (g d) -> p g d", d=HD),
                                           r, ALU.mult), normed)
                    step(dve.tensor_tensor(qn[:, GQA, :, :], qn[:, GQA, :, :],
                                           gk[:, :].unsqueeze(1).broadcast_to([NB, NKV, HD]), ALU.mult), kn_ready)
                    dve.wait_ge(transposed, 1)
                    dve.wait_ge(cleared, 4)
                    for kv in range(NKV):
                        half = slice(kv * HD, (kv + 1) * HD)
                        dve.tensor_copy(st.Qz[half, :, kv * GQA:(kv + 1) * GQA],
                                        t_ps[half, 0:GQA, :].rearrange("p g b -> p b g"))
                    dve.tensor_copy(st.KnT[:, 0, :], t_ps[:, 4, :])
                    dve.tensor_copy(QiT[:, :, :], i_ps[:, 0:IDXH, :].rearrange("p i b -> p b i"))
                    dve.tensor_copy(KiN[:, :], i_ps[:, IDXH, :])
            clear_signals(nc, sems)

        V = tile_of(nc, c, "s_V", [P, NB * PAGES, P])

        def load(sp, b, K, V, Ki, keys_loaded, kidx_loaded):
            page_loads(sp, G, b, kv_cache, [
                (lambda j: K[:, j, :], lambda page: kv_cache[page, :, 0:KVW], keys_loaded),
                (lambda j: V[:, bass.ds(b * PAGES + j, 1), :], lambda page: kv_cache[page, :, KVW:A_KV].unsqueeze(1), keys_loaded),
                (lambda j: Ki[:, j, :], lambda page: ki_cache[page], kidx_loaded),
            ])

        sample_logits(nc, G, st, "a", load, PAGES, 0, V, (QiT, KiN))

        with ExitStack() as c2:
            rel = tile_of(nc, c2, "s_rel_rows", [NB, IDXH, PAST + 1])
            score = tile_of(nc, c2, "s_score", [NB, PAST + 1])
            top8 = tile_of(nc, c2, "s_top8", [NB, 8])
            m_ps = bank_of(nc, c2, "s_m_ps", [R, 3, 512])
            sems = signals(nc, c2, "rel_loaded scored picked mask_made spread")
            rel_loaded, scored, picked, mask_made, spread = sems
            spans = ((0, 512), (512, 1024), (1024, 1025))
            with nc.Block() as block:

                @block.sync
                def _(sp):
                    sp.dma_start(rel[:, :, :], G["s_rel"]).then_inc(rel_loaded, 16)

                @block.vector
                def _(dve):
                    step = InOrder(dve)
                    dve.wait_ge(rel_loaded, 16)
                    step(dve.tensor_scalar(score[:, :], rel[:, 0, :], wi[:, 0:1], None, ALU.mult), scored)
                    for i in range(1, IDXH):
                        step(dve.scalar_tensor_tensor(score[:, :], rel[:, i, :], wi[:, i:i + 1], score[:, :],
                                                      ALU.mult, ALU.add), scored)
                    for _ in range(TOPK // 8):
                        step(dve.max(top8[:, :], score[:, :]), picked)
                        step(dve.match_replace(score[:, :], top8[:, :], score[:, :], TAKEN), picked)
                    step(dve.tensor_scalar(score[:, :], score[:, :], TAKEN / 2, NEG, ALU.is_gt, ALU.mult), mask_made)
                    dve.wait_ge(spread, 1)
                    for i, (a, e) in enumerate(spans):
                        dve.tensor_copy(st.mask[:, a:e], m_ps[:, i, 0:e - a])

                @block.tensor
                def _(pe):
                    pe.wait_ge(mask_made, 1)
                    for i, (a, e) in enumerate(spans):
                        last = pe.matmul(m_ps[:, i, 0:e - a], expand[:, :], score[:, a:e], start=True, stop=True)
                    last.then_inc(spread, 1)
            clear_signals(nc, sems)

        sample_attend(nc, G, st, PAGES, 0, V, 0, 0, False)
        sample_concat(nc, G, st)


BLOCKS = -(-2 * TOK // ROUTE_BLOCK) + NEXP
NT = TILES + 1
EPG = NEXP // NGRP


def rank_of(step, dve, rank, flags, x, n, sem):
    step(dve.memset(rank, 0.0), sem)
    for r in range(1, n):
        f = flags[:, :, 0:n - r]
        step(dve.tensor_tensor(f, x[:, :, 0:n - r], x[:, :, r:n], ALU.is_ge), sem)
        step(dve.tensor_tensor(rank[:, :, r:n], rank[:, :, r:n], f, ALU.add), sem)
        step(dve.tensor_scalar(f, f, -1.0, 1.0, ALU.mult, ALU.add), sem)
        step(dve.tensor_tensor(rank[:, :, 0:n - r], rank[:, :, 0:n - r], f, ALU.add), sem)


def stage_route(nc, G, M):
    featT, ones = G["featT"], G["ones"]
    E3 = NT * NEXP
    with ExitStack() as c:
        wr = tile_of(nc, c, "w_router_sb", [P, KC, NEXP])
        br = tile_of(nc, c, "b_router_sb", [P, NEXP])
        tri = tile_of(nc, c, "tri", [P, P])
        valid = tile_of(nc, c, "valid", [P, NT])
        ids = tile_of(nc, c, "token_ids", [P, NT], I32)
        zero_ids = tile_of(nc, c, "zero_ids", [P, BLOCKS], I32)
        kth = tile_of(nc, c, "block_number", [P, BLOCKS, 1], I32)
        kthf = tile_of(nc, c, "block_number_f", [P, BLOCKS, 1])
        s = tile_of(nc, c, "r_s", [P, NT, NEXP])
        sel = tile_of(nc, c, "r_sel", [P, NT, NEXP])
        rank = tile_of(nc, c, "r_rank", [P, NT * NGRP, EPG])
        flags = tile_of(nc, c, "r_flags", [P, NT * NGRP, EPG])
        pairs = tile_of(nc, c, "r_pairs", [P, NT * NGRP, 6])
        grp = tile_of(nc, c, "r_grp", [P, NT, NGRP])
        grank = tile_of(nc, c, "r_grank", [P, NT, NGRP])
        gflags = tile_of(nc, c, "r_gflags", [P, NT, NGRP])
        took = tile_of(nc, c, "r_took", [P, NT, NEXP])
        w = tile_of(nc, c, "r_w", [P, NT, NEXP])
        wsum = tile_of(nc, c, "r_wsum", [P, NT])
        pos = tile_of(nc, c, "r_pos", [P, NT, NEXP])
        tot = tile_of(nc, c, "r_tot", [P, NT, NEXP])
        blk = tile_of(nc, c, "r_blk", [P, NT, NEXP])
        count = tile_of(nc, c, "r_count", [P, NEXP])
        nblk = tile_of(nc, c, "r_nblk", [P, NEXP])
        ends = [tile_of(nc, c, f"r_ends{i}", [P, NEXP]) for i in range(2)]
        slot = tile_of(nc, c, "r_slot", [P, NT, NEXP])
        tmp = tile_of(nc, c, "r_tmp", [P, NT, NEXP])
        dst = tile_of(nc, c, "r_dst", [P, NT, 2])
        be = tile_of(nc, c, "r_be", [P, BLOCKS, NEXP])
        bef = tile_of(nc, c, "r_bef", [P, BLOCKS])
        bei = tile_of(nc, c, "r_bei", [P, BLOCKS], I32)
        l_ps = bank_of(nc, c, "r_l_ps", [P, NT, NEXP])
        pos_ps = bank_of(nc, c, "r_pos_ps", [P, E3])
        tot_ps = bank_of(nc, c, "r_tot_ps", [P, E3])
        sems = signals(nc, c, "w_loaded filled cut s_cleared r_summed sigmoid_done chain took_made pos_summed idx_made "
                              "slots_cleared be_made be_stored scattered")
        (w_loaded, filled, cut, s_cleared, r_summed, sigmoid_done, chain, took_made, pos_summed, idx_made,
         slots_cleared, be_made, be_stored, scattered) = sems
        with nc.Block() as block:

            @block.sync
            def _(sp):
                sp.dma_start(wr[:, :, :], G["w_router"].rearrange("(k p) e -> p k e", p=P)).then_inc(w_loaded, 16)
                sp.dma_start(br[:, :], G["b_router"].partition_broadcast(P)).then_inc(w_loaded, 16)
                sp.wait_ge(filled, 7)
                sp.dma_start(G["slot_token"].rearrange("(p k) one -> p (k one)", p=P), zero_ids[:, :])\
                  .then_inc(slots_cleared, 16)
                sp.wait_ge(be_made, 1)
                sp.dma_start(G["block_expert"], bei[0:1, :]).then_inc(be_stored, 16)
                sp.wait_ge(be_stored, 16)
                sp.wait_ge(slots_cleared, 16)

            @block.gpsimd
            def _(pool):
                pool.memset(tri[:, :], 1.0).then_inc(filled, 1)
                pool.memset(valid[:, :], 1.0).then_inc(filled, 1)
                pool.memset(s[:, :, :], 0.0).then_inc(filled, 1)
                pool.memset(M.idx[:, :, :], 0).then_inc(filled, 1)
                pool.iota(ids[:, :], pattern=[[P, NT]], base=0, channel_multiplier=1).then_inc(filled, 1)
                pool.iota(kth[:, :, :], pattern=[[1, BLOCKS], [0, 1]], base=0, channel_multiplier=0).then_inc(filled, 1)
                pool.memset(zero_ids[:, :], 0).then_inc(filled, 1)
                pool.wait_ge(filled, 7)
                pool.affine_select(out=tri[:, :], in_=tri[:, :], compare_op=ALU.is_gt, fill=0.0, base=0,
                                   pattern=[[1, P]], channel_multiplier=-1).then_inc(cut, 1)
                pool.affine_select(out=valid[:, TILES:NT], in_=valid[:, TILES:NT], compare_op=ALU.is_ge, fill=0.0,
                                   base=NB - 1, pattern=[[0, 1]], channel_multiplier=-1).then_inc(cut, 1)
                pool.wait_ge(idx_made, 1)
                pool.wait_ge(slots_cleared, 16)
                for t in range(NT):
                    rows = P if t < TILES else NB
                    for j in range(2):
                        pool.indirect_dma_start(
                            out=G["slot_token"], out_offset=bass.IndirectOffsetOnAxis(ap=M.idx[0:rows, t, j:j + 1], axis=0),
                            in_=ids[0:rows, t:t + 1], in_offset=None).then_inc(scattered, 16)
                pool.wait_ge(scattered, 16 * 2 * NT)

            @block.tensor
            def _(pe):
                pe.wait_ge(w_loaded, 32)
                for t in range(NT):
                    rows = P if t < TILES else NB
                    for k in range(KC):
                        last = pe.matmul(l_ps[0:rows, t, :], featT[:, k, t * P:t * P + rows], wr[:, k, :],
                                         start=(k == 0), stop=(k == KC - 1))
                last.then_inc(r_summed, 1)
                pe.wait_ge(took_made, 1)
                pe.wait_ge(cut, 2)
                took2 = took[:, :, :].rearrange("p t e -> p (t e)")
                pe.matmul(pos_ps[:, :], tri[:, :], took2, start=True, stop=True)
                pe.matmul(tot_ps[:, :], ones[:, :], took2, start=True, stop=True).then_inc(pos_summed, 1)

            @block.scalar
            def _(act):
                act.wait_ge(r_summed, 1)
                act.wait_ge(filled, 7)
                act.activation(s[:, 0:TILES, :], l_ps[:, 0:TILES, :], ACT.Sigmoid).then_inc(sigmoid_done, 1)
                act.activation(s[0:NB, TILES, :], l_ps[0:NB, TILES, :], ACT.Sigmoid).then_inc(sigmoid_done, 1)

            @block.vector
            def _(dve):
                step = InOrder(dve)
                dve.wait_ge(w_loaded, 32)
                dve.wait_ge(filled, 7)
                dve.wait_ge(sigmoid_done, 2)
                dve.wait_ge(cut, 2)
                step(dve.tensor_copy(kthf[:, :, :], kth[:, :, :]), chain)
                step(dve.tensor_tensor(sel[:, :, :], s[:, :, :], br[:, :].unsqueeze(1).broadcast_to([P, NT, NEXP]),
                                       ALU.add), chain)
                x = sel[:, :, :].rearrange("p t (g e) -> p (t g) e", e=EPG)
                at = 0
                for r in range(1, EPG):
                    n = EPG - r
                    step(dve.tensor_tensor(pairs[:, :, at:at + n], x[:, :, 0:n], x[:, :, r:EPG], ALU.add), chain)
                    at += n
                step(dve.tensor_reduce(grp[:, :, :].rearrange("p t g -> p (t g)"), pairs[:, :, :], AX.X, ALU.max), chain)
                rank_of(step, dve, grank[:, :, :], gflags[:, :, :], grp[:, :, :], NGRP, chain)
                step(dve.tensor_scalar(grank[:, :, :], grank[:, :, :], 0.5, None, ALU.is_lt), chain)
                step(dve.tensor_tensor(grank[:, :, :], grank[:, :, :],
                                       valid[:, :].unsqueeze(2).broadcast_to([P, NT, NGRP]), ALU.mult), chain)
                rank_of(step, dve, rank[:, :, :], flags[:, :, :], x, EPG, chain)
                step(dve.tensor_scalar(rank[:, :, :], rank[:, :, :], 1.5, None, ALU.is_lt), chain)
                step(dve.tensor_tensor(took[:, :, :].rearrange("p t (g e) -> p (t g) e", e=EPG), rank[:, :, :],
                                       grank[:, :, :].rearrange("p t g -> p (t g)").unsqueeze(2)
                                       .broadcast_to([P, NT * NGRP, EPG]), ALU.mult), took_made)
                step(dve.tensor_tensor(w[:, :, :], s[:, :, :], took[:, :, :], ALU.mult), chain)
                step(dve.tensor_reduce(wsum[:, :], w[:, :, :], AX.X, ALU.add), chain)
                step(dve.tensor_scalar(wsum[:, :], wsum[:, :], 1e-38, None, ALU.max), chain)
                step(dve.reciprocal(wsum[:, :], wsum[:, :]), chain)
                step(dve.tensor_tensor(w[:, :, :], w[:, :, :], wsum[:, :].unsqueeze(2).broadcast_to([P, NT, NEXP]),
                                       ALU.mult), chain)
                dve.wait_ge(pos_summed, 1)
                step(dve.tensor_copy(pos[:, :, :].rearrange("p t e -> p (t e)"), pos_ps[:, :]), chain)
                step(dve.tensor_copy(tot[:, :, :].rearrange("p t e -> p (t e)"), tot_ps[:, :]), chain)
                step(dve.tensor_copy(count[:, :], tot[:, 0, :]), chain)
                for t in range(1, NT):
                    step(dve.tensor_tensor(pos[:, t, :], pos[:, t, :], count[:, :], ALU.add), chain)
                    step(dve.tensor_tensor(count[:, :], count[:, :], tot[:, t, :], ALU.add), chain)
                step(dve.tensor_scalar(nblk[:, :], count[:, :], 0.5, None, ALU.is_gt), chain)
                for i in range(1, NT):
                    step(dve.scalar_tensor_tensor(nblk[:, :], count[:, :], i * P + 0.5, nblk[:, :], ALU.is_gt,
                                                  ALU.add), chain)
                step(dve.tensor_copy(ends[0][:, :], nblk[:, :]), chain)
                a = 0
                for r in (1, 2, 4, 8):
                    step(dve.tensor_copy(ends[1 - a][:, 0:r], ends[a][:, 0:r]), chain)
                    step(dve.tensor_tensor(ends[1 - a][:, r:NEXP], ends[a][:, r:NEXP], ends[a][:, 0:NEXP - r],
                                           ALU.add), chain)
                    a = 1 - a
                end = ends[a]
                step(dve.tensor_tensor(be[:, :, :], kthf[:, :, :].broadcast_to([P, BLOCKS, NEXP]),
                                       end[:, :].unsqueeze(1).broadcast_to([P, BLOCKS, NEXP]), ALU.is_ge), chain)
                step(dve.tensor_reduce(bef[:, :], be[:, :, :], AX.X, ALU.add), chain)
                step(dve.tensor_scalar(bef[:, :], bef[:, :], NEXP - 1.0, None, ALU.min), chain)
                step(dve.tensor_copy(bei[:, :], bef[:, :]), be_made)
                step(dve.tensor_scalar(blk[:, :, :], pos[:, :, :], P - 0.5, None, ALU.is_gt), chain)
                for i in range(2, NT):
                    step(dve.scalar_tensor_tensor(blk[:, :, :], pos[:, :, :], i * P - 0.5, blk[:, :, :], ALU.is_gt,
                                                  ALU.add), chain)
                step(dve.scalar_tensor_tensor(slot[:, :, :], blk[:, :, :], -float(P), pos[:, :, :], ALU.mult, ALU.add),
                     chain)
                step(dve.scalar_tensor_tensor(slot[:, :, :], slot[:, :, :], float(BLOCKS), blk[:, :, :], ALU.mult,
                                              ALU.add), chain)
                step(dve.tensor_tensor(nblk[:, :], end[:, :], nblk[:, :], ALU.subtract), chain)
                step(dve.tensor_tensor(slot[:, :, :], slot[:, :, :],
                                       nblk[:, :].unsqueeze(1).broadcast_to([P, NT, NEXP]), ALU.add), chain)
                for j in range(2):
                    big = 1e6
                    eidx = kthf[:, 0:NEXP, 0].unsqueeze(1).broadcast_to([P, NT, NEXP])
                    if j == 0:
                        step(dve.tensor_scalar(tmp[:, :, :], took[:, :, :], -big, big, ALU.mult, ALU.add), chain)
                        step(dve.tensor_tensor(tmp[:, :, :], tmp[:, :, :], eidx, ALU.add), chain)
                        step(dve.tensor_reduce(wsum[:, :], tmp[:, :, :], AX.X, ALU.min), chain)
                    else:
                        step(dve.tensor_scalar(tmp[:, :, :], took[:, :, :], big, -big, ALU.mult, ALU.add), chain)
                        step(dve.tensor_tensor(tmp[:, :, :], tmp[:, :, :], eidx, ALU.add), chain)
                        step(dve.tensor_reduce(wsum[:, :], tmp[:, :, :], AX.X, ALU.max), chain)
                    step(dve.tensor_tensor(tmp[:, :, :], eidx, wsum[:, :].unsqueeze(2).broadcast_to([P, NT, NEXP]),
                                           ALU.is_equal), chain)
                    step(dve.tensor_tensor(be[:, 0:NT, :], tmp[:, :, :], slot[:, :, :], ALU.mult), chain)
                    step(dve.tensor_reduce(dst[:, :, j:j + 1].rearrange("p t one -> p (t one)"), be[:, 0:NT, :], AX.X, ALU.add), chain)
                    step(dve.tensor_tensor(be[:, 0:NT, :], tmp[:, :, :], w[:, :, :], ALU.mult), chain)
                    step(dve.tensor_reduce(M.wts[:, :, j:j + 1].rearrange("p t one -> p (t one)"), be[:, 0:NT, :], AX.X, ALU.add), chain)
                step(dve.tensor_copy(M.idx[:, 0:TILES, :], dst[:, 0:TILES, :]), chain)
                step(dve.tensor_copy(M.idx[0:NB, TILES, :], dst[0:NB, TILES, :]), idx_made)
        clear_signals(nc, sems, [scattered])


def stage_experts(nc, G, layer):
    ident = G["ident"]
    FC = DEXP // P
    views = [G["w_expert_gate"][layer].rearrange("e (k p) f -> p e k f", p=P),
             G["w_expert_up"][layer].rearrange("e (k p) f -> p e k f", p=P),
             G["w_expert_down"][layer].rearrange("e (k p) n -> p e k n", p=P)]
    y_slots = G["y_slots"].rearrange("(p k) n -> p k n", p=P)
    with ExitStack() as c:
        wg = tile_of(nc, c, "wg", [P, 2, KC, DEXP])
        wu = tile_of(nc, c, "wu", [P, 2, KC, DEXP])
        wd = tile_of(nc, c, "wd", [P, 2, FC, D])
        slots = tile_of(nc, c, "slots", [P, BLOCKS], I32)
        sid = tile_of(nc, c, "slot_ids", [P, 1], I32)
        xb = tile_of(nc, c, "xb", [P, D])
        xT = tile_of(nc, c, "xT", [P, KC, P])
        sg = tile_of(nc, c, "sg", [P, DEXP])
        hid = tile_of(nc, c, "hid", [P, DEXP])
        hT = tile_of(nc, c, "hT", [P, FC, P])
        y = tile_of(nc, c, "y", [P, D])
        xT_ps = bank_of(nc, c, "xT_ps", [P, KC, P])
        g_ps = bank_of(nc, c, "g_ps", [P, DEXP])
        u_ps = bank_of(nc, c, "u_ps", [P, DEXP])
        hT_ps = bank_of(nc, c, "hT2_ps", [P, FC, P])
        y_ps = bank_of(nc, c, "y_ps", [P, D])
        (loaded,) = setup = signals(nc, c, "slots_loaded")

        def load_weights(sp, k, half, sem):
            e = sp.value_load(G["block_expert"][0:1, bass.ds(k, 1)], min_val=0, max_val=NEXP - 1)
            for view, dst in zip(views, (wg, wu, wd)):
                sp.dma_start(dst[:, bass.ds(half, 1), :, :], view[:, bass.ds(e, 1), :, :]).then_inc(sem, 16)

        with nc.Block() as block:

            @block.sync
            def _(sp):
                sp.dma_start(slots[:, :], G["slot_token"].rearrange("(p k) one -> p (k one)", p=P)).then_inc(loaded, 16)
                load_weights(sp, 0, 0, loaded)
                sp.wait_ge(loaded, 64)
        clear_signals(nc, setup)

        sems = signals(nc, c, "sid_ready x_gathered x_transposed xT_dve xT_act g_summed u_summed silu_done hid_made "
                              "hid_transposed hT_copied y_summed y_dve y_act y_stored next_loaded")
        (sid_ready, x_gathered, x_transposed, xT_dve, xT_act, g_summed, u_summed, silu_done, hid_made, hid_transposed,
         hT_copied, y_summed, y_dve, y_act, y_stored, next_loaded) = sems

        def one_block(k, half, more):
            with nc.Block() as block:

                @block.sync
                def _(sp):
                    if more:
                        load_weights(sp, k + 1, 1 - half, next_loaded)
                    for n in range(2):
                        sp.wait_ge((y_dve, y_act)[n], 1)
                        cols = slice(n * 512, (n + 1) * 512)
                        sp.dma_start(y_slots[:, bass.ds(k, 1), cols], y[:, cols].unsqueeze(1)).then_inc(y_stored, 16)
                    sp.wait_ge(y_stored, 32)
                    if more:
                        sp.wait_ge(next_loaded, 48)

                @block.gpsimd
                def _(pool):
                    pool.wait_ge(sid_ready, 1)
                    pool.indirect_dma_start(out=xb[:, :], out_offset=None, in_=G["h_rows"],
                                            in_offset=bass.IndirectOffsetOnAxis(ap=sid[:, 0:1], axis=0))\
                        .then_inc(x_gathered, 16)
                    pool.wait_ge(x_gathered, 16)

                @block.tensor
                def _(pe):
                    pe.wait_ge(x_gathered, 16)
                    for j in range(KC):
                        last = pe.transpose(xT_ps[:, j, :], xb[:, j * P:(j + 1) * P], ident[:, :])
                        if j % 4 == 3:
                            last.then_inc(x_transposed, 1)
                    pe.wait_ge(xT_dve, 1)
                    pe.wait_ge(xT_act, 1)
                    for ps, wt, sem in ((g_ps, wg, g_summed), (u_ps, wu, u_summed)):
                        for j in range(KC):
                            last = pe.matmul(ps[:, :], xT[:, j, :], wt[:, half, j, :], start=(j == 0), stop=(j == KC - 1))
                        last.then_inc(sem, 1)
                    pe.wait_ge(hid_made, 1)
                    for f in range(FC):
                        last = pe.transpose(hT_ps[:, f, :], hid[:, f * P:(f + 1) * P], ident[:, :])
                    last.then_inc(hid_transposed, 1)
                    pe.wait_ge(hT_copied, 1)
                    for n in range(2):
                        for f in range(FC):
                            last = pe.matmul(y_ps[:, n * 512:(n + 1) * 512], hT[:, f, :],
                                             wd[:, half, f, n * 512:(n + 1) * 512], start=(f == 0), stop=(f == FC - 1))
                        last.then_inc(y_summed, 1)

                @block.scalar
                def _(act):
                    act.wait_ge(x_transposed, 2)
                    act.copy(xT[:, 4:8, :], xT_ps[:, 4:8, :]).then_inc(xT_act, 1)
                    act.wait_ge(g_summed, 1)
                    act.activation(sg[:, :], g_ps[:, :], ACT.Silu).then_inc(silu_done, 1)
                    act.wait_ge(y_summed, 2)
                    act.copy(y[:, 512:D], y_ps[:, 512:D]).then_inc(y_act, 1)

                @block.vector
                def _(dve):
                    dve.tensor_copy(sid[:, 0:1], slots[:, bass.ds(k, 1)]).then_inc(sid_ready, 1)
                    dve.wait_ge(x_transposed, 1)
                    dve.tensor_copy(xT[:, 0:4, :], xT_ps[:, 0:4, :]).then_inc(xT_dve, 1)
                    dve.wait_ge(silu_done, 1)
                    dve.wait_ge(u_summed, 1)
                    dve.tensor_tensor(hid[:, :], sg[:, :], u_ps[:, :], ALU.mult).then_inc(hid_made, 1)
                    dve.wait_ge(hid_transposed, 1)
                    dve.tensor_copy(hT[:, :, :], hT_ps[:, :, :]).then_inc(hT_copied, 1)
                    dve.wait_ge(y_summed, 1)
                    dve.tensor_copy(y[:, 0:512], y_ps[:, 0:512]).then_inc(y_dve, 1)
            clear_signals(nc, sems, [x_gathered])

        with nc.Fori(0, BLOCKS // 2) as pair:
            for half in range(2):
                one_block(pair * 2 + half, half, True)
        one_block(BLOCKS - 1, 0, False)


def stage_combine(nc, G, layer, M, gate_row):
    x = G["x"]
    with ExitStack() as c:
        gate = tile_of(nc, c, "m_gate", [P, 2, D])
        sid = [tile_of(nc, c, f"m_sid{j}", [P, 1], I32) for j in range(2)]
        wt = tile_of(nc, c, "m_wt", [P, 2])
        y = [tile_of(nc, c, f"m_y{j}", [P, D]) for j in range(2)]
        (loaded,) = setup = signals(nc, c, "gate_loaded")
        with nc.Block() as block:

            @block.sync
            def _(sp):
                cols = slice(gate_row * D, (gate_row + 1) * D)
                sp.dma_start(gate[:, 0, :], G["mod"][0, layer, cols].partition_broadcast(P)).then_inc(loaded, 16)
                sp.dma_start(gate[0:NB, 1, :], G["mod"][1:1 + NB, layer, cols]).then_inc(loaded, 16)
                sp.wait_ge(loaded, 32)
        clear_signals(nc, setup)
        staged, gathered, summed = sems = signals(nc, c, "staged y_gathered y_weighted")

        def one_tile(t, rows, kind):
            with nc.Block() as block:

                @block.vector
                def _(dve):
                    step = InOrder(dve)
                    for j in range(2):
                        dve.tensor_copy(sid[j][0:rows, :], M.idx[0:rows, t, j:j + 1]).then_inc(staged, 1)
                    dve.tensor_copy(wt[0:rows, :], M.wts[0:rows, t, :]).then_inc(staged, 1)
                    dve.wait_ge(staged, 3)
                    dve.wait_ge(gathered, 32)
                    step(dve.tensor_scalar(y[0][0:rows, :], y[0][0:rows, :], wt[0:rows, 0:1], None, ALU.mult), summed)
                    step(dve.scalar_tensor_tensor(y[0][0:rows, :], y[1][0:rows, :], wt[0:rows, 1:2], y[0][0:rows, :],
                                                  ALU.mult, ALU.add), summed)
                    step(dve.tensor_tensor(y[0][0:rows, :], y[0][0:rows, :], gate[0:rows, kind, :], ALU.mult), summed)
                    step(dve.tensor_tensor(x[0:rows, t, :], x[0:rows, t, :], y[0][0:rows, :], ALU.add), summed)

                @block.gpsimd
                def _(pool):
                    pool.wait_ge(staged, 3)
                    for j in range(2):
                        pool.indirect_dma_start(out=y[j][0:rows, :], out_offset=None, in_=G["y_slots"],
                                                in_offset=bass.IndirectOffsetOnAxis(ap=sid[j][0:rows, 0:1], axis=0))\
                            .then_inc(gathered, 16)
                    pool.wait_ge(gathered, 32)
            clear_signals(nc, sems, [gathered])

        with nc.Fori(0, TILES) as t:
            one_tile(t, P, 0)
        one_tile(TILES, NB, 1)


class Routing:
    def __init__(self, nc, c):
        self.idx = tile_of(nc, c, "moe_idx", [P, NT, 2], I32)
        self.wts = tile_of(nc, c, "moe_wts", [P, NT, 2])


def moe_sublayer(nc, G, layer):
    with ExitStack() as c:
        M = Routing(nc, c)
        with ExitStack() as c2:
            G["featT"] = tile_of(nc, c2, "featT_ffn", [P, KC, TOK])
            stage_modulate(nc, G, layer, G["g_norm_ffn"][layer], 3, G["h_rows"])
            stage_route(nc, G, M)
        stage_experts(nc, G, layer)
        stage_combine(nc, G, layer, M, 5)


RQ_R, RQ_K, RQ_V, RQ_KK, RQ_B, RQ_SW, RQ_G = range(7)
DECAY = float(np.exp(np.float32(-0.5)))


class RwkvWeights:
    def __init__(self, nc, c):
        self.mu = tile_of(nc, c, "c_mu_b", [P, P_C])
        self.w0 = tile_of(nc, c, "c_w0_b", [P, RW])
        self.a0 = tile_of(nc, c, "c_a0_b", [P, RW])
        self.kk = tile_of(nc, c, "c_kk_b", [P, RW])
        self.ka = tile_of(nc, c, "c_ka_b", [P, RW])
        self.up = tile_of(nc, c, "c_up", [P, RW])
        self.g_up = tile_of(nc, c, "c_gup", [P, RW])

    def load(self, sp, G, sem):
        for dst, src in ((self.mu, G["c_mu"]), (self.w0, G["c_w0"]), (self.a0, G["c_a0"]), (self.kk, G["c_k_k"]),
                         (self.ka, G["c_k_a"])):
            sp.dma_start(dst[:, :], src[0].partition_broadcast(P)).then_inc(sem, 16)
        sp.dma_start(self.up[0:64, :], G["c_w_up"][0]).then_inc(sem, 16)
        sp.dma_start(self.up[64:128, :], G["c_a_up"][0]).then_inc(sem, 16)
        sp.dma_start(self.g_up[:, :], G["c_g_up"][0]).then_inc(sem, 16)


class RwkvInputs:

    def __init__(self, nc, c, bank_a, bank_b, bank_c, bank_t):
        self.z = tile_of(nc, c, "rw_z", [P, P_C])
        self.prev = tile_of(nc, c, "rw_prev", [P, P_C])
        self.q = tile_of(nc, c, "rw_q", [P, 7, RW])
        self.low = tile_of(nc, c, "rw_low", [P, 2, P])
        self.lowT = tile_of(nc, c, "rw_lowT", [P, 2, P])
        self.a = tile_of(nc, c, "rw_a", [P, RW])
        self.nrm = tile_of(nc, c, "rw_nrm", [P, 2, NH])
        self.w_ps, self.a_ps, self.g_ps, self.t_ps = bank_a, bank_b, bank_c, bank_t
        self.sems = signals(nc, c, "rw_z_loaded rw_mixed rw_low_made rw_low_T rw_lowT_copied rw_up_summed rw_sig_w "
                                   "rw_sig_a rw_a_shifted rw_w_shifted rw_sq_made rw_norm_made rw_chain rw_g_copied")

    def emit(self, nc, G, W, rows, load):
        (z_loaded, mixed, low_made, low_T, lowT_copied, up_summed, sig_w, sig_a, a_shifted, w_shifted, sq_made,
         norm_made, chain, g_copied) = self.sems
        R = slice(0, rows)
        z, prev, q, a = self.z, self.prev, self.q, self.a
        ident = G["ident"]
        with nc.Block() as block:

            @block.sync
            def _(sp):
                load(sp, z, prev, z_loaded)

            @block.vector
            def _(dve):
                step = InOrder(dve)
                dve.wait_ge(z_loaded, 32)
                step(dve.tensor_tensor(prev[R, :], prev[R, :], z[R, :], ALU.subtract), chain)
                step(dve.tensor_tensor(prev[R, :], prev[R, :], W.mu[R, :], ALU.mult), chain)
                step(dve.tensor_tensor(z[R, :], z[R, :], prev[R, :], ALU.add), mixed)
                k = z[R, O_K:O_V]
                kk3 = q[R, RQ_KK, :].rearrange("p (h d) -> p h d", d=HD)
                step(dve.tensor_tensor(q[R, RQ_KK, :], k, W.kk[R, :], ALU.mult), chain)
                step(dve.tensor_tensor(prev[R, 0:RW], q[R, RQ_KK, :], q[R, RQ_KK, :], ALU.mult), chain)
                step(dve.tensor_reduce(self.nrm[R, 0, :], prev[R, 0:RW].rearrange("p (h d) -> p h d", d=HD), AX.X,
                                       ALU.add), sq_made)
                dve.wait_ge(norm_made, 1)
                step(dve.tensor_scalar(self.nrm[R, 1, :], self.nrm[R, 1, :], 1e-12, None, ALU.max), chain)
                step(dve.reciprocal(self.nrm[R, 0, :], self.nrm[R, 1, :]), chain)
                step(dve.tensor_tensor(kk3, kk3, self.nrm[R, 0, :].unsqueeze(2).broadcast_to([rows, NH, HD]),
                                       ALU.mult), chain)
                dve.wait_ge(low_T, 2)
                step(dve.tensor_copy(self.lowT[:, :, R], self.t_ps[:, 0:2, R]), lowT_copied)
                dve.wait_ge(up_summed, 3)
                step(dve.tensor_tensor(a[R, :], self.a_ps[R, :], W.a0[R, :], ALU.add), a_shifted)
                step(dve.tensor_tensor(q[R, RQ_SW, :], self.w_ps[R, :], W.w0[R, :], ALU.add), w_shifted)
                step(dve.tensor_copy(q[R, RQ_R, :], z[R, O_R:O_K]), chain)
                step(dve.tensor_copy(q[R, RQ_V, :], z[R, O_V:O_WD]), chain)
                dve.wait_ge(sig_a, 1)
                step(dve.tensor_tensor(q[R, RQ_B, :], q[R, RQ_KK, :], a[R, :], ALU.mult), chain)
                step(dve.scalar_tensor_tensor(prev[R, 0:RW], a[R, :], -1.0, W.ka[R, :], ALU.add, ALU.mult), chain)
                step(dve.scalar_tensor_tensor(q[R, RQ_K, :], prev[R, 0:RW], 1.0, k, ALU.add, ALU.mult), chain)

            @block.scalar
            def _(act):
                act.wait_ge(mixed, 1)
                act.activation(self.low[R, 0, 0:64], z[R, O_WD:O_AD], ACT.Tanh).then_inc(low_made, 1)
                act.copy(self.low[R, 0, 64:128], z[R, O_AD:O_GD]).then_inc(low_made, 1)
                act.activation(self.low[R, 1, :], z[R, O_GD:P_C], ACT.Sigmoid).then_inc(low_made, 1)
                act.wait_ge(sq_made, 1)
                act.activation(self.nrm[R, 1, :], self.nrm[R, 0, :], ACT.Sqrt).then_inc(norm_made, 1)
                act.wait_ge(up_summed, 3)
                act.copy(q[R, RQ_G, :], self.g_ps[R, :]).then_inc(g_copied, 1)
                act.wait_ge(a_shifted, 1)
                act.activation(a[R, :], a[R, :], ACT.Sigmoid).then_inc(sig_a, 1)
                act.wait_ge(w_shifted, 1)
                act.activation(q[R, RQ_SW, :], q[R, RQ_SW, :], ACT.Sigmoid).then_inc(sig_w, 1)

            @block.tensor
            def _(pe):
                pe.wait_ge(low_made, 3)
                for j in range(2):
                    pe.transpose(self.t_ps[:, j, R], self.low[R, j, :], ident[R, R]).then_inc(low_T, 1)
                pe.wait_ge(lowT_copied, 1)
                pe.matmul(self.w_ps[R, :], self.lowT[0:64, 0, R], W.up[0:64, :], start=True, stop=True)\
                  .then_inc(up_summed, 1)
                pe.matmul(self.a_ps[R, :], self.lowT[64:128, 0, R], W.up[64:128, :], start=True, stop=True)\
                  .then_inc(up_summed, 1)
                pe.matmul(self.g_ps[R, :], self.lowT[:, 1, R], W.g_up[:, :], start=True, stop=True)\
                  .then_inc(up_summed, 1)


def stage_rwkv_prompt(nc, G):
    ident, featT, z = G["ident"], G["featT"], G["z_odd"]
    NC = P // CH
    HG = 4
    with ExitStack() as c:
        W = RwkvWeights(nc, c)
        banks = [bank_of(nc, c, f"rw_ps{i}", [P, 512]) for i in range(8)]
        b4 = [b[:, :].rearrange("p (h s) -> p h s", h=HG) for b in banks]
        I = RwkvInputs(nc, c, banks[0], banks[1], banks[2], b4[3])
        rk = tile_of(nc, c, "c_rk_b", [P, RW])
        lnw = tile_of(nc, c, "c_lnw_b", [P, RW])
        lnb = tile_of(nc, c, "c_lnb_b", [P, RW])
        incl = tile_of(nc, c, "m_incl", [P, P])
        excl = tile_of(nc, c, "m_excl", [P, P])
        after = tile_of(nc, c, "m_after", [P, P])
        nlow = tile_of(nc, c, "m_nlow", [P, P])
        nup = tile_of(nc, c, "m_nup", [P, P])
        inchunk = tile_of(nc, c, "m_inchunk", [P, NC])
        H = tile_of(nc, c, "rw_H", [HD, NC + 1, NH, HD])
        fac = tile_of(nc, c, "rw_fac", [P, 4, RW])
        RT, KT_, BH, KH, BB, KB = range(6)
        sc = tile_of(nc, c, "rw_sc", [P, 6, RW])
        WCT = tile_of(nc, c, "rw_WCT", [HD, NH, NC])
        T4 = tile_of(nc, c, "rw_T4", [HD, 4, HG, P])
        A = [tile_of(nc, c, f"rw_A{i}", [P, HG, P]) for i in range(2)]
        AT = [tile_of(nc, c, f"rw_AT{i}", [P, HG, P]) for i in range(2)]
        MT = tile_of(nc, c, "rw_MT", [P, HG, P])
        ArbT = tile_of(nc, c, "rw_ArbT", [P, HG, P])
        ArkT = tile_of(nc, c, "rw_ArkT", [P, HG, P])
        X = tile_of(nc, c, "rw_X", [P, HG, 2, HD])
        PT = tile_of(nc, c, "rw_PT", [HD, HG, P])
        GF = tile_of(nc, c, "rw_GF", [HD, NC, 2 * HG, HD])
        gf_banks = [banks[1], banks[2], banks[5], banks[6]]
        HW = tile_of(nc, c, "rw_HW", [HD, HG, HD])
        yT = tile_of(nc, c, "rw_yT", [HD, HG, P])
        y = tile_of(nc, c, "rw_y", [P, NH, HD])
        st = tile_of(nc, c, "rw_st", [P, 4, NH])
        tmp = tile_of(nc, c, "rw_tmp", [P, RW])

        loaded, filled, cut, made = setup = signals(nc, c, "rw_loaded rw_filled rw_cut rw_masks")
        with nc.Block() as block:

            @block.sync
            def _(sp):
                W.load(sp, G, loaded)
                sp.dma_start(rk[:, :], G["c_r_k"][0].rearrange("h d -> (h d)").partition_broadcast(P)).then_inc(loaded, 16)
                sp.dma_start(lnw[:, :], G["c_ln_w"][0].partition_broadcast(P)).then_inc(loaded, 16)
                sp.dma_start(lnb[:, :], G["c_ln_b"][0].partition_broadcast(P)).then_inc(loaded, 16)
                sp.wait_ge(loaded, 16 * 11)

            @block.gpsimd
            def _(pool):
                step = InOrder(pool)
                for m in (incl, excl, after):
                    step(pool.memset(m[:, :], 1.0), filled)
                step(pool.memset(inchunk[:, :], 1.0), filled)
                step(pool.memset(H[:, :, :, :], 0.0), filled)
                for m, op, s in ((incl, ALU.is_ge, 1), (excl, ALU.is_gt, 1), (after, ALU.is_gt, -1)):
                    step(pool.affine_select(out=m[:, :], in_=m[:, :], compare_op=op, fill=0.0, base=0,
                                            pattern=[[s, P]], channel_multiplier=-s), cut)
                    m3 = m[:, :].rearrange("p (c s) -> p c s", s=CH)
                    step(pool.affine_select(out=m3, in_=m3, compare_op=ALU.is_ge, fill=0.0, base=0,
                                            pattern=[[-CH, NC], [0, CH]], channel_multiplier=1), cut)
                    step(pool.affine_select(out=m3, in_=m3, compare_op=ALU.is_ge, fill=0.0, base=CH - 1,
                                            pattern=[[CH, NC], [0, CH]], channel_multiplier=-1), cut)
                step(pool.affine_select(out=inchunk[:, :], in_=inchunk[:, :], compare_op=ALU.is_ge, fill=0.0, base=0,
                                        pattern=[[-CH, NC]], channel_multiplier=1), cut)
                step(pool.affine_select(out=inchunk[:, :], in_=inchunk[:, :], compare_op=ALU.is_ge, fill=0.0,
                                        base=CH - 1, pattern=[[CH, NC]], channel_multiplier=-1), cut)

            @block.vector
            def _(dve):
                dve.wait_ge(cut, 11)
                dve.tensor_scalar(nup[:, :], excl[:, :], -1.0, None, ALU.mult)
                dve.tensor_scalar(nlow[:, :], after[:, :], -1.0, None, ALU.mult)
        clear_signals(nc, setup)

        names = signals(nc, c, "rc_cum rc_fac rc_wct rc_scaled rc_chain rc_T rc_Tcopied rc_outer rc_masked rc_pow rc_powA "
                               "rc_powAT rc_app rc_X rc_mv rc_gt rc_gtc rc_h rc_H rc_p rc_P rc_yT rc_yTc rc_y rc_yc rc_sq "
                               "rc_rms rc_out rc_outT rc_hw")
        (cum_summed, fac_made, wct_made, scaled, chain, transposed, T_copied, outer, masked, pow_summed, powA_copied,
         powAT_copied, applied, X_made, mv_summed, gt_summed, gt_copied, h_summed, H_made, p_summed, P_made, yT_summed,
         yT_copied, y_summed, y_copied, sq_made, rms_made, out_made, out_T, hw_made) = names
        NPOW = 4
        bc = [P, HG, P]

        with nc.Fori(0, TILES) as t:

            def load(sp, zt, prev, sem):
                sp.dma_start(zt[:, :], z[bass.ds(t * P + LEAD, P), 0:P_C]).then_inc(sem, 16)
                sp.dma_start(prev[:, :], z[bass.ds(t * P + LEAD - 1, P), 0:P_C]).then_inc(sem, 16)

            I.emit(nc, G, W, P, load)
            q = I.q

            with nc.Block() as block:

                @block.tensor
                def _(pe):
                    sw = q[:, RQ_SW, :]
                    pe.matmul(banks[0][:, :], incl[:, :], sw, start=True, stop=True).then_inc(cum_summed, 1)
                    pe.matmul(banks[1][:, :], excl[:, :], sw, start=True, stop=True).then_inc(cum_summed, 1)
                    pe.matmul(banks[2][:, :], after[:, :], sw, start=True, stop=True).then_inc(cum_summed, 1)
                    for h in range(NH):
                        last = pe.matmul(banks[3][0:HD, h * NC:(h + 1) * NC], q[:, RQ_SW, h * HD:(h + 1) * HD],
                                         inchunk[:, :], start=True, stop=True)
                    last.then_inc(cum_summed, 1)
                    for g in range(2):
                        n = g + 1
                        heads = range(g * HG, (g + 1) * HG)
                        pe.wait_ge(scaled, 4)
                        if g == 0:
                            pe.wait_ge(fac_made, 4)
                            pe.wait_ge(wct_made, 1)
                        else:
                            pe.wait_ge(T_copied, 4)
                            pe.wait_ge(y_copied, 1)
                        for i in range(4):
                            for j, h in enumerate(heads):
                                last = pe.transpose(b4[i][0:HD, j, :], sc[:, i, h * HD:(h + 1) * HD], ident[:, :])
                            last.then_inc(transposed, 1)
                        pe.wait_ge(T_copied, 4 * n)
                        for i, (l, r) in enumerate(((KT_, BH), (BH, KT_), (KH, KT_), (BH, RT), (KH, RT))):
                            for j in range(HG):
                                last = pe.matmul(b4[i + 3][:, j, :], T4[:, l, j, :], T4[:, r, j, :],
                                                 start=True, stop=True)
                            last.then_inc(outer, 1)
                        pe.wait_ge(masked, 5 * g + 3)
                        for j, h in enumerate(heads):
                            last = pe.matmul(b4[0][:, j, 0:HD], MT[:, j, :], q[:, RQ_V, h * HD:(h + 1) * HD],
                                             start=True, stop=True)
                        last.then_inc(mv_summed, 1)
                        for s in range(NPOW + 1):
                            a, at = A[s % 2], AT[s % 2]
                            pe.wait_ge(X_made, (NPOW + 2) * g + s + 1)
                            if s:
                                pe.wait_ge(powAT_copied, NPOW * g + s)
                            for j in range(HG):
                                last = pe.matmul(b4[0][:, j, :], at[:, j, :],
                                                 X[:, j, :, :].rearrange("p a d -> p (a d)"), start=True, stop=True)
                            last.then_inc(applied, 1)
                            if s < NPOW:
                                if s:
                                    pe.wait_ge(powA_copied, (NPOW - 1) * g + s)
                                for j in range(HG):
                                    last = pe.matmul(b4[1][:, j, :], a[:, j, :], at[:, j, :], start=True, stop=True)
                                last.then_inc(pow_summed, 1)
                                if s < NPOW - 1:
                                    for j in range(HG):
                                        last = pe.matmul(b4[2][:, j, :], at[:, j, :], a[:, j, :], start=True, stop=True)
                                    last.then_inc(pow_summed, 1)
                        pe.wait_ge(X_made, (NPOW + 2) * n)
                        pe.wait_ge(masked, 5 * n)
                        for j in range(HG):
                            last = pe.matmul(b4[0][0:HD, j, :], X[:, j, 1, :], ArbT[:, j, :], start=True, stop=True)
                        last.then_inc(p_summed, 1)
                        pe.wait_ge(hw_made, 2)
                        for k in range(NC):
                            rows = slice(k * CH, (k + 1) * CH)
                            for j, h in enumerate(heads):
                                cols = slice(h * HD, (h + 1) * HD)
                                f = gf_banks[k][0:HD, (HG + j) * HD:(HG + j + 1) * HD]
                                pe.matmul(gf_banks[k][0:HD, j * HD:(j + 1) * HD], X[rows, j, 1, :], sc[rows, BB, cols],
                                          start=True, stop=True)
                                pe.matmul(f, sc[rows, BB, cols], X[rows, j, 0, :], start=True, stop=False)
                                last = pe.matmul(f, sc[rows, KB, cols], q[rows, RQ_V, cols], start=False, stop=True)
                            last.then_inc(gt_summed, 1)
                        pe.wait_ge(gt_copied, NC * n)
                        for k in range(NC):
                            if k:
                                pe.wait_ge(H_made, NC * g + k)
                            for j, h in enumerate(heads):
                                last = pe.matmul(banks[3 + k % 2][0:HD, j * HD:(j + 1) * HD], GF[:, k, j, :],
                                                 H[:, k, h, :], start=True, stop=True)
                            last.then_inc(h_summed, 1)
                        pe.wait_ge(P_made, n)
                        pe.wait_ge(H_made, NC * n)
                        for j, h in enumerate(heads):
                            cols = slice(h * HD, (h + 1) * HD)
                            pe.matmul(b4[5][0:HD, j, :], X[:, j, 0, :], ArbT[:, j, :], start=True, stop=False)
                            pe.matmul(b4[5][0:HD, j, :], q[:, RQ_V, cols], ArkT[:, j, :], start=False, stop=False)
                            for k in range(NC):
                                s = slice(k * CH, (k + 1) * CH)
                                last = pe.matmul(b4[5][0:HD, j, s], H[:, k, h, :], PT[:, j, s], start=False,
                                                 stop=(k == NC - 1))
                        last.then_inc(yT_summed, 1)
                        pe.wait_ge(yT_copied, n)
                        for j in range(HG):
                            last = pe.transpose(banks[6][:, j * HD:(j + 1) * HD], yT[:, j, :], ident[0:HD, 0:HD])
                        last.then_inc(y_summed, 1)
                    pe.wait_ge(out_made, 1)
                    for j in range(4):
                        last = pe.transpose(b4[7][:, j, :], tmp[:, j * P:(j + 1) * P], ident[:, :])
                    last.then_inc(out_T, 1)

                @block.scalar
                def _(act):
                    for i, (b, s) in enumerate(((0, -DECAY), (1, -DECAY), (0, DECAY), (2, -DECAY))):
                        act.wait_ge(cum_summed, b + 1)
                        act.activation(fac[:, i, :], banks[b][:, :], ACT.Exp, scale=s).then_inc(fac_made, 1)
                    act.wait_ge(cum_summed, 4)
                    act.activation(WCT[:, :, :].rearrange("k h c -> k (h c)"), banks[3][0:HD, 0:NH * NC], ACT.Exp,
                                   scale=-DECAY).then_inc(wct_made, 1)
                    for g in range(2):
                        n = g + 1
                        for i in range(4):
                            act.wait_ge(transposed, 4 * g + i + 1)
                            act.copy(T4[:, i, :, :], b4[i][0:HD, :, :]).then_inc(T_copied, 1)
                        for s in range(NPOW):
                            at = (2 * NPOW - 1) * g + 2 * s
                            act.wait_ge(pow_summed, at + 1)
                            act.copy(AT[1 - s % 2][:, :, :], b4[1]).then_inc(powAT_copied, 1)
                            if s < NPOW - 1:
                                act.wait_ge(pow_summed, at + 2)
                                act.copy(A[1 - s % 2][:, :, :], b4[2]).then_inc(powA_copied, 1)
                        for k in range(NC):
                            act.wait_ge(gt_summed, NC * g + k + 1)
                            act.copy(GF[:, k, :, :].rearrange("k h v -> k (h v)"), gf_banks[k][0:HD, :])\
                               .then_inc(gt_copied, 1)
                        act.wait_ge(yT_summed, n)
                        act.copy(yT[:, :, :], b4[5][0:HD, :, :]).then_inc(yT_copied, 1)
                        act.wait_ge(y_summed, n)
                        act.copy(y[:, g * HG:(g + 1) * HG, :].rearrange("p h d -> p (h d)"), banks[6][:, 0:HG * HD])\
                           .then_inc(y_copied, 1)
                    act.wait_ge(sq_made, 1)
                    act.activation(st[:, 2, :], st[:, 1, :], ACT.Sqrt).then_inc(rms_made, 1)

                @block.gpsimd
                def _(pool):
                    pool.wait_ge(fac_made, 4)
                    pool.tensor_tensor(sc[:, BB, :], q[:, RQ_B, :], fac[:, 3, :], ALU.mult).then_inc(hw_made, 1)
                    pool.tensor_tensor(sc[:, KB, :], q[:, RQ_K, :], fac[:, 3, :], ALU.mult).then_inc(hw_made, 1)

                @block.vector
                def _(dve):
                    step = InOrder(dve)
                    dve.wait_ge(fac_made, 4)
                    for i, (src, f) in enumerate(((RQ_R, 0), (RQ_KK, 1), (RQ_B, 2), (RQ_K, 2))):
                        step(dve.tensor_tensor(sc[:, i, :], q[:, src, :], fac[:, f, :], ALU.mult), scaled)
                    for g in range(2):
                        n = g + 1
                        heads = slice(g * HG, (g + 1) * HG)
                        cols = slice(g * HG * HD, (g + 1) * HG * HD)
                        for i, (dst, mask) in enumerate(((A[0], nlow), (AT[0], nup), (MT, nup), (ArbT, incl),
                                                         (ArkT, incl))):
                            dve.wait_ge(outer, 5 * g + i + 1)
                            step(dve.tensor_tensor(dst[:, :, :], b4[3 + i], mask[:, :].unsqueeze(1).broadcast_to(bc),
                                                   ALU.mult), masked)
                        step(dve.tensor_scalar(X[:, :, 1, :], sc[:, KT_, cols].rearrange("p (h d) -> p h d", d=HD),
                                               -1.0, None, ALU.mult), chain)
                        dve.wait_ge(mv_summed, n)
                        step(dve.tensor_copy(X[:, :, 0, :], b4[0][:, :, 0:HD]), X_made)
                        for s in range(NPOW + 1):
                            dve.wait_ge(applied, (NPOW + 1) * g + s + 1)
                            X4 = X[:, :, :, :].rearrange("p h a d -> p h (a d)")
                            step(dve.tensor_tensor(X4, X4, b4[0], ALU.add), X_made)
                        dve.wait_ge(p_summed, n)
                        step(dve.tensor_tensor(PT[:, :, :], T4[:, RT, :, :], b4[0][0:HD, :, :], ALU.add), P_made)
                        for k in range(NC):
                            step(dve.tensor_tensor(HW[:, :, :], H[:, k, heads, :],
                                                   WCT[:, heads, k:k + 1].broadcast_to([HD, HG, HD]), ALU.mult), chain)
                            dve.wait_ge(gt_copied, NC * g + k + 1)
                            step(dve.tensor_tensor(HW[:, :, :], HW[:, :, :], GF[:, k, HG:2 * HG, :], ALU.add), chain)
                            dve.wait_ge(h_summed, NC * g + k + 1)
                            step(dve.tensor_tensor(H[:, k + 1, heads, :], HW[:, :, :],
                                                   banks[3 + k % 2][0:HD, 0:HG * HD].rearrange("k (h v) -> k h v", v=HD),
                                                   ALU.add), H_made)
                    dve.wait_ge(y_copied, 2)
                    step(dve.tensor_copy(H[:, 0, :, :], H[:, NC, :, :]), chain)
                    full = [P, NH, HD]
                    y3 = y[:, :, :]
                    t3 = tmp[:, :].rearrange("p (h d) -> p h d", d=HD)
                    step(dve.tensor_reduce(st[:, 0, :], y3, AX.X, ALU.add), chain)
                    step(dve.tensor_scalar(st[:, 0, :], st[:, 0, :], 1.0 / HD, None, ALU.mult), chain)
                    step(dve.tensor_tensor(y3, y3, st[:, 0, :].unsqueeze(2).broadcast_to(full), ALU.subtract), chain)
                    step(dve.tensor_tensor(t3, y3, y3, ALU.mult), chain)
                    step(dve.tensor_reduce(st[:, 1, :], t3, AX.X, ALU.add), chain)
                    step(dve.tensor_scalar(st[:, 1, :], st[:, 1, :], 1.0 / HD, GN_EPS, ALU.mult, ALU.add), sq_made)
                    dve.wait_ge(rms_made, 1)
                    step(dve.reciprocal(st[:, 3, :], st[:, 2, :]), chain)
                    step(dve.tensor_tensor(y3, y3, st[:, 3, :].unsqueeze(2).broadcast_to(full), ALU.mult), chain)
                    yf = y[:, :, :].rearrange("p h d -> p (h d)")
                    step(dve.tensor_tensor(yf, yf, lnw[:, :], ALU.mult), chain)
                    step(dve.tensor_tensor(yf, yf, lnb[:, :], ALU.add), chain)
                    step(dve.tensor_tensor(tmp[:, :], q[:, RQ_R, :], q[:, RQ_K, :], ALU.mult), chain)
                    step(dve.tensor_tensor(tmp[:, :], tmp[:, :], rk[:, :], ALU.mult), chain)
                    step(dve.tensor_reduce(st[:, 0, :], t3, AX.X, ALU.add), chain)
                    step(dve.tensor_tensor(t3, q[:, RQ_V, :].rearrange("p (h d) -> p h d", d=HD),
                                           st[:, 0, :].unsqueeze(2).broadcast_to(full), ALU.mult), chain)
                    step(dve.tensor_tensor(yf, yf, tmp[:, :], ALU.add), chain)
                    step(dve.tensor_tensor(tmp[:, :], yf, q[:, RQ_G, :], ALU.mult), out_made)
                    dve.wait_ge(out_T, 1)
                    dve.tensor_copy(featT[:, 0:4, bass.ds(t * P, P)], b4[7])
            clear_signals(nc, names + I.sems)

        h_T, h_copied, h_stored = tail = signals(nc, c, "rw_hT rw_hTc rw_hst")
        with nc.Block() as block:

            @block.tensor
            def _(pe):
                for h in range(NH):
                    last = pe.transpose(banks[0][0:HD, h * HD:(h + 1) * HD], H[:, 0, h, :], ident[0:HD, 0:HD])
                last.then_inc(h_T, 1)

            @block.vector
            def _(dve):
                dve.wait_ge(h_T, 1)
                dve.tensor_copy(I.z[0:HD, 0:NH * HD], banks[0][0:HD, 0:NH * HD]).then_inc(h_copied, 1)

            @block.sync
            def _(sp):
                sp.dma_start(G["c_shift_p"][0], z[Z_S - 1:Z_S, 0:P_C]).then_inc(h_stored, 16)
                sp.wait_ge(h_copied, 1)
                sp.dma_start(G["c_wkv_p"][0, 0].rearrange("h v k -> v h k"),
                             I.z[0:HD, 0:NH * HD].rearrange("v (h k) -> v h k", k=HD)).then_inc(h_stored, 16)
                sp.wait_ge(h_stored, 32)
        clear_signals(nc, tail)


def stage_rwkv_sample(nc, G):
    z = G["z_odd"]
    R = NB * NH
    with ExitStack() as c:
        W = RwkvWeights(nc, c)
        banks = [bank_of(nc, c, f"rs_ps{i}", [P, 512]) for i in range(4)]
        I = RwkvInputs(nc, c, banks[0], banks[1], banks[2], banks[3][:, :].rearrange("p (h s) -> p h s", h=4))
        (loaded,) = setup = signals(nc, c, "rs_loaded")
        with nc.Block() as block:

            @block.sync
            def _(sp):
                W.load(sp, G, loaded)
                sp.wait_ge(loaded, 16 * 8)
        clear_signals(nc, setup)

        def load(sp, zt, prev, sem):
            sp.dma_start(zt[0:NB, :], z[Z_S:Z_S + NB, 0:P_C]).then_inc(sem, 16)
            sp.dma_start(prev[0:NB, :], G["state_c_shift"][0]).then_inc(sem, 16)

        I.emit(nc, G, W, NB, load)
        clear_signals(nc, I.sems)

        S = tile_of(nc, c, "rs_S", [R, HD, HD])
        big = tile_of(nc, c, "rs_big", [R, HD, HD])
        v7 = tile_of(nc, c, "rs_q", [R, 7, HD])
        ln = tile_of(nc, c, "rs_ln", [R, 3, HD])
        sa = tile_of(nc, c, "rs_sa", [R, 4, HD])
        st = tile_of(nc, c, "rs_st", [R, 4])
        sems = signals(nc, c, "q_stored q_spread s_loaded decay_made chain sq_made rms_made state_made row_made stored")
        q_stored, q_spread, s_loaded, decay_made, chain, sq_made, rms_made, state_made, row_made, stored = sems
        with nc.Block() as block:

            @block.sync
            def _(sp):
                sp.dma_start(G["s_rq"], I.q[0:NB, :, :]).then_inc(q_stored, 16)
                sp.dma_start(S[:, :, :], G["state_c_wkv"][0].rearrange("b h v k -> (b h) v k")).then_inc(s_loaded, 16)
                for b in range(NB):
                    rows = slice(b * NH, (b + 1) * NH)
                    for i, src in enumerate((G["c_ln_w"][0].rearrange("(h d) -> h d", d=HD),
                                             G["c_ln_b"][0].rearrange("(h d) -> h d", d=HD), G["c_r_k"][0])):
                        sp.dma_start(ln[rows, i, :], src).then_inc(s_loaded, 16)
                sp.dma_start(G["c_shift_s"][0], z[Z_S:Z_S + NB, 0:P_C]).then_inc(stored, 16)
                sp.wait_ge(q_stored, 16)
                for b in range(NB):
                    sp.dma_start(v7[b * NH:(b + 1) * NH, :, :],
                                 G["s_rq"][b].rearrange("i (h d) -> h i d", d=HD)).then_inc(q_spread, 16)
                sp.wait_ge(state_made, 1)
                sp.dma_start(G["c_wkv_s"][0].rearrange("b h v k -> (b h) v k"), S[:, :, :]).then_inc(stored, 16)
                sp.wait_ge(row_made, 1)
                sp.dma_start(G["s_rows_c"], sa[:, 1, :]).then_inc(stored, 16)
                sp.wait_ge(stored, 48)

            @block.scalar
            def _(act):
                act.wait_ge(q_spread, 16 * NB)
                act.activation(v7[:, RQ_SW, :], v7[:, RQ_SW, :], ACT.Exp, scale=-DECAY).then_inc(decay_made, 1)
                act.wait_ge(sq_made, 1)
                act.activation(st[:, 2:3], st[:, 1:2], ACT.Sqrt).then_inc(rms_made, 1)

            @block.vector
            def _(dve):
                step = InOrder(dve)
                full = [R, HD, HD]

                def over_v(i):
                    return v7[:, i, :].unsqueeze(1).broadcast_to(full)

                dve.wait_ge(q_spread, 16 * NB)
                dve.wait_ge(s_loaded, 16 * (1 + 3 * NB))
                dve.wait_ge(decay_made, 1)
                step(dve.tensor_tensor(big[:, :, :], S[:, :, :], over_v(RQ_KK), ALU.mult), chain)
                step(dve.tensor_reduce(sa[:, 0, :], big[:, :, :], AX.X, ALU.add, negate=True), chain)
                step(dve.tensor_tensor(S[:, :, :], S[:, :, :], over_v(RQ_SW), ALU.mult), chain)
                step(dve.tensor_tensor(big[:, :, :], sa[:, 0, :].unsqueeze(2).broadcast_to(full), over_v(RQ_B),
                                       ALU.mult), chain)
                step(dve.tensor_tensor(S[:, :, :], S[:, :, :], big[:, :, :], ALU.add), chain)
                step(dve.tensor_tensor(big[:, :, :], v7[:, RQ_V, :].unsqueeze(2).broadcast_to(full), over_v(RQ_K),
                                       ALU.mult), chain)
                step(dve.tensor_tensor(S[:, :, :], S[:, :, :], big[:, :, :], ALU.add), state_made)
                step(dve.tensor_tensor(big[:, :, :], S[:, :, :], over_v(RQ_R), ALU.mult), chain)
                step(dve.tensor_reduce(sa[:, 1, :], big[:, :, :], AX.X, ALU.add), chain)
                yv, t = sa[:, 1, :], sa[:, 2, :]
                step(dve.tensor_reduce(st[:, 0:1], yv, AX.X, ALU.add), chain)
                step(dve.tensor_scalar(st[:, 0:1], st[:, 0:1], 1.0 / HD, None, ALU.mult), chain)
                step(dve.tensor_scalar(yv, yv, st[:, 0:1], None, ALU.subtract), chain)
                step(dve.tensor_tensor(t, yv, yv, ALU.mult), chain)
                step(dve.tensor_reduce(st[:, 1:2], t, AX.X, ALU.add), chain)
                step(dve.tensor_scalar(st[:, 1:2], st[:, 1:2], 1.0 / HD, GN_EPS, ALU.mult, ALU.add), sq_made)
                dve.wait_ge(rms_made, 1)
                step(dve.reciprocal(st[:, 3:4], st[:, 2:3]), chain)
                step(dve.scalar_tensor_tensor(yv, yv, st[:, 3:4], ln[:, 0, :], ALU.mult, ALU.mult), chain)
                step(dve.tensor_tensor(yv, yv, ln[:, 1, :], ALU.add), chain)
                step(dve.tensor_tensor(t, v7[:, RQ_R, :], v7[:, RQ_K, :], ALU.mult), chain)
                step(dve.tensor_tensor(t, t, ln[:, 2, :], ALU.mult), chain)
                step(dve.tensor_reduce(st[:, 0:1], t, AX.X, ALU.add), chain)
                step(dve.scalar_tensor_tensor(yv, v7[:, RQ_V, :], st[:, 0:1], yv, ALU.mult, ALU.add), chain)
                step(dve.tensor_tensor(yv, yv, v7[:, RQ_G, :], ALU.mult), row_made)
        clear_signals(nc, sems)


class Compressed:
    def __init__(self, nc, c):
        self.KT = tile_of(nc, c, "cmp_KT", [P, 1 + NB, NCMP])
        self.V = tile_of(nc, c, "cmp_V", [NCMP, 1 + NB, P])
        self.V4 = tile_of(nc, c, "cmp_V4", [P, P])


def stage_compress(nc, G, C):
    ident = G["ident"]
    cache = G["cache_d_cmp"][0].rearrange("n s two kv d -> n s (two kv d)")
    with ExitStack() as c:
        w = tile_of(nc, c, "cmp_w_sb", [P, 2, CMP, HD])
        pe_rows = tile_of(nc, c, "cmp_pe_rows", [CMP, 2, 2, HD])
        peT = tile_of(nc, c, "cmp_peT", [P, 2, CMP])
        gain = tile_of(nc, c, "cmp_gain", [NCMP, HD])
        rows = tile_of(nc, c, "cmp_rows", [P, PAGES, A_KV])
        rawT = tile_of(nc, c, "cmp_rawT", [P, 2, SEQ])
        kc = tile_of(nc, c, "cmp_kc", [NCMP, NKV, HD])
        sq = tile_of(nc, c, "cmp_sq", [NCMP, NKV, HD])
        rms = tile_of(nc, c, "cmp_rms", [NCMP, 3, NKV])
        t_ps = [bank_of(nc, c, f"cmp_t_ps{i}", [P, PAGES, P]) for i in range(2)]
        c_ps = [bank_of(nc, c, f"cmp_c_ps{i}", [NCMP, 2, HD]) for i in range(NKV)]
        kT_ps = bank_of(nc, c, "cmp_kT_ps", [P, 2 * CMP])
        loaded, pe_transposed = setup = signals(nc, c, "cmp_loaded cmp_peT")
        with nc.Block() as block:

            @block.sync
            def _(sp):
                for a in range(2):
                    for kv in range(NKV):
                        sp.dma_start(w[kv * HD:(kv + 1) * HD, a, :, :],
                                     G["d_cmp_w"][0, a].rearrange("(r d) e -> d r e", d=HD)).then_inc(loaded, 16)
                        sp.dma_start(pe_rows[:, a, kv, :], G["d_cmp_pe"][0, a]).then_inc(loaded, 16)
                sp.dma_start(gain[:, :], G["d_k_norm"][0, 0].partition_broadcast(NCMP)).then_inc(loaded, 16)
                sp.wait_ge(loaded, 16 * 9)

            @block.tensor
            def _(pe):
                pe.wait_ge(loaded, 16 * 9)
                for a in range(2):
                    last = pe.transpose(kT_ps[:, a * CMP:(a + 1) * CMP],
                                        pe_rows[:, a, :, :].rearrange("r k d -> r (k d)"), ident[0:CMP, 0:CMP])
                last.then_inc(pe_transposed, 1)

            @block.vector
            def _(dve):
                dve.wait_ge(pe_transposed, 1)
                dve.tensor_copy(peT[:, :, :].rearrange("p a r -> p (a r)"), kT_ps[:, :])
        clear_signals(nc, setup)

        names = signals(nc, c, "cmp_rows_loaded cmp_transposed cmp_pe_added cmp_summed cmp_kc cmp_sqd cmp_rms "
                               "cmp_kc_ready cmp_kT cmp_v4")
        (rows_loaded, transposed, pe_added, summed, kc_copied, sq_made, rms_made, kc_ready, kT_made, v4_stored) = names

        def one_sequence(seq, load):
            with nc.Block() as block:

                @block.sync
                def _(sp):
                    load(sp, rows_loaded)

                @block.tensor
                def _(pe):
                    pe.wait_ge(rows_loaded, 16 * PAGES)
                    for a in range(2):
                        for j in range(PAGES):
                            last = pe.transpose(t_ps[a][:, j, :], rows[:, j, a * P:(a + 1) * P], ident[:, :])
                        last.then_inc(transposed, 1)
                    for a in range(2):
                        pe.wait_ge(pe_added, a + 1)
                        for kv in range(NKV):
                            half = slice(kv * HD, (kv + 1) * HD)
                            x = rawT[half, a, :].rearrange("p (n r) -> p r n", r=CMP)
                            for r in range(CMP):
                                last = pe.matmul(c_ps[kv][:, a, :], x[:, r, :], w[half, a, r, :],
                                                 start=(r == 0), stop=(r == CMP - 1))
                    last.then_inc(summed, 1)
                    pe.wait_ge(kc_ready, 1)
                    pe.transpose(kT_ps[:, 0:NCMP], kc[:, :, :].rearrange("n k e -> n (k e)"), ident[0:NCMP, 0:NCMP])\
                      .then_inc(kT_made, 1)

                @block.vector
                def _(dve):
                    step = InOrder(dve)
                    for a in range(2):
                        dve.wait_ge(transposed, a + 1)
                        step(dve.tensor_tensor(rawT[:, a, :].rearrange("p (n r) -> p n r", r=CMP),
                                               t_ps[a][:, :, :].rearrange("p j (m r) -> p (j m) r", r=CMP),
                                               peT[:, a, :].unsqueeze(1).broadcast_to([P, NCMP, CMP]), ALU.add),
                             pe_added)
                    dve.wait_ge(summed, 1)
                    for kv in range(NKV):
                        step(dve.tensor_copy(kc[:, kv, :], c_ps[kv][:, 0, :]), kc_copied)
                        step(dve.tensor_copy(C.V[:, seq, kv * HD:(kv + 1) * HD], c_ps[kv][:, 1, :]), kc_copied)
                    step(dve.tensor_tensor(sq[:, :, :], kc[:, :, :], kc[:, :, :], ALU.mult), kc_copied)
                    step(dve.tensor_reduce(rms[:, 0, :], sq[:, :, :], AX.X, ALU.add), kc_copied)
                    step(dve.tensor_scalar(rms[:, 0, :], rms[:, 0, :], 1.0 / HD, RMS_EPS, ALU.mult, ALU.add), sq_made)
                    dve.wait_ge(rms_made, 1)
                    step(dve.reciprocal(rms[:, 2, :], rms[:, 1, :]), kc_copied)
                    step(dve.tensor_tensor(kc[:, :, :], kc[:, :, :],
                                           rms[:, 2, :].unsqueeze(2).broadcast_to([NCMP, NKV, HD]), ALU.mult), kc_copied)
                    step(dve.tensor_tensor(kc[:, :, :], kc[:, :, :],
                                           gain[:, :].unsqueeze(1).broadcast_to([NCMP, NKV, HD]), ALU.mult), kc_ready)
                    dve.wait_ge(kT_made, 1)
                    dve.tensor_copy(C.KT[:, seq, :], kT_ps[:, 0:NCMP])

                @block.scalar
                def _(act):
                    act.wait_ge(sq_made, 1)
                    act.activation(rms[:, 1, :], rms[:, 0, :], ACT.Sqrt).then_inc(rms_made, 1)
            clear_signals(nc, names)

        def load_prompt(sp, sem):
            for j in range(PAGES):
                sp.dma_start(rows[:, j, :], G["z_odd"][LEAD + j * P:LEAD + (j + 1) * P, O_KVC:O_KVS]).then_inc(sem, 16)

        one_sequence(0, load_prompt)
        with nc.Fori(0, NB) as b:
            one_sequence(b + 1, lambda sp, sem: page_loads(
                sp, G, b, cache, [(lambda j: rows[:, j, :], lambda page: cache[page], sem)]))
        with nc.Block() as block:

            @block.sync
            def _(sp):
                for i in range(P // NCMP):
                    sp.dma_start(C.V4[i * NCMP:(i + 1) * NCMP, :], C.V[:, 0, :]).then_inc(v4_stored, 16)
                sp.wait_ge(v4_stored, 16 * (P // NCMP))
        clear_signals(nc, [v4_stored])


ZQ = O_Q


def stage_nsa_prompt(nc, G, C):
    ident, featT, near, far_mask, z = G["ident"], G["featT"], G["near"], G["far_mask"], G["z_odd"]
    cmp_bias = G["cmp_bias"]
    cmp_out = G["d_cmp_p"][0, 0].rearrange("s two kv d -> s (two kv d)")
    slc_out = G["d_slc_p"][0, 0].rearrange("s two kv d -> s (two kv d)")
    win_out = G["d_win_p"][0, 0].rearrange("s two kv d -> s (two kv d)")
    WW = WINDOW + P
    with ExitStack() as c:
        zt = tile_of(nc, c, "zt", [P, P_ODD - ZQ])
        gq = tile_of(nc, c, "gq", [P, HD])
        gk = tile_of(nc, c, "gk", [P, 2, HD])
        sq = tile_of(nc, c, "sq", [P, 12, HD])
        rms = tile_of(nc, c, "rms", [P, 3, 12])
        qn = tile_of(nc, c, "qn", [P, 6, NKV, HD])
        gates = tile_of(nc, c, "gates", [P, 3 * NH])
        qTz = tile_of(nc, c, "qTz", [P, NH, P])
        KsT = tile_of(nc, c, "KsT", [P, SEQ])
        KwT = tile_of(nc, c, "KwT", [P, WINDOW + SEQ])
        Vs = tile_of(nc, c, "Vs", [P, TILES, P])
        Vw = tile_of(nc, c, "Vw", [P, WINDOW // P + TILES, P])
        smask = [tile_of(nc, c, f"smask{kv}", [P, SEQ]) for kv in range(NKV)]
        win_bank = tile_of(nc, c, "win_bank", [P, WW])
        pad_bank = tile_of(nc, c, "pad_bank", [P, 7 * P + WW])
        wmask = tile_of(nc, c, "wmask", [P, WW])
        vis = tile_of(nc, c, "cmp_visible", [P, 64])
        keep = tile_of(nc, c, "sel_keep", [P, 32])
        force = tile_of(nc, c, "sel_force", [P, 32])
        pc = tile_of(nc, c, "pc", [P, NH, NCMP])
        pcT = tile_of(nc, c, "pcT", [P, 2, P])
        cst = tile_of(nc, c, "cmp_st", [P, 3, NH])
        ps = tile_of(nc, c, "ps", [P, NKV, NCMP])
        score = tile_of(nc, c, "sel_score", [P, NKV, NSEL])
        top8 = tile_of(nc, c, "top8", [P, 8])
        o = tile_of(nc, c, "nsa_o", [P, NH, HD])
        att = Attend(nc, c)
        t_ps, lg_ps = att.t_ps, att.lg_ps

        loaded, cleared, cut, forced, scaled = setup = signals(nc, c, "w_loaded cleared cut forced scaled")
        with nc.Block() as block:

            @block.sync
            def _(sp):
                sp.dma_start(gq[:, :], G["d_q_norm"][0].partition_broadcast(P)).then_inc(loaded, 16)
                for i in range(2):
                    sp.dma_start(gk[:, i, :], G["d_k_norm"][0, 1 + i].partition_broadcast(P)).then_inc(loaded, 16)

            @block.gpsimd
            def _(pool):
                for buf in (qTz[:, :, :], KsT[:, :], KwT[:, :], Vs[:, :, :], Vw[:, :, :], att.lg[0][:, :],
                            att.lg[1][:, :], win_bank[:, :], pad_bank[:, :]):
                    pool.memset(buf, 0.0).then_inc(cleared, 1)
                pool.memset(vis[:, :], 1.0).then_inc(cleared, 1)
                pool.wait_ge(cleared, 10)
                step = InOrder(pool)
                step(pool.memset(pad_bank[:, 0:WINDOW], NEG), cut)
                step(pool.affine_select(out=win_bank[:, :], in_=win_bank[:, :], compare_op=ALU.is_ge, fill=NEG,
                                        base=WINDOW, pattern=[[-1, WW]], channel_multiplier=1), cut)
                step(pool.affine_select(out=win_bank[:, :], in_=win_bank[:, :], compare_op=ALU.is_gt, fill=NEG,
                                        base=0, pattern=[[1, WW]], channel_multiplier=-1), cut)
                step(pool.affine_select(out=vis[:, :], in_=vis[:, :], compare_op=ALU.is_ge, fill=0.0, base=865,
                                        pattern=[[-CMP, 64]], channel_multiplier=1), cut)
                step(pool.affine_select(out=cmp_bias[:, :, :], in_=cmp_bias[:, :, :], compare_op=ALU.is_ge, fill=NEG,
                                        base=865, pattern=[[0, NH], [-CMP, 64]], channel_multiplier=1), cut)

            @block.vector
            def _(dve):
                step = InOrder(dve)
                for half, own in ((slice(0, 64), 14), (slice(64, 128), 15)):
                    step(dve.memset(keep[half, 0:own - 1], 1.0), forced)
                    step(dve.memset(keep[half, own - 1:32], 0.0), forced)
                    step(dve.memset(force[half, 0:own - 1], 0.0), forced)
                    step(dve.memset(force[half, own - 1:own + 1], FORCE), forced)
                    step(dve.memset(force[half, own + 1:32], NEG), forced)
                dve.wait_ge(loaded, 48)
                dve.tensor_scalar(gq[:, :], gq[:, :], HD ** -0.5, None, ALU.mult).then_inc(scaled, 1)
        clear_signals(nc, setup)

        names = signals(nc, c, "z_loaded normed kn_ready mean_made rms_made v_copied gates_made qk_transposed q_copied "
                               "keys_copied c_summed c_shifted c_exp c_ready c_transposed c_copied c_pv c_out chain "
                               "masks_ready stored o_T")
        (z_loaded, normed, kn_ready, mean_made, rms_made, v_copied, gates_made, qk_transposed, q_copied, keys_copied,
         c_summed, c_shifted, c_exp, c_ready, c_transposed, c_copied, c_pv, c_out, chain, masks_ready, stored,
         o_T) = names

        with nc.Fori(0, TILES) as t:
            units = []
            for h in range(NH):
                cols = slice((h // GQA) * HD, (h // GQA + 1) * HD)
                units.append((qTz[:, h, :], [(KsT[:, 0:512], 512), (KsT[:, 512:1024], 512)], smask[h // GQA][:, :],
                              t * P, h, [Vs[:, j, cols] for j in range(TILES)], NH + h))
                units.append((qTz[:, h, :], [(KwT[:, bass.ds(t * P, 512)], 512), (KwT[:, bass.ds(t * P + 512, P)], P)],
                              wmask[:, :], WINDOW, h, [Vw[:, t + j, cols] for j in range(WW // P)], 2 * NH + h))
            rows = bass.ds(t * P, P)
            with nc.Block() as block:

                @block.sync
                def _(sp):
                    sp.dma_start(zt[:, :], z[bass.ds(t * P + LEAD, P), ZQ:P_ODD]).then_inc(z_loaded, 16)
                    sp.wait_ge(z_loaded, 16)
                    sp.dma_start(cmp_out[rows, :], zt[:, O_KVC - ZQ:O_KVS - ZQ]).then_inc(stored, 16)
                    sp.dma_start(slc_out[rows, KVW:A_KV], zt[:, O_KVS - ZQ + KVW:O_KVW - ZQ]).then_inc(stored, 16)
                    sp.dma_start(G["win_rows"][rows, KVW:A_KV], zt[:, O_KVW - ZQ + KVW:O_G - ZQ]).then_inc(stored, 16)
                    sp.wait_ge(kn_ready, 1)
                    sp.dma_start(slc_out[rows, 0:KVW], qn[:, 4, :, :].rearrange("p a d -> p (a d)")).then_inc(stored, 16)
                    sp.dma_start(G["win_rows"][rows, 0:KVW], qn[:, 5, :, :].rearrange("p a d -> p (a d)"))\
                      .then_inc(stored, 16)
                    sp.wait_ge(stored, 80)

                @block.scalar
                def _(act):
                    act.wait_ge(z_loaded, 16)
                    act.activation(gates[:, :], zt[:, O_G - ZQ:P_ODD - ZQ], ACT.Sigmoid).then_inc(gates_made, 1)
                    act.copy(Vs[:, t, :], zt[:, O_KVS - ZQ + KVW:O_KVW - ZQ]).then_inc(v_copied, 1)
                    act.copy(Vw[:, t + WINDOW // P, :], zt[:, O_KVW - ZQ + KVW:O_G - ZQ]).then_inc(v_copied, 1)
                    act.wait_ge(mean_made, 1)
                    act.activation(rms[:, 1, :], rms[:, 0, :], ACT.Sqrt).then_inc(rms_made, 1)
                    act.wait_ge(qk_transposed, 1)
                    act.copy(KsT[:, rows], t_ps[:, 4, :]).then_inc(keys_copied, 1)
                    act.copy(KwT[:, bass.ds(t * P + WINDOW, P)], t_ps[:, 5, :]).then_inc(keys_copied, 1)
                    act.wait_ge(c_shifted, 1)
                    act.activation(pc[:, :, :], pc[:, :, :], ACT.Exp).then_inc(c_exp, 1)
                    act.wait_ge(c_transposed, 1)
                    act.copy(pcT[:, :, :], t_ps[:, 6:8, :]).then_inc(c_copied, 1)
                    att.scalar(act, units)

                @block.tensor
                def _(pe):
                    pe.wait_ge(kn_ready, 1)
                    for g in range(6):
                        last = pe.transpose(t_ps[:, g, :], qn[:, g, :, :].rearrange("p a d -> p (a d)"), ident[:, :])
                    last.then_inc(qk_transposed, 1)
                    pe.wait_ge(q_copied, 2)
                    for h in range(NH):
                        last = pe.matmul(lg_ps[0][:, h * NCMP:(h + 1) * NCMP], qTz[:, h, :], C.KT[:, 0, :],
                                         start=True, stop=True)
                    last.then_inc(c_summed, 1)
                    pe.wait_ge(c_ready, 1)
                    pe.wait_ge(keys_copied, 2)
                    for a in range(2):
                        last = pe.transpose(t_ps[:, 6 + a, :],
                                            pc[:, 4 * a:4 * a + 4, :].rearrange("p h n -> p (h n)"), ident[:, :])
                    last.then_inc(c_transposed, 1)
                    pe.wait_ge(c_copied, 1)
                    for i in range(4):
                        part = slice(i * NCMP, (i + 1) * NCMP)
                        for a in range(2):
                            at = (i % 2) * 512 + a * HD
                            last = pe.matmul(lg_ps[i // 2][:, at:at + HD], pcT[part, a, :],
                                             C.V4[part, a * HD:(a + 1) * HD], start=True, stop=True)
                    last.then_inc(c_pv, 1)
                    pe.wait_ge(c_out, NH)
                    pe.wait_ge(v_copied, 2)
                    att.tensor(pe, units, ident)
                    pe.wait_ge(att.o_scaled, 2 * NH)
                    for k in range(4):
                        last = pe.transpose(t_ps[:, k, :], o[:, 2 * k:2 * k + 2, :].rearrange("p h d -> p (h d)"),
                                            ident[:, :])
                    last.then_inc(o_T, 1)

                @block.vector
                def _(dve):
                    step = InOrder(dve)
                    dve.wait_ge(z_loaded, 16)
                    q3 = zt[:, 0:A_Q].rearrange("p (h d) -> p h d", d=HD)
                    ks3 = zt[:, O_KVS - ZQ:O_KVS - ZQ + KVW].rearrange("p (h d) -> p h d", d=HD)
                    kw3 = zt[:, O_KVW - ZQ:O_KVW - ZQ + KVW].rearrange("p (h d) -> p h d", d=HD)
                    step(dve.tensor_tensor(sq[:, 0:NH, :], q3, q3, ALU.mult), normed)
                    step(dve.tensor_tensor(sq[:, NH:NH + 2, :], ks3, ks3, ALU.mult), normed)
                    step(dve.tensor_tensor(sq[:, NH + 2:NH + 4, :], kw3, kw3, ALU.mult), normed)
                    step(dve.tensor_reduce(rms[:, 0, :], sq[:, :, :], AX.X, ALU.add), normed)
                    step(dve.tensor_scalar(rms[:, 0, :], rms[:, 0, :], 1.0 / HD, RMS_EPS, ALU.mult, ALU.add),
                         mean_made)
                    dve.wait_ge(rms_made, 1)
                    step(dve.reciprocal(rms[:, 2, :], rms[:, 1, :]), normed)
                    for kv in range(NKV):
                        cols = slice(kv * GQA * HD, (kv + 1) * GQA * HD)
                        r = rms[:, 2, kv * GQA:(kv + 1) * GQA].unsqueeze(2).broadcast_to([P, GQA, HD])
                        step(dve.tensor_tensor(qn[:, 0:GQA, kv, :], zt[:, cols].rearrange("p (g d) -> p g d", d=HD),
                                               r, ALU.mult), normed)
                        step(dve.tensor_tensor(qn[:, 0:GQA, kv, :], qn[:, 0:GQA, kv, :],
                                               gq[:, :].unsqueeze(1).broadcast_to([P, GQA, HD]), ALU.mult), normed)
                    for i, k3 in enumerate((ks3, kw3)):
                        r = rms[:, 2, NH + 2 * i:NH + 2 * i + 2].unsqueeze(2).broadcast_to([P, NKV, HD])
                        step(dve.tensor_tensor(qn[:, GQA + i, :, :], k3, r, ALU.mult), normed)
                        step(dve.tensor_tensor(qn[:, GQA + i, :, :], qn[:, GQA + i, :, :],
                                               gk[:, i, :].unsqueeze(1).broadcast_to([P, NKV, HD]), ALU.mult),
                             normed if i == 0 else kn_ready)
                    dve.wait_ge(qk_transposed, 1)
                    for kv in range(NKV):
                        half = slice(kv * HD, (kv + 1) * HD)
                        step(dve.tensor_copy(qTz[half, kv * GQA:(kv + 1) * GQA, :], t_ps[half, 0:GQA, :]), q_copied)
                    full = [P, NH, NCMP]
                    dve.wait_ge(c_summed, 1)
                    step(dve.tensor_tensor(pc[:, :, :], lg_ps[0][:, 0:NH * NCMP].rearrange("p (h n) -> p h n", h=NH),
                                           cmp_bias[:, :, bass.ds(28 - 4 * t, NCMP)], ALU.add), chain)
                    step(dve.tensor_reduce(cst[:, 0, :], pc[:, :, :], AX.X, ALU.max), chain)
                    step(dve.tensor_tensor(pc[:, :, :], pc[:, :, :], cst[:, 0, :].unsqueeze(2).broadcast_to(full),
                                           ALU.subtract), c_shifted)
                    dve.wait_ge(c_exp, 1)
                    step(dve.tensor_reduce(cst[:, 1, :], pc[:, :, :], AX.X, ALU.add), chain)
                    step(dve.reciprocal(cst[:, 2, :], cst[:, 1, :]), chain)
                    step(dve.tensor_tensor(pc[:, :, :], pc[:, :, :], cst[:, 2, :].unsqueeze(2).broadcast_to(full),
                                           ALU.mult), chain)
                    step(dve.tensor_tensor(pc[:, :, :], pc[:, :, :],
                                           vis[:, bass.ds(28 - 4 * t, NCMP)].unsqueeze(1).broadcast_to(full), ALU.mult),
                         c_ready)
                    p4 = pc[:, :, :].rearrange("p (k g) n -> p k g n", g=GQA)
                    step(dve.tensor_tensor(ps[:, :, :], p4[:, :, 0, :], p4[:, :, 1, :], ALU.add), chain)
                    for g in range(2, GQA):
                        step(dve.tensor_tensor(ps[:, :, :], ps[:, :, :], p4[:, :, g, :], ALU.add), chain)
                    pair = ps[:, :, :].rearrange("p k (n two) -> p k n two", two=2)
                    step(dve.tensor_tensor(score[:, :, :], pair[:, :, :, 0], pair[:, :, :, 1], ALU.add), chain)
                    sl = bass.ds(14 - 2 * t, NSEL)
                    wide = [P, NKV, NSEL]
                    step(dve.tensor_tensor(score[:, :, :], score[:, :, :], keep[:, sl].unsqueeze(1).broadcast_to(wide),
                                           ALU.mult), chain)
                    step(dve.tensor_tensor(score[:, :, :], score[:, :, :], force[:, sl].unsqueeze(1).broadcast_to(wide),
                                           ALU.add), chain)
                    step(dve.memset(score[:, :, 0:1], FORCE), chain)
                    for kv in range(NKV):
                        step(dve.max(top8[:, :], score[:, kv, :]), chain)
                        step(dve.match_replace(score[:, kv, :], top8[:, :], score[:, kv, :], TAKEN), chain)
                    step(dve.tensor_scalar(score[:, :, :], score[:, :, :], TAKEN / 2, NEG, ALU.is_gt, ALU.mult), chain)
                    causal = far_mask[:, bass.ds(896 - t * P, SEQ)].rearrange("p (n s) -> p n s", s=SEL)
                    for kv in range(NKV):
                        step(dve.tensor_tensor(smask[kv][:, :].rearrange("p (n s) -> p n s", s=SEL), causal,
                                               score[:, kv, :].unsqueeze(2).broadcast_to([P, NSEL, SEL]), ALU.add),
                             masks_ready)
                    step(dve.tensor_tensor(wmask[:, :], win_bank[:, :], pad_bank[:, bass.ds(t * P, WW)], ALU.add),
                         masks_ready)
                    dve.wait_ge(c_pv, 1)
                    dve.wait_ge(gates_made, 1)
                    for h in range(NH):
                        a, i = h // 4, h % 4
                        at = (i % 2) * 512 + a * HD
                        step(dve.tensor_scalar(o[:, h, :], lg_ps[i // 2][:, at:at + HD], gates[:, h:h + 1], None,
                                               ALU.mult), c_out)
                    att.vector(dve, step, units, near, o, gates)
                    dve.wait_ge(o_T, 1)
                    dve.tensor_copy(featT[:, 4:8, rows], t_ps[:, 0:4, :])
            clear_signals(nc, names + att.sems)

        (copied,) = tail = signals(nc, c, "win_copied")
        with nc.Block() as block:

            @block.sync
            def _(sp):
                sp.dma_start(win_out, G["win_rows"][SEQ - WINDOW:SEQ, :]).then_inc(copied, 16)
                sp.wait_ge(copied, 16)
        clear_signals(nc, tail)


def stage_nsa_sample(nc, G, C):
    ident, z, row_bias = G["ident"], G["z_odd"], G["row_bias"]
    cmp_out = G["d_cmp_s"][0].rearrange("b one two kv d -> b (one two kv d)")
    slc_out = G["d_slc_s"][0].rearrange("b one two kv d -> b (one two kv d)")
    win_out = G["d_win_s"][0].rearrange("b s two kv d -> b s (two kv d)")
    win_in = G["cache_d_win"][0].rearrange("b s two kv d -> b s (two kv d)")
    slc_cache = G["cache_d_slc"][0].rearrange("n s two kv d -> n s (two kv d)")
    R = NB * NH
    G2 = NB * NKV
    NS = NSEL + 1
    with ExitStack() as c:
        st = SampleState(nc, c)
        QzAll = st.Qz

        with ExitStack() as c2:
            zs = tile_of(nc, c2, "s_z", [NB, P_ODD - ZQ])
            gq = tile_of(nc, c2, "s_gq", [NB, HD])
            gk = tile_of(nc, c2, "s_gk", [NB, 2, HD])
            qn = tile_of(nc, c2, "s_qn", [NB, 6, NKV, HD])
            sq = tile_of(nc, c2, "s_sq", [NB, 12, HD])
            rms = tile_of(nc, c2, "s_rms", [NB, 3, 12])
            expand = tile_of(nc, c2, "s_expand16", [G2, R])
            cbias_rows = tile_of(nc, c2, "s_cbias_rows", [R, NCMP])
            cbias = tile_of(nc, c2, "s_cbias", [G2, GQA, NCMP])
            lc8 = tile_of(nc, c2, "s_lc8", [NH, NB, NCMP])
            lc = tile_of(nc, c2, "s_lc", [G2, GQA, NCMP])
            lcT = tile_of(nc, c2, "s_lcT", [NCMP, NB, NKV, GQA])
            cs = tile_of(nc, c2, "s_cs", [G2, 3, GQA])
            cgate = tile_of(nc, c2, "s_cgate", [G2, GQA])
            ps = tile_of(nc, c2, "s_ps", [G2, NCMP])
            score = tile_of(nc, c2, "s_sscore", [G2, NS])
            top8 = tile_of(nc, c2, "s_stop8", [G2, 8])
            m17 = tile_of(nc, c2, "s_m17", [R, NS])
            t_ps = bank_of(nc, c2, "n_prep_ps", [P, 6, NB])
            c_ps = bank_of(nc, c2, "n_c_ps", [NH, NB * NCMP])
            pT_ps = bank_of(nc, c2, "n_pT_ps", [NCMP, GQA, G2])
            o_ps = bank_of(nc, c2, "n_o_ps", [P, R])
            m_ps = bank_of(nc, c2, "n_m_ps", [R, NS])
            names = signals(nc, c2, "z_loaded w_loaded cleared cut1 expand_made normed mean_made rms_made kn_ready "
                                    "transposed q_ready c_summed c_copied bias_copied bounced c_loaded c_shifted c_exp "
                                    "c_ready c_T c_Tcopied c_pv m_made m_spread chain stored gates_loaded gates_made")
            (z_loaded, w_loaded, cleared, cut1, expand_made, normed, mean_made, rms_made, kn_ready, transposed, q_ready,
             c_summed, c_copied, bias_copied, bounced, c_loaded, c_shifted, c_exp, c_ready, c_T, c_Tcopied, c_pv,
             m_made, m_spread, chain, stored, gates_loaded, gates_made) = names
            with nc.Block() as block:

                @block.sync
                def _(sp):
                    sp.dma_start(zs[:, :], z[Z_S:Z_S + NB, ZQ:P_ODD]).then_inc(z_loaded, 16)
                    for i, col in enumerate((O_KVS + KVW, O_KVW + KVW)):
                        sp.dma_start(st.Vn[0:1, i, :, :], z[Z_S:Z_S + NB, col:col + KVW].unsqueeze(0))\
                          .then_inc(z_loaded, 16)
                    sp.dma_start(gq[:, :], G["d_q_norm"][0].partition_broadcast(NB)).then_inc(w_loaded, 16)
                    for i in range(2):
                        sp.dma_start(gk[:, i, :], G["d_k_norm"][0, 1 + i].partition_broadcast(NB)).then_inc(w_loaded, 16)
                    for b in range(NB):
                        g = z[Z_S + b, O_G:P_ODD].rearrange("(r h) -> h r", h=NH)
                        sp.dma_start(st.scale[b * NH:(b + 1) * NH, :], g, allow_slow_non_contiguous=True)\
                          .then_inc(gates_loaded, 16)
                        sp.dma_start(cgate[b * NKV:(b + 1) * NKV, :], z[Z_S + b, O_G:O_G + NH]
                                     .rearrange("(k g) -> k g", g=GQA)).then_inc(gates_loaded, 16)
                    sp.dma_start(win_out[:, 0:WINDOW - 1, :], win_in[:, 1:WINDOW, :]).then_inc(stored, 16)
                    sp.wait_ge(z_loaded, 48)
                    sp.dma_start(cmp_out, zs[:, O_KVC - ZQ:O_KVS - ZQ]).then_inc(stored, 16)
                    sp.dma_start(slc_out[:, KVW:A_KV], zs[:, O_KVS - ZQ + KVW:O_KVW - ZQ]).then_inc(stored, 16)
                    sp.dma_start(win_out[:, WINDOW - 1, KVW:A_KV], zs[:, O_KVW - ZQ + KVW:O_G - ZQ]).then_inc(stored, 16)
                    sp.wait_ge(kn_ready, 1)
                    sp.dma_start(slc_out[:, 0:KVW], qn[:, 4, :, :].rearrange("p a d -> p (a d)")).then_inc(stored, 16)
                    sp.dma_start(win_out[:, WINDOW - 1, 0:KVW], qn[:, 5, :, :].rearrange("p a d -> p (a d)"))\
                      .then_inc(stored, 16)
                    sp.wait_ge(bias_copied, 1)
                    sp.dma_start(G["s_cbias_d"], cbias_rows[:, :]).then_inc(bounced, 16)
                    sp.wait_ge(c_copied, 1)
                    sp.dma_start(G["s_lc_d"].rearrange("b h n -> h b n"), lc8[:, :, :]).then_inc(bounced, 16)
                    sp.wait_ge(bounced, 32)
                    sp.dma_start(cbias[:, :, :], G["s_cbias_d"].rearrange("(r g) n -> r g n", g=GQA)).then_inc(c_loaded, 16)
                    sp.dma_start(lc[:, :, :], G["s_lc_d"].rearrange("b (k g) n -> (b k) g n", g=GQA)).then_inc(c_loaded, 16)
                    sp.wait_ge(stored, 96)

                @block.gpsimd
                def _(pool):
                    step = InOrder(pool)
                    pool.memset(st.mask[:, :], 0.0).then_inc(cleared, 1)
                    pool.memset(st.Qz[:, :, :], 0.0).then_inc(cleared, 1)
                    pool.memset(expand[:, :], 1.0).then_inc(cleared, 1)
                    pool.wait_ge(cleared, 3)
                    step(pool.affine_select(out=expand[:, :], in_=expand[:, :], compare_op=ALU.is_ge, fill=0.0,
                                            base=0, pattern=[[1, R]], channel_multiplier=-GQA), cut1)
                    step(pool.affine_select(out=expand[:, :], in_=expand[:, :], compare_op=ALU.is_ge, fill=0.0,
                                            base=GQA - 1, pattern=[[-1, R]], channel_multiplier=GQA), expand_made)

                @block.scalar
                def _(act):
                    act.copy(cbias_rows[:, :], row_bias[:, CMP - 1:PAST:CMP]).then_inc(bias_copied, 1)
                    act.wait_ge(gates_loaded, 16 * 2 * NB)
                    act.activation(st.scale[:, :], st.scale[:, :], ACT.Sigmoid).then_inc(gates_made, 1)
                    act.activation(cgate[:, :], cgate[:, :], ACT.Sigmoid).then_inc(gates_made, 1)
                    act.wait_ge(mean_made, 1)
                    act.activation(rms[:, 1, :], rms[:, 0, :], ACT.Sqrt).then_inc(rms_made, 1)
                    act.wait_ge(c_shifted, 1)
                    act.activation(lc[:, :, :], lc[:, :, :], ACT.Exp).then_inc(c_exp, 1)

                @block.tensor
                def _(pe):
                    pe.wait_ge(kn_ready, 1)
                    for g in range(6):
                        last = pe.transpose(t_ps[:, g, :], qn[:, g, :, :].rearrange("p a d -> p (a d)"), ident[0:NB, 0:NB])
                    last.then_inc(transposed, 1)
                    pe.wait_ge(q_ready, 4)
                    for b in range(NB):
                        last = pe.matmul(c_ps[:, b * NCMP:(b + 1) * NCMP], QzAll[:, b, :], C.KT[:, 1 + b, :],
                                         start=True, stop=True)
                    last.then_inc(c_summed, 1)
                    pe.wait_ge(c_ready, 1)
                    for g in range(GQA):
                        last = pe.transpose(pT_ps[:, g, :], lc[:, g, :], ident[0:G2, 0:G2])
                    last.then_inc(c_T, 1)
                    pe.wait_ge(c_Tcopied, 1)
                    for b in range(NB):
                        last = pe.matmul(o_ps[:, b * NH:(b + 1) * NH], C.V[:, 1 + b, :],
                                         lcT[:, b, :, :].rearrange("n k g -> n (k g)"), start=True, stop=True)
                    last.then_inc(c_pv, 1)
                    pe.wait_ge(m_made, 1)
                    pe.wait_ge(expand_made, 1)
                    pe.matmul(m_ps[:, :], expand[:, :], score[:, :], start=True, stop=True).then_inc(m_spread, 1)

                @block.vector
                def _(dve):
                    step = InOrder(dve)
                    dve.wait_ge(z_loaded, 48)
                    dve.wait_ge(w_loaded, 48)
                    step(dve.tensor_scalar(gq[:, :], gq[:, :], HD ** -0.5, None, ALU.mult), normed)
                    q3 = zs[:, 0:A_Q].rearrange("p (h d) -> p h d", d=HD)
                    ks3 = zs[:, O_KVS - ZQ:O_KVS - ZQ + KVW].rearrange("p (h d) -> p h d", d=HD)
                    kw3 = zs[:, O_KVW - ZQ:O_KVW - ZQ + KVW].rearrange("p (h d) -> p h d", d=HD)
                    step(dve.tensor_tensor(sq[:, 0:NH, :], q3, q3, ALU.mult), normed)
                    step(dve.tensor_tensor(sq[:, NH:NH + 2, :], ks3, ks3, ALU.mult), normed)
                    step(dve.tensor_tensor(sq[:, NH + 2:NH + 4, :], kw3, kw3, ALU.mult), normed)
                    step(dve.tensor_reduce(rms[:, 0, :], sq[:, :, :], AX.X, ALU.add), normed)
                    step(dve.tensor_scalar(rms[:, 0, :], rms[:, 0, :], 1.0 / HD, RMS_EPS, ALU.mult, ALU.add),
                         mean_made)
                    dve.wait_ge(rms_made, 1)
                    step(dve.reciprocal(rms[:, 2, :], rms[:, 1, :]), normed)
                    for kv in range(NKV):
                        cols = slice(kv * GQA * HD, (kv + 1) * GQA * HD)
                        r = rms[:, 2, kv * GQA:(kv + 1) * GQA].unsqueeze(2).broadcast_to([NB, GQA, HD])
                        step(dve.tensor_tensor(qn[:, 0:GQA, kv, :], zs[:, cols].rearrange("p (g d) -> p g d", d=HD),
                                               r, ALU.mult), normed)
                        step(dve.tensor_tensor(qn[:, 0:GQA, kv, :], qn[:, 0:GQA, kv, :],
                                               gq[:, :].unsqueeze(1).broadcast_to([NB, GQA, HD]), ALU.mult), normed)
                    for i, k3 in enumerate((ks3, kw3)):
                        r = rms[:, 2, NH + 2 * i:NH + 2 * i + 2].unsqueeze(2).broadcast_to([NB, NKV, HD])
                        step(dve.tensor_tensor(qn[:, GQA + i, :, :], k3, r, ALU.mult), normed)
                        step(dve.tensor_tensor(qn[:, GQA + i, :, :], qn[:, GQA + i, :, :],
                                               gk[:, i, :].unsqueeze(1).broadcast_to([NB, NKV, HD]), ALU.mult),
                             normed if i == 0 else kn_ready)
                    dve.wait_ge(transposed, 1)
                    dve.wait_ge(cleared, 3)
                    for kv in range(NKV):
                        half = slice(kv * HD, (kv + 1) * HD)
                        step(dve.tensor_copy(st.Qz[half, :, kv * GQA:(kv + 1) * GQA],
                                             t_ps[half, 0:GQA, :].rearrange("p g b -> p b g")), q_ready)
                    for i in range(2):
                        step(dve.tensor_copy(st.KnT[:, i, :], t_ps[:, 4 + i, :]), q_ready)
                    dve.wait_ge(c_summed, 1)
                    step(dve.tensor_copy(lc8[:, :, :].rearrange("h b n -> h (b n)"), c_ps[:, :]), c_copied)
                    full = [G2, GQA, NCMP]
                    dve.wait_ge(c_loaded, 32)
                    step(dve.tensor_tensor(lc[:, :, :], lc[:, :, :], cbias[:, :, :], ALU.add), chain)
                    step(dve.tensor_reduce(cs[:, 0, :], lc[:, :, :], AX.X, ALU.max), chain)
                    step(dve.tensor_tensor(lc[:, :, :], lc[:, :, :], cs[:, 0, :].unsqueeze(2).broadcast_to(full),
                                           ALU.subtract), c_shifted)
                    dve.wait_ge(c_exp, 1)
                    step(dve.tensor_reduce(cs[:, 1, :], lc[:, :, :], AX.X, ALU.add), chain)
                    step(dve.reciprocal(cs[:, 2, :], cs[:, 1, :]), chain)
                    step(dve.tensor_tensor(lc[:, :, :], lc[:, :, :], cs[:, 2, :].unsqueeze(2).broadcast_to(full),
                                           ALU.mult), chain)
                    step(dve.tensor_tensor(ps[:, :], lc[:, 0, :], lc[:, 1, :], ALU.add), chain)
                    for g in range(2, GQA):
                        step(dve.tensor_tensor(ps[:, :], ps[:, :], lc[:, g, :], ALU.add), chain)
                    dve.wait_ge(gates_made, 2)
                    step(dve.tensor_tensor(lc[:, :, :], lc[:, :, :], cgate[:, :].unsqueeze(2).broadcast_to(full),
                                           ALU.mult), c_ready)
                    pair = ps[:, :].rearrange("p (n two) -> p n two", two=2)
                    step(dve.tensor_tensor(score[:, 0:NSEL], pair[:, :, 0], pair[:, :, 1], ALU.add), chain)
                    step(dve.memset(score[:, 0:1], FORCE), chain)
                    step(dve.memset(score[:, NSEL - 1:NS], FORCE), chain)
                    step(dve.max(top8[:, :], score[:, :]), chain)
                    step(dve.match_replace(score[:, :], top8[:, :], score[:, :], TAKEN), chain)
                    step(dve.tensor_scalar(score[:, :], score[:, :], TAKEN / 2, NEG, ALU.is_gt, ALU.mult), m_made)
                    dve.wait_ge(c_T, 1)
                    for g in range(GQA):
                        step(dve.tensor_copy(lcT[:, :, :, g], pT_ps[:, g, :].rearrange("n (b k) -> n b k", k=NKV)),
                             chain if g < GQA - 1 else c_Tcopied)
                    dve.wait_ge(c_pv, 1)
                    step(dve.tensor_copy(st.oT[:, :], o_ps[:, :]), chain)
                    dve.wait_ge(m_spread, 1)
                    step(dve.tensor_copy(m17[:, :], m_ps[:, :]), chain)
                    step(dve.tensor_tensor(st.mask[:, 0:PAST].rearrange("p (n s) -> p n s", s=SEL),
                                           st.mask[:, 0:PAST].rearrange("p (n s) -> p n s", s=SEL),
                                           m17[:, 0:NSEL].unsqueeze(2).broadcast_to([R, NSEL, SEL]), ALU.add), chain)
                    step(dve.tensor_copy(st.mask[:, PAST:PAST + 1], m17[:, NSEL:NS]), chain)
            clear_signals(nc, names)

        V = tile_of(nc, c, "s_V", [P, NB * PAGES, P])

        def load_selected(sp, b, K, V, Ki, keys_loaded, kidx_loaded):
            page_loads(sp, G, b, slc_cache, [
                (lambda j: K[:, j, :], lambda page: slc_cache[page, :, 0:KVW], keys_loaded),
                (lambda j: V[:, bass.ds(b * PAGES + j, 1), :],
                 lambda page: slc_cache[page, :, KVW:A_KV].unsqueeze(1), keys_loaded),
            ])

        sample_logits(nc, G, st, "slc", load_selected, PAGES, 0, V)
        sample_attend(nc, G, st, PAGES, 0, V, 0, 1, True)

        NW = WINDOW // P
        (cleared,) = sems = signals(nc, c, "mask_cleared")
        with nc.Block() as block:

            @block.vector
            def _(dve):
                step = InOrder(dve)
                step(dve.memset(st.mask[:, PAST - WINDOW:PAST + 1], 0.0), cleared)
                step(dve.memset(st.mask[:, PAST - WINDOW:PAST - WINDOW + 1], NEG), cleared)
        clear_signals(nc, sems)

        def load_window(sp, b, K, V, Ki, keys_loaded, kidx_loaded):
            for j in range(NW):
                rows = slice(j * P, (j + 1) * P)
                sp.dma_start(K[:, j, :], win_in[b, rows, 0:KVW]).then_inc(keys_loaded, 16)
                sp.dma_start(V[:, bass.ds(b * NW + j, 1), :], win_in[b, rows, KVW:A_KV].unsqueeze(1))\
                  .then_inc(keys_loaded, 16)

        sample_logits(nc, G, st, "win", load_window, NW, 1, V)
        sample_attend(nc, G, st, NW, 1, V, PAST - WINDOW, 2, True)

        sample_concat(nc, G, st, "odd")


def stage_outputs(nc, G):
    with ExitStack() as c:
        (stored,) = signals(nc, c, "y_stored")
        with nc.Block() as block:

            @block.sync
            def _(sp):
                sp.dma_start(G["y_prompt"][0].rearrange("(t p) d -> p t d", p=P), G["x"][:, 0:TILES, :])\
                  .then_inc(stored, 16)
                sp.dma_start(G["y_sample"][:, 0, :], G["x"][0:NB, TILES, :]).then_inc(stored, 16)
                sp.wait_ge(stored, 32)


def build_program(nc, dram):
    G = dict(dram)

    def scratch(name, shape, dt=F32):
        G[name] = nc.dram_tensor(name, shape, dt).ap()

    scratch("mod", [1 + NB, DEPTH, 6 * D])
    scratch("z_even", [LEAD + TOK, P_EVEN])
    scratch("z_odd", [LEAD + TOK, P_ODD])
    scratch("s_logits", [NB * NH, PAST + 1])
    scratch("s_rel", [NB, IDXH, PAST + 1])
    scratch("s_rows", [NB * NH, P])
    scratch("s_rq", [NB, 7, RW])
    scratch("s_rows_c", [NB * NH, HD])
    scratch("s_cbias_d", [NB * NH, NCMP])
    scratch("s_lc_d", [NB, NH, NCMP])
    scratch("win_rows", [SEQ, A_KV])
    scratch("h_rows", [TOK, D])
    scratch("slot_token", [P * BLOCKS, 1], I32)
    scratch("block_expert", [1, BLOCKS], I32)
    scratch("y_slots", [P * BLOCKS, D])
    with ExitStack() as c:
        G["ident"] = tile_of(nc, c, "ident", [P, P])
        G["ones"] = tile_of(nc, c, "ones", [P, P])
        G["x"] = tile_of(nc, c, "x", [P, TILES + 1, D])
        with ExitStack() as c2:
            G["featT"] = tile_of(nc, c2, "featT", [P, KC, TOK])
            stage_constants(nc, G)
            stage_ada(nc, G)
            stage_modulate(nc, G, 0, G["g_norm_mix"][0], 0)
            stage_project(nc, G, G["e_w_in"][0], P_EVEN, G["z_even"][LEAD:Z_S], G["z_even"][Z_S:Z_S + NB])
            with ExitStack() as c3:
                alloc_banks(nc, c3, G)
                stage_banks(nc, G)
                stage_even_prompt(nc, G)
                stage_even_sample(nc, G)
            stage_residual_project(nc, G, 0, G["e_w_out"][0], 2)
        moe_sublayer(nc, G, 0)
        with ExitStack() as c2:
            G["featT"] = tile_of(nc, c2, "featT", [P, KC, TOK])
            stage_modulate(nc, G, 1, G["g_norm_mix"][1], 0)
            stage_project(nc, G, G["o_w_in"][0], P_ODD, G["z_odd"][LEAD:Z_S], G["z_odd"][Z_S:Z_S + NB])
            stage_rwkv_prompt(nc, G)
            stage_rwkv_sample(nc, G)
            with ExitStack() as c3:
                alloc_banks(nc, c3, G)
                G["cmp_bias"] = tile_of(nc, c3, "cmp_bias", [P, NH, 64])
                stage_banks(nc, G, G["cmp_bias"])
                C = Compressed(nc, c3)
                stage_compress(nc, G, C)
                stage_nsa_prompt(nc, G, C)
                stage_nsa_sample(nc, G, C)
            stage_residual_project(nc, G, 1, G["o_w_out"][0], 2)
        moe_sublayer(nc, G, 1)
        stage_outputs(nc, G)


_OUTS = [
    ("y_prompt", (1, SEQ, D)), ("y_sample", (NB, 1, D)),
    ("a_kv_p", (1, 1, SEQ, 2, NKV, HD)), ("a_kidx_p", (1, 1, SEQ, HD)), ("b_conv_p", (1, 1, 2, CONV)),
    ("c_wkv_p", (1, 1, NH, HD, HD)), ("c_shift_p", (1, 1, P_C)), ("d_cmp_p", (1, 1, SEQ, 2, NKV, HD)),
    ("d_slc_p", (1, 1, SEQ, 2, NKV, HD)), ("d_win_p", (1, 1, WINDOW, 2, NKV, HD)),
    ("a_kv_s", (1, NB, 1, 2, NKV, HD)), ("a_kidx_s", (1, NB, 1, HD)), ("b_conv_s", (1, NB, 2, CONV)),
    ("c_wkv_s", (1, NB, NH, HD, HD)), ("c_shift_s", (1, NB, P_C)), ("d_cmp_s", (1, NB, 1, 2, NKV, HD)),
    ("d_slc_s", (1, NB, 1, 2, NKV, HD)), ("d_win_s", (1, NB, WINDOW, 2, NKV, HD)),
]


def kernel(**inputs):
    import concourse.bacc as bacc
    from concourse.bass_utils import run_bass_kernel_spmd

    nc = bacc.Bacc("TRN2", target_bir_lowering=False, num_devices=1)
    given = dict(inputs)
    given["t5_onehot"] = t5_onehot()
    given["t5_onehot_rev"] = np.ascontiguousarray(given["t5_onehot"][:, OH0:OH0 + PAST + 1][:, ::-1])
    arrays, dram = {}, {}
    for name in given:
        a = np.ascontiguousarray(given[name])
        arrays[f"in_{name}"] = a
        dram[name] = nc.dram_tensor(f"in_{name}", a.shape, mybir.dt.from_np(a.dtype), kind="ExternalInput").ap()
    for name, shape in _OUTS:
        dram[name] = nc.dram_tensor(f"out_{name}", shape, F32, kind="ExternalOutput").ap()
    build_program(nc, dram)
    result = run_bass_kernel_spmd(nc, [arrays], core_ids=[0]).results[0]
    return tuple(result[f"out_{name}"] for name, _ in _OUTS)
```

```python
from contextlib import ExitStack

import numpy as np

import concourse.bass as bass
from concourse import mybir

F32 = mybir.dt.float32
U32 = mybir.dt.uint32
I32 = mybir.dt.int32
ALU = mybir.AluOpType
ACT = mybir.ActivationFunctionType
AX = mybir.AxisListType

P = 128
D = 1024
SEQ = 1024
DEPTH = 2
NB = 8
TILES = SEQ // P
TOK = SEQ + NB
KC = D // P
HD = 64
NH = 8
NKV = 2
GQA = NH // NKV
PAST = 1024
PAGE = 128
PAGES = PAST // PAGE
A_Q = NH * HD
KVW = NKV * HD
A_KV = 2 * KVW
IDXH = 4
TOPK = 256
CONV = 512
P_EVEN = A_Q + A_KV + IDXH * HD + HD + IDXH + 3 * CONV
RW = 512
P_C = 3 * RW + 64 + 64 + 128
P_ODD = P_C + A_Q + 3 * A_KV + 3 * NH
CMP = 32
NCMP = SEQ // CMP
SEL = 64
NSEL = SEQ // SEL
WINDOW = 512
NBUCK = 32
NEXP = 16
NGRP = 4
DEXP = 512
ROUTE_BLOCK = 128
RMS_EPS = 1e-6
GN_EPS = 64e-5
NEG = -1e30
FORCE = 1e9
TAKEN = -3e38
CH = 32

E_Q, E_K, E_V, E_QI, E_KI, E_WI = 0, 512, 640, 768, 1024, 1088
E_BG, E_CG, E_XIN = 1092, 1604, 2116
O_R, O_K, O_V, O_WD, O_AD, O_GD = 0, 512, 1024, 1536, 1600, 1664
O_Q, O_KVC, O_KVS, O_KVW, O_G = 1792, 2304, 2560, 2816, 3072

LEAD = 2
Z_S = LEAD + SEQ

OH0 = 1280
OH_W = OH0 + 1280


def t5_onehot():
    dist = np.maximum(np.arange(OH_W) - OH0, 0)
    exact = NBUCK // 2
    far = exact + (np.log(np.maximum(dist, 1).astype(np.float32) / np.float32(exact))
                   / np.float32(np.log(128 / exact)) * np.float32(NBUCK - exact)).astype(np.int32)
    bucket = np.where(dist < exact, dist, np.minimum(far, NBUCK - 1))
    return (bucket[None, :] == np.arange(NBUCK)[:, None]).astype(np.float32)


def signals(nc, ctx, names):
    return [ctx.enter_context(nc.semaphore(n)) for n in names.split()]


def tile_of(nc, ctx, name, shape, dt=F32):
    return ctx.enter_context(nc.sbuf_tensor(name, shape, dt, allow_name_mangling=True))


def bank_of(nc, ctx, name, shape):
    return ctx.enter_context(nc.psum_tensor(name, shape, F32, allow_name_mangling=True))


def clear_signals(nc, sems, pool_dma=()):
    for s in pool_dma:
        nc.gpsimd.dma_reset(range(s.num, s.num + 1))
    for s in sems:
        nc.gpsimd.sem_clear(s)
    nc.all_engine_barrier()


class InOrder:

    def __init__(self, eng):
        self.eng = eng
        self.count = {}

    def __call__(self, ins, sem, n=1):
        ins.then_inc(sem, n)
        self.count[sem.num] = self.count.get(sem.num, 0) + n
        self.eng.wait_ge(sem, self.count[sem.num])


def turns(eng, count, turn, one):
    for s in range(turn):
        one(0, s)
    with eng.Fori(1, count // turn - 1) as i:
        for s in range(turn):
            one(i, s)
    for s in range(turn):
        one(count // turn - 1, s)


def has(i, s, turn, back):
    return not isinstance(i, int) or i * turn + s >= back


def stage_constants(nc, G):
    with ExitStack() as c:
        zeroed, made, stored, started = signals(nc, c, "zeroed ident_made lead_stored x_loaded")
        with nc.Block() as block:

            @block.gpsimd
            def _(pool):
                pool.memset(G["ident"][:, :], 0.0).then_inc(zeroed, 1)
                pool.memset(G["ones"][:, :], 1.0).then_inc(zeroed, 1)
                pool.memset(G["featT"][0:LEAD, :, :], 0.0).then_inc(zeroed, 1)
                pool.wait_ge(zeroed, 3)
                pool.affine_select(out=G["ident"][:, :], in_=G["ident"][:, :], compare_op=ALU.not_equal,
                                   fill=1.0, base=0, pattern=[[-1, P]], channel_multiplier=1).then_inc(made, 1)
                pool.wait_ge(made, 1)

            @block.sync
            def _(sp):
                sp.dma_start(G["x"][:, 0:TILES, :],
                             G["x_prompt"][0].rearrange("(t p) d -> p t d", p=P)).then_inc(started, 16)
                sp.dma_start(G["x"][0:NB, TILES, :], G["x_sample"][:, 0, :]).then_inc(started, 16)
                sp.dma_start(G["pages"][:, :], G["page_table"].rearrange("b j -> (b j)").unsqueeze(0))\
                  .then_inc(started, 16)
                sp.wait_ge(zeroed, 3)
                lead = G["featT"][0:LEAD, :, :].rearrange("p k n -> p (k n)")
                sp.dma_start(G["z_even"][0:LEAD, :], lead[:, 0:P_EVEN])\
                  .then_inc(stored, 16)
                sp.dma_start(G["z_odd"][0:LEAD, :], lead[:, 0:P_ODD])\
                  .then_inc(stored, 16)
                sp.wait_ge(stored, 32)
                sp.wait_ge(started, 48)
        clear_signals(nc, [zeroed, made, stored, started])


def stage_ada(nc, G):
    N = 6 * D
    NQ = 4
    rows = 1 + NB
    with ExitStack() as c:
        c_sb = tile_of(nc, c, "c_rows", [rows, D])
        cT = tile_of(nc, c, "cT", [P, KC, rows])
        ct_ps = bank_of(nc, c, "cT_ps", [P, KC, rows])
        sems = signals(nc, c, "c_loaded silu_done cT_transposed cT_ready")
        c_loaded, silu_done, cT_transposed, cT_ready = sems
        with nc.Block() as block:

            @block.sync
            def _(sp):
                sp.dma_start(c_sb[0:1, :], G["c_prompt"]).then_inc(c_loaded, 16)
                sp.dma_start(c_sb[1:rows, :], G["c_sample"]).then_inc(c_loaded, 16)

            @block.scalar
            def _(act):
                act.wait_ge(c_loaded, 32)
                act.activation(c_sb[:, :], c_sb[:, :], ACT.Silu).then_inc(silu_done, 1)

            @block.tensor
            def _(pe):
                pe.wait_ge(silu_done, 1)
                for k in range(KC):
                    last = pe.transpose(ct_ps[:, k, :], c_sb[:, k * P:(k + 1) * P], G["ident"][0:rows, 0:rows])
                last.then_inc(cT_transposed, 1)

            @block.vector
            def _(dve):
                dve.wait_ge(cT_transposed, 1)
                dve.tensor_copy(cT[:, :, :], ct_ps[:, :, :]).then_inc(cT_ready, 1)
                dve.wait_ge(cT_ready, 1)
        clear_signals(nc, sems)

        w = [tile_of(nc, c, f"w_ada{i}", [P, KC, 512]) for i in range(NQ)]
        bias = tile_of(nc, c, "b_ada_rows", [rows, NQ * 512])
        m_sb = tile_of(nc, c, "mod_rows", [rows, NQ * 512])
        acc = [bank_of(nc, c, f"mod_ps{i}", [rows, 512]) for i in range(NQ)]
        sems = signals(nc, c, "w0 w1 w2 w3 b_loaded mod_summed mod_ready mod_stored")
        w_loaded, (b_loaded, mod_summed, mod_ready, mod_stored) = sems[0:4], sems[4:]
        for layer in range(DEPTH):
            w_view = G["w_ada"][layer].rearrange("(k p) n -> p k n", p=P)
            with nc.Fori(0, N // (NQ * 512)) as j:
                with nc.Block() as block:

                    @block.sync
                    def _(sp):
                        for q in range(NQ):
                            sp.dma_start(w[q][:, :, :], w_view[:, :, bass.ds(j * (NQ * 512) + q * 512, 512)])\
                              .then_inc(w_loaded[q], 16)
                            if q == 0:
                                sp.dma_start(bias[:, :], G["b_ada"][layer, bass.ds(j * (NQ * 512), NQ * 512)]
                                             .partition_broadcast(rows)).then_inc(b_loaded, 16)
                        sp.wait_ge(mod_ready, NQ)
                        sp.dma_start(G["mod"][:, layer, bass.ds(j * (NQ * 512), NQ * 512)], m_sb[:, :])\
                          .then_inc(mod_stored, 16)
                        sp.wait_ge(mod_stored, 16)

                    @block.tensor
                    def _(pe):
                        for q in range(NQ):
                            pe.wait_ge(w_loaded[q], 16)
                            for k in range(KC):
                                last = pe.matmul(acc[q][:, :], cT[:, k, :], w[q][:, k, :],
                                                 start=(k == 0), stop=(k == KC - 1))
                            last.then_inc(mod_summed, 1)

                    @block.vector
                    def _(dve):
                        dve.wait_ge(b_loaded, 16)
                        for q in range(NQ):
                            dve.wait_ge(mod_summed, q + 1)
                            dve.tensor_tensor(m_sb[:, q * 512:(q + 1) * 512], acc[q][:, :],
                                              bias[:, q * 512:(q + 1) * 512], ALU.add).then_inc(mod_ready, 1)
                clear_signals(nc, sems)


def stage_modulate(nc, G, layer, gain_dram, first, rows_dram=None):
    x, featT = G["x"], G["featT"]
    with ExitStack() as c:
        gain = tile_of(nc, c, "gain_b", [P, D])
        amp = tile_of(nc, c, "amp_b", [P, 2, D])
        shift = tile_of(nc, c, "shift_b", [P, 2, D])
        h = [tile_of(nc, c, f"h_tile{i}", [P, D]) for i in range(2)]
        junk = tile_of(nc, c, "sq_rows", [P, D])
        ss = [tile_of(nc, c, f"h_ss{i}", [P, 4]) for i in range(2)]
        hT_ps = [bank_of(nc, c, f"hT_ps{i}", [P, KC, P]) for i in range(2)]
        loaded, made = setup = signals(nc, c, "mod_loaded amp_made")
        with nc.Block() as block:

            @block.sync
            def _(sp):
                sp.dma_start(gain[:, :], gain_dram.partition_broadcast(P)).then_inc(loaded, 16)
                for j, dst in ((first + 1, amp), (first, shift)):
                    cols = slice(j * D, (j + 1) * D)
                    sp.dma_start(dst[:, 0, :], G["mod"][0, layer, cols].partition_broadcast(P)).then_inc(loaded, 16)
                    sp.dma_start(dst[0:NB, 1, :], G["mod"][1:1 + NB, layer, cols]).then_inc(loaded, 16)

            @block.vector
            def _(dve):
                dve.wait_ge(loaded, 16 * 5)
                for kind, rows in ((0, P), (1, NB)):
                    dve.scalar_tensor_tensor(amp[0:rows, kind, :], amp[0:rows, kind, :], 1.0, gain[0:rows, :],
                                             ALU.add, ALU.mult).then_inc(made, 1)
                dve.wait_ge(made, 2)
        clear_signals(nc, setup)

        names = "squares_summed mean_made rms_made rstd_made h_scaled h_made h_transposed copied_dve copied_act h_stored " \
                "act_passed dve_passed sp_passed"
        sems = signals(nc, c, names)
        (squares_summed, mean_made, rms_made, rstd_made, h_scaled, h_made, h_transposed, copied_dve, copied_act,
         h_stored, act_passed, dve_passed, sp_passed) = sems

        def tiles(eng, one):
            turns(eng, TILES, 2, one)
            one(TILES // 2, 0)

        def kind_of(i):
            return (NB, 1) if isinstance(i, int) and i == TILES // 2 else (P, 0)

        def at(i, s):
            return i * 2 + s

        def halves(eng, copy, chunks, copied, passed, sem_count):
            def copy_tile(i, s):
                b, rows = at(i, s), kind_of(i)[0]
                eng.wait_ge(h_transposed, b * 2 + sem_count)
                eng.sem_inc(passed, 1)
                copy(featT[:, chunks, bass.ds(b * P, rows)], hT_ps[s][:, chunks, 0:rows]).then_inc(copied, 1)
            return copy_tile

        def previous(i, s):
            return (i, 0) if s == 1 else (i - 1, 1)

        with nc.Block() as block:

            @block.scalar
            def _(act):
                copy_tile = halves(act, act.copy, slice(KC // 2, KC), copied_act, act_passed, 2)

                def one(i, s):
                    b, rows = at(i, s), kind_of(i)[0]
                    if has(i, s, 2, 2):
                        act.wait_ge(h_made, b - 1)
                        act.sem_inc(act_passed, 1)
                    act.activation(junk[0:rows, :], x[0:rows, b, :], ACT.Square, accum_out=ss[s][0:rows, 0:1])\
                       .then_inc(squares_summed, 1)
                    act.wait_ge(mean_made, b + 1)
                    act.activation(ss[s][0:rows, 2:3], ss[s][0:rows, 1:2], ACT.Sqrt).then_inc(rms_made, 1)
                    if has(i, s, 2, 1):
                        copy_tile(*previous(i, s))

                tiles(act, one)
                copy_tile(TILES // 2, 0)

            @block.vector
            def _(dve):
                copy_tile = halves(dve, dve.tensor_copy, slice(0, KC // 2), copied_dve, dve_passed, 1)

                def one(i, s):
                    b, (rows, kind) = at(i, s), kind_of(i)
                    hs, r = h[s][0:rows, :], ss[s][0:rows, 3:4]
                    dve.wait_ge(squares_summed, b + 1)
                    dve.tensor_scalar(ss[s][0:rows, 1:2], ss[s][0:rows, 0:1], 1.0 / D, RMS_EPS, ALU.mult, ALU.add)\
                       .then_inc(mean_made, 1)
                    dve.wait_ge(rms_made, b + 1)
                    dve.reciprocal(r, ss[s][0:rows, 2:3]).then_inc(rstd_made, 1)
                    if has(i, s, 2, 2):
                        dve.wait_ge(h_transposed, (b - 1) * 2)
                        if rows_dram is not None:
                            dve.wait_ge(h_stored, (b - 1) * 16)
                    dve.wait_ge(rstd_made, b + 1)
                    dve.scalar_tensor_tensor(hs, x[0:rows, b, :], r, amp[0:rows, kind, :], ALU.mult, ALU.mult)\
                       .then_inc(h_scaled, 1)
                    dve.wait_ge(h_scaled, b + 1)
                    dve.tensor_tensor(hs, hs, shift[0:rows, kind, :], ALU.add).then_inc(h_made, 1)
                    if has(i, s, 2, 1):
                        copy_tile(*previous(i, s))

                tiles(dve, one)
                copy_tile(TILES // 2, 0)

            @block.tensor
            def _(pe):
                def one(i, s):
                    b, rows = at(i, s), kind_of(i)[0]
                    if has(i, s, 2, 2):
                        pe.wait_ge(copied_dve, b - 1)
                        pe.wait_ge(copied_act, b - 1)
                    pe.wait_ge(h_made, b + 1)
                    for k in range(KC):
                        last = pe.transpose(hT_ps[s][:, k, 0:rows], h[s][0:rows, k * P:(k + 1) * P],
                                            G["ident"][0:rows, 0:rows])
                        if k in (KC // 2 - 1, KC - 1):
                            last.then_inc(h_transposed, 1)

                tiles(pe, one)

            @block.sync
            def _(sp):
                def one(i, s):
                    b, rows = at(i, s), kind_of(i)[0]
                    if has(i, s, 2, 1):
                        sp.wait_ge(h_stored, b * 16)
                        sp.sem_inc(sp_passed, 1)
                    sp.wait_ge(h_made, b + 1)
                    sp.sem_inc(sp_passed, 1)
                    sp.dma_start(rows_dram[bass.ds(b * P, rows), :], h[s][0:rows, :]).then_inc(h_stored, 16)

                if rows_dram is not None:
                    tiles(sp, one)
                    sp.wait_ge(h_stored, 16 * (TILES + 1))
        clear_signals(nc, sems)


def stage_project(nc, G, w_dram, width, prompt_rows, sample_rows):
    featT = G["featT"]
    w_view = w_dram.rearrange("(k p) n -> p k n", p=P)
    NM = TILES + 1
    with ExitStack() as c:
        w = [tile_of(nc, c, f"w_cols{i}", [P, KC, 512]) for i in range(2)]
        out = [tile_of(nc, c, f"z_cols{i}", [P, NM, 512]) for i in range(2)]
        acc = [bank_of(nc, c, f"z_ps{i}", [P, 512]) for i in range(4)]
        sems = signals(nc, c, "w_loaded0 w_loaded1 z_summed z_copied_dve z_copied_act z_stored next_loaded")
        w_loaded, (z_summed, copied_dve, copied_act, z_stored, next_loaded) = sems[0:2], sems[2:]

        def load(eng, half, c0, n, sem):
            for part in range(2):
                ks = slice(part * KC // 2, (part + 1) * KC // 2)
                eng.dma_start(w[half][:, ks, 0:n], w_view[:, ks, bass.ds(c0, n)]).then_inc(sem, 16)

        def chunks(items, following):
            ms = [(i, m) for i in range(len(items)) for m in range(NM)]
            by_dve = [m % 2 == 0 for _, m in ms]

            def copied(q, eng):
                same = sum(d == by_dve[q] for d in by_dve[:q + 1])
                eng.wait_ge(copied_dve if by_dve[q] else copied_act, same)

            with nc.Block() as block:

                @block.sync
                def _(sp):
                    if len(items) > 1:
                        load(sp, 1, *items[1], w_loaded[1])
                    for q, (i, m) in enumerate(ms):
                        c0, n = items[i]
                        copied(q, sp)
                        if m < TILES:
                            sp.dma_start(prompt_rows[m * P:(m + 1) * P, bass.ds(c0, n)], out[i][:, m, 0:n])\
                              .then_inc(z_stored, 16)
                        else:
                            sp.dma_start(sample_rows[:, bass.ds(c0, n)], out[i][0:NB, TILES, 0:n])\
                              .then_inc(z_stored, 16)
                        if i == 0 and m == NM - 1 and following:
                            load(sp, 0, *following, next_loaded)
                    sp.wait_ge(z_stored, 16 * len(ms))
                    if following:
                        sp.wait_ge(next_loaded, 32)

                @block.tensor
                def _(pe):
                    for q, (i, m) in enumerate(ms):
                        n = items[i][1]
                        rows = P if m < TILES else NB
                        if i == 1 and m == 0:
                            pe.wait_ge(w_loaded[1], 32)
                        if q >= 4:
                            copied(q - 4, pe)
                        for k in range(KC):
                            last = pe.matmul(acc[q % 4][0:rows, 0:n], featT[:, k, m * P:m * P + rows],
                                             w[i][:, k, 0:n], start=(k == 0), stop=(k == KC - 1))
                        last.then_inc(z_summed, 1)

                def copy_out(eng, copy, mine, sem):
                    for q, (i, m) in enumerate(ms):
                        if by_dve[q] == mine:
                            n = items[i][1]
                            rows = P if m < TILES else NB
                            eng.wait_ge(z_summed, q + 1)
                            copy(out[i][0:rows, m, 0:n], acc[q % 4][0:rows, 0:n]).then_inc(sem, 1)

                @block.vector
                def _(dve):
                    copy_out(dve, dve.tensor_copy, True, copied_dve)

                @block.scalar
                def _(act):
                    copy_out(act, act.copy, False, copied_act)
            clear_signals(nc, sems)

        full = width // 512
        tail = [(full * 512, width % 512)] if width % 512 else []
        with nc.Block() as block:

            @block.sync
            def _(sp):
                load(sp, 0, 0, 512, w_loaded[0])
                sp.wait_ge(w_loaded[0], 32)
        clear_signals(nc, [w_loaded[0]])
        looped = (full - 1) // 2
        rest = [(i * 512, 512) for i in range(2 * looped, full)] + tail
        with nc.Fori(0, looped) as j:
            chunks([(j * 1024, 512), (j * 1024 + 512, 512)], (j * 1024 + 1024, 512))
        while rest:
            chunks(rest[0:2], rest[2] if len(rest) > 2 else None)
            rest = rest[2:]
def stage_residual_project(nc, G, layer, w_dram, gate_row):
    featT, x = G["featT"], G["x"]
    w_view = w_dram.rearrange("(k p) n -> p k n", p=P)
    NM = TILES + 1
    halves = [slice(c0, c0 + 512) for c0 in range(0, D, 512)]
    with ExitStack() as c:
        w = [tile_of(nc, c, f"w_out_cols{i}", [P, KC, 512]) for i in range(2)]
        gate = tile_of(nc, c, "gate_cols", [P, 2, D])
        gated = [tile_of(nc, c, f"gated{i}", [P, 512]) for i in range(2)]
        acc = [bank_of(nc, c, f"mix_ps{i}", [P, 512]) for i in range(4)]
        sems = signals(nc, c, "w_loaded0 w_loaded1 gate_loaded mix_summed mix_gated x_added")
        w_loaded, (gate_loaded, mix_summed, mix_gated, x_added) = sems[0:2], sems[2:]
        sums = [(half, m) for half in range(2) for m in range(NM)]
        with nc.Block() as block:

            @block.sync
            def _(sp):
                cols = slice(gate_row * D, (gate_row + 1) * D)
                for half in range(2):
                    for k in range(0, KC, KC // 2):
                        sp.dma_start(w[half][:, k:k + KC // 2, :], w_view[:, k:k + KC // 2, halves[half]])\
                          .then_inc(w_loaded[half], 16)
                    if half == 0:
                        sp.dma_start(gate[:, 0, :], G["mod"][0, layer, cols].partition_broadcast(P))\
                          .then_inc(gate_loaded, 16)
                        sp.dma_start(gate[0:NB, 1, :], G["mod"][1:1 + NB, layer, cols]).then_inc(gate_loaded, 16)

            @block.tensor
            def _(pe):
                for q, (half, m) in enumerate(sums):
                    rows = P if m < TILES else NB
                    if m == 0:
                        pe.wait_ge(w_loaded[half], 32)
                    if q >= 4:
                        pe.wait_ge(mix_gated, q - 3)
                    for k in range(KC):
                        last = pe.matmul(acc[q % 4][0:rows, :], featT[:, k, m * P:m * P + rows], w[half][:, k, :],
                                         start=(k == 0), stop=(k == KC - 1))
                    last.then_inc(mix_summed, 1)

            @block.vector
            def _(dve):
                step = InOrder(dve)
                dve.wait_ge(gate_loaded, 32)
                for q, (half, m) in enumerate(sums):
                    rows, kind = (P, 0) if m < TILES else (NB, 1)
                    dve.wait_ge(mix_summed, q + 1)
                    step(dve.tensor_tensor(gated[q % 2][0:rows, :], acc[q % 4][0:rows, :],
                                           gate[0:rows, kind, halves[half]], ALU.mult), mix_gated)
                    step(dve.tensor_tensor(x[0:rows, m, halves[half]], x[0:rows, m, halves[half]],
                                           gated[q % 2][0:rows, :], ALU.add), x_added)
        clear_signals(nc, sems)


def alloc_banks(nc, c, G):
    G["near"] = tile_of(nc, c, "near_bias", [P, NH, 2 * P])
    G["far_mask"] = tile_of(nc, c, "causal_bank", [P, 15 * P])
    G["row_bias"] = tile_of(nc, c, "row_bias", [NB * NH, PAST + 1])


def make_far_mask(pool, far_mask, filled, masked):
    pool.memset(far_mask[:, :], 0.0).then_inc(filled, 1)
    pool.wait_ge(filled, 1)
    pool.affine_select(out=far_mask[:, :], in_=far_mask[:, :], compare_op=ALU.is_ge, fill=NEG,
                       base=896, pattern=[[-1, 15 * P]], channel_multiplier=1).then_inc(masked, 1)
    pool.wait_ge(masked, 1)


def stage_load_banks(nc, G, cmp_bias):
    with ExitStack() as c:
        loaded, filled, masked = sems = signals(nc, c, "banks_loaded filled masked")
        with nc.Block() as block:

            @block.gpsimd
            def _(pool):
                make_far_mask(pool, G["far_mask"], filled, masked)

            @block.sync
            def _(sp):
                sp.dma_start(G["near"][:, :, :], G["near_d"]).then_inc(loaded, 16)
                sp.dma_start(cmp_bias[:, :, :], G["cmp_bias_d"]).then_inc(loaded, 16)
                sp.dma_start(G["row_bias"][:, :], G["row_bias_d"]).then_inc(loaded, 16)
                sp.wait_ge(loaded, 48)
        clear_signals(nc, sems)


def stage_banks(nc, G):
    near, far_mask, row_bias = G["near"], G["far_mask"], G["row_bias"]
    with ExitStack() as c:
        cmp_bias = tile_of(nc, c, "cmp_bias_made", [P, NH, 64])
        oh = tile_of(nc, c, "t5_oh", [NBUCK, OH_W])
        rev = tile_of(nc, c, "t5_rev", [NBUCK, PAST + 1])
        table = tile_of(nc, c, "bias_table", [NBUCK, NH])
        farthest = tile_of(nc, c, "bias_far", [NBUCK, NH])
        rel8 = tile_of(nc, c, "bias_rel8", [NBUCK, NB, NH])
        col_ps = [bank_of(nc, c, f"near_ps{i}", [P, 64, NH]) for i in range(2)]
        row_ps = bank_of(nc, c, "row_ps", [NB * NH, 512])
        sems = signals(nc, c, "tables_loaded table_made cols_summed cols_copied row_summed row_copied filled masked "
                              "banks_stored")
        tables_loaded, table_made, cols_summed, cols_copied, row_summed, row_copied, filled, masked, \
            banks_stored = sems
        near_groups = [(near[:, :, g * 64:(g + 1) * 64], [P - (g * 64 + i) for i in range(64)]) for g in range(4)]
        near_groups.append((cmp_bias[:, :, :], [865 - CMP * i for i in range(64)]))

        with nc.Block() as block:

            @block.gpsimd
            def _(pool):
                make_far_mask(pool, far_mask, filled, masked)

            @block.sync
            def _(sp):
                sp.dma_start(oh[:, :], G["t5_onehot"]).then_inc(tables_loaded, 16)
                sp.dma_start(rev[:, :], G["t5_onehot_rev"]).then_inc(tables_loaded, 16)
                sp.dma_start(table[:, :], G["rel_bias"]).then_inc(tables_loaded, 16)
                sp.dma_start(farthest[:, :], G["rel_bias"][NBUCK - 1].partition_broadcast(NBUCK))\
                  .then_inc(tables_loaded, 16)
                sp.wait_ge(cols_copied, len(near_groups) - 1)
                sp.dma_start(G["near_d"], near[:, :, :]).then_inc(banks_stored, 16)
                sp.wait_ge(cols_copied, len(near_groups))
                sp.dma_start(G["cmp_bias_d"], cmp_bias[:, :, :]).then_inc(banks_stored, 16)
                sp.wait_ge(row_copied, 3)
                sp.dma_start(G["row_bias_d"], row_bias[:, :]).then_inc(banks_stored, 16)
                sp.wait_ge(banks_stored, 48)

            @block.vector
            def _(dve):
                step = InOrder(dve)
                dve.wait_ge(tables_loaded, 64)
                step(dve.tensor_tensor(table[:, :], table[:, :], farthest[:, :], ALU.subtract), table_made)
                for b in range(NB):
                    step(dve.tensor_copy(rel8[:, b, :], table[:, :]), table_made)
                for i, (dst, dist) in enumerate(near_groups):
                    dve.wait_ge(cols_summed, i + 1)
                    step(dve.tensor_copy(dst, col_ps[i % 2][:, 0:len(dist), :].rearrange("p x h -> p h x")), cols_copied)

            @block.tensor
            def _(pe):
                pe.wait_ge(table_made, 1 + NB)
                for i, (dst, dist) in enumerate(near_groups):
                    if i >= 2:
                        pe.wait_ge(cols_copied, i - 1)
                    for x, d in enumerate(dist):
                        last = pe.matmul(col_ps[i % 2][:, x, :], oh[:, OH0 + d:OH0 + d + P], table[:, :],
                                         start=True, stop=True)
                    last.then_inc(cols_summed, 1)
                for i, (a, b) in enumerate(((0, 512), (512, 1024), (1024, 1025))):
                    if i:
                        pe.wait_ge(row_copied, i)
                    pe.matmul(row_ps[:, 0:b - a], rel8[:, :, :].rearrange("r b h -> r (b h)"), rev[:, a:b],
                              start=True, stop=True).then_inc(row_summed, 1)

            @block.scalar
            def _(act):
                for i, (a, b) in enumerate(((0, 512), (512, 1024), (1024, 1025))):
                    act.wait_ge(row_summed, i + 1)
                    act.copy(row_bias[:, a:b], row_ps[:, 0:b - a]).then_inc(row_copied, 1)
        clear_signals(nc, sems)


TILE_GROUP = 2


def by_width(nc, one_tile):
    for t0 in range(0, TILES, TILE_GROUP):
        with nc.Fori(t0, t0 + TILE_GROUP) as t:
            one_tile(t, (t0 + TILE_GROUP) * P)


def key_chunks(KT, width):
    return [(KT[:, a:min(a + 512, width)], min(512, width - a)) for a in range(0, width, 512)]


class Attend:
    def __init__(self, nc, c):
        self.lg_ps = [bank_of(nc, c, f"lg_ps{i}", [P, 1024]) for i in range(2)]
        self.t_ps = bank_of(nc, c, "t_ps", [P, 8, P])
        self.o_ps = [bank_of(nc, c, f"o_ps{i}", [P, HD]) for i in range(2)]
        self.lg = [tile_of(nc, c, f"lg{i}", [P, 1024]) for i in range(2)]
        self.biased = [tile_of(nc, c, f"biased{i}", [P, P + 1024]) for i in range(2)]
        self.prob = [tile_of(nc, c, f"prob{i}", [P, 1024]) for i in range(2)]
        self.probT = [tile_of(nc, c, f"probT{i}", [P, 8, P]) for i in range(2)]
        self.nmax = tile_of(nc, c, "nmax", [P, 2])
        self.sum = tile_of(nc, c, "esum", [P, 16])
        self.rsum = tile_of(nc, c, "rsum", [P, 2])
        self.sems = signals(nc, c, "lg_summed lg_masked masks_made mask_kept bias_made exp_done p_transposed "
                                   "pT_copied pv_summed o_scaled o_added")
        (self.lg_summed, self.lg_masked, self.masks_made, self.mask_kept, self.bias_made, self.exp_done,
         self.p_transposed, self.pT_copied, self.pv_summed, self.o_scaled, self.o_added) = self.sems

    def gpsimd(self, pool, units, near, masks):
        step = InOrder(pool)
        pool.wait_ge(self.masks_made, masks)
        for i, (_, _, mask, mask_near, at, head, values, _) in enumerate(units):
            buf = self.biased[i % 2]
            if i >= 2:
                pool.wait_ge(self.lg_masked, i - 1)
            if mask is not None:
                step(pool.tensor_copy(buf[:, P:P + len(values) * P], mask), self.mask_kept)
            pool.tensor_tensor(buf[:, bass.ds(at, 2 * P)], mask_near, near[:, head, :], ALU.add)\
                .then_inc(self.bias_made, 1)

    def tensor(self, pe, units, ident):
        n = len(units)
        for i in range(n + 2):
            if i < n:
                lhsT, keys = units[i][0], units[i][1]
                if i >= 2:
                    pe.wait_ge(self.lg_masked, i - 1)
                at = 0
                for ap, width in keys:
                    last = pe.matmul(self.lg_ps[i % 2][:, at:at + width], lhsT, ap, start=True, stop=True)
                    at += width
                last.then_inc(self.lg_summed, 1)
            if 1 <= i <= n:
                u = i - 1
                pe.wait_ge(self.exp_done, u + 1)
                if u >= 1:
                    pe.wait_ge(self.pT_copied, u)
                for j in range(len(units[u][6])):
                    last = pe.transpose(self.t_ps[:, j, :], self.prob[u % 2][:, j * P:(j + 1) * P], ident[:, :])
                last.then_inc(self.p_transposed, 1)
            if i >= 2:
                u = i - 2
                pe.wait_ge(self.pT_copied, u + 1)
                if u >= 2:
                    pe.wait_ge(self.o_scaled, u - 1)
                values = units[u][6]
                for j, v in enumerate(values):
                    last = pe.matmul(self.o_ps[u % 2][:, :], self.probT[u % 2][:, j, :], v,
                                     start=(j == 0), stop=(j == len(values) - 1))
                last.then_inc(self.pv_summed, 1)

    def vector(self, dve, step, units, out, gates):
        n = len(units)
        for i in range(n + 2):
            if i < n:
                width = len(units[i][6]) * P
                dve.wait_ge(self.lg_summed, i + 1)
                if i >= 2:
                    dve.wait_ge(self.exp_done, i - 1)
                dve.wait_ge(self.bias_made, i + 1)
                dve.tensor_tensor_reduce(self.lg[i % 2][:, 0:width], self.lg_ps[i % 2][:, 0:width],
                                         self.biased[i % 2][:, P:P + width], -1.0, 3e38, ALU.add, ALU.min,
                                         self.nmax[:, i % 2:i % 2 + 1]).then_inc(self.lg_masked, 1)
            if i >= 2:
                u = i - 2
                head, gate = units[u][5], units[u][7]
                r = self.rsum[:, u % 2:u % 2 + 1]
                step(dve.reciprocal(r, self.sum[:, u:u + 1]), self.o_added)
                if gates is not None:
                    step(dve.tensor_tensor(r, r, gates[:, gate:gate + 1], ALU.mult), self.o_added)
                dve.wait_ge(self.pv_summed, u + 1)
                if gates is None:
                    step(dve.tensor_scalar(out[:, head, :], self.o_ps[u % 2][:, :], r, None, ALU.mult), self.o_scaled)
                else:
                    step(dve.scalar_tensor_tensor(out[:, head, :], self.o_ps[u % 2][:, :], r, out[:, head, :],
                                                  ALU.mult, ALU.add), self.o_scaled)

    def scalar(self, act, units):
        n = len(units)
        for i in range(n + 1):
            if i < n:
                width = len(units[i][6]) * P
                act.wait_ge(self.lg_masked, i + 1)
                if i >= 2:
                    act.wait_ge(self.p_transposed, i - 1)
                act.activation(self.prob[i % 2][:, 0:width], self.lg[i % 2][:, 0:width], ACT.Exp,
                               bias=self.nmax[:, i % 2:i % 2 + 1], scale=-1.0, accum_out=self.sum[:, i:i + 1])\
                   .then_inc(self.exp_done, 1)
            if i >= 1:
                u = i - 1
                nb = len(units[u][6])
                act.wait_ge(self.p_transposed, u + 1)
                if u >= 2:
                    act.wait_ge(self.pv_summed, u - 1)
                act.copy(self.probT[u % 2][:, 0:nb, :], self.t_ps[:, 0:nb, :]).then_inc(self.pT_copied, 1)


def stage_even_prompt(nc, G):
    ident, featT, near, far_mask, z = G["ident"], G["featT"], G["near"], G["far_mask"], G["z_even"]
    kv_out = G["a_kv_p"][0, 0].rearrange("s two kv d -> s (two kv d)")
    with ExitStack() as c:
        zt = tile_of(nc, c, "zt", [P, E_BG])
        cx = [tile_of(nc, c, f"cx{j}", [P, 2, CONV]) for j in range(3)]
        bg = tile_of(nc, c, "bg", [P, CONV])
        cw = tile_of(nc, c, "cw", [P, 4, CONV])
        gq = tile_of(nc, c, "gq", [P, HD])
        gk = tile_of(nc, c, "gk", [P, HD])
        sq = tile_of(nc, c, "sq", [P, 10, HD])
        rms = tile_of(nc, c, "rms", [P, 3, 10])
        qn = tile_of(nc, c, "qn", [P, 5, NKV, HD])
        kid = tile_of(nc, c, "kid", [P, 2, HD])
        qTz = tile_of(nc, c, "qTz", [P, NH, P])
        qiT = tile_of(nc, c, "qiT", [P, 2, P])
        KT = tile_of(nc, c, "KT", [P, SEQ])
        KiT = tile_of(nc, c, "KiT", [P, SEQ])
        V = tile_of(nc, c, "V", [P, TILES, P])
        rel = tile_of(nc, c, "rel", [P, SEQ])
        score = tile_of(nc, c, "score", [P, P + SEQ])
        top8 = tile_of(nc, c, "top8", [P, 8])
        wi = tile_of(nc, c, "wi", [P, IDXH])
        cat = tile_of(nc, c, "cat", [P, D])
        o = cat[:, 0:A_Q].rearrange("p (h d) -> p h d", h=NH)
        att = Attend(nc, c)
        t_ps = att.t_ps

        loaded, cleared, scaled = setup = signals(nc, c, "weights_loaded buffers_cleared gain_scaled")
        with nc.Block() as block:

            @block.sync
            def _(sp):
                for j in range(3):
                    sp.dma_start(cw[:, j, :], G["b_conv_w"][0, j].partition_broadcast(P)).then_inc(loaded, 16)
                sp.dma_start(cw[:, 3, :], G["b_conv_b"][0].partition_broadcast(P)).then_inc(loaded, 16)
                sp.dma_start(gq[:, :], G["a_q_norm"][0].partition_broadcast(P)).then_inc(loaded, 16)
                sp.dma_start(gk[:, :], G["a_k_norm"][0].partition_broadcast(P)).then_inc(loaded, 16)

            @block.gpsimd
            def _(pool):
                for buf in (qTz[:, :, :], KT[:, :], KiT[:, :], V[:, :, :], att.biased[0][:, :], att.biased[1][:, :],
                            score[:, 0:P]):
                    pool.memset(buf, 0.0).then_inc(cleared, 1)

            @block.vector
            def _(dve):
                dve.wait_ge(loaded, 96)
                dve.tensor_scalar(gq[:, :], gq[:, :], HD ** -0.5, None, ALU.mult).then_inc(scaled, 1)
        clear_signals(nc, setup)

        names = signals(nc, c, "z_loaded conv_loaded normed kn_ready mean_made rms_made kid_copied v_copied "
                               "qk_transposed q_copied keys_copied idx_summed idx_relu score_step picked "
                               "u_made conv_step conv_made kv_stored cat_transposed")
        (z_loaded, conv_loaded, normed, kn_ready, mean_made, rms_made, kid_copied, v_copied, qk_transposed,
         q_copied, keys_copied, idx_summed, idx_relu, score_step, picked, u_made, conv_step, conv_made, kv_stored,
         cat_transposed) = names

        def load_rows(sp, t):
            sp.dma_start(zt[:, :], z[bass.ds(t * P + LEAD, P), 0:E_BG]).then_inc(z_loaded, 16)

        def load_conv(sp, t):
            for j in range(3):
                sp.dma_start(cx[j][:, :, :].rearrange("p a n -> p (a n)"),
                             z[bass.ds(t * P + LEAD - j, P), E_CG:P_EVEN]).then_inc(conv_loaded, 16)
            sp.dma_start(bg[:, :], z[bass.ds(t * P + LEAD, P), E_BG:E_CG]).then_inc(conv_loaded, 16)

        with nc.Block() as block:

            @block.sync
            def _(sp):
                load_rows(sp, 0)
                load_conv(sp, 0)
                sp.wait_ge(z_loaded, 16)
                sp.wait_ge(conv_loaded, 64)
        clear_signals(nc, [z_loaded, conv_loaded])

        def one_tile(t, width):
            causal = far_mask[:, bass.ds(896 - t * P, width)]
            select = width > TOPK
            mask = score[:, P:P + width] if select else causal
            mask_near = score[:, bass.ds(t * P, 2 * P)] if select else far_mask[:, 896 - P:896 + P]
            units = [(qTz[:, h, :], key_chunks(KT, width), mask if h < 2 else None, mask_near, t * P, h,
                      [V[:, j, (h // GQA) * HD:(h // GQA + 1) * HD] for j in range(width // P)], None)
                     for h in range(NH)]
            with nc.Block() as block:

                @block.sync
                def _(sp):
                    sp.dma_start(kv_out[bass.ds(t * P, P), KVW:A_KV], zt[:, E_V:E_QI]).then_inc(kv_stored, 16)
                    sp.dma_start(G["a_kidx_p"][0, 0, bass.ds(t * P, P), :], zt[:, E_KI:E_WI]).then_inc(kv_stored, 16)
                    sp.wait_ge(kn_ready, 1)
                    sp.dma_start(kv_out[bass.ds(t * P, P), 0:KVW], qn[:, 4, :, :].rearrange("p a d -> p (a d)"))\
                      .then_inc(kv_stored, 16)
                    sp.wait_ge(u_made, 3)
                    sp.dma_start(G["b_conv_p"][0, 0], cx[0][P - 2:P, 0, :]).then_inc(kv_stored, 16)
                    sp.wait_ge(kv_stored, 64)
                    sp.wait_ge(v_copied, 1)
                    sp.wait_ge(qk_transposed, 1)
                    load_rows(sp, (t + 1) % TILES)
                    sp.wait_ge(conv_made, 1)
                    load_conv(sp, (t + 1) % TILES)
                    sp.wait_ge(z_loaded, 16)
                    sp.wait_ge(conv_loaded, 64)

                @block.gpsimd
                def _(pool):
                    step = InOrder(pool)
                    for j in range(3):
                        step(pool.tensor_tensor(cx[j][:, 0, :], cx[j][:, 0, :], cx[j][:, 1, :], ALU.mult), u_made)
                    for j in (2, 1, 0):
                        step(pool.tensor_tensor(cx[j][:, 1, :], cx[j][:, 0, :], cw[:, 2 - j, :], ALU.mult), conv_step)
                    step(pool.tensor_tensor(cx[2][:, 1, :], cx[2][:, 1, :], cw[:, 3, :], ALU.add), conv_step)
                    step(pool.tensor_tensor(cx[2][:, 1, :], cx[2][:, 1, :], cx[1][:, 1, :], ALU.add), conv_step)
                    step(pool.tensor_tensor(cx[2][:, 1, :], cx[2][:, 1, :], cx[0][:, 1, :], ALU.add), conv_step)
                    step(pool.tensor_tensor(cat[:, A_Q:D], cx[2][:, 1, :], bg[:, :], ALU.mult), conv_made)
                    att.gpsimd(pool, units, near, 1)

                @block.scalar
                def _(act):
                    for a in range(2):
                        act.copy(kid[:, a, :], zt[:, E_KI:E_WI]).then_inc(kid_copied, 1)
                    act.copy(V[:, t, :], zt[:, E_V:E_QI]).then_inc(v_copied, 1)
                    act.wait_ge(mean_made, 1)
                    act.activation(rms[:, 1, :], rms[:, 0, :], ACT.Sqrt).then_inc(rms_made, 1)
                    act.wait_ge(qk_transposed, 1)
                    act.copy(KT[:, bass.ds(t * P, P)], t_ps[:, 4, :]).then_inc(keys_copied, 1)
                    act.copy(qiT[:, :, :], t_ps[:, 5:7, :]).then_inc(keys_copied, 1)
                    act.copy(KiT[:, bass.ds(t * P, P)], t_ps[:, 7, :]).then_inc(keys_copied, 1)
                    for i in range(IDXH if select else 0):
                        act.wait_ge(idx_summed, i + 1)
                        if i:
                            act.wait_ge(score_step, i)
                        act.activation(rel[:, 0:width], att.lg_ps[i % 2][:, 0:width], ACT.Relu).then_inc(idx_relu, 1)
                    att.scalar(act, units)
                    act.wait_ge(cat_transposed, 1)
                    act.copy(featT[:, KC // 2:KC, bass.ds(t * P, P)], t_ps[:, KC // 2:KC, :])

                @block.tensor
                def _(pe):
                    pe.wait_ge(kn_ready, 1)
                    for g in range(5):
                        pe.transpose(t_ps[:, g, :], qn[:, g, :, :].rearrange("p a d -> p (a d)"), ident[:, :])
                    for g in range(2):
                        pe.transpose(t_ps[:, 5 + g, :], zt[:, E_QI + g * P:E_QI + (g + 1) * P], ident[:, :])
                    pe.wait_ge(kid_copied, 2)
                    pe.transpose(t_ps[:, 7, :], kid[:, :, :].rearrange("p a d -> p (a d)"), ident[:, :])\
                      .then_inc(qk_transposed, 1)
                    pe.wait_ge(keys_copied, 3)
                    for i in range(IDXH if select else 0):
                        if i >= 2:
                            pe.wait_ge(idx_relu, i - 1)
                        half = slice((i % 2) * HD, (i % 2 + 1) * HD)
                        for a in range(0, width, 512):
                            b = min(a + 512, width)
                            last = pe.matmul(att.lg_ps[i % 2][:, a:b], qiT[half, i // 2, :], KiT[half, a:b],
                                             start=True, stop=True)
                        last.then_inc(idx_summed, 1)
                    pe.wait_ge(q_copied, 2)
                    if select:
                        pe.wait_ge(idx_relu, IDXH)
                    pe.wait_ge(v_copied, 1)
                    att.tensor(pe, units, ident)
                    pe.wait_ge(att.o_scaled, NH)
                    pe.wait_ge(conv_made, 1)
                    for k in range(KC):
                        last = pe.transpose(t_ps[:, k, :], cat[:, k * P:(k + 1) * P], ident[:, :])
                    last.then_inc(cat_transposed, 1)

                @block.vector
                def _(dve):
                    step = InOrder(dve)
                    qk = zt[:, 0:10 * HD].rearrange("p (h d) -> p h d", d=HD)
                    step(dve.tensor_tensor(sq[:, :, :], qk, qk, ALU.mult), normed)
                    step(dve.tensor_reduce(rms[:, 0, :], sq[:, :, :], AX.X, ALU.add), normed)
                    step(dve.tensor_scalar(rms[:, 0, :], rms[:, 0, :], 1.0 / HD, RMS_EPS, ALU.mult, ALU.add),
                         mean_made)
                    step(dve.tensor_scalar(wi[:, :], zt[:, E_WI:E_BG], (IDXH * HD) ** -0.5, None, ALU.mult), normed)
                    dve.wait_ge(rms_made, 1)
                    step(dve.reciprocal(rms[:, 2, :], rms[:, 1, :]), normed)
                    for kv in range(NKV):
                        cols = slice(kv * GQA * HD, (kv + 1) * GQA * HD)
                        r = rms[:, 2, kv * GQA:(kv + 1) * GQA].unsqueeze(2).broadcast_to([P, GQA, HD])
                        step(dve.tensor_tensor(qn[:, 0:GQA, kv, :], zt[:, cols].rearrange("p (g d) -> p g d", d=HD),
                                               r, ALU.mult), normed)
                        step(dve.tensor_tensor(qn[:, 0:GQA, kv, :], qn[:, 0:GQA, kv, :],
                                               gq[:, :].unsqueeze(1).broadcast_to([P, GQA, HD]), ALU.mult), normed)
                    r = rms[:, 2, NH:NH + NKV].unsqueeze(2).broadcast_to([P, NKV, HD])
                    step(dve.tensor_tensor(qn[:, GQA, :, :], zt[:, E_K:E_V].rearrange("p (g d) -> p g d", d=HD),
                                           r, ALU.mult), normed)
                    step(dve.tensor_tensor(qn[:, GQA, :, :], qn[:, GQA, :, :],
                                           gk[:, :].unsqueeze(1).broadcast_to([P, NKV, HD]), ALU.mult), kn_ready)
                    dve.wait_ge(qk_transposed, 1)
                    for kv in range(NKV):
                        half = slice(kv * HD, (kv + 1) * HD)
                        step(dve.tensor_copy(qTz[half, kv * GQA:(kv + 1) * GQA, :], t_ps[half, 0:GQA, :]), q_copied)
                    if select:
                        for i in range(IDXH):
                            dve.wait_ge(idx_relu, i + 1)
                            step(dve.scalar_tensor_tensor(mask, rel[:, 0:width], wi[:, i:i + 1],
                                                          causal if i == 0 else mask, ALU.mult, ALU.add), score_step)
                        for _ in range(TOPK // 8):
                            step(dve.max(top8[:, :], mask), picked)
                            step(dve.match_replace(mask, top8[:, :], mask, TAKEN), picked)
                        step(dve.tensor_scalar(mask, mask, TAKEN / 2, NEG, ALU.is_gt, ALU.mult), picked)
                        step(dve.tensor_tensor(mask, mask, causal, ALU.add), picked)
                    dve.sem_inc(att.masks_made, 1)
                    att.vector(dve, step, units, o, None)
                    dve.wait_ge(cat_transposed, 1)
                    dve.tensor_copy(featT[:, 0:KC // 2, bass.ds(t * P, P)], t_ps[:, 0:KC // 2, :])
            clear_signals(nc, names + att.sems)

        by_width(nc, one_tile)
class SampleState:

    def __init__(self, nc, c):
        self.Qz = tile_of(nc, c, "Qz", [P, NB, NH])
        self.KnT = tile_of(nc, c, "KnT", [P, 2, NB])
        self.Vn = tile_of(nc, c, "Vn", [1, 2, NB, P])
        self.mask = tile_of(nc, c, "s_mask", [NB * NH, PAST + 1])
        self.scale = tile_of(nc, c, "s_scale", [NB * NH, 3])
        self.oT = tile_of(nc, c, "s_oT", [P, NB * NH])
        self.cat = tile_of(nc, c, "s_cat", [NB, D])


def sample_logits(nc, G, st, name, load_keys, n_tiles, branch, V, kidx=None):
    ident = G["ident"]
    past = n_tiles * P
    Ls, Rs = G["s_logits"], G["s_rel"]
    TURN = 2
    stores = 32 if kidx else 16
    steps = 4 if kidx else 2
    with ExitStack() as c:
        K = [tile_of(nc, c, f"s_K{i}", [P, n_tiles, P]) for i in range(TURN)]
        Ki = [tile_of(nc, c, f"s_Ki{i}", [P, n_tiles, HD]) for i in range(TURN)]
        KT = tile_of(nc, c, "s_KT", [P, past + 1])
        Qb = tile_of(nc, c, "s_Qb", [P, NH])
        L = [tile_of(nc, c, f"s_L{i}", [NH, past + 1]) for i in range(TURN)]
        KiT = tile_of(nc, c, "s_KiT", [HD, past + 1])
        Qib = tile_of(nc, c, "s_Qib", [HD, IDXH])
        R = [tile_of(nc, c, f"s_R{i}", [IDXH, past + 1]) for i in range(TURN)]
        t_ps = bank_of(nc, c, "s_t_ps", [P, 8, P])
        ti_ps = bank_of(nc, c, "s_ti_ps", [HD, 8, P])
        l_ps = bank_of(nc, c, "s_l_ps", [NH, 1024])
        new_ps = bank_of(nc, c, "s_new_ps", [NH, 2])
        sems = signals(nc, c, "keys_loaded0 keys_loaded1 kidx_loaded0 kidx_loaded1 staged k_transposed kT_copied "
                              "ki_transposed kiT_copied l_summed l_copied r_summed r_copied l_stored sp_passed pe_passed")
        keys_loaded, kidx_loaded = sems[0:2], sems[2:4]
        (staged, k_transposed, kT_copied, ki_transposed, kiT_copied, l_summed, l_copied, r_summed, r_copied,
         l_stored, sp_passed, pe_passed) = sems[4:]
        spans = [(a, min(a + 512, past)) for a in range(0, past, 512)]

        with nc.Block() as block:

            @block.sync
            def _(sp):
                def one(i, s):
                    b = i * TURN + s
                    if has(i, s, TURN, TURN):
                        sp.wait_ge(k_transposed, b - 1)
                        sp.sem_inc(sp_passed, 1)
                        if kidx:
                            sp.wait_ge(ki_transposed, b - 1)
                            sp.sem_inc(sp_passed, 1)
                    load_keys(sp, b, K[s], V, Ki[s], keys_loaded[s], kidx_loaded[s])

                turns(sp, NB, TURN, one)
                sp.wait_ge(l_stored, stores * NB)

            @block.vector
            def _(dve):
                def one(i, s):
                    b = i * TURN + s
                    if kidx and has(i, s, TURN, 1):
                        dve.wait_ge(r_summed, b)
                    dve.tensor_copy(Qb[:, :], st.Qz[:, bass.ds(b, 1), :].rearrange("p one h -> p (one h)"))\
                       .then_inc(staged, 1)
                    dve.tensor_copy(KT[:, past:past + 1], st.KnT[:, branch, bass.ds(b, 1)]).then_inc(staged, 1)
                    if kidx:
                        dve.tensor_copy(Qib[:, :], kidx[0][:, bass.ds(b, 1), :].rearrange("p one i -> p (one i)"))\
                           .then_inc(staged, 1)
                        dve.tensor_copy(KiT[:, past:past + 1], kidx[1][:, bass.ds(b, 1)]).then_inc(staged, 1)
                        dve.wait_ge(ki_transposed, b + 1)
                        dve.tensor_copy(KiT[:, 0:past], ti_ps[:, 0:n_tiles, :].rearrange("p j s -> p (j s)"))\
                           .then_inc(kiT_copied, 1)
                    if has(i, s, TURN, TURN):
                        dve.wait_ge(l_stored, (b - 1) * stores)
                    dve.wait_ge(l_summed, b + 1)
                    dve.tensor_copy(L[s][:, 0:past], l_ps[:, 0:past]).then_inc(l_copied, 1)
                    dve.tensor_copy(L[s][:, past:past + 1], new_ps[:, 0:1]).then_inc(l_copied, 1)

                turns(dve, NB, TURN, one)

            @block.scalar
            def _(act):
                def one(i, s):
                    b = i * TURN + s
                    act.wait_ge(k_transposed, b + 1)
                    act.copy(KT[:, 0:past], t_ps[:, 0:n_tiles, :].rearrange("p j s -> p (j s)")).then_inc(kT_copied, 1)
                    if kidx:
                        act.wait_ge(r_summed, b + 1)
                        act.activation(R[s][:, 0:past], l_ps[0:IDXH, 0:past], ACT.Relu).then_inc(r_copied, 1)
                        act.activation(R[s][:, past:past + 1], new_ps[0:IDXH, 1:2], ACT.Relu).then_inc(r_copied, 1)
                    if has(i, s, TURN, 1):
                        act.wait_ge(l_stored, b * stores)
                    act.wait_ge(l_copied, (b + 1) * 2)
                    act.dma_start(Ls[bass.ds(b * NH, NH), 0:past + 1], L[s][:, :]).then_inc(l_stored, 16)
                    if kidx:
                        act.wait_ge(r_copied, (b + 1) * 2)
                        act.dma_start(Rs[bass.ds(b, 1)].rearrange("one i n -> (one i) n"), R[s][:, :])\
                           .then_inc(l_stored, 16)

                turns(act, NB, TURN, one)

            @block.tensor
            def _(pe):
                def one(i, s):
                    b = i * TURN + s
                    if has(i, s, TURN, 1):
                        pe.wait_ge(kT_copied, b)
                    pe.wait_ge(keys_loaded[s], (i + 1) * (16 * 2 * n_tiles))
                    for j in range(n_tiles):
                        last = pe.transpose(t_ps[:, j, :], K[s][:, j, :], ident[:, :])
                    last.then_inc(k_transposed, 1)
                    if kidx:
                        if has(i, s, TURN, 1):
                            pe.wait_ge(kiT_copied, b)
                        pe.wait_ge(kidx_loaded[s], (i + 1) * (16 * n_tiles))
                        pe.sem_inc(pe_passed, 1)
                        for j in range(n_tiles):
                            last = pe.transpose(ti_ps[:, j, :], Ki[s][:, j, :], ident[:, :])
                        last.then_inc(ki_transposed, 1)
                    pe.wait_ge(staged, (b + 1) * steps)
                    if has(i, s, TURN, 1):
                        pe.wait_ge(r_copied if kidx else l_copied, b * 2)
                    pe.wait_ge(kT_copied, b + 1)
                    for a, e in spans:
                        pe.matmul(l_ps[:, a:e], Qb[:, :], KT[:, a:e], start=True, stop=True)
                    pe.matmul(new_ps[:, 0:1], Qb[:, :], KT[:, past:past + 1], start=True, stop=True)\
                      .then_inc(l_summed, 1)
                    if kidx:
                        pe.wait_ge(kiT_copied, b + 1)
                        pe.wait_ge(l_copied, (b + 1) * 2)
                        pe.sem_inc(pe_passed, 1)
                        for a, e in spans:
                            pe.matmul(l_ps[0:IDXH, a:e], Qib[:, :], KiT[:, a:e], start=True, stop=True)
                        pe.matmul(new_ps[0:IDXH, 1:2], Qib[:, :], KiT[:, past:past + 1], start=True, stop=True)\
                          .then_inc(r_summed, 1)

                turns(pe, NB, TURN, one)
        clear_signals(nc, sems)


def sample_attend(nc, G, st, n_tiles, branch, V, first_key, gate, accumulate):
    ident, row_bias = G["ident"], G["row_bias"]
    past = n_tiles * P
    W = past + 1
    R = NB * NH
    with ExitStack() as c:
        S = tile_of(nc, c, "s_S", [R, W])
        PT = tile_of(nc, c, "s_PT", [P, n_tiles, R])
        PTn = tile_of(nc, c, "s_PTn", [1, R])
        mx = tile_of(nc, c, "s_mx", [R, 4])
        t_ps = bank_of(nc, c, "s_pt_ps", [P, n_tiles, R])
        tn_ps = bank_of(nc, c, "s_ptn_ps", [1, R])
        o_ps = bank_of(nc, c, "s_o_ps", [P, R])
        sems = signals(nc, c, "l_loaded masked max_made exp_done scaled transposed pT_copied o_summed")
        l_loaded, masked, max_made, exp_done, scaled, transposed, pT_copied, o_summed = sems
        with nc.Block() as block:

            @block.sync
            def _(sp):
                sp.dma_start(S[:, :], G["s_logits"][:, 0:W]).then_inc(l_loaded, 16)

            @block.vector
            def _(dve):
                step = InOrder(dve)
                dve.wait_ge(l_loaded, 16)
                step(dve.tensor_tensor(S[:, :], S[:, :], row_bias[:, first_key:first_key + W], ALU.add), masked)
                step(dve.tensor_tensor(S[:, :], S[:, :], st.mask[:, first_key:first_key + W], ALU.add), masked)
                step(dve.tensor_reduce(mx[:, 0:1], S[:, :], AX.X, ALU.max, negate=True), max_made)
                dve.wait_ge(exp_done, 1)
                step(dve.reciprocal(mx[:, 2:3], mx[:, 1:2]), masked)
                step(dve.tensor_scalar(S[:, :], S[:, :], mx[:, 2:3], st.scale[:, gate:gate + 1], ALU.mult, ALU.mult),
                     scaled)
                dve.wait_ge(transposed, 1)
                dve.tensor_copy(PT[:, :, :], t_ps[:, :, :]).then_inc(pT_copied, 1)
                dve.tensor_copy(PTn[:, :], tn_ps[:, :]).then_inc(pT_copied, 1)
                dve.wait_ge(o_summed, 1)
                if accumulate:
                    step(dve.tensor_tensor(st.oT[:, :], st.oT[:, :], o_ps[:, :], ALU.add), masked)
                else:
                    step(dve.tensor_copy(st.oT[:, :], o_ps[:, :]), masked)

            @block.scalar
            def _(act):
                act.wait_ge(max_made, 1)
                act.activation(S[:, :], S[:, :], ACT.Exp, bias=mx[:, 0:1], accum_out=mx[:, 1:2]).then_inc(exp_done, 1)

            @block.tensor
            def _(pe):
                pe.wait_ge(scaled, 1)
                for j in range(n_tiles):
                    pe.transpose(t_ps[:, j, :], S[:, j * P:(j + 1) * P], ident[0:R, 0:R])
                pe.transpose(tn_ps[:, :], S[:, past:W], ident[0:R, 0:R]).then_inc(transposed, 1)
                pe.wait_ge(pT_copied, 2)
                for b in range(NB):
                    cols = slice(b * NH, (b + 1) * NH)
                    for j in range(n_tiles):
                        pe.matmul(o_ps[:, cols], V[:, b * n_tiles + j, :], PT[:, j, cols], start=(j == 0), stop=False)
                    last = pe.matmul(o_ps[:, cols], st.Vn[0:1, branch, b, :], PTn[:, cols], start=False, stop=True)
                last.then_inc(o_summed, 1)
        clear_signals(nc, sems)


def sample_concat(nc, G, st, layer_kind="even"):
    ident, featT = G["ident"], G["featT"]
    R = NB * NH
    with ExitStack() as c:
        rows = tile_of(nc, c, "s_orow", [R, P])
        o_ps = bank_of(nc, c, "s_or_ps", [R, P])
        t_ps = bank_of(nc, c, "s_cat_ps", [P, KC, NB])
        sems = signals(nc, c, "o_transposed o_copied o_stored cat_loaded cat_transposed")
        o_transposed, o_copied, o_stored, cat_loaded, cat_transposed = sems
        odd = layer_kind == "odd"
        at = A_Q if odd else 0
        with nc.Block() as block:

            @block.tensor
            def _(pe):
                pe.transpose(o_ps[:, :], st.oT[:, :], ident[:, :]).then_inc(o_transposed, 1)
                pe.wait_ge(cat_loaded, 48 if odd else 32)
                for k in range(KC):
                    last = pe.transpose(t_ps[:, k, :], st.cat[:, k * P:(k + 1) * P], ident[0:NB, 0:NB])
                last.then_inc(cat_transposed, 1)

            @block.vector
            def _(dve):
                dve.wait_ge(o_transposed, 1)
                dve.tensor_copy(rows[:, :], o_ps[:, :]).then_inc(o_copied, 1)
                dve.wait_ge(cat_transposed, 1)
                dve.tensor_copy(featT[:, :, SEQ:TOK], t_ps[:, :, :])

            @block.sync
            def _(sp):
                sp.wait_ge(o_copied, 1)
                sp.dma_start(G["s_rows"], rows[:, :]).then_inc(o_stored, 16)
                sp.wait_ge(o_stored, 16)
                for kv in range(NKV):
                    src = G["s_rows"].rearrange("(b a g) n -> b a g n", b=NB, a=NKV)[:, kv, :, kv * HD:(kv + 1) * HD]
                    cols = slice(at + kv * GQA * HD, at + (kv + 1) * GQA * HD)
                    sp.dma_start(st.cat[:, cols].rearrange("b (g d) -> b g d", d=HD), src).then_inc(cat_loaded, 16)
                if odd:
                    sp.dma_start(st.cat[:, 0:RW].rearrange("b (h d) -> b h d", d=HD),
                                 G["s_rows_c"].rearrange("(b h) d -> b h d", h=NH)).then_inc(cat_loaded, 16)
        clear_signals(nc, sems)


def page_loads(sp, G, b, cache, sources):
    n_pool = cache.shape[0]
    for j in range(PAGES):
        page = sp.value_load(G["pages"][0:1, bass.ds(b * PAGES + j, 1)], min_val=0, max_val=n_pool - 1)
        for dst, cache_view, sem in sources:
            sp.dma_start(dst(j), cache_view(page)).then_inc(sem, 16)


def stage_even_sample(nc, G):
    ident = G["ident"]
    z = G["z_even"]
    kv_cache = G["cache_a_kv"][0].rearrange("n s two kv d -> n s (two kv d)")
    ki_cache = G["cache_a_kidx"][0]
    kv_out = G["a_kv_s"][0].rearrange("b one two kv d -> b (one two kv d)")
    R = NB * NH
    with ExitStack() as c:
        st = SampleState(nc, c)
        wi = tile_of(nc, c, "s_wi", [NB, IDXH])
        QiT = tile_of(nc, c, "s_QiT", [HD, NB, IDXH])
        KiN = tile_of(nc, c, "s_KiN", [HD, NB])
        expand = tile_of(nc, c, "s_expand", [NB, R])

        with ExitStack() as c2:
            zs = tile_of(nc, c2, "s_z", [NB, P_EVEN])
            buf = tile_of(nc, c2, "s_buf", [NB, 2, CONV])
            cw = tile_of(nc, c2, "s_cw", [NB, 4, CONV])
            tmp = tile_of(nc, c2, "s_tmp", [NB, 3, CONV])
            gq = tile_of(nc, c2, "s_gq", [NB, HD])
            gk = tile_of(nc, c2, "s_gk", [NB, HD])
            qn = tile_of(nc, c2, "s_qn", [NB, 5, NKV, HD])
            sq = tile_of(nc, c2, "s_sq", [NB, 10, HD])
            rms = tile_of(nc, c2, "s_rms", [NB, 3, 10])
            t_ps = bank_of(nc, c2, "s_prep_ps", [P, 5, NB])
            i_ps = bank_of(nc, c2, "s_prepi_ps", [HD, 5, NB])
            sems = signals(nc, c2, "z_loaded w_loaded cleared expand_cut1 expand_made normed mean_made rms_made kn_ready "
                                   "transposed conv_step u_made conv_made stored")
            (z_loaded, w_loaded, cleared, expand_cut1, expand_made, normed, mean_made, rms_made, kn_ready, transposed,
             conv_step, u_made, conv_made, stored) = sems
            with nc.Block() as block:

                @block.sync
                def _(sp):
                    sp.dma_start(zs[:, :], z[Z_S:Z_S + NB, :]).then_inc(z_loaded, 16)
                    sp.dma_start(st.Vn[0:1, 0, :, :], z[Z_S:Z_S + NB, E_V:E_QI].unsqueeze(0)).then_inc(z_loaded, 16)
                    for j in range(3):
                        sp.dma_start(cw[:, j, :], G["b_conv_w"][0, j].partition_broadcast(NB)).then_inc(w_loaded, 16)
                    sp.dma_start(cw[:, 3, :], G["b_conv_b"][0].partition_broadcast(NB)).then_inc(w_loaded, 16)
                    sp.dma_start(gq[:, :], G["a_q_norm"][0].partition_broadcast(NB)).then_inc(w_loaded, 16)
                    sp.dma_start(gk[:, :], G["a_k_norm"][0].partition_broadcast(NB)).then_inc(w_loaded, 16)
                    sp.dma_start(buf[:, :, :], G["state_b_conv"][0]).then_inc(w_loaded, 16)
                    sp.wait_ge(z_loaded, 32)
                    sp.wait_ge(w_loaded, 112)
                    sp.dma_start(kv_out[:, KVW:A_KV], zs[:, E_V:E_QI]).then_inc(stored, 16)
                    sp.dma_start(G["a_kidx_s"][0, :, 0, :], zs[:, E_KI:E_WI]).then_inc(stored, 16)
                    sp.dma_start(G["b_conv_s"][0, :, 0, :], buf[:, 1, :]).then_inc(stored, 16)
                    sp.wait_ge(kn_ready, 1)
                    sp.dma_start(kv_out[:, 0:KVW], qn[:, 4, :, :].rearrange("p a d -> p (a d)")).then_inc(stored, 16)
                    sp.wait_ge(u_made, 1)
                    sp.dma_start(G["b_conv_s"][0, :, 1, :], tmp[:, 0, :]).then_inc(stored, 16)
                    sp.wait_ge(stored, 80)

                @block.gpsimd
                def _(pool):
                    step = InOrder(pool)
                    pool.memset(st.mask[:, :], 0.0).then_inc(cleared, 1)
                    pool.memset(st.scale[:, :], 1.0).then_inc(cleared, 1)
                    pool.memset(expand[:, :], 1.0).then_inc(cleared, 1)
                    pool.memset(st.Qz[:, :, :], 0.0).then_inc(cleared, 1)
                    pool.wait_ge(cleared, 4)
                    step(pool.affine_select(out=expand[:, :], in_=expand[:, :], compare_op=ALU.is_ge, fill=0.0,
                                            base=0, pattern=[[1, R]], channel_multiplier=-NH), expand_cut1)
                    step(pool.affine_select(out=expand[:, :], in_=expand[:, :], compare_op=ALU.is_ge, fill=0.0,
                                            base=NH - 1, pattern=[[-1, R]], channel_multiplier=NH), expand_made)
                    pool.wait_ge(z_loaded, 32)
                    pool.wait_ge(w_loaded, 112)
                    step(pool.tensor_tensor(tmp[:, 0, :], zs[:, E_CG:E_XIN], zs[:, E_XIN:P_EVEN], ALU.mult), u_made)
                    step(pool.tensor_tensor(tmp[:, 1, :], buf[:, 0, :], cw[:, 0, :], ALU.mult), conv_step)
                    step(pool.tensor_tensor(tmp[:, 1, :], tmp[:, 1, :], cw[:, 3, :], ALU.add), conv_step)
                    step(pool.tensor_tensor(tmp[:, 2, :], buf[:, 1, :], cw[:, 1, :], ALU.mult), conv_step)
                    step(pool.tensor_tensor(tmp[:, 1, :], tmp[:, 1, :], tmp[:, 2, :], ALU.add), conv_step)
                    step(pool.tensor_tensor(tmp[:, 2, :], tmp[:, 0, :], cw[:, 2, :], ALU.mult), conv_step)
                    step(pool.tensor_tensor(tmp[:, 1, :], tmp[:, 1, :], tmp[:, 2, :], ALU.add), conv_step)
                    step(pool.tensor_tensor(st.cat[:, A_Q:D], tmp[:, 1, :], zs[:, E_BG:E_CG], ALU.mult), conv_made)

                @block.scalar
                def _(act):
                    act.wait_ge(mean_made, 1)
                    act.activation(rms[:, 1, :], rms[:, 0, :], ACT.Sqrt).then_inc(rms_made, 1)

                @block.tensor
                def _(pe):
                    pe.wait_ge(kn_ready, 1)
                    for g in range(5):
                        pe.transpose(t_ps[:, g, :], qn[:, g, :, :].rearrange("p a d -> p (a d)"), ident[0:NB, 0:NB])
                    for g in range(5):
                        last = pe.transpose(i_ps[:, g, :], zs[:, E_QI + g * HD:E_QI + (g + 1) * HD], ident[0:NB, 0:NB])
                    last.then_inc(transposed, 1)

                @block.vector
                def _(dve):
                    step = InOrder(dve)
                    dve.wait_ge(z_loaded, 32)
                    dve.wait_ge(w_loaded, 112)
                    step(dve.tensor_scalar(gq[:, :], gq[:, :], HD ** -0.5, None, ALU.mult), normed)
                    qk = zs[:, 0:10 * HD].rearrange("p (h d) -> p h d", d=HD)
                    step(dve.tensor_tensor(sq[:, :, :], qk, qk, ALU.mult), normed)
                    step(dve.tensor_reduce(rms[:, 0, :], sq[:, :, :], AX.X, ALU.add), normed)
                    step(dve.tensor_scalar(rms[:, 0, :], rms[:, 0, :], 1.0 / HD, RMS_EPS, ALU.mult, ALU.add),
                         mean_made)
                    step(dve.tensor_scalar(wi[:, :], zs[:, E_WI:E_BG], (IDXH * HD) ** -0.5, None, ALU.mult), normed)
                    dve.wait_ge(rms_made, 1)
                    step(dve.reciprocal(rms[:, 2, :], rms[:, 1, :]), normed)
                    for kv in range(NKV):
                        cols = slice(kv * GQA * HD, (kv + 1) * GQA * HD)
                        r = rms[:, 2, kv * GQA:(kv + 1) * GQA].unsqueeze(2).broadcast_to([NB, GQA, HD])
                        step(dve.tensor_tensor(qn[:, 0:GQA, kv, :], zs[:, cols].rearrange("p (g d) -> p g d", d=HD),
                                               r, ALU.mult), normed)
                        step(dve.tensor_tensor(qn[:, 0:GQA, kv, :], qn[:, 0:GQA, kv, :],
                                               gq[:, :].unsqueeze(1).broadcast_to([NB, GQA, HD]), ALU.mult), normed)
                    r = rms[:, 2, NH:NH + NKV].unsqueeze(2).broadcast_to([NB, NKV, HD])
                    step(dve.tensor_tensor(qn[:, GQA, :, :], zs[:, E_K:E_V].rearrange("p (g d) -> p g d", d=HD),
                                           r, ALU.mult), normed)
                    step(dve.tensor_tensor(qn[:, GQA, :, :], qn[:, GQA, :, :],
                                           gk[:, :].unsqueeze(1).broadcast_to([NB, NKV, HD]), ALU.mult), kn_ready)
                    dve.wait_ge(transposed, 1)
                    dve.wait_ge(cleared, 4)
                    for kv in range(NKV):
                        half = slice(kv * HD, (kv + 1) * HD)
                        dve.tensor_copy(st.Qz[half, :, kv * GQA:(kv + 1) * GQA],
                                        t_ps[half, 0:GQA, :].rearrange("p g b -> p b g"))
                    dve.tensor_copy(st.KnT[:, 0, :], t_ps[:, 4, :])
                    dve.tensor_copy(QiT[:, :, :], i_ps[:, 0:IDXH, :].rearrange("p i b -> p b i"))
                    dve.tensor_copy(KiN[:, :], i_ps[:, IDXH, :])
            clear_signals(nc, sems)

        V = tile_of(nc, c, "s_V", [P, NB * PAGES, P])

        def load(sp, b, K, V, Ki, keys_loaded, kidx_loaded):
            page_loads(sp, G, b, kv_cache, [
                (lambda j: K[:, j, :], lambda page: kv_cache[page, :, 0:KVW], keys_loaded),
                (lambda j: V[:, bass.ds(b * PAGES + j, 1), :], lambda page: kv_cache[page, :, KVW:A_KV].unsqueeze(1), keys_loaded),
                (lambda j: Ki[:, j, :], lambda page: ki_cache[page], kidx_loaded),
            ])

        sample_logits(nc, G, st, "a", load, PAGES, 0, V, (QiT, KiN))

        with ExitStack() as c2:
            rel = tile_of(nc, c2, "s_rel_rows", [NB, IDXH, PAST + 1])
            score = tile_of(nc, c2, "s_score", [NB, PAST + 1])
            top8 = tile_of(nc, c2, "s_top8", [NB, 8])
            m_ps = bank_of(nc, c2, "s_m_ps", [R, 3, 512])
            sems = signals(nc, c2, "rel_loaded scored picked mask_made spread")
            rel_loaded, scored, picked, mask_made, spread = sems
            spans = ((0, 512), (512, 1024), (1024, 1025))
            with nc.Block() as block:

                @block.sync
                def _(sp):
                    sp.dma_start(rel[:, :, :], G["s_rel"]).then_inc(rel_loaded, 16)

                @block.vector
                def _(dve):
                    step = InOrder(dve)
                    dve.wait_ge(rel_loaded, 16)
                    step(dve.tensor_scalar(score[:, :], rel[:, 0, :], wi[:, 0:1], None, ALU.mult), scored)
                    for i in range(1, IDXH):
                        step(dve.scalar_tensor_tensor(score[:, :], rel[:, i, :], wi[:, i:i + 1], score[:, :],
                                                      ALU.mult, ALU.add), scored)
                    for _ in range(TOPK // 8):
                        step(dve.max(top8[:, :], score[:, :]), picked)
                        step(dve.match_replace(score[:, :], top8[:, :], score[:, :], TAKEN), picked)
                    step(dve.tensor_scalar(score[:, :], score[:, :], TAKEN / 2, NEG, ALU.is_gt, ALU.mult), mask_made)
                    dve.wait_ge(spread, 1)
                    for i, (a, e) in enumerate(spans):
                        dve.tensor_copy(st.mask[:, a:e], m_ps[:, i, 0:e - a])

                @block.tensor
                def _(pe):
                    pe.wait_ge(mask_made, 1)
                    for i, (a, e) in enumerate(spans):
                        last = pe.matmul(m_ps[:, i, 0:e - a], expand[:, :], score[:, a:e], start=True, stop=True)
                    last.then_inc(spread, 1)
            clear_signals(nc, sems)

        sample_attend(nc, G, st, PAGES, 0, V, 0, 0, False)
        sample_concat(nc, G, st)


BLOCKS = -(-2 * TOK // ROUTE_BLOCK) + NEXP
NT = TILES + 1
EPG = NEXP // NGRP
PLAN_EXPERT, PLAN_NEXT, PLAN_HALF, PLAN_OTHER, PLAN_FIRST, PLAN_LOADED, PLAN_RUN = range(7)
PLAN_ROWS = 7
BLOCK_TURN = 3
ALWAYS = -(-(-(-2 * TOK // ROUTE_BLOCK)) // BLOCK_TURN) * BLOCK_TURN
LOAD_COUNT = 3 * 16


def rank_of(step, dve, rank, flags, x, n, sem):
    step(dve.memset(rank, 0.0), sem)
    for r in range(1, n):
        f = flags[:, :, 0:n - r]
        step(dve.tensor_tensor(f, x[:, :, 0:n - r], x[:, :, r:n], ALU.is_ge), sem)
        step(dve.tensor_tensor(rank[:, :, r:n], rank[:, :, r:n], f, ALU.add), sem)
        step(dve.tensor_scalar(f, f, -1.0, 1.0, ALU.mult, ALU.add), sem)
        step(dve.tensor_tensor(rank[:, :, 0:n - r], rank[:, :, 0:n - r], f, ALU.add), sem)


def stage_route(nc, G, M, fill):
    featT, ones = G["featT"], G["ones"]
    E3 = NT * NEXP
    with ExitStack() as c:
        wr = tile_of(nc, c, "w_router_sb", [P, KC, NEXP])
        br = tile_of(nc, c, "b_router_sb", [P, NEXP])
        tri = tile_of(nc, c, "tri", [P, P])
        valid = tile_of(nc, c, "valid", [P, NT])
        ids = tile_of(nc, c, "token_ids", [P, NT], I32)
        zero_rows = tile_of(nc, c, "zero_rows", [P, D])
        zero_ids = tile_of(nc, c, "zero_ids", [P, BLOCKS], I32)
        kth = tile_of(nc, c, "block_number", [P, BLOCKS, 1], I32)
        turn_first = tile_of(nc, c, "turn_first", [P, BLOCKS // BLOCK_TURN, BLOCK_TURN], I32)
        kthf = tile_of(nc, c, "block_number_f", [P, BLOCKS, 1])
        s = tile_of(nc, c, "r_s", [P, NT, NEXP])
        sel = tile_of(nc, c, "r_sel", [P, NT, NEXP])
        rank = tile_of(nc, c, "r_rank", [P, NT * NGRP, EPG])
        flags = tile_of(nc, c, "r_flags", [P, NT * NGRP, EPG])
        pairs = tile_of(nc, c, "r_pairs", [P, NT * NGRP, 6])
        grp = tile_of(nc, c, "r_grp", [P, NT, NGRP])
        grank = tile_of(nc, c, "r_grank", [P, NT, NGRP])
        gflags = tile_of(nc, c, "r_gflags", [P, NT, NGRP])
        took = tile_of(nc, c, "r_took", [P, NT, NEXP])
        w = tile_of(nc, c, "r_w", [P, NT, NEXP])
        wsum = tile_of(nc, c, "r_wsum", [P, NT])
        pos = tile_of(nc, c, "r_pos", [P, NT, NEXP])
        tot = tile_of(nc, c, "r_tot", [P, NT, NEXP])
        blk = tile_of(nc, c, "r_blk", [P, NT, NEXP])
        count = tile_of(nc, c, "r_count", [P, NEXP])
        nblk = tile_of(nc, c, "r_nblk", [P, NEXP])
        ends = [tile_of(nc, c, f"r_ends{i}", [P, NEXP]) for i in range(2)]
        slot = tile_of(nc, c, "r_slot", [P, NT, NEXP])
        tmp = tile_of(nc, c, "r_tmp", [P, NT, NEXP])
        dst = tile_of(nc, c, "r_dst", [P, NT, 2])
        be = tile_of(nc, c, "r_be", [P, BLOCKS, NEXP])
        bef = tile_of(nc, c, "r_bef", [P, BLOCKS])
        be2 = tile_of(nc, c, "r_be2", [P, BLOCKS, NEXP])
        plan = tile_of(nc, c, "r_plan", [P, PLAN_ROWS, BLOCKS])
        nonempty = tile_of(nc, c, "r_nonempty", [P, NEXP])
        count_k = tile_of(nc, c, "r_count_k", [P, BLOCKS])
        l_ps = bank_of(nc, c, "r_l_ps", [P, NT, NEXP])
        pos_ps = bank_of(nc, c, "r_pos_ps", [P, E3])
        tot_ps = bank_of(nc, c, "r_tot_ps", [P, E3])
        sems = signals(nc, c, "w_loaded filled cut s_cleared r_summed sigmoid_done chain took_made pos_summed idx_made "
                              "slots_cleared scattered outputs_filled")
        (w_loaded, filled, cut, s_cleared, r_summed, sigmoid_done, chain, took_made, pos_summed, idx_made,
         slots_cleared, scattered, outputs_filled) = sems
        with nc.Block() as block:

            @block.sync
            def _(sp):
                sp.dma_start(wr[:, :, :], G["w_router"].rearrange("(k p) e -> p k e", p=P)).then_inc(w_loaded, 16)
                sp.dma_start(br[:, :], G["b_router"].partition_broadcast(P)).then_inc(w_loaded, 16)
                sp.wait_ge(filled, 9)
                sp.dma_start(G["slot_token"].rearrange("(p k) one -> p (k one)", p=P), zero_ids[:, :])\
                  .then_inc(slots_cleared, 16)
                if fill:
                    rest = G["y_slots"].rearrange("(p k) n -> p k n", p=P)[:, ALWAYS:BLOCKS, :]
                    sp.dma_start(rest, zero_rows[:, :].unsqueeze(1).broadcast_to([P, BLOCKS - ALWAYS, D]))\
                      .then_inc(outputs_filled, 16)
                    sp.wait_ge(outputs_filled, 16)
                sp.wait_ge(slots_cleared, 16)

            @block.gpsimd
            def _(pool):
                pool.memset(tri[:, :], 1.0).then_inc(filled, 1)
                pool.memset(valid[:, :], 1.0).then_inc(filled, 1)
                pool.memset(s[:, :, :], 0.0).then_inc(filled, 1)
                pool.memset(M.idx[:, :, :], 0).then_inc(filled, 1)
                pool.iota(ids[:, :], pattern=[[P, NT]], base=0, channel_multiplier=1).then_inc(filled, 1)
                pool.iota(kth[:, :, :], pattern=[[1, BLOCKS], [0, 1]], base=0, channel_multiplier=0).then_inc(filled, 1)
                pool.iota(turn_first[:, :, :], pattern=[[BLOCK_TURN, BLOCKS // BLOCK_TURN], [0, BLOCK_TURN]], base=0,
                          channel_multiplier=0).then_inc(filled, 1)
                pool.memset(zero_ids[:, :], 0).then_inc(filled, 1)
                pool.memset(zero_rows[:, :], 0.0).then_inc(filled, 1)
                pool.wait_ge(filled, 9)
                pool.affine_select(out=tri[:, :], in_=tri[:, :], compare_op=ALU.is_gt, fill=0.0, base=0,
                                   pattern=[[1, P]], channel_multiplier=-1).then_inc(cut, 1)
                pool.affine_select(out=valid[:, TILES:NT], in_=valid[:, TILES:NT], compare_op=ALU.is_ge, fill=0.0,
                                   base=NB - 1, pattern=[[0, 1]], channel_multiplier=-1).then_inc(cut, 1)
                pool.wait_ge(idx_made, 1)
                pool.wait_ge(slots_cleared, 16)
                for t in range(NT):
                    rows = P if t < TILES else NB
                    for j in range(2):
                        pool.indirect_dma_start(
                            out=G["slot_token"], out_offset=bass.IndirectOffsetOnAxis(ap=M.idx[0:rows, t, j:j + 1], axis=0),
                            in_=ids[0:rows, t:t + 1], in_offset=None).then_inc(scattered, 16)
                pool.wait_ge(scattered, 16 * 2 * NT)

            @block.tensor
            def _(pe):
                pe.wait_ge(w_loaded, 32)
                for t in range(NT):
                    rows = P if t < TILES else NB
                    for k in range(KC):
                        last = pe.matmul(l_ps[0:rows, t, :], featT[:, k, t * P:t * P + rows], wr[:, k, :],
                                         start=(k == 0), stop=(k == KC - 1))
                last.then_inc(r_summed, 1)
                pe.wait_ge(took_made, 1)
                pe.wait_ge(cut, 2)
                took2 = took[:, :, :].rearrange("p t e -> p (t e)")
                pe.matmul(pos_ps[:, :], tri[:, :], took2, start=True, stop=True)
                pe.matmul(tot_ps[:, :], ones[:, :], took2, start=True, stop=True).then_inc(pos_summed, 1)

            @block.scalar
            def _(act):
                act.wait_ge(r_summed, 1)
                act.wait_ge(filled, 9)
                act.activation(s[:, 0:TILES, :], l_ps[:, 0:TILES, :], ACT.Sigmoid).then_inc(sigmoid_done, 1)
                act.activation(s[0:NB, TILES, :], l_ps[0:NB, TILES, :], ACT.Sigmoid).then_inc(sigmoid_done, 1)

            @block.vector
            def _(dve):
                step = InOrder(dve)
                dve.wait_ge(w_loaded, 32)
                dve.wait_ge(filled, 9)
                dve.wait_ge(sigmoid_done, 2)
                dve.wait_ge(cut, 2)
                step(dve.tensor_copy(kthf[:, :, :], kth[:, :, :]), chain)
                step(dve.tensor_tensor(sel[:, :, :], s[:, :, :], br[:, :].unsqueeze(1).broadcast_to([P, NT, NEXP]),
                                       ALU.add), chain)
                x = sel[:, :, :].rearrange("p t (g e) -> p (t g) e", e=EPG)
                at = 0
                for r in range(1, EPG):
                    n = EPG - r
                    step(dve.tensor_tensor(pairs[:, :, at:at + n], x[:, :, 0:n], x[:, :, r:EPG], ALU.add), chain)
                    at += n
                step(dve.tensor_reduce(grp[:, :, :].rearrange("p t g -> p (t g)"), pairs[:, :, :], AX.X, ALU.max), chain)
                rank_of(step, dve, grank[:, :, :], gflags[:, :, :], grp[:, :, :], NGRP, chain)
                step(dve.tensor_scalar(grank[:, :, :], grank[:, :, :], 0.5, None, ALU.is_lt), chain)
                step(dve.tensor_tensor(grank[:, :, :], grank[:, :, :],
                                       valid[:, :].unsqueeze(2).broadcast_to([P, NT, NGRP]), ALU.mult), chain)
                rank_of(step, dve, rank[:, :, :], flags[:, :, :], x, EPG, chain)
                step(dve.tensor_scalar(rank[:, :, :], rank[:, :, :], 1.5, None, ALU.is_lt), chain)
                step(dve.tensor_tensor(took[:, :, :].rearrange("p t (g e) -> p (t g) e", e=EPG), rank[:, :, :],
                                       grank[:, :, :].rearrange("p t g -> p (t g)").unsqueeze(2)
                                       .broadcast_to([P, NT * NGRP, EPG]), ALU.mult), took_made)
                step(dve.tensor_tensor(w[:, :, :], s[:, :, :], took[:, :, :], ALU.mult), chain)
                step(dve.tensor_reduce(wsum[:, :], w[:, :, :], AX.X, ALU.add), chain)
                step(dve.tensor_scalar(wsum[:, :], wsum[:, :], 1e-38, None, ALU.max), chain)
                step(dve.reciprocal(wsum[:, :], wsum[:, :]), chain)
                step(dve.tensor_tensor(w[:, :, :], w[:, :, :], wsum[:, :].unsqueeze(2).broadcast_to([P, NT, NEXP]),
                                       ALU.mult), chain)
                dve.wait_ge(pos_summed, 1)
                step(dve.tensor_copy(pos[:, :, :].rearrange("p t e -> p (t e)"), pos_ps[:, :]), chain)
                step(dve.tensor_copy(tot[:, :, :].rearrange("p t e -> p (t e)"), tot_ps[:, :]), chain)
                step(dve.tensor_copy(count[:, :], tot[:, 0, :]), chain)
                for t in range(1, NT):
                    step(dve.tensor_tensor(pos[:, t, :], pos[:, t, :], count[:, :], ALU.add), chain)
                    step(dve.tensor_tensor(count[:, :], count[:, :], tot[:, t, :], ALU.add), chain)
                step(dve.tensor_scalar(nblk[:, :], count[:, :], 0.5, None, ALU.is_gt), chain)
                for i in range(1, NT):
                    step(dve.scalar_tensor_tensor(nblk[:, :], count[:, :], i * P + 0.5, nblk[:, :], ALU.is_gt,
                                                  ALU.add), chain)
                step(dve.tensor_copy(ends[0][:, :], nblk[:, :]), chain)
                a = 0
                for r in (1, 2, 4, 8):
                    step(dve.tensor_copy(ends[1 - a][:, 0:r], ends[a][:, 0:r]), chain)
                    step(dve.tensor_tensor(ends[1 - a][:, r:NEXP], ends[a][:, r:NEXP], ends[a][:, 0:NEXP - r],
                                           ALU.add), chain)
                    a = 1 - a
                end = ends[a]
                step(dve.tensor_tensor(be[:, :, :], kthf[:, :, :].broadcast_to([P, BLOCKS, NEXP]),
                                       end[:, :].unsqueeze(1).broadcast_to([P, BLOCKS, NEXP]), ALU.is_ge), chain)
                step(dve.tensor_reduce(bef[:, :], be[:, :, :], AX.X, ALU.add), chain)
                step(dve.tensor_scalar(plan[:, PLAN_EXPERT, :], bef[:, :], NEXP - 1.0, None, ALU.min), chain)
                end_k = end[:, :].unsqueeze(1).broadcast_to([P, BLOCKS, NEXP])
                step(dve.tensor_tensor(be2[:, :, :], be[:, :, :], end_k, ALU.mult), chain)
                step(dve.tensor_reduce(bef[:, :], be2[:, :, :], AX.X, ALU.max), chain)
                step(dve.tensor_scalar(plan[:, PLAN_LOADED, :], bef[:, :], float(LOAD_COUNT), float(LOAD_COUNT),
                                       ALU.mult, ALU.add), chain)
                step(dve.tensor_scalar(nonempty[:, :], nblk[:, :], 0.5, None, ALU.is_gt), chain)
                step(dve.tensor_tensor(be2[:, :, :], be[:, :, :],
                                       nonempty[:, :].unsqueeze(1).broadcast_to([P, BLOCKS, NEXP]), ALU.mult), chain)
                half = plan[:, PLAN_HALF, :]
                step(dve.tensor_reduce(half, be2[:, :, :], AX.X, ALU.add), chain)
                step(dve.memset(plan[:, PLAN_FIRST, 0:1], 1.0), chain)
                step(dve.tensor_tensor(plan[:, PLAN_FIRST, 1:BLOCKS], half[:, 1:BLOCKS], half[:, 0:BLOCKS - 1],
                                       ALU.subtract), chain)
                for bit in (16, 8, 4, 2):
                    step(dve.tensor_scalar(count_k[:, :], half, bit - 0.5, -float(bit), ALU.is_gt, ALU.mult), chain)
                    step(dve.tensor_tensor(half, half, count_k[:, :], ALU.add), chain)
                step(dve.tensor_scalar(plan[:, PLAN_OTHER, :], half, -1.0, 1.0, ALU.mult, ALU.add), chain)
                step(dve.scalar_tensor_tensor(be2[:, :, :], be[:, :, :], 1e6, end_k, ALU.mult, ALU.add), chain)
                step(dve.tensor_reduce(bef[:, :], be2[:, :, :], AX.X, ALU.min), chain)
                step(dve.tensor_tensor(be2[:, :, :], bef[:, :].unsqueeze(2).broadcast_to([P, BLOCKS, NEXP]), end_k,
                                       ALU.is_ge), chain)
                step(dve.tensor_reduce(bef[:, :], be2[:, :, :], AX.X, ALU.add), chain)
                step(dve.tensor_scalar(plan[:, PLAN_NEXT, :], bef[:, :], NEXP - 1.0, None, ALU.min), chain)
                run = plan[:, PLAN_RUN, :]
                step(dve.tensor_copy(run, turn_first[:, :, :].rearrange("p n s -> p (n s)")), chain)
                step(dve.tensor_scalar(run, run, end[:, NEXP - 1:NEXP], None, ALU.is_lt), chain)
                step(dve.tensor_copy(M.plan[:, :, :], plan[0:1, :, :]), chain)
                step(dve.tensor_scalar(blk[:, :, :], pos[:, :, :], P - 0.5, None, ALU.is_gt), chain)
                for i in range(2, NT):
                    step(dve.scalar_tensor_tensor(blk[:, :, :], pos[:, :, :], i * P - 0.5, blk[:, :, :], ALU.is_gt,
                                                  ALU.add), chain)
                step(dve.scalar_tensor_tensor(slot[:, :, :], blk[:, :, :], -float(P), pos[:, :, :], ALU.mult, ALU.add),
                     chain)
                step(dve.scalar_tensor_tensor(slot[:, :, :], slot[:, :, :], float(BLOCKS), blk[:, :, :], ALU.mult,
                                              ALU.add), chain)
                step(dve.tensor_tensor(nblk[:, :], end[:, :], nblk[:, :], ALU.subtract), chain)
                step(dve.tensor_tensor(slot[:, :, :], slot[:, :, :],
                                       nblk[:, :].unsqueeze(1).broadcast_to([P, NT, NEXP]), ALU.add), chain)
                for j in range(2):
                    big = 1e6
                    eidx = kthf[:, 0:NEXP, 0].unsqueeze(1).broadcast_to([P, NT, NEXP])
                    if j == 0:
                        step(dve.tensor_scalar(tmp[:, :, :], took[:, :, :], -big, big, ALU.mult, ALU.add), chain)
                        step(dve.tensor_tensor(tmp[:, :, :], tmp[:, :, :], eidx, ALU.add), chain)
                        step(dve.tensor_reduce(wsum[:, :], tmp[:, :, :], AX.X, ALU.min), chain)
                    else:
                        step(dve.tensor_scalar(tmp[:, :, :], took[:, :, :], big, -big, ALU.mult, ALU.add), chain)
                        step(dve.tensor_tensor(tmp[:, :, :], tmp[:, :, :], eidx, ALU.add), chain)
                        step(dve.tensor_reduce(wsum[:, :], tmp[:, :, :], AX.X, ALU.max), chain)
                    step(dve.tensor_tensor(tmp[:, :, :], eidx, wsum[:, :].unsqueeze(2).broadcast_to([P, NT, NEXP]),
                                           ALU.is_equal), chain)
                    step(dve.tensor_tensor(be[:, 0:NT, :], tmp[:, :, :], slot[:, :, :], ALU.mult), chain)
                    step(dve.tensor_reduce(dst[:, :, j:j + 1].rearrange("p t one -> p (t one)"), be[:, 0:NT, :], AX.X, ALU.add), chain)
                    step(dve.tensor_tensor(be[:, 0:NT, :], tmp[:, :, :], w[:, :, :], ALU.mult), chain)
                    step(dve.tensor_reduce(M.wts[:, :, j:j + 1].rearrange("p t one -> p (t one)"), be[:, 0:NT, :], AX.X, ALU.add), chain)
                step(dve.tensor_copy(M.idx[:, 0:TILES, :], dst[:, 0:TILES, :]), chain)
                step(dve.tensor_copy(M.idx[0:NB, TILES, :], dst[0:NB, TILES, :]), idx_made)
        clear_signals(nc, sems, [scattered])


def stage_experts(nc, G, layer, M):
    ident = G["ident"]
    FC = DEXP // P
    TURN = BLOCK_TURN
    assert BLOCKS % TURN == 0
    views = [G["w_expert_gate"][layer].rearrange("e (k p) f -> p e k f", p=P),
             G["w_expert_up"][layer].rearrange("e (k p) f -> p e k f", p=P),
             G["w_expert_down"][layer].rearrange("e (k p) n -> p e k n", p=P)]
    y_slots = G["y_slots"].rearrange("(p k) n -> p k n", p=P)
    with ExitStack() as c:
        wg = tile_of(nc, c, "wg", [P, 2, KC, DEXP])
        wu = tile_of(nc, c, "wu", [P, 2, KC, DEXP])
        wd = tile_of(nc, c, "wd", [P, 2, FC, D])
        slots = tile_of(nc, c, "slots", [P, BLOCKS], I32)
        sid = [tile_of(nc, c, f"slot_ids{i}", [P, 1], I32) for i in range(TURN)]
        xb = [tile_of(nc, c, f"xb{i}", [P, D]) for i in range(TURN)]
        y = [tile_of(nc, c, f"y{i}", [P, D]) for i in range(TURN)]
        xT = tile_of(nc, c, "xT", [P, KC, P])
        sg = tile_of(nc, c, "sg", [P, DEXP])
        hid = tile_of(nc, c, "hid", [P, DEXP])
        hT = tile_of(nc, c, "hT", [P, FC, P])
        xT_ps = bank_of(nc, c, "xT_ps", [P, KC, P])
        g_ps = bank_of(nc, c, "g_ps", [P, DEXP])
        u_ps = bank_of(nc, c, "u_ps", [P, DEXP])
        hT_ps = bank_of(nc, c, "hT2_ps", [P, FC, P])
        y_ps = bank_of(nc, c, "y_ps", [P, D])

        sems = signals(nc, c, "slots_loaded sid_ready x_gathered x_transposed xT_dve xT_act g_summed u_summed "
                              "silu_done hid_made hid_transposed hT_copied y_summed y_dve y_act y_stored w_loaded sp_passed "
                              "pool_passed")
        (slots_loaded, sid_ready, x_gathered, x_transposed, xT_dve, xT_act, g_summed, u_summed, silu_done, hid_made,
         hid_transposed, hT_copied, y_summed, y_dve, y_act, y_stored, w_loaded, sp_passed,
         pool_passed) = sems


        def turns(eng, one):
            for s in range(TURN):
                one(s, s)
            with eng.Fori(1, BLOCKS // TURN - 1) as i:
                with eng.If(planned(eng, PLAN_RUN, i * TURN, 1) > 0):
                    for s in range(TURN):
                        one(i * TURN + s, s)
            with eng.If(planned(eng, PLAN_RUN, BLOCKS - TURN, 1) > 0):
                for s in range(TURN):
                    one(BLOCKS - TURN + s, s)

        def is_first_turn(b):
            return isinstance(b, int) and b < TURN

        def planned(eng, row, b, top):
            return eng.value_load(M.plan[0:1, row, bass.ds(b, 1)], min_val=0, max_val=top)

        with nc.Block() as block:

            @block.sync
            def _(sp):
                sp.dma_start(slots[:, :], G["slot_token"].rearrange("(p k) one -> p (k one)", p=P))\
                  .then_inc(slots_loaded, 16)
                e = planned(sp, PLAN_EXPERT, 0, NEXP - 1)
                for view, dst in zip(views, (wg, wu, wd)):
                    sp.dma_start(dst[:, 0:1, :, :], view[:, bass.ds(e, 1), :, :]).then_inc(w_loaded, 16)

                def one(b, s):
                    e = planned(sp, PLAN_NEXT, b, NEXP - 1)
                    other = planned(sp, PLAN_OTHER, b, 1)
                    first = planned(sp, PLAN_FIRST, b, 1)
                    loaded = planned(sp, PLAN_LOADED, b, LOAD_COUNT * (BLOCKS + 1))
                    if not (isinstance(b, int) and b == 0):
                        sp.wait_ge(y_summed, b * 2)
                    sp.wait_ge(w_loaded, loaded)
                    sp.sem_inc(sp_passed, 1)
                    for view, dst in zip(views, (wg, wu, wd)):
                        sp.dma_start(dst[:, bass.ds(other, 1), :, :], view[:, bass.ds(e, 1), :, :], cond=first)\
                          .then_inc(w_loaded, 16)
                    if not (isinstance(b, int) and b == 0):
                        sp.wait_ge(y_stored, b * 32)
                        sp.sem_inc(sp_passed, 1)
                    for n in range(2):
                        sp.wait_ge((y_dve, y_act)[n], b + 1)
                        sp.sem_inc(sp_passed, 1)
                        cols = slice(n * 512, (n + 1) * 512)
                        sp.dma_start(y_slots[:, bass.ds(b, 1), cols], y[s][:, cols].unsqueeze(1))\
                          .then_inc(y_stored, 16)
                    if s == TURN - 1:
                        sp.wait_ge(y_stored, (b + 1) * 32)
                        sp.wait_ge(w_loaded, (b + 2) * LOAD_COUNT)
                        sp.sem_inc(sp_passed, 1)

                turns(sp, one)

            @block.gpsimd
            def _(pool):
                pool.wait_ge(slots_loaded, 16)

                def gather(b, s):
                    pool.tensor_copy(sid[s][:, 0:1], slots[:, bass.ds(b, 1)]).then_inc(sid_ready, 1)
                    if not is_first_turn(b):
                        pool.wait_ge(x_transposed, (b - (TURN - 1)) * 2)
                    pool.wait_ge(sid_ready, b + 1)
                    pool.sem_inc(pool_passed, 1)
                    pool.indirect_dma_start(out=xb[s][:, :], out_offset=None, in_=G["h_rows"],
                                            in_offset=bass.IndirectOffsetOnAxis(ap=sid[s][:, 0:1], axis=0))\
                        .then_inc(x_gathered, 16)
                    pool.wait_ge(x_gathered, (b + 1) * 16)
                    pool.sem_inc(pool_passed, 1)

                def one(b, s):
                    if not (isinstance(b, int) and b == BLOCKS - 1):
                        gather(b + 1, (s + 1) % TURN)

                gather(0, 0)
                turns(pool, one)

            @block.tensor
            def _(pe):
                def transpose_rows(b, s):
                    pe.wait_ge(x_gathered, (b + 1) * 16)
                    for j in range(KC):
                        last = pe.transpose(xT_ps[:, j, :], xb[s][:, j * P:(j + 1) * P], ident[:, :])
                        if j % 4 == 3:
                            last.then_inc(x_transposed, 1)

                def one(b, s):
                    half = planned(pe, PLAN_HALF, b, 1)
                    loaded = planned(pe, PLAN_LOADED, b, LOAD_COUNT * (BLOCKS + 1))
                    pe.wait_ge(w_loaded, loaded)
                    pe.wait_ge(xT_dve, b + 1)
                    pe.wait_ge(xT_act, b + 1)
                    for ps, wt, sem in ((g_ps, wg, g_summed), (u_ps, wu, u_summed)):
                        for j in range(KC):
                            last = pe.matmul(ps[:, :], xT[:, j, :], wt[:, bass.ds(half, 1), j, :]
                                             .rearrange("p one f -> p (one f)"), start=(j == 0), stop=(j == KC - 1))
                        last.then_inc(sem, 1)
                    if not (isinstance(b, int) and b == BLOCKS - 1):
                        transpose_rows(b + 1, (s + 1) % TURN)
                    pe.wait_ge(hid_made, b + 1)
                    for f in range(FC):
                        last = pe.transpose(hT_ps[:, f, :], hid[:, f * P:(f + 1) * P], ident[:, :])
                    last.then_inc(hid_transposed, 1)
                    if not (isinstance(b, int) and b == 0):
                        pe.wait_ge(y_dve, b)
                        pe.wait_ge(y_act, b)
                    pe.wait_ge(hT_copied, b + 1)
                    for n in range(2):
                        for f in range(FC):
                            last = pe.matmul(y_ps[:, n * 512:(n + 1) * 512], hT[:, f, :],
                                             wd[:, bass.ds(half, 1), f, n * 512:(n + 1) * 512]
                                             .rearrange("p one f -> p (one f)"), start=(f == 0), stop=(f == FC - 1))
                        last.then_inc(y_summed, 1)

                transpose_rows(0, 0)
                turns(pe, one)

            @block.scalar
            def _(act):
                def copy_rows(b):
                    act.wait_ge(x_transposed, (b + 1) * 2)
                    act.copy(xT[:, 4:8, :], xT_ps[:, 4:8, :]).then_inc(xT_act, 1)

                def one(b, s):
                    act.wait_ge(g_summed, b + 1)
                    act.activation(sg[:, :], g_ps[:, :], ACT.Silu).then_inc(silu_done, 1)
                    if not (isinstance(b, int) and b == BLOCKS - 1):
                        copy_rows(b + 1)
                    if not is_first_turn(b):
                        act.wait_ge(y_stored, (b - (TURN - 1)) * 32)
                    act.wait_ge(y_summed, (b + 1) * 2)
                    act.copy(y[s][:, 512:D], y_ps[:, 512:D]).then_inc(y_act, 1)

                copy_rows(0)
                turns(act, one)

            @block.vector
            def _(dve):
                def copy_rows(b):
                    dve.wait_ge(x_transposed, b * 2 + 1)
                    dve.tensor_copy(xT[:, 0:4, :], xT_ps[:, 0:4, :]).then_inc(xT_dve, 1)

                def one(b, s):
                    dve.wait_ge(silu_done, b + 1)
                    dve.wait_ge(u_summed, b + 1)
                    dve.tensor_tensor(hid[:, :], sg[:, :], u_ps[:, :], ALU.mult).then_inc(hid_made, 1)
                    if not (isinstance(b, int) and b == BLOCKS - 1):
                        copy_rows(b + 1)
                    dve.wait_ge(hid_transposed, b + 1)
                    dve.tensor_copy(hT[:, :, :], hT_ps[:, :, :]).then_inc(hT_copied, 1)
                    if not is_first_turn(b):
                        dve.wait_ge(y_stored, (b - (TURN - 1)) * 32)
                    dve.wait_ge(y_summed, b * 2 + 1)
                    dve.tensor_copy(y[s][:, 0:512], y_ps[:, 0:512]).then_inc(y_dve, 1)

                copy_rows(0)
                turns(dve, one)
        clear_signals(nc, sems, [x_gathered])


def stage_combine(nc, G, layer, M, gate_row):
    x = G["x"]
    with ExitStack() as c:
        gate = tile_of(nc, c, "m_gate", [P, 2, D])
        sid = [[tile_of(nc, c, f"m_sid{s}{j}", [P, 1], I32) for j in range(2)] for s in range(2)]
        y = [[tile_of(nc, c, f"m_y{s}{j}", [P, D]) for j in range(2)] for s in range(2)]
        (loaded,) = setup = signals(nc, c, "gate_loaded")
        with nc.Block() as block:

            @block.sync
            def _(sp):
                cols = slice(gate_row * D, (gate_row + 1) * D)
                sp.dma_start(gate[:, 0, :], G["mod"][0, layer, cols].partition_broadcast(P)).then_inc(loaded, 16)
                sp.dma_start(gate[0:NB, 1, :], G["mod"][1:1 + NB, layer, cols]).then_inc(loaded, 16)
                sp.wait_ge(loaded, 32)
        clear_signals(nc, setup)
        sems = signals(nc, c, "staged y_gathered y_weighted y_summed y_gated x_added pool_passed")
        staged, gathered, weighted, summed, gated, x_added, pool_passed = sems

        def tiles(eng, one):
            turns(eng, TILES, 2, lambda i, s: one(i, s, P, 0))
            one(TILES // 2, 0, NB, 1)

        with nc.Block() as block:

            @block.gpsimd
            def _(pool):
                def one(i, s, rows, kind):
                    b = i * 2 + s
                    if has(i, s, 2, 2):
                        pool.wait_ge(x_added, b - 1)
                        pool.sem_inc(pool_passed, 1)
                    for j in range(2):
                        pool.tensor_copy(sid[s][j][0:rows, :], M.idx[0:rows, bass.ds(b, 1), j:j + 1]
                                         .rearrange("p one j -> p (one j)")).then_inc(staged, 1)
                    pool.wait_ge(staged, (b + 1) * 2)
                    pool.sem_inc(pool_passed, 1)
                    for j in range(2):
                        pool.indirect_dma_start(out=y[s][j][0:rows, :], out_offset=None, in_=G["y_slots"],
                                                in_offset=bass.IndirectOffsetOnAxis(ap=sid[s][j][0:rows, 0:1], axis=0))\
                            .then_inc(gathered, 16)
                    pool.wait_ge(gathered, (b + 1) * 32)
                    pool.sem_inc(pool_passed, 1)

                tiles(pool, one)

            @block.vector
            def _(dve):
                def one(i, s, rows, kind):
                    b = i * 2 + s
                    first, second = y[s][0][0:rows, :], y[s][1][0:rows, :]
                    w1, w2 = [M.wts[0:rows, bass.ds(b, 1), j:j + 1].rearrange("p one j -> p (one j)") for j in range(2)]
                    dve.wait_ge(gathered, (b + 1) * 32)
                    dve.tensor_scalar(first, first, w1, None, ALU.mult).then_inc(weighted, 1)
                    dve.wait_ge(weighted, b + 1)
                    dve.scalar_tensor_tensor(first, second, w2, first, ALU.mult, ALU.add).then_inc(summed, 1)
                    dve.wait_ge(summed, b + 1)
                    dve.tensor_tensor(first, first, gate[0:rows, kind, :], ALU.mult).then_inc(gated, 1)
                    dve.wait_ge(gated, b + 1)
                    row = x[0:rows, bass.ds(b, 1), :].rearrange("p one d -> p (one d)")
                    dve.tensor_tensor(row, row, first, ALU.add).then_inc(x_added, 1)

                tiles(dve, one)
        clear_signals(nc, sems, [gathered])


class Routing:
    def __init__(self, nc, c):
        self.idx = tile_of(nc, c, "moe_idx", [P, NT, 2], I32)
        self.plan = tile_of(nc, c, "moe_plan", [1, PLAN_ROWS, BLOCKS], I32)
        self.wts = tile_of(nc, c, "moe_wts", [P, NT, 2])


def moe_sublayer(nc, G, layer):
    with ExitStack() as c:
        M = Routing(nc, c)
        with ExitStack() as c2:
            G["featT"] = tile_of(nc, c2, "featT_ffn", [P, KC, TOK])
            stage_modulate(nc, G, layer, G["g_norm_ffn"][layer], 3, G["h_rows"])
            stage_route(nc, G, M, layer == 0)
        stage_experts(nc, G, layer, M)
        stage_combine(nc, G, layer, M, 5)


RQ_R, RQ_K, RQ_V, RQ_KK, RQ_B, RQ_SW, RQ_G = range(7)
DECAY = float(np.exp(np.float32(-0.5)))


class RwkvWeights:
    def __init__(self, nc, c):
        self.mu = tile_of(nc, c, "c_mu_b", [P, P_C])
        self.w0 = tile_of(nc, c, "c_w0_b", [P, RW])
        self.a0 = tile_of(nc, c, "c_a0_b", [P, RW])
        self.kk = tile_of(nc, c, "c_kk_b", [P, RW])
        self.ka = tile_of(nc, c, "c_ka_b", [P, RW])
        self.up = tile_of(nc, c, "c_up", [P, RW])
        self.g_up = tile_of(nc, c, "c_gup", [P, RW])

    def load(self, sp, G, sem):
        for dst, src in ((self.mu, G["c_mu"]), (self.w0, G["c_w0"]), (self.a0, G["c_a0"]), (self.kk, G["c_k_k"]),
                         (self.ka, G["c_k_a"])):
            sp.dma_start(dst[:, :], src[0].partition_broadcast(P)).then_inc(sem, 16)
        sp.dma_start(self.up[0:64, :], G["c_w_up"][0]).then_inc(sem, 16)
        sp.dma_start(self.up[64:128, :], G["c_a_up"][0]).then_inc(sem, 16)
        sp.dma_start(self.g_up[:, :], G["c_g_up"][0]).then_inc(sem, 16)


class RwkvInputs:

    def __init__(self, nc, c, bank_a, bank_b, bank_c, bank_t):
        self.z = tile_of(nc, c, "rw_z", [P, P_C])
        self.prev = tile_of(nc, c, "rw_prev", [P, P_C])
        self.q = tile_of(nc, c, "rw_q", [P, 7, RW])
        self.low = tile_of(nc, c, "rw_low", [P, 2, P])
        self.lowT = tile_of(nc, c, "rw_lowT", [P, 2, P])
        self.a = tile_of(nc, c, "rw_a", [P, RW])
        self.nrm = tile_of(nc, c, "rw_nrm", [P, 2, NH])
        self.w_ps, self.a_ps, self.g_ps, self.t_ps = bank_a, bank_b, bank_c, bank_t
        self.sems = signals(nc, c, "rw_z_loaded rw_mixed rw_low_made rw_low_T rw_lowT_copied rw_up_summed rw_sig_w "
                                   "rw_sig_a rw_a_shifted rw_w_shifted rw_sq_made rw_norm_made rw_chain rw_g_copied")

    def emit(self, nc, G, W, rows, load):
        (z_loaded, mixed, low_made, low_T, lowT_copied, up_summed, sig_w, sig_a, a_shifted, w_shifted, sq_made,
         norm_made, chain, g_copied) = self.sems
        R = slice(0, rows)
        z, prev, q, a = self.z, self.prev, self.q, self.a
        ident = G["ident"]
        with nc.Block() as block:

            @block.sync
            def _(sp):
                if load is not None:
                    load(sp, z, prev, z_loaded)

            @block.gpsimd
            def _(pool):
                pool.wait_ge(mixed, 1)
                pool.tensor_copy(q[R, RQ_R, :], z[R, O_R:O_K])
                pool.tensor_copy(q[R, RQ_V, :], z[R, O_V:O_WD])

            @block.vector
            def _(dve):
                step = InOrder(dve)
                if load is not None:
                    dve.wait_ge(z_loaded, 32)
                step(dve.tensor_tensor(prev[R, :], prev[R, :], z[R, :], ALU.subtract), chain)
                step(dve.tensor_tensor(prev[R, :], prev[R, :], W.mu[R, :], ALU.mult), chain)
                step(dve.tensor_tensor(z[R, :], z[R, :], prev[R, :], ALU.add), mixed)
                k = z[R, O_K:O_V]
                kk3 = q[R, RQ_KK, :].rearrange("p (h d) -> p h d", d=HD)
                step(dve.tensor_tensor(q[R, RQ_KK, :], k, W.kk[R, :], ALU.mult), chain)
                step(dve.tensor_tensor(prev[R, 0:RW], q[R, RQ_KK, :], q[R, RQ_KK, :], ALU.mult), chain)
                step(dve.tensor_reduce(self.nrm[R, 0, :], prev[R, 0:RW].rearrange("p (h d) -> p h d", d=HD), AX.X,
                                       ALU.add), sq_made)
                dve.wait_ge(norm_made, 1)
                step(dve.tensor_scalar(self.nrm[R, 1, :], self.nrm[R, 1, :], 1e-12, None, ALU.max), chain)
                step(dve.reciprocal(self.nrm[R, 0, :], self.nrm[R, 1, :]), chain)
                step(dve.tensor_tensor(kk3, kk3, self.nrm[R, 0, :].unsqueeze(2).broadcast_to([rows, NH, HD]),
                                       ALU.mult), chain)
                dve.wait_ge(low_T, 2)
                step(dve.tensor_copy(self.lowT[:, :, R], self.t_ps[:, 0:2, R]), lowT_copied)
                dve.wait_ge(up_summed, 3)
                step(dve.tensor_tensor(a[R, :], self.a_ps[R, :], W.a0[R, :], ALU.add), a_shifted)
                step(dve.tensor_tensor(q[R, RQ_SW, :], self.w_ps[R, :], W.w0[R, :], ALU.add), w_shifted)
                dve.wait_ge(sig_a, 1)
                step(dve.tensor_tensor(q[R, RQ_B, :], q[R, RQ_KK, :], a[R, :], ALU.mult), chain)
                step(dve.scalar_tensor_tensor(prev[R, 0:RW], a[R, :], -1.0, W.ka[R, :], ALU.add, ALU.mult), chain)
                step(dve.scalar_tensor_tensor(q[R, RQ_K, :], prev[R, 0:RW], 1.0, k, ALU.add, ALU.mult), chain)

            @block.scalar
            def _(act):
                act.wait_ge(mixed, 1)
                act.activation(self.low[R, 0, 0:64], z[R, O_WD:O_AD], ACT.Tanh).then_inc(low_made, 1)
                act.copy(self.low[R, 0, 64:128], z[R, O_AD:O_GD]).then_inc(low_made, 1)
                act.activation(self.low[R, 1, :], z[R, O_GD:P_C], ACT.Sigmoid).then_inc(low_made, 1)
                act.wait_ge(sq_made, 1)
                act.activation(self.nrm[R, 1, :], self.nrm[R, 0, :], ACT.Sqrt).then_inc(norm_made, 1)
                act.wait_ge(up_summed, 3)
                act.copy(q[R, RQ_G, :], self.g_ps[R, :]).then_inc(g_copied, 1)
                act.wait_ge(a_shifted, 1)
                act.activation(a[R, :], a[R, :], ACT.Sigmoid).then_inc(sig_a, 1)
                act.wait_ge(w_shifted, 1)
                act.activation(q[R, RQ_SW, :], q[R, RQ_SW, :], ACT.Sigmoid).then_inc(sig_w, 1)

            @block.tensor
            def _(pe):
                pe.wait_ge(low_made, 3)
                for j in range(2):
                    pe.transpose(self.t_ps[:, j, R], self.low[R, j, :], ident[R, R]).then_inc(low_T, 1)
                pe.wait_ge(lowT_copied, 1)
                pe.matmul(self.w_ps[R, :], self.lowT[0:64, 0, R], W.up[0:64, :], start=True, stop=True)\
                  .then_inc(up_summed, 1)
                pe.matmul(self.a_ps[R, :], self.lowT[64:128, 0, R], W.up[64:128, :], start=True, stop=True)\
                  .then_inc(up_summed, 1)
                pe.matmul(self.g_ps[R, :], self.lowT[:, 1, R], W.g_up[:, :], start=True, stop=True)\
                  .then_inc(up_summed, 1)


def stage_rwkv_prompt(nc, G):
    ident, featT, z = G["ident"], G["featT"], G["z_odd"]
    NC = P // CH
    HG = 4
    with ExitStack() as c:
        W = RwkvWeights(nc, c)
        banks = [bank_of(nc, c, f"rw_ps{i}", [P, 512]) for i in range(8)]
        b4 = [b[:, :].rearrange("p (h s) -> p h s", h=HG) for b in banks]
        I = RwkvInputs(nc, c, banks[0], banks[1], banks[2], b4[3])
        rk = tile_of(nc, c, "c_rk_b", [P, RW])
        lnw = tile_of(nc, c, "c_lnw_b", [P, RW])
        lnb = tile_of(nc, c, "c_lnb_b", [P, RW])
        incl = tile_of(nc, c, "m_incl", [P, P])
        excl = tile_of(nc, c, "m_excl", [P, P])
        after = tile_of(nc, c, "m_after", [P, P])
        nlow = tile_of(nc, c, "m_nlow", [P, P])
        nup = tile_of(nc, c, "m_nup", [P, P])
        inchunk = tile_of(nc, c, "m_inchunk", [P, NC])
        H = tile_of(nc, c, "rw_H", [HD, NC + 1, NH, HD])
        fac = tile_of(nc, c, "rw_fac", [P, 4, RW])
        RT, KT_, BH, KH, BB, KB = range(6)
        sc = tile_of(nc, c, "rw_sc", [P, 6, RW])
        WCT = tile_of(nc, c, "rw_WCT", [HD, NH, NC])
        T4 = tile_of(nc, c, "rw_T4", [HD, 4, HG, P])
        A = [tile_of(nc, c, f"rw_A{i}", [P, HG, P]) for i in range(2)]
        AT = [tile_of(nc, c, f"rw_AT{i}", [P, HG, P]) for i in range(2)]
        MT = tile_of(nc, c, "rw_MT", [P, HG, P])
        ArbT = tile_of(nc, c, "rw_ArbT", [P, HG, P])
        ArkT = tile_of(nc, c, "rw_ArkT", [P, HG, P])
        X = tile_of(nc, c, "rw_X", [P, HG, 2, HD])
        PT = tile_of(nc, c, "rw_PT", [HD, HG, P])
        GF = tile_of(nc, c, "rw_GF", [HD, NC, 2 * HG, HD])
        gf_banks = [banks[1], banks[2], banks[5], banks[6]]
        HW = tile_of(nc, c, "rw_HW", [HD, HG, HD])
        yT = tile_of(nc, c, "rw_yT", [HD, HG, P])
        y = tile_of(nc, c, "rw_y", [P, NH, HD])
        st = tile_of(nc, c, "rw_st", [P, 4, NH])
        tmp = tile_of(nc, c, "rw_tmp", [P, RW])
        bonus = tile_of(nc, c, "rw_bonus", [P, RW])
        rkv = tile_of(nc, c, "rw_rkv", [P, NH])

        loaded, filled, cut, made = setup = signals(nc, c, "rw_loaded rw_filled rw_cut rw_masks")
        with nc.Block() as block:

            @block.sync
            def _(sp):
                W.load(sp, G, loaded)
                sp.dma_start(rk[:, :], G["c_r_k"][0].rearrange("h d -> (h d)").partition_broadcast(P)).then_inc(loaded, 16)
                sp.dma_start(lnw[:, :], G["c_ln_w"][0].partition_broadcast(P)).then_inc(loaded, 16)
                sp.dma_start(lnb[:, :], G["c_ln_b"][0].partition_broadcast(P)).then_inc(loaded, 16)
                sp.wait_ge(loaded, 16 * 11)

            @block.gpsimd
            def _(pool):
                step = InOrder(pool)
                for m in (incl, excl, after):
                    step(pool.memset(m[:, :], 1.0), filled)
                step(pool.memset(inchunk[:, :], 1.0), filled)
                step(pool.memset(H[:, :, :, :], 0.0), filled)
                for m, op, s in ((incl, ALU.is_ge, 1), (excl, ALU.is_gt, 1), (after, ALU.is_gt, -1)):
                    step(pool.affine_select(out=m[:, :], in_=m[:, :], compare_op=op, fill=0.0, base=0,
                                            pattern=[[s, P]], channel_multiplier=-s), cut)
                    m3 = m[:, :].rearrange("p (c s) -> p c s", s=CH)
                    step(pool.affine_select(out=m3, in_=m3, compare_op=ALU.is_ge, fill=0.0, base=0,
                                            pattern=[[-CH, NC], [0, CH]], channel_multiplier=1), cut)
                    step(pool.affine_select(out=m3, in_=m3, compare_op=ALU.is_ge, fill=0.0, base=CH - 1,
                                            pattern=[[CH, NC], [0, CH]], channel_multiplier=-1), cut)
                step(pool.affine_select(out=inchunk[:, :], in_=inchunk[:, :], compare_op=ALU.is_ge, fill=0.0, base=0,
                                        pattern=[[-CH, NC]], channel_multiplier=1), cut)
                step(pool.affine_select(out=inchunk[:, :], in_=inchunk[:, :], compare_op=ALU.is_ge, fill=0.0,
                                        base=CH - 1, pattern=[[CH, NC]], channel_multiplier=-1), cut)

            @block.vector
            def _(dve):
                dve.wait_ge(cut, 11)
                dve.tensor_scalar(nup[:, :], excl[:, :], -1.0, None, ALU.mult)
                dve.tensor_scalar(nlow[:, :], after[:, :], -1.0, None, ALU.mult)
        clear_signals(nc, setup)

        names = signals(nc, c, "rc_cum rc_fac rc_wct rc_scaled rc_chain rc_T rc_Tcopied rc_outer rc_masked rc_pow rc_powA "
                               "rc_powAT rc_app rc_X rc_mv rc_gt rc_gtc rc_h rc_H rc_p rc_P rc_yT rc_yTc rc_y rc_yc rc_sq "
                               "rc_rms rc_out rc_outT rc_hw rc_rows rc_bonus rc_bonus_made")
        (cum_summed, fac_made, wct_made, scaled, chain, transposed, T_copied, outer, masked, pow_summed, powA_copied,
         powAT_copied, applied, X_made, mv_summed, gt_summed, gt_copied, h_summed, H_made, p_summed, P_made, yT_summed,
         yT_copied, y_summed, y_copied, sq_made, rms_made, out_made, out_T, hw_made, rows_loaded, bonus_step,
         bonus_made) = names
        NPOW = 4
        bc = [P, HG, P]

        def load_rows(sp, t, sem):
            sp.dma_start(I.z[:, :], z[bass.ds(t * P + LEAD, P), 0:P_C]).then_inc(sem, 16)
            sp.dma_start(I.prev[:, :], z[bass.ds(t * P + LEAD - 1, P), 0:P_C]).then_inc(sem, 16)

        with nc.Block() as block:

            @block.sync
            def _(sp):
                load_rows(sp, 0, rows_loaded)
                sp.wait_ge(rows_loaded, 32)
        clear_signals(nc, [rows_loaded])

        with nc.Fori(0, TILES) as t:
            I.emit(nc, G, W, P, None)
            q = I.q

            with nc.Block() as block:

                @block.sync
                def _(sp):
                    load_rows(sp, (t + 1) % TILES, rows_loaded)
                    sp.wait_ge(rows_loaded, 32)

                @block.tensor
                def _(pe):
                    sw = q[:, RQ_SW, :]
                    pe.matmul(banks[0][:, :], incl[:, :], sw, start=True, stop=True).then_inc(cum_summed, 1)
                    pe.matmul(banks[1][:, :], excl[:, :], sw, start=True, stop=True).then_inc(cum_summed, 1)
                    pe.matmul(banks[2][:, :], after[:, :], sw, start=True, stop=True).then_inc(cum_summed, 1)
                    for h in range(NH):
                        last = pe.matmul(banks[3][0:HD, h * NC:(h + 1) * NC], q[:, RQ_SW, h * HD:(h + 1) * HD],
                                         inchunk[:, :], start=True, stop=True)
                    last.then_inc(cum_summed, 1)
                    for g in range(2):
                        n = g + 1
                        heads = range(g * HG, (g + 1) * HG)
                        pe.wait_ge(scaled, 4)
                        if g == 0:
                            pe.wait_ge(fac_made, 4)
                            pe.wait_ge(wct_made, 1)
                        else:
                            pe.wait_ge(T_copied, 4)
                            pe.wait_ge(y_copied, 1)
                        for i in range(4):
                            for j, h in enumerate(heads):
                                last = pe.transpose(b4[i][0:HD, j, :], sc[:, i, h * HD:(h + 1) * HD], ident[:, :])
                            last.then_inc(transposed, 1)
                        pe.wait_ge(T_copied, 4 * n)
                        for i, (l, r) in enumerate(((KT_, BH), (BH, KT_), (KH, KT_), (BH, RT), (KH, RT))):
                            for j in range(HG):
                                last = pe.matmul(b4[i + 3][:, j, :], T4[:, l, j, :], T4[:, r, j, :],
                                                 start=True, stop=True)
                            last.then_inc(outer, 1)
                        pe.wait_ge(masked, 5 * g + 3)
                        for j, h in enumerate(heads):
                            last = pe.matmul(b4[0][:, j, 0:HD], MT[:, j, :], q[:, RQ_V, h * HD:(h + 1) * HD],
                                             start=True, stop=True)
                        last.then_inc(mv_summed, 1)
                        for s in range(NPOW + 1):
                            a, at = A[s % 2], AT[s % 2]
                            pe.wait_ge(X_made, (NPOW + 2) * g + s + 1)
                            if s:
                                pe.wait_ge(powAT_copied, NPOW * g + s)
                            for j in range(HG):
                                last = pe.matmul(b4[0][:, j, :], at[:, j, :],
                                                 X[:, j, :, :].rearrange("p a d -> p (a d)"), start=True, stop=True)
                            last.then_inc(applied, 1)
                            if s < NPOW:
                                if s:
                                    pe.wait_ge(powA_copied, (NPOW - 1) * g + s)
                                for j in range(HG):
                                    last = pe.matmul(b4[1][:, j, :], a[:, j, :], at[:, j, :], start=True, stop=True)
                                last.then_inc(pow_summed, 1)
                                if s < NPOW - 1:
                                    for j in range(HG):
                                        last = pe.matmul(b4[2][:, j, :], at[:, j, :], a[:, j, :], start=True, stop=True)
                                    last.then_inc(pow_summed, 1)
                        pe.wait_ge(X_made, (NPOW + 2) * n)
                        pe.wait_ge(masked, 5 * n)
                        for j in range(HG):
                            last = pe.matmul(b4[0][0:HD, j, :], X[:, j, 1, :], ArbT[:, j, :], start=True, stop=True)
                        last.then_inc(p_summed, 1)
                        pe.wait_ge(hw_made, 2)
                        for k in range(NC):
                            rows = slice(k * CH, (k + 1) * CH)
                            for j, h in enumerate(heads):
                                cols = slice(h * HD, (h + 1) * HD)
                                f = gf_banks[k][0:HD, (HG + j) * HD:(HG + j + 1) * HD]
                                pe.matmul(gf_banks[k][0:HD, j * HD:(j + 1) * HD], X[rows, j, 1, :], sc[rows, BB, cols],
                                          start=True, stop=True)
                                pe.matmul(f, sc[rows, BB, cols], X[rows, j, 0, :], start=True, stop=False)
                                last = pe.matmul(f, sc[rows, KB, cols], q[rows, RQ_V, cols], start=False, stop=True)
                            last.then_inc(gt_summed, 1)
                        pe.wait_ge(gt_copied, NC * n)
                        for k in range(NC):
                            if k:
                                pe.wait_ge(H_made, NC * g + k)
                            for j, h in enumerate(heads):
                                last = pe.matmul(banks[3 + k % 2][0:HD, j * HD:(j + 1) * HD], GF[:, k, j, :],
                                                 H[:, k, h, :], start=True, stop=True)
                            last.then_inc(h_summed, 1)
                        pe.wait_ge(P_made, n)
                        pe.wait_ge(H_made, NC * n)
                        for j, h in enumerate(heads):
                            cols = slice(h * HD, (h + 1) * HD)
                            pe.matmul(b4[5][0:HD, j, :], X[:, j, 0, :], ArbT[:, j, :], start=True, stop=False)
                            pe.matmul(b4[5][0:HD, j, :], q[:, RQ_V, cols], ArkT[:, j, :], start=False, stop=False)
                            for k in range(NC):
                                s = slice(k * CH, (k + 1) * CH)
                                last = pe.matmul(b4[5][0:HD, j, s], H[:, k, h, :], PT[:, j, s], start=False,
                                                 stop=(k == NC - 1))
                        last.then_inc(yT_summed, 1)
                        pe.wait_ge(yT_copied, n)
                        for j in range(HG):
                            last = pe.transpose(banks[6][:, j * HD:(j + 1) * HD], yT[:, j, :], ident[0:HD, 0:HD])
                        last.then_inc(y_summed, 1)
                    pe.wait_ge(out_made, 1)
                    for j in range(4):
                        last = pe.transpose(b4[7][:, j, :], tmp[:, j * P:(j + 1) * P], ident[:, :])
                    last.then_inc(out_T, 1)

                @block.scalar
                def _(act):
                    for i, (b, s) in enumerate(((0, -DECAY), (1, -DECAY), (0, DECAY), (2, -DECAY))):
                        act.wait_ge(cum_summed, b + 1)
                        act.activation(fac[:, i, :], banks[b][:, :], ACT.Exp, scale=s).then_inc(fac_made, 1)
                    act.wait_ge(cum_summed, 4)
                    act.activation(WCT[:, :, :].rearrange("k h c -> k (h c)"), banks[3][0:HD, 0:NH * NC], ACT.Exp,
                                   scale=-DECAY).then_inc(wct_made, 1)
                    for g in range(2):
                        n = g + 1
                        for i in range(4):
                            act.wait_ge(transposed, 4 * g + i + 1)
                            act.copy(T4[:, i, :, :], b4[i][0:HD, :, :]).then_inc(T_copied, 1)
                        for s in range(NPOW):
                            at = (2 * NPOW - 1) * g + 2 * s
                            act.wait_ge(pow_summed, at + 1)
                            act.copy(AT[1 - s % 2][:, :, :], b4[1]).then_inc(powAT_copied, 1)
                            if s < NPOW - 1:
                                act.wait_ge(pow_summed, at + 2)
                                act.copy(A[1 - s % 2][:, :, :], b4[2]).then_inc(powA_copied, 1)
                        for k in range(NC):
                            act.wait_ge(gt_summed, NC * g + k + 1)
                            act.copy(GF[:, k, :, :].rearrange("k h v -> k (h v)"), gf_banks[k][0:HD, :])\
                               .then_inc(gt_copied, 1)
                        act.wait_ge(yT_summed, n)
                        act.copy(yT[:, :, :], b4[5][0:HD, :, :]).then_inc(yT_copied, 1)
                        act.wait_ge(y_summed, n)
                        act.copy(y[:, g * HG:(g + 1) * HG, :].rearrange("p h d -> p (h d)"), banks[6][:, 0:HG * HD])\
                           .then_inc(y_copied, 1)
                    act.wait_ge(sq_made, 1)
                    act.activation(st[:, 2, :], st[:, 1, :], ACT.Sqrt).then_inc(rms_made, 1)

                @block.gpsimd
                def _(pool):
                    pool.wait_ge(fac_made, 4)
                    pool.tensor_tensor(sc[:, BB, :], q[:, RQ_B, :], fac[:, 3, :], ALU.mult).then_inc(hw_made, 1)
                    pool.tensor_tensor(sc[:, KB, :], q[:, RQ_K, :], fac[:, 3, :], ALU.mult).then_inc(hw_made, 1)
                    step = InOrder(pool)
                    b3 = bonus[:, :].rearrange("p (h d) -> p h d", d=HD)
                    step(pool.tensor_tensor(bonus[:, :], q[:, RQ_R, :], q[:, RQ_K, :], ALU.mult), bonus_step)
                    step(pool.tensor_tensor(bonus[:, :], bonus[:, :], rk[:, :], ALU.mult), bonus_step)
                    n = HD // 2
                    while n:
                        step(pool.tensor_tensor(b3[:, :, 0:n], b3[:, :, 0:n], b3[:, :, n:2 * n], ALU.add), bonus_step)
                        n //= 2
                    step(pool.tensor_copy(rkv[:, :], b3[:, :, 0]), bonus_step)
                    step(pool.tensor_tensor(b3, q[:, RQ_V, :].rearrange("p (h d) -> p h d", d=HD),
                                            rkv[:, :].unsqueeze(2).broadcast_to([P, NH, HD]), ALU.mult), bonus_made)

                @block.vector
                def _(dve):
                    step = InOrder(dve)
                    dve.wait_ge(fac_made, 4)
                    for i, (src, f) in enumerate(((RQ_R, 0), (RQ_KK, 1), (RQ_B, 2), (RQ_K, 2))):
                        step(dve.tensor_tensor(sc[:, i, :], q[:, src, :], fac[:, f, :], ALU.mult), scaled)
                    for g in range(2):
                        n = g + 1
                        heads = slice(g * HG, (g + 1) * HG)
                        cols = slice(g * HG * HD, (g + 1) * HG * HD)
                        for i, (dst, mask) in enumerate(((A[0], nlow), (AT[0], nup), (MT, nup), (ArbT, incl),
                                                         (ArkT, incl))):
                            dve.wait_ge(outer, 5 * g + i + 1)
                            step(dve.tensor_tensor(dst[:, :, :], b4[3 + i], mask[:, :].unsqueeze(1).broadcast_to(bc),
                                                   ALU.mult), masked)
                        step(dve.tensor_scalar(X[:, :, 1, :], sc[:, KT_, cols].rearrange("p (h d) -> p h d", d=HD),
                                               -1.0, None, ALU.mult), chain)
                        dve.wait_ge(mv_summed, n)
                        step(dve.tensor_copy(X[:, :, 0, :], b4[0][:, :, 0:HD]), X_made)
                        for s in range(NPOW + 1):
                            dve.wait_ge(applied, (NPOW + 1) * g + s + 1)
                            X4 = X[:, :, :, :].rearrange("p h a d -> p h (a d)")
                            step(dve.tensor_tensor(X4, X4, b4[0], ALU.add), X_made)
                        dve.wait_ge(p_summed, n)
                        step(dve.tensor_tensor(PT[:, :, :], T4[:, RT, :, :], b4[0][0:HD, :, :], ALU.add), P_made)
                        for k in range(NC):
                            step(dve.tensor_tensor(HW[:, :, :], H[:, k, heads, :],
                                                   WCT[:, heads, k:k + 1].broadcast_to([HD, HG, HD]), ALU.mult), chain)
                            dve.wait_ge(gt_copied, NC * g + k + 1)
                            step(dve.tensor_tensor(HW[:, :, :], HW[:, :, :], GF[:, k, HG:2 * HG, :], ALU.add), chain)
                            dve.wait_ge(h_summed, NC * g + k + 1)
                            step(dve.tensor_tensor(H[:, k + 1, heads, :], HW[:, :, :],
                                                   banks[3 + k % 2][0:HD, 0:HG * HD].rearrange("k (h v) -> k h v", v=HD),
                                                   ALU.add), H_made)
                    dve.wait_ge(y_copied, 2)
                    step(dve.tensor_copy(H[:, 0, :, :], H[:, NC, :, :]), chain)
                    full = [P, NH, HD]
                    y3 = y[:, :, :]
                    t3 = tmp[:, :].rearrange("p (h d) -> p h d", d=HD)
                    step(dve.tensor_reduce(st[:, 0, :], y3, AX.X, ALU.add), chain)
                    step(dve.tensor_scalar(st[:, 0, :], st[:, 0, :], 1.0 / HD, None, ALU.mult), chain)
                    step(dve.tensor_tensor(y3, y3, st[:, 0, :].unsqueeze(2).broadcast_to(full), ALU.subtract), chain)
                    step(dve.tensor_tensor(t3, y3, y3, ALU.mult), chain)
                    step(dve.tensor_reduce(st[:, 1, :], t3, AX.X, ALU.add), chain)
                    step(dve.tensor_scalar(st[:, 1, :], st[:, 1, :], 1.0 / HD, GN_EPS, ALU.mult, ALU.add), sq_made)
                    dve.wait_ge(rms_made, 1)
                    step(dve.reciprocal(st[:, 3, :], st[:, 2, :]), chain)
                    step(dve.tensor_tensor(y3, y3, st[:, 3, :].unsqueeze(2).broadcast_to(full), ALU.mult), chain)
                    yf = y[:, :, :].rearrange("p h d -> p (h d)")
                    step(dve.tensor_tensor(yf, yf, lnw[:, :], ALU.mult), chain)
                    step(dve.tensor_tensor(yf, yf, lnb[:, :], ALU.add), chain)
                    dve.wait_ge(bonus_made, 1)
                    step(dve.tensor_tensor(yf, yf, bonus[:, :], ALU.add), chain)
                    step(dve.tensor_tensor(tmp[:, :], yf, q[:, RQ_G, :], ALU.mult), out_made)
                    dve.wait_ge(out_T, 1)
                    dve.tensor_copy(featT[:, 0:4, bass.ds(t * P, P)], b4[7])
            clear_signals(nc, names + I.sems)

        h_T, h_copied, h_stored = tail = signals(nc, c, "rw_hT rw_hTc rw_hst")
        with nc.Block() as block:

            @block.tensor
            def _(pe):
                for h in range(NH):
                    last = pe.transpose(banks[0][0:HD, h * HD:(h + 1) * HD], H[:, 0, h, :], ident[0:HD, 0:HD])
                last.then_inc(h_T, 1)

            @block.vector
            def _(dve):
                dve.wait_ge(h_T, 1)
                dve.tensor_copy(I.z[0:HD, 0:NH * HD], banks[0][0:HD, 0:NH * HD]).then_inc(h_copied, 1)

            @block.sync
            def _(sp):
                sp.dma_start(G["c_shift_p"][0], z[Z_S - 1:Z_S, 0:P_C]).then_inc(h_stored, 16)
                sp.wait_ge(h_copied, 1)
                sp.dma_start(G["c_wkv_p"][0, 0].rearrange("h v k -> v h k"),
                             I.z[0:HD, 0:NH * HD].rearrange("v (h k) -> v h k", k=HD)).then_inc(h_stored, 16)
                sp.wait_ge(h_stored, 32)
        clear_signals(nc, tail)


def stage_rwkv_sample(nc, G):
    z = G["z_odd"]
    R = NB * NH
    with ExitStack() as c:
        W = RwkvWeights(nc, c)
        banks = [bank_of(nc, c, f"rs_ps{i}", [P, 512]) for i in range(4)]
        I = RwkvInputs(nc, c, banks[0], banks[1], banks[2], banks[3][:, :].rearrange("p (h s) -> p h s", h=4))
        (loaded,) = setup = signals(nc, c, "rs_loaded")
        with nc.Block() as block:

            @block.sync
            def _(sp):
                W.load(sp, G, loaded)
                sp.wait_ge(loaded, 16 * 8)
        clear_signals(nc, setup)

        def load(sp, zt, prev, sem):
            sp.dma_start(zt[0:NB, :], z[Z_S:Z_S + NB, 0:P_C]).then_inc(sem, 16)
            sp.dma_start(prev[0:NB, :], G["state_c_shift"][0]).then_inc(sem, 16)

        I.emit(nc, G, W, NB, load)
        clear_signals(nc, I.sems)

        S = tile_of(nc, c, "rs_S", [R, HD, HD])
        big = tile_of(nc, c, "rs_big", [R, HD, HD])
        v7 = tile_of(nc, c, "rs_q", [R, 7, HD])
        ln = tile_of(nc, c, "rs_ln", [R, 3, HD])
        sa = tile_of(nc, c, "rs_sa", [R, 4, HD])
        st = tile_of(nc, c, "rs_st", [R, 4])
        sems = signals(nc, c, "q_stored q_spread s_loaded decay_made chain sq_made rms_made state_made row_made stored")
        q_stored, q_spread, s_loaded, decay_made, chain, sq_made, rms_made, state_made, row_made, stored = sems
        with nc.Block() as block:

            @block.sync
            def _(sp):
                sp.dma_start(G["s_rq"], I.q[0:NB, :, :]).then_inc(q_stored, 16)
                sp.dma_start(S[:, :, :], G["state_c_wkv"][0].rearrange("b h v k -> (b h) v k")).then_inc(s_loaded, 16)
                for b in range(NB):
                    rows = slice(b * NH, (b + 1) * NH)
                    for i, src in enumerate((G["c_ln_w"][0].rearrange("(h d) -> h d", d=HD),
                                             G["c_ln_b"][0].rearrange("(h d) -> h d", d=HD), G["c_r_k"][0])):
                        sp.dma_start(ln[rows, i, :], src).then_inc(s_loaded, 16)
                sp.dma_start(G["c_shift_s"][0], z[Z_S:Z_S + NB, 0:P_C]).then_inc(stored, 16)
                sp.wait_ge(q_stored, 16)
                for b in range(NB):
                    sp.dma_start(v7[b * NH:(b + 1) * NH, :, :],
                                 G["s_rq"][b].rearrange("i (h d) -> h i d", d=HD)).then_inc(q_spread, 16)
                sp.wait_ge(state_made, 1)
                sp.dma_start(G["c_wkv_s"][0].rearrange("b h v k -> (b h) v k"), S[:, :, :]).then_inc(stored, 16)
                sp.wait_ge(row_made, 1)
                sp.dma_start(G["s_rows_c"], sa[:, 1, :]).then_inc(stored, 16)
                sp.wait_ge(stored, 48)

            @block.scalar
            def _(act):
                act.wait_ge(q_spread, 16 * NB)
                act.activation(v7[:, RQ_SW, :], v7[:, RQ_SW, :], ACT.Exp, scale=-DECAY).then_inc(decay_made, 1)
                act.wait_ge(sq_made, 1)
                act.activation(st[:, 2:3], st[:, 1:2], ACT.Sqrt).then_inc(rms_made, 1)

            @block.vector
            def _(dve):
                step = InOrder(dve)
                full = [R, HD, HD]

                def over_v(i):
                    return v7[:, i, :].unsqueeze(1).broadcast_to(full)

                dve.wait_ge(q_spread, 16 * NB)
                dve.wait_ge(s_loaded, 16 * (1 + 3 * NB))
                dve.wait_ge(decay_made, 1)
                step(dve.tensor_tensor(big[:, :, :], S[:, :, :], over_v(RQ_KK), ALU.mult), chain)
                step(dve.tensor_reduce(sa[:, 0, :], big[:, :, :], AX.X, ALU.add, negate=True), chain)
                step(dve.tensor_tensor(S[:, :, :], S[:, :, :], over_v(RQ_SW), ALU.mult), chain)
                step(dve.tensor_tensor(big[:, :, :], sa[:, 0, :].unsqueeze(2).broadcast_to(full), over_v(RQ_B),
                                       ALU.mult), chain)
                step(dve.tensor_tensor(S[:, :, :], S[:, :, :], big[:, :, :], ALU.add), chain)
                step(dve.tensor_tensor(big[:, :, :], v7[:, RQ_V, :].unsqueeze(2).broadcast_to(full), over_v(RQ_K),
                                       ALU.mult), chain)
                step(dve.tensor_tensor(S[:, :, :], S[:, :, :], big[:, :, :], ALU.add), state_made)
                step(dve.tensor_tensor(big[:, :, :], S[:, :, :], over_v(RQ_R), ALU.mult), chain)
                step(dve.tensor_reduce(sa[:, 1, :], big[:, :, :], AX.X, ALU.add), chain)
                yv, t = sa[:, 1, :], sa[:, 2, :]
                step(dve.tensor_reduce(st[:, 0:1], yv, AX.X, ALU.add), chain)
                step(dve.tensor_scalar(st[:, 0:1], st[:, 0:1], 1.0 / HD, None, ALU.mult), chain)
                step(dve.tensor_scalar(yv, yv, st[:, 0:1], None, ALU.subtract), chain)
                step(dve.tensor_tensor(t, yv, yv, ALU.mult), chain)
                step(dve.tensor_reduce(st[:, 1:2], t, AX.X, ALU.add), chain)
                step(dve.tensor_scalar(st[:, 1:2], st[:, 1:2], 1.0 / HD, GN_EPS, ALU.mult, ALU.add), sq_made)
                dve.wait_ge(rms_made, 1)
                step(dve.reciprocal(st[:, 3:4], st[:, 2:3]), chain)
                step(dve.scalar_tensor_tensor(yv, yv, st[:, 3:4], ln[:, 0, :], ALU.mult, ALU.mult), chain)
                step(dve.tensor_tensor(yv, yv, ln[:, 1, :], ALU.add), chain)
                step(dve.tensor_tensor(t, v7[:, RQ_R, :], v7[:, RQ_K, :], ALU.mult), chain)
                step(dve.tensor_tensor(t, t, ln[:, 2, :], ALU.mult), chain)
                step(dve.tensor_reduce(st[:, 0:1], t, AX.X, ALU.add), chain)
                step(dve.scalar_tensor_tensor(yv, v7[:, RQ_V, :], st[:, 0:1], yv, ALU.mult, ALU.add), chain)
                step(dve.tensor_tensor(yv, yv, v7[:, RQ_G, :], ALU.mult), row_made)
        clear_signals(nc, sems)


class Compressed:
    def __init__(self, nc, c):
        self.KT = tile_of(nc, c, "cmp_KT", [P, 1 + NB, NCMP])
        self.V = tile_of(nc, c, "cmp_V", [NCMP, 1 + NB, P])
        self.V4 = tile_of(nc, c, "cmp_V4", [P, P])


def stage_compress(nc, G, C):
    ident = G["ident"]
    cache = G["cache_d_cmp"][0].rearrange("n s two kv d -> n s (two kv d)")
    with ExitStack() as c:
        w = tile_of(nc, c, "cmp_w_sb", [P, 2, CMP, HD])
        pe_rows = tile_of(nc, c, "cmp_pe_rows", [CMP, 2, 2, HD])
        peT = tile_of(nc, c, "cmp_peT", [P, 2, CMP])
        gain = tile_of(nc, c, "cmp_gain", [NCMP, HD])
        rows = [tile_of(nc, c, f"cmp_rows{i}", [P, PAGES, A_KV]) for i in range(2)]
        rawT = tile_of(nc, c, "cmp_rawT", [P, 2, SEQ])
        kc = tile_of(nc, c, "cmp_kc", [NCMP, NKV, HD])
        sq = tile_of(nc, c, "cmp_sq", [NCMP, NKV, HD])
        rms = tile_of(nc, c, "cmp_rms", [NCMP, 3, NKV])
        t_ps = [bank_of(nc, c, f"cmp_t_ps{i}", [P, PAGES, P]) for i in range(2)]
        c_ps = [bank_of(nc, c, f"cmp_c_ps{i}", [NCMP, 2, HD]) for i in range(NKV)]
        kT_ps = bank_of(nc, c, "cmp_kT_ps", [P, 2 * CMP])
        loaded, pe_transposed = setup = signals(nc, c, "cmp_loaded cmp_peT")
        with nc.Block() as block:

            @block.sync
            def _(sp):
                for a in range(2):
                    for kv in range(NKV):
                        sp.dma_start(w[kv * HD:(kv + 1) * HD, a, :, :],
                                     G["d_cmp_w"][0, a].rearrange("(r d) e -> d r e", d=HD)).then_inc(loaded, 16)
                        sp.dma_start(pe_rows[:, a, kv, :], G["d_cmp_pe"][0, a]).then_inc(loaded, 16)
                sp.dma_start(gain[:, :], G["d_k_norm"][0, 0].partition_broadcast(NCMP)).then_inc(loaded, 16)
                sp.wait_ge(loaded, 16 * 9)

            @block.tensor
            def _(pe):
                pe.wait_ge(loaded, 16 * 9)
                for a in range(2):
                    last = pe.transpose(kT_ps[:, a * CMP:(a + 1) * CMP],
                                        pe_rows[:, a, :, :].rearrange("r k d -> r (k d)"), ident[0:CMP, 0:CMP])
                last.then_inc(pe_transposed, 1)

            @block.vector
            def _(dve):
                dve.wait_ge(pe_transposed, 1)
                dve.tensor_copy(peT[:, :, :].rearrange("p a r -> p (a r)"), kT_ps[:, :])
        clear_signals(nc, setup)

        names = signals(nc, c, "cmp_rows_loaded cmp_transposed cmp_pe_added cmp_summed cmp_kc cmp_sqd cmp_rms "
                               "cmp_kc_ready cmp_kT cmp_v4")
        (rows_loaded, transposed, pe_added, summed, kc_copied, sq_made, rms_made, kc_ready, kT_made, v4_stored) = names

        def one_sequence(seq, odd, next_sample):
            with nc.Block() as block:

                @block.sync
                def _(sp):
                    if next_sample is not None:
                        load_sample(sp, next_sample, rows[1 - odd])
                        sp.wait_ge(rows_loaded, 16 * PAGES)

                @block.tensor
                def _(pe):
                    for a in range(2):
                        for j in range(PAGES):
                            last = pe.transpose(t_ps[a][:, j, :], rows[odd][:, j, a * P:(a + 1) * P], ident[:, :])
                        last.then_inc(transposed, 1)
                    for a in range(2):
                        pe.wait_ge(pe_added, a + 1)
                        for kv in range(NKV):
                            half = slice(kv * HD, (kv + 1) * HD)
                            x = rawT[half, a, :].rearrange("p (n r) -> p r n", r=CMP)
                            for r in range(CMP):
                                last = pe.matmul(c_ps[kv][:, a, :], x[:, r, :], w[half, a, r, :],
                                                 start=(r == 0), stop=(r == CMP - 1))
                    last.then_inc(summed, 1)
                    pe.wait_ge(kc_ready, 1)
                    pe.transpose(kT_ps[:, 0:NCMP], kc[:, :, :].rearrange("n k e -> n (k e)"), ident[0:NCMP, 0:NCMP])\
                      .then_inc(kT_made, 1)

                @block.vector
                def _(dve):
                    step = InOrder(dve)
                    for a in range(2):
                        dve.wait_ge(transposed, a + 1)
                        step(dve.tensor_tensor(rawT[:, a, :].rearrange("p (n r) -> p n r", r=CMP),
                                               t_ps[a][:, :, :].rearrange("p j (m r) -> p (j m) r", r=CMP),
                                               peT[:, a, :].unsqueeze(1).broadcast_to([P, NCMP, CMP]), ALU.add),
                             pe_added)
                    dve.wait_ge(summed, 1)
                    for kv in range(NKV):
                        step(dve.tensor_copy(kc[:, kv, :], c_ps[kv][:, 0, :]), kc_copied)
                        step(dve.tensor_copy(C.V[:, seq, kv * HD:(kv + 1) * HD], c_ps[kv][:, 1, :]), kc_copied)
                    step(dve.tensor_tensor(sq[:, :, :], kc[:, :, :], kc[:, :, :], ALU.mult), kc_copied)
                    step(dve.tensor_reduce(rms[:, 0, :], sq[:, :, :], AX.X, ALU.add), kc_copied)
                    step(dve.tensor_scalar(rms[:, 0, :], rms[:, 0, :], 1.0 / HD, RMS_EPS, ALU.mult, ALU.add), sq_made)
                    dve.wait_ge(rms_made, 1)
                    step(dve.reciprocal(rms[:, 2, :], rms[:, 1, :]), kc_copied)
                    step(dve.tensor_tensor(kc[:, :, :], kc[:, :, :],
                                           rms[:, 2, :].unsqueeze(2).broadcast_to([NCMP, NKV, HD]), ALU.mult), kc_copied)
                    step(dve.tensor_tensor(kc[:, :, :], kc[:, :, :],
                                           gain[:, :].unsqueeze(1).broadcast_to([NCMP, NKV, HD]), ALU.mult), kc_ready)
                    dve.wait_ge(kT_made, 1)
                    dve.tensor_copy(C.KT[:, seq, :], kT_ps[:, 0:NCMP])

                @block.scalar
                def _(act):
                    act.wait_ge(sq_made, 1)
                    act.activation(rms[:, 1, :], rms[:, 0, :], ACT.Sqrt).then_inc(rms_made, 1)
            clear_signals(nc, names)

        def load_sample(sp, b, dst):
            page_loads(sp, G, b, cache, [(lambda j: dst[:, j, :], lambda page: cache[page], rows_loaded)])

        with nc.Block() as block:

            @block.sync
            def _(sp):
                sp.dma_start(rows[0][:, :, :], G["z_odd"][LEAD:LEAD + SEQ, O_KVC:O_KVS]
                             .rearrange("(j p) n -> p j n", p=P)).then_inc(rows_loaded, 16)
                sp.wait_ge(rows_loaded, 16)
        clear_signals(nc, [rows_loaded])

        one_sequence(0, 0, 0)
        with nc.Fori(0, NB // 2 - 1) as i:
            one_sequence(i * 2 + 1, 1, i * 2 + 1)
            one_sequence(i * 2 + 2, 0, i * 2 + 2)
        one_sequence(NB - 1, 1, NB - 1)
        one_sequence(NB, 0, None)
        with nc.Block() as block:

            @block.sync
            def _(sp):
                for i in range(P // NCMP):
                    sp.dma_start(C.V4[i * NCMP:(i + 1) * NCMP, :], C.V[:, 0, :]).then_inc(v4_stored, 16)
                sp.wait_ge(v4_stored, 16 * (P // NCMP))
        clear_signals(nc, [v4_stored])


ZQ = O_Q


def stage_nsa_prompt(nc, G, C):
    ident, featT, near, far_mask, z = G["ident"], G["featT"], G["near"], G["far_mask"], G["z_odd"]
    cmp_bias = G["cmp_bias"]
    cmp_out = G["d_cmp_p"][0, 0].rearrange("s two kv d -> s (two kv d)")
    slc_out = G["d_slc_p"][0, 0].rearrange("s two kv d -> s (two kv d)")
    win_out = G["d_win_p"][0, 0].rearrange("s two kv d -> s (two kv d)")
    WW = WINDOW + P
    with ExitStack() as c:
        zt = tile_of(nc, c, "zt", [P, P_ODD - ZQ])
        gq = tile_of(nc, c, "gq", [P, HD])
        gk = tile_of(nc, c, "gk", [P, 2, HD])
        sq = tile_of(nc, c, "sq", [P, 12, HD])
        rms = tile_of(nc, c, "rms", [P, 3, 12])
        qn = tile_of(nc, c, "qn", [P, 6, NKV, HD])
        gates = tile_of(nc, c, "gates", [P, 3 * NH])
        qTz = tile_of(nc, c, "qTz", [P, NH, P])
        KsT = tile_of(nc, c, "KsT", [P, SEQ])
        KwT = tile_of(nc, c, "KwT", [P, WINDOW + SEQ])
        Vs = tile_of(nc, c, "Vs", [P, TILES, P])
        Vw = tile_of(nc, c, "Vw", [P, WINDOW // P + TILES, P])
        smask = [tile_of(nc, c, f"smask{kv}", [P, P + SEQ]) for kv in range(NKV)]
        win_bank = tile_of(nc, c, "win_bank", [P, WW])
        pad_bank = tile_of(nc, c, "pad_bank", [P, 7 * P + WW])
        wmask = tile_of(nc, c, "wmask", [P, WW])
        vis = tile_of(nc, c, "cmp_visible", [P, 64])
        keep = tile_of(nc, c, "sel_keep", [P, 32])
        force = tile_of(nc, c, "sel_force", [P, 32])
        pc = tile_of(nc, c, "pc", [P, NH, NCMP])
        pcT = tile_of(nc, c, "pcT", [P, 2, P])
        cst = tile_of(nc, c, "cmp_st", [P, 3, NH])
        ps = tile_of(nc, c, "ps", [P, NKV, NCMP])
        score = tile_of(nc, c, "sel_score", [P, NKV, NSEL])
        top8 = tile_of(nc, c, "top8", [P, 8])
        o = tile_of(nc, c, "nsa_o", [P, NH, HD])
        att = Attend(nc, c)
        t_ps, lg_ps = att.t_ps, att.lg_ps

        loaded, cleared, cut, forced, scaled = setup = signals(nc, c, "w_loaded cleared cut forced scaled")
        with nc.Block() as block:

            @block.sync
            def _(sp):
                sp.dma_start(gq[:, :], G["d_q_norm"][0].partition_broadcast(P)).then_inc(loaded, 16)
                for i in range(2):
                    sp.dma_start(gk[:, i, :], G["d_k_norm"][0, 1 + i].partition_broadcast(P)).then_inc(loaded, 16)

            @block.gpsimd
            def _(pool):
                for buf in (qTz[:, :, :], KsT[:, :], KwT[:, :], Vs[:, :, :], Vw[:, :, :], att.biased[0][:, :],
                            att.biased[1][:, :], win_bank[:, :], pad_bank[:, :], smask[0][:, 0:P], smask[1][:, 0:P]):
                    pool.memset(buf, 0.0).then_inc(cleared, 1)
                pool.memset(vis[:, :], 1.0).then_inc(cleared, 1)
                pool.wait_ge(cleared, 12)
                step = InOrder(pool)
                step(pool.memset(pad_bank[:, 0:WINDOW], NEG), cut)
                step(pool.affine_select(out=win_bank[:, :], in_=win_bank[:, :], compare_op=ALU.is_ge, fill=NEG,
                                        base=WINDOW, pattern=[[-1, WW]], channel_multiplier=1), cut)
                step(pool.affine_select(out=win_bank[:, :], in_=win_bank[:, :], compare_op=ALU.is_gt, fill=NEG,
                                        base=0, pattern=[[1, WW]], channel_multiplier=-1), cut)
                step(pool.affine_select(out=vis[:, :], in_=vis[:, :], compare_op=ALU.is_ge, fill=0.0, base=865,
                                        pattern=[[-CMP, 64]], channel_multiplier=1), cut)
                step(pool.affine_select(out=cmp_bias[:, :, :], in_=cmp_bias[:, :, :], compare_op=ALU.is_ge, fill=NEG,
                                        base=865, pattern=[[0, NH], [-CMP, 64]], channel_multiplier=1), cut)

            @block.vector
            def _(dve):
                step = InOrder(dve)
                for half, own in ((slice(0, 64), 14), (slice(64, 128), 15)):
                    step(dve.memset(keep[half, 0:own - 1], 1.0), forced)
                    step(dve.memset(keep[half, own - 1:32], 0.0), forced)
                    step(dve.memset(force[half, 0:own - 1], 0.0), forced)
                    step(dve.memset(force[half, own - 1:own + 1], FORCE), forced)
                    step(dve.memset(force[half, own + 1:32], NEG), forced)
                dve.wait_ge(loaded, 48)
                dve.tensor_scalar(gq[:, :], gq[:, :], HD ** -0.5, None, ALU.mult).then_inc(scaled, 1)
        clear_signals(nc, setup)

        names = signals(nc, c, "z_loaded normed kn_ready mean_made rms_made v_copied gates_made qk_transposed q_copied "
                               "keys_copied c_summed c_shifted c_exp c_ready c_transposed c_copied c_pv c_out chain "
                               "stored o_T")
        (z_loaded, normed, kn_ready, mean_made, rms_made, v_copied, gates_made, qk_transposed, q_copied, keys_copied,
         c_summed, c_shifted, c_exp, c_ready, c_transposed, c_copied, c_pv, c_out, chain, stored,
         o_T) = names

        def load_rows(sp, t):
            sp.dma_start(zt[:, :], z[bass.ds(t * P + LEAD, P), ZQ:P_ODD]).then_inc(z_loaded, 16)

        with nc.Block() as block:

            @block.sync
            def _(sp):
                load_rows(sp, 0)
                sp.wait_ge(z_loaded, 16)
        clear_signals(nc, [z_loaded])

        def one_tile(t, width):
            skip = max(0, WINDOW // P - (width // P - 1))
            units = []
            for h in range(NH):
                cols = slice((h // GQA) * HD, (h // GQA + 1) * HD)
                units.append((qTz[:, h, :], key_chunks(KsT, width),
                              smask[h // GQA][:, P:P + width] if h % GQA == 0 else None,
                              smask[h // GQA][:, bass.ds(t * P, 2 * P)], t * P, h, [Vs[:, j, cols] for j in range(width // P)], NH + h))
                first, seen = skip * P, WW - skip * P
                keys = [(KwT[:, bass.ds(t * P + first + a, min(512, seen - a))], min(512, seen - a))
                        for a in range(0, seen, 512)]
                units.append((qTz[:, h, :], keys, wmask[:, first:WW] if h == 0 else None,
                              wmask[:, WINDOW - P:WINDOW + P], WINDOW - first, h,
                              [Vw[:, t + skip + j, cols] for j in range(seen // P)], 2 * NH + h))
            rows = bass.ds(t * P, P)
            with nc.Block() as block:

                @block.sync
                def _(sp):
                    sp.dma_start(cmp_out[rows, :], zt[:, O_KVC - ZQ:O_KVS - ZQ]).then_inc(stored, 16)
                    sp.dma_start(slc_out[rows, KVW:A_KV], zt[:, O_KVS - ZQ + KVW:O_KVW - ZQ]).then_inc(stored, 16)
                    sp.dma_start(G["win_rows"][rows, KVW:A_KV], zt[:, O_KVW - ZQ + KVW:O_G - ZQ]).then_inc(stored, 16)
                    sp.wait_ge(kn_ready, 1)
                    sp.dma_start(slc_out[rows, 0:KVW], qn[:, 4, :, :].rearrange("p a d -> p (a d)")).then_inc(stored, 16)
                    sp.dma_start(G["win_rows"][rows, 0:KVW], qn[:, 5, :, :].rearrange("p a d -> p (a d)"))\
                      .then_inc(stored, 16)
                    sp.wait_ge(stored, 80)
                    sp.wait_ge(gates_made, 1)
                    sp.wait_ge(v_copied, 2)
                    load_rows(sp, (t + 1) % TILES)
                    sp.wait_ge(z_loaded, 16)

                @block.gpsimd
                def _(pool):
                    att.gpsimd(pool, units, near, 3)

                @block.scalar
                def _(act):
                    act.activation(gates[:, :], zt[:, O_G - ZQ:P_ODD - ZQ], ACT.Sigmoid).then_inc(gates_made, 1)
                    act.copy(Vs[:, t, :], zt[:, O_KVS - ZQ + KVW:O_KVW - ZQ]).then_inc(v_copied, 1)
                    act.copy(Vw[:, t + WINDOW // P, :], zt[:, O_KVW - ZQ + KVW:O_G - ZQ]).then_inc(v_copied, 1)
                    act.wait_ge(mean_made, 1)
                    act.activation(rms[:, 1, :], rms[:, 0, :], ACT.Sqrt).then_inc(rms_made, 1)
                    act.wait_ge(qk_transposed, 1)
                    act.copy(KsT[:, rows], t_ps[:, 4, :]).then_inc(keys_copied, 1)
                    act.copy(KwT[:, bass.ds(t * P + WINDOW, P)], t_ps[:, 5, :]).then_inc(keys_copied, 1)
                    act.wait_ge(c_shifted, 1)
                    act.activation(pc[:, :, :], pc[:, :, :], ACT.Exp).then_inc(c_exp, 1)
                    act.wait_ge(c_transposed, 1)
                    act.copy(pcT[:, :, :], t_ps[:, 6:8, :]).then_inc(c_copied, 1)
                    att.scalar(act, units)

                @block.tensor
                def _(pe):
                    pe.wait_ge(kn_ready, 1)
                    for g in range(6):
                        last = pe.transpose(t_ps[:, g, :], qn[:, g, :, :].rearrange("p a d -> p (a d)"), ident[:, :])
                    last.then_inc(qk_transposed, 1)
                    pe.wait_ge(q_copied, 2)
                    for h in range(NH):
                        last = pe.matmul(lg_ps[0][:, h * NCMP:(h + 1) * NCMP], qTz[:, h, :], C.KT[:, 0, :],
                                         start=True, stop=True)
                    last.then_inc(c_summed, 1)
                    pe.wait_ge(c_ready, 1)
                    pe.wait_ge(keys_copied, 2)
                    for a in range(2):
                        last = pe.transpose(t_ps[:, 6 + a, :],
                                            pc[:, 4 * a:4 * a + 4, :].rearrange("p h n -> p (h n)"), ident[:, :])
                    last.then_inc(c_transposed, 1)
                    pe.wait_ge(c_copied, 1)
                    for i in range(4):
                        part = slice(i * NCMP, (i + 1) * NCMP)
                        for a in range(2):
                            at = (i % 2) * 512 + a * HD
                            last = pe.matmul(lg_ps[i // 2][:, at:at + HD], pcT[part, a, :],
                                             C.V4[part, a * HD:(a + 1) * HD], start=True, stop=True)
                    last.then_inc(c_pv, 1)
                    pe.wait_ge(c_out, NH)
                    pe.wait_ge(v_copied, 2)
                    att.tensor(pe, units, ident)
                    pe.wait_ge(att.o_scaled, 2 * NH)
                    for k in range(4):
                        last = pe.transpose(t_ps[:, k, :], o[:, 2 * k:2 * k + 2, :].rearrange("p h d -> p (h d)"),
                                            ident[:, :])
                    last.then_inc(o_T, 1)

                @block.vector
                def _(dve):
                    step = InOrder(dve)
                    q3 = zt[:, 0:A_Q].rearrange("p (h d) -> p h d", d=HD)
                    ks3 = zt[:, O_KVS - ZQ:O_KVS - ZQ + KVW].rearrange("p (h d) -> p h d", d=HD)
                    kw3 = zt[:, O_KVW - ZQ:O_KVW - ZQ + KVW].rearrange("p (h d) -> p h d", d=HD)
                    step(dve.tensor_tensor(sq[:, 0:NH, :], q3, q3, ALU.mult), normed)
                    step(dve.tensor_tensor(sq[:, NH:NH + 2, :], ks3, ks3, ALU.mult), normed)
                    step(dve.tensor_tensor(sq[:, NH + 2:NH + 4, :], kw3, kw3, ALU.mult), normed)
                    step(dve.tensor_reduce(rms[:, 0, :], sq[:, :, :], AX.X, ALU.add), normed)
                    step(dve.tensor_scalar(rms[:, 0, :], rms[:, 0, :], 1.0 / HD, RMS_EPS, ALU.mult, ALU.add),
                         mean_made)
                    dve.wait_ge(rms_made, 1)
                    step(dve.reciprocal(rms[:, 2, :], rms[:, 1, :]), normed)
                    for kv in range(NKV):
                        cols = slice(kv * GQA * HD, (kv + 1) * GQA * HD)
                        r = rms[:, 2, kv * GQA:(kv + 1) * GQA].unsqueeze(2).broadcast_to([P, GQA, HD])
                        step(dve.tensor_tensor(qn[:, 0:GQA, kv, :], zt[:, cols].rearrange("p (g d) -> p g d", d=HD),
                                               r, ALU.mult), normed)
                        step(dve.tensor_tensor(qn[:, 0:GQA, kv, :], qn[:, 0:GQA, kv, :],
                                               gq[:, :].unsqueeze(1).broadcast_to([P, GQA, HD]), ALU.mult), normed)
                    for i, k3 in enumerate((ks3, kw3)):
                        r = rms[:, 2, NH + 2 * i:NH + 2 * i + 2].unsqueeze(2).broadcast_to([P, NKV, HD])
                        step(dve.tensor_tensor(qn[:, GQA + i, :, :], k3, r, ALU.mult), normed)
                        step(dve.tensor_tensor(qn[:, GQA + i, :, :], qn[:, GQA + i, :, :],
                                               gk[:, i, :].unsqueeze(1).broadcast_to([P, NKV, HD]), ALU.mult),
                             normed if i == 0 else kn_ready)
                    dve.wait_ge(qk_transposed, 1)
                    for kv in range(NKV):
                        half = slice(kv * HD, (kv + 1) * HD)
                        step(dve.tensor_copy(qTz[half, kv * GQA:(kv + 1) * GQA, :], t_ps[half, 0:GQA, :]), q_copied)
                    full = [P, NH, NCMP]
                    dve.wait_ge(c_summed, 1)
                    step(dve.tensor_tensor(pc[:, :, :], lg_ps[0][:, 0:NH * NCMP].rearrange("p (h n) -> p h n", h=NH),
                                           cmp_bias[:, :, bass.ds(28 - 4 * t, NCMP)], ALU.add), chain)
                    step(dve.tensor_reduce(cst[:, 0, :], pc[:, :, :], AX.X, ALU.max), chain)
                    step(dve.tensor_tensor(pc[:, :, :], pc[:, :, :], cst[:, 0, :].unsqueeze(2).broadcast_to(full),
                                           ALU.subtract), c_shifted)
                    dve.wait_ge(c_exp, 1)
                    step(dve.tensor_reduce(cst[:, 1, :], pc[:, :, :], AX.X, ALU.add), chain)
                    step(dve.reciprocal(cst[:, 2, :], cst[:, 1, :]), chain)
                    step(dve.tensor_tensor(pc[:, :, :], pc[:, :, :], cst[:, 2, :].unsqueeze(2).broadcast_to(full),
                                           ALU.mult), chain)
                    step(dve.tensor_tensor(pc[:, :, :], pc[:, :, :],
                                           vis[:, bass.ds(28 - 4 * t, NCMP)].unsqueeze(1).broadcast_to(full), ALU.mult),
                         c_ready)
                    p4 = pc[:, :, :].rearrange("p (k g) n -> p k g n", g=GQA)
                    step(dve.tensor_tensor(ps[:, :, :], p4[:, :, 0, :], p4[:, :, 1, :], ALU.add), chain)
                    for g in range(2, GQA):
                        step(dve.tensor_tensor(ps[:, :, :], ps[:, :, :], p4[:, :, g, :], ALU.add), chain)
                    pair = ps[:, :, :].rearrange("p k (n two) -> p k n two", two=2)
                    step(dve.tensor_tensor(score[:, :, :], pair[:, :, :, 0], pair[:, :, :, 1], ALU.add), chain)
                    sl = bass.ds(14 - 2 * t, NSEL)
                    wide = [P, NKV, NSEL]
                    step(dve.tensor_tensor(score[:, :, :], score[:, :, :], keep[:, sl].unsqueeze(1).broadcast_to(wide),
                                           ALU.mult), chain)
                    step(dve.tensor_tensor(score[:, :, :], score[:, :, :], force[:, sl].unsqueeze(1).broadcast_to(wide),
                                           ALU.add), chain)
                    step(dve.memset(score[:, :, 0:1], FORCE), chain)
                    for kv in range(NKV):
                        step(dve.max(top8[:, :], score[:, kv, :]), chain)
                        step(dve.match_replace(score[:, kv, :], top8[:, :], score[:, kv, :], TAKEN), chain)
                    step(dve.tensor_scalar(score[:, :, :], score[:, :, :], TAKEN / 2, NEG, ALU.is_gt, ALU.mult), chain)
                    causal = far_mask[:, bass.ds(896 - t * P, width)].rearrange("p (n s) -> p n s", s=SEL)
                    seen = width // SEL
                    for kv in range(NKV):
                        step(dve.tensor_tensor(smask[kv][:, P:P + width].rearrange("p (n s) -> p n s", s=SEL), causal,
                                               score[:, kv, 0:seen].unsqueeze(2).broadcast_to([P, seen, SEL]), ALU.add),
                             att.masks_made)
                    step(dve.tensor_tensor(wmask[:, :], win_bank[:, :], pad_bank[:, bass.ds(t * P, WW)], ALU.add),
                         att.masks_made)
                    dve.wait_ge(c_pv, 1)
                    dve.wait_ge(gates_made, 1)
                    for h in range(NH):
                        a, i = h // 4, h % 4
                        at = (i % 2) * 512 + a * HD
                        step(dve.tensor_scalar(o[:, h, :], lg_ps[i // 2][:, at:at + HD], gates[:, h:h + 1], None,
                                               ALU.mult), c_out)
                    att.vector(dve, step, units, o, gates)
                    dve.wait_ge(o_T, 1)
                    dve.tensor_copy(featT[:, 4:8, rows], t_ps[:, 0:4, :])
            clear_signals(nc, names + att.sems)

        by_width(nc, one_tile)
        (copied,) = tail = signals(nc, c, "win_copied")
        with nc.Block() as block:

            @block.sync
            def _(sp):
                sp.dma_start(win_out, G["win_rows"][SEQ - WINDOW:SEQ, :]).then_inc(copied, 16)
                sp.wait_ge(copied, 16)
        clear_signals(nc, tail)


def stage_nsa_sample(nc, G, C):
    ident, z, row_bias = G["ident"], G["z_odd"], G["row_bias"]
    cmp_out = G["d_cmp_s"][0].rearrange("b one two kv d -> b (one two kv d)")
    slc_out = G["d_slc_s"][0].rearrange("b one two kv d -> b (one two kv d)")
    win_out = G["d_win_s"][0].rearrange("b s two kv d -> b s (two kv d)")
    win_in = G["cache_d_win"][0].rearrange("b s two kv d -> b s (two kv d)")
    slc_cache = G["cache_d_slc"][0].rearrange("n s two kv d -> n s (two kv d)")
    R = NB * NH
    G2 = NB * NKV
    NS = NSEL + 1
    with ExitStack() as c:
        st = SampleState(nc, c)
        QzAll = st.Qz

        with ExitStack() as c2:
            zs = tile_of(nc, c2, "s_z", [NB, P_ODD - ZQ])
            gq = tile_of(nc, c2, "s_gq", [NB, HD])
            gk = tile_of(nc, c2, "s_gk", [NB, 2, HD])
            qn = tile_of(nc, c2, "s_qn", [NB, 6, NKV, HD])
            sq = tile_of(nc, c2, "s_sq", [NB, 12, HD])
            rms = tile_of(nc, c2, "s_rms", [NB, 3, 12])
            expand = tile_of(nc, c2, "s_expand16", [G2, R])
            cbias_rows = tile_of(nc, c2, "s_cbias_rows", [R, NCMP])
            cbias = tile_of(nc, c2, "s_cbias", [G2, GQA, NCMP])
            lc8 = tile_of(nc, c2, "s_lc8", [NH, NB, NCMP])
            lc = tile_of(nc, c2, "s_lc", [G2, GQA, NCMP])
            lcT = tile_of(nc, c2, "s_lcT", [NCMP, NB, NKV, GQA])
            cs = tile_of(nc, c2, "s_cs", [G2, 3, GQA])
            cgate = tile_of(nc, c2, "s_cgate", [G2, GQA])
            ps = tile_of(nc, c2, "s_ps", [G2, NCMP])
            score = tile_of(nc, c2, "s_sscore", [G2, NS])
            top8 = tile_of(nc, c2, "s_stop8", [G2, 8])
            m17 = tile_of(nc, c2, "s_m17", [R, NS])
            t_ps = bank_of(nc, c2, "n_prep_ps", [P, 6, NB])
            c_ps = bank_of(nc, c2, "n_c_ps", [NH, NB * NCMP])
            pT_ps = bank_of(nc, c2, "n_pT_ps", [NCMP, GQA, G2])
            o_ps = bank_of(nc, c2, "n_o_ps", [P, R])
            m_ps = bank_of(nc, c2, "n_m_ps", [R, NS])
            names = signals(nc, c2, "z_loaded w_loaded cleared cut1 expand_made normed mean_made rms_made kn_ready "
                                    "transposed q_ready c_summed c_copied bias_copied bounced c_loaded c_shifted c_exp "
                                    "c_ready c_T c_Tcopied c_pv m_made m_spread chain stored gates_loaded gates_made")
            (z_loaded, w_loaded, cleared, cut1, expand_made, normed, mean_made, rms_made, kn_ready, transposed, q_ready,
             c_summed, c_copied, bias_copied, bounced, c_loaded, c_shifted, c_exp, c_ready, c_T, c_Tcopied, c_pv,
             m_made, m_spread, chain, stored, gates_loaded, gates_made) = names
            with nc.Block() as block:

                @block.sync
                def _(sp):
                    sp.dma_start(zs[:, :], z[Z_S:Z_S + NB, ZQ:P_ODD]).then_inc(z_loaded, 16)
                    for i, col in enumerate((O_KVS + KVW, O_KVW + KVW)):
                        sp.dma_start(st.Vn[0:1, i, :, :], z[Z_S:Z_S + NB, col:col + KVW].unsqueeze(0))\
                          .then_inc(z_loaded, 16)
                    sp.dma_start(gq[:, :], G["d_q_norm"][0].partition_broadcast(NB)).then_inc(w_loaded, 16)
                    for i in range(2):
                        sp.dma_start(gk[:, i, :], G["d_k_norm"][0, 1 + i].partition_broadcast(NB)).then_inc(w_loaded, 16)
                    for b in range(NB):
                        g = z[Z_S + b, O_G:P_ODD].rearrange("(r h) -> h r", h=NH)
                        sp.dma_start(st.scale[b * NH:(b + 1) * NH, :], g, allow_slow_non_contiguous=True)\
                          .then_inc(gates_loaded, 16)
                        sp.dma_start(cgate[b * NKV:(b + 1) * NKV, :], z[Z_S + b, O_G:O_G + NH]
                                     .rearrange("(k g) -> k g", g=GQA)).then_inc(gates_loaded, 16)
                    sp.dma_start(win_out[:, 0:WINDOW - 1, :], win_in[:, 1:WINDOW, :]).then_inc(stored, 16)
                    sp.wait_ge(z_loaded, 48)
                    sp.dma_start(cmp_out, zs[:, O_KVC - ZQ:O_KVS - ZQ]).then_inc(stored, 16)
                    sp.dma_start(slc_out[:, KVW:A_KV], zs[:, O_KVS - ZQ + KVW:O_KVW - ZQ]).then_inc(stored, 16)
                    sp.dma_start(win_out[:, WINDOW - 1, KVW:A_KV], zs[:, O_KVW - ZQ + KVW:O_G - ZQ]).then_inc(stored, 16)
                    sp.wait_ge(kn_ready, 1)
                    sp.dma_start(slc_out[:, 0:KVW], qn[:, 4, :, :].rearrange("p a d -> p (a d)")).then_inc(stored, 16)
                    sp.dma_start(win_out[:, WINDOW - 1, 0:KVW], qn[:, 5, :, :].rearrange("p a d -> p (a d)"))\
                      .then_inc(stored, 16)
                    sp.wait_ge(bias_copied, 1)
                    sp.dma_start(G["s_cbias_d"], cbias_rows[:, :]).then_inc(bounced, 16)
                    sp.wait_ge(c_copied, 1)
                    sp.dma_start(G["s_lc_d"].rearrange("b h n -> h b n"), lc8[:, :, :]).then_inc(bounced, 16)
                    sp.wait_ge(bounced, 32)
                    sp.dma_start(cbias[:, :, :], G["s_cbias_d"].rearrange("(r g) n -> r g n", g=GQA)).then_inc(c_loaded, 16)
                    sp.dma_start(lc[:, :, :], G["s_lc_d"].rearrange("b (k g) n -> (b k) g n", g=GQA)).then_inc(c_loaded, 16)
                    sp.wait_ge(stored, 96)

                @block.gpsimd
                def _(pool):
                    step = InOrder(pool)
                    pool.memset(st.mask[:, :], 0.0).then_inc(cleared, 1)
                    pool.memset(st.Qz[:, :, :], 0.0).then_inc(cleared, 1)
                    pool.memset(expand[:, :], 1.0).then_inc(cleared, 1)
                    pool.wait_ge(cleared, 3)
                    step(pool.affine_select(out=expand[:, :], in_=expand[:, :], compare_op=ALU.is_ge, fill=0.0,
                                            base=0, pattern=[[1, R]], channel_multiplier=-GQA), cut1)
                    step(pool.affine_select(out=expand[:, :], in_=expand[:, :], compare_op=ALU.is_ge, fill=0.0,
                                            base=GQA - 1, pattern=[[-1, R]], channel_multiplier=GQA), expand_made)

                @block.scalar
                def _(act):
                    act.copy(cbias_rows[:, :], row_bias[:, CMP - 1:PAST:CMP]).then_inc(bias_copied, 1)
                    act.wait_ge(gates_loaded, 16 * 2 * NB)
                    act.activation(st.scale[:, :], st.scale[:, :], ACT.Sigmoid).then_inc(gates_made, 1)
                    act.activation(cgate[:, :], cgate[:, :], ACT.Sigmoid).then_inc(gates_made, 1)
                    act.wait_ge(mean_made, 1)
                    act.activation(rms[:, 1, :], rms[:, 0, :], ACT.Sqrt).then_inc(rms_made, 1)
                    act.wait_ge(c_shifted, 1)
                    act.activation(lc[:, :, :], lc[:, :, :], ACT.Exp).then_inc(c_exp, 1)

                @block.tensor
                def _(pe):
                    pe.wait_ge(kn_ready, 1)
                    for g in range(6):
                        last = pe.transpose(t_ps[:, g, :], qn[:, g, :, :].rearrange("p a d -> p (a d)"), ident[0:NB, 0:NB])
                    last.then_inc(transposed, 1)
                    pe.wait_ge(q_ready, 4)
                    for b in range(NB):
                        last = pe.matmul(c_ps[:, b * NCMP:(b + 1) * NCMP], QzAll[:, b, :], C.KT[:, 1 + b, :],
                                         start=True, stop=True)
                    last.then_inc(c_summed, 1)
                    pe.wait_ge(c_ready, 1)
                    for g in range(GQA):
                        last = pe.transpose(pT_ps[:, g, :], lc[:, g, :], ident[0:G2, 0:G2])
                    last.then_inc(c_T, 1)
                    pe.wait_ge(c_Tcopied, 1)
                    for b in range(NB):
                        last = pe.matmul(o_ps[:, b * NH:(b + 1) * NH], C.V[:, 1 + b, :],
                                         lcT[:, b, :, :].rearrange("n k g -> n (k g)"), start=True, stop=True)
                    last.then_inc(c_pv, 1)
                    pe.wait_ge(m_made, 1)
                    pe.wait_ge(expand_made, 1)
                    pe.matmul(m_ps[:, :], expand[:, :], score[:, :], start=True, stop=True).then_inc(m_spread, 1)

                @block.vector
                def _(dve):
                    step = InOrder(dve)
                    dve.wait_ge(z_loaded, 48)
                    dve.wait_ge(w_loaded, 48)
                    step(dve.tensor_scalar(gq[:, :], gq[:, :], HD ** -0.5, None, ALU.mult), normed)
                    q3 = zs[:, 0:A_Q].rearrange("p (h d) -> p h d", d=HD)
                    ks3 = zs[:, O_KVS - ZQ:O_KVS - ZQ + KVW].rearrange("p (h d) -> p h d", d=HD)
                    kw3 = zs[:, O_KVW - ZQ:O_KVW - ZQ + KVW].rearrange("p (h d) -> p h d", d=HD)
                    step(dve.tensor_tensor(sq[:, 0:NH, :], q3, q3, ALU.mult), normed)
                    step(dve.tensor_tensor(sq[:, NH:NH + 2, :], ks3, ks3, ALU.mult), normed)
                    step(dve.tensor_tensor(sq[:, NH + 2:NH + 4, :], kw3, kw3, ALU.mult), normed)
                    step(dve.tensor_reduce(rms[:, 0, :], sq[:, :, :], AX.X, ALU.add), normed)
                    step(dve.tensor_scalar(rms[:, 0, :], rms[:, 0, :], 1.0 / HD, RMS_EPS, ALU.mult, ALU.add),
                         mean_made)
                    dve.wait_ge(rms_made, 1)
                    step(dve.reciprocal(rms[:, 2, :], rms[:, 1, :]), normed)
                    for kv in range(NKV):
                        cols = slice(kv * GQA * HD, (kv + 1) * GQA * HD)
                        r = rms[:, 2, kv * GQA:(kv + 1) * GQA].unsqueeze(2).broadcast_to([NB, GQA, HD])
                        step(dve.tensor_tensor(qn[:, 0:GQA, kv, :], zs[:, cols].rearrange("p (g d) -> p g d", d=HD),
                                               r, ALU.mult), normed)
                        step(dve.tensor_tensor(qn[:, 0:GQA, kv, :], qn[:, 0:GQA, kv, :],
                                               gq[:, :].unsqueeze(1).broadcast_to([NB, GQA, HD]), ALU.mult), normed)
                    for i, k3 in enumerate((ks3, kw3)):
                        r = rms[:, 2, NH + 2 * i:NH + 2 * i + 2].unsqueeze(2).broadcast_to([NB, NKV, HD])
                        step(dve.tensor_tensor(qn[:, GQA + i, :, :], k3, r, ALU.mult), normed)
                        step(dve.tensor_tensor(qn[:, GQA + i, :, :], qn[:, GQA + i, :, :],
                                               gk[:, i, :].unsqueeze(1).broadcast_to([NB, NKV, HD]), ALU.mult),
                             normed if i == 0 else kn_ready)
                    dve.wait_ge(transposed, 1)
                    dve.wait_ge(cleared, 3)
                    for kv in range(NKV):
                        half = slice(kv * HD, (kv + 1) * HD)
                        step(dve.tensor_copy(st.Qz[half, :, kv * GQA:(kv + 1) * GQA],
                                             t_ps[half, 0:GQA, :].rearrange("p g b -> p b g")), q_ready)
                    for i in range(2):
                        step(dve.tensor_copy(st.KnT[:, i, :], t_ps[:, 4 + i, :]), q_ready)
                    dve.wait_ge(c_summed, 1)
                    step(dve.tensor_copy(lc8[:, :, :].rearrange("h b n -> h (b n)"), c_ps[:, :]), c_copied)
                    full = [G2, GQA, NCMP]
                    dve.wait_ge(c_loaded, 32)
                    step(dve.tensor_tensor(lc[:, :, :], lc[:, :, :], cbias[:, :, :], ALU.add), chain)
                    step(dve.tensor_reduce(cs[:, 0, :], lc[:, :, :], AX.X, ALU.max), chain)
                    step(dve.tensor_tensor(lc[:, :, :], lc[:, :, :], cs[:, 0, :].unsqueeze(2).broadcast_to(full),
                                           ALU.subtract), c_shifted)
                    dve.wait_ge(c_exp, 1)
                    step(dve.tensor_reduce(cs[:, 1, :], lc[:, :, :], AX.X, ALU.add), chain)
                    step(dve.reciprocal(cs[:, 2, :], cs[:, 1, :]), chain)
                    step(dve.tensor_tensor(lc[:, :, :], lc[:, :, :], cs[:, 2, :].unsqueeze(2).broadcast_to(full),
                                           ALU.mult), chain)
                    step(dve.tensor_tensor(ps[:, :], lc[:, 0, :], lc[:, 1, :], ALU.add), chain)
                    for g in range(2, GQA):
                        step(dve.tensor_tensor(ps[:, :], ps[:, :], lc[:, g, :], ALU.add), chain)
                    dve.wait_ge(gates_made, 2)
                    step(dve.tensor_tensor(lc[:, :, :], lc[:, :, :], cgate[:, :].unsqueeze(2).broadcast_to(full),
                                           ALU.mult), c_ready)
                    pair = ps[:, :].rearrange("p (n two) -> p n two", two=2)
                    step(dve.tensor_tensor(score[:, 0:NSEL], pair[:, :, 0], pair[:, :, 1], ALU.add), chain)
                    step(dve.memset(score[:, 0:1], FORCE), chain)
                    step(dve.memset(score[:, NSEL - 1:NS], FORCE), chain)
                    step(dve.max(top8[:, :], score[:, :]), chain)
                    step(dve.match_replace(score[:, :], top8[:, :], score[:, :], TAKEN), chain)
                    step(dve.tensor_scalar(score[:, :], score[:, :], TAKEN / 2, NEG, ALU.is_gt, ALU.mult), m_made)
                    dve.wait_ge(c_T, 1)
                    for g in range(GQA):
                        step(dve.tensor_copy(lcT[:, :, :, g], pT_ps[:, g, :].rearrange("n (b k) -> n b k", k=NKV)),
                             chain if g < GQA - 1 else c_Tcopied)
                    dve.wait_ge(c_pv, 1)
                    step(dve.tensor_copy(st.oT[:, :], o_ps[:, :]), chain)
                    dve.wait_ge(m_spread, 1)
                    step(dve.tensor_copy(m17[:, :], m_ps[:, :]), chain)
                    step(dve.tensor_tensor(st.mask[:, 0:PAST].rearrange("p (n s) -> p n s", s=SEL),
                                           st.mask[:, 0:PAST].rearrange("p (n s) -> p n s", s=SEL),
                                           m17[:, 0:NSEL].unsqueeze(2).broadcast_to([R, NSEL, SEL]), ALU.add), chain)
                    step(dve.tensor_copy(st.mask[:, PAST:PAST + 1], m17[:, NSEL:NS]), chain)
            clear_signals(nc, names)

        V = tile_of(nc, c, "s_V", [P, NB * PAGES, P])

        def load_selected(sp, b, K, V, Ki, keys_loaded, kidx_loaded):
            page_loads(sp, G, b, slc_cache, [
                (lambda j: K[:, j, :], lambda page: slc_cache[page, :, 0:KVW], keys_loaded),
                (lambda j: V[:, bass.ds(b * PAGES + j, 1), :],
                 lambda page: slc_cache[page, :, KVW:A_KV].unsqueeze(1), keys_loaded),
            ])

        sample_logits(nc, G, st, "slc", load_selected, PAGES, 0, V)
        sample_attend(nc, G, st, PAGES, 0, V, 0, 1, True)

        NW = WINDOW // P
        (cleared,) = sems = signals(nc, c, "mask_cleared")
        with nc.Block() as block:

            @block.vector
            def _(dve):
                step = InOrder(dve)
                step(dve.memset(st.mask[:, PAST - WINDOW:PAST + 1], 0.0), cleared)
                step(dve.memset(st.mask[:, PAST - WINDOW:PAST - WINDOW + 1], NEG), cleared)
        clear_signals(nc, sems)

        def load_window(sp, b, K, V, Ki, keys_loaded, kidx_loaded):
            for j in range(NW):
                rows = slice(j * P, (j + 1) * P)
                sp.dma_start(K[:, j:j + 1, :], win_in[bass.ds(b, 1), rows, 0:KVW].rearrange("one s n -> s one n"))\
                  .then_inc(keys_loaded, 16)
                sp.dma_start(V[:, bass.ds(b * NW + j, 1), :],
                             win_in[bass.ds(b, 1), rows, KVW:A_KV].rearrange("one s n -> s one n"))\
                  .then_inc(keys_loaded, 16)

        sample_logits(nc, G, st, "win", load_window, NW, 1, V)
        sample_attend(nc, G, st, NW, 1, V, PAST - WINDOW, 2, True)

        sample_concat(nc, G, st, "odd")


def stage_outputs(nc, G):
    with ExitStack() as c:
        (stored,) = signals(nc, c, "y_stored")
        with nc.Block() as block:

            @block.sync
            def _(sp):
                sp.dma_start(G["y_prompt"][0].rearrange("(t p) d -> p t d", p=P), G["x"][:, 0:TILES, :])\
                  .then_inc(stored, 16)
                sp.dma_start(G["y_sample"][:, 0, :], G["x"][0:NB, TILES, :]).then_inc(stored, 16)
                sp.wait_ge(stored, 32)


def build_program(nc, dram):
    G = dict(dram)

    def scratch(name, shape, dt=F32):
        G[name] = nc.dram_tensor(name, shape, dt).ap()

    scratch("mod", [1 + NB, DEPTH, 6 * D])
    scratch("z_even", [LEAD + TOK, P_EVEN])
    scratch("z_odd", [LEAD + TOK, P_ODD])
    scratch("s_logits", [NB * NH, PAST + 1])
    scratch("s_rel", [NB, IDXH, PAST + 1])
    scratch("s_rows", [NB * NH, P])
    scratch("s_rq", [NB, 7, RW])
    scratch("s_rows_c", [NB * NH, HD])
    scratch("s_cbias_d", [NB * NH, NCMP])
    scratch("s_lc_d", [NB, NH, NCMP])
    scratch("win_rows", [SEQ, A_KV])
    scratch("near_d", [P, NH, 2 * P])
    scratch("cmp_bias_d", [P, NH, 64])
    scratch("row_bias_d", [NB * NH, PAST + 1])
    scratch("h_rows", [TOK, D])
    scratch("slot_token", [P * BLOCKS, 1], I32)
    scratch("y_slots", [P * BLOCKS, D])
    with ExitStack() as c:
        G["ident"] = tile_of(nc, c, "ident", [P, P])
        G["ones"] = tile_of(nc, c, "ones", [P, P])
        G["pages"] = tile_of(nc, c, "pages", [1, NB * PAGES], I32)
        G["x"] = tile_of(nc, c, "x", [P, TILES + 1, D])
        with ExitStack() as c2:
            G["featT"] = tile_of(nc, c2, "featT", [P, KC, TOK])
            stage_constants(nc, G)
            stage_ada(nc, G)
            stage_modulate(nc, G, 0, G["g_norm_mix"][0], 0)
            stage_project(nc, G, G["e_w_in"][0], P_EVEN, G["z_even"][LEAD:Z_S], G["z_even"][Z_S:Z_S + NB])
            with ExitStack() as c3:
                alloc_banks(nc, c3, G)
                stage_banks(nc, G)
                stage_even_prompt(nc, G)
                stage_even_sample(nc, G)
            stage_residual_project(nc, G, 0, G["e_w_out"][0], 2)
        moe_sublayer(nc, G, 0)
        with ExitStack() as c2:
            G["featT"] = tile_of(nc, c2, "featT", [P, KC, TOK])
            stage_modulate(nc, G, 1, G["g_norm_mix"][1], 0)
            stage_project(nc, G, G["o_w_in"][0], P_ODD, G["z_odd"][LEAD:Z_S], G["z_odd"][Z_S:Z_S + NB])
            stage_rwkv_prompt(nc, G)
            stage_rwkv_sample(nc, G)
            with ExitStack() as c3:
                alloc_banks(nc, c3, G)
                G["cmp_bias"] = tile_of(nc, c3, "cmp_bias", [P, NH, 64])
                stage_load_banks(nc, G, G["cmp_bias"])
                C = Compressed(nc, c3)
                stage_compress(nc, G, C)
                stage_nsa_prompt(nc, G, C)
                stage_nsa_sample(nc, G, C)
            stage_residual_project(nc, G, 1, G["o_w_out"][0], 2)
        moe_sublayer(nc, G, 1)
        stage_outputs(nc, G)


_OUTS = [
    ("y_prompt", (1, SEQ, D)), ("y_sample", (NB, 1, D)),
    ("a_kv_p", (1, 1, SEQ, 2, NKV, HD)), ("a_kidx_p", (1, 1, SEQ, HD)), ("b_conv_p", (1, 1, 2, CONV)),
    ("c_wkv_p", (1, 1, NH, HD, HD)), ("c_shift_p", (1, 1, P_C)), ("d_cmp_p", (1, 1, SEQ, 2, NKV, HD)),
    ("d_slc_p", (1, 1, SEQ, 2, NKV, HD)), ("d_win_p", (1, 1, WINDOW, 2, NKV, HD)),
    ("a_kv_s", (1, NB, 1, 2, NKV, HD)), ("a_kidx_s", (1, NB, 1, HD)), ("b_conv_s", (1, NB, 2, CONV)),
    ("c_wkv_s", (1, NB, NH, HD, HD)), ("c_shift_s", (1, NB, P_C)), ("d_cmp_s", (1, NB, 1, 2, NKV, HD)),
    ("d_slc_s", (1, NB, 1, 2, NKV, HD)), ("d_win_s", (1, NB, WINDOW, 2, NKV, HD)),
]


def kernel(**inputs):
    import concourse.bacc as bacc
    from concourse.bass_utils import run_bass_kernel_spmd

    nc = bacc.Bacc("TRN2", target_bir_lowering=False, num_devices=1)
    given = dict(inputs)
    given["t5_onehot"] = t5_onehot()
    given["t5_onehot_rev"] = np.ascontiguousarray(given["t5_onehot"][:, OH0:OH0 + PAST + 1][:, ::-1])
    arrays, dram = {}, {}
    for name in given:
        a = np.ascontiguousarray(given[name])
        arrays[f"in_{name}"] = a
        dram[name] = nc.dram_tensor(f"in_{name}", a.shape, mybir.dt.from_np(a.dtype), kind="ExternalInput").ap()
    for name, shape in _OUTS:
        dram[name] = nc.dram_tensor(f"out_{name}", shape, F32, kind="ExternalOutput").ap()
    build_program(nc, dram)
    result = run_bass_kernel_spmd(nc, [arrays], core_ids=[0]).results[0]
    return tuple(result[f"out_{name}"] for name, _ in _OUTS)
```
